# Optimizing a Trainium2 kernel written in Bass

```python
import math
import jax
import jax.numpy as jnp
from jax import lax
import numpy as np

D_MODEL = 1024
BATCH = 1
SEQ = 1024
DEPTH = 1
DEC_BATCH = 8
DEC_SEQ = 1
PAST_LEN = 2048
PAGE_SIZE = 128

ATT_HEADS = 16
ATT_KV_HEADS = 4
ATT_HEAD_DIM = 64
ATT_GROUP = ATT_HEADS // ATT_KV_HEADS
ATT_WIDTH = ATT_HEADS * ATT_HEAD_DIM
KV_WIDTH = ATT_KV_HEADS * ATT_HEAD_DIM
WINDOW = 128
ATT_BLOCK = WINDOW
N_BUCKETS = 32
MAX_DISTANCE = 128

SSD_HEADS = 16
SSD_HEAD_DIM = 64
SSD_WIDTH = SSD_HEADS * SSD_HEAD_DIM
SSD_GROUPS = 2
SSD_HPG = SSD_HEADS // SSD_GROUPS
D_STATE = 128
CONV_WIDTH = 4
CONV_DIM = SSD_WIDTH + 2 * SSD_GROUPS * D_STATE
SSD_CHUNK = 128

MIX_WIDTH = ATT_WIDTH + SSD_WIDTH
IN_SPLITS = (ATT_WIDTH, KV_WIDTH, KV_WIDTH, SSD_WIDTH, CONV_DIM, SSD_HEADS)
IN_COLS = sum(IN_SPLITS)

N_MEM = 256
MEM_HEADS = 4
MEM_HEAD_DIM = D_MODEL // MEM_HEADS

PEER_HEADS = 8
N_KEYS = 128
N_EXPERTS = N_KEYS * N_KEYS
PEER_TOPK = 16
PEER_QDIM = 256
PEER_HALF = PEER_QDIM // 2
PEER_BLOCK = 128

EPS = 1e-6

kernel_name = 'hymba_swa_ssd_peer_memory_step'

def rmsnorm(x, w):
    xf = x.astype(jnp.float32)
    y = xf * lax.rsqrt(jnp.mean(xf * xf, axis=-1, keepdims=True) + EPS)
    return (y * w.astype(jnp.float32)).astype(x.dtype)

def split_in(proj):
    offs = np.cumsum(IN_SPLITS)[:-1].tolist()
    return jnp.split(proj, offs, axis=-1)

def t5_bucket(dist):
    n = jnp.maximum(dist, 0)
    max_exact = N_BUCKETS // 2
    nf = jnp.maximum(n, 1).astype(jnp.float32)
    large = max_exact + (jnp.log(nf / max_exact) / math.log(MAX_DISTANCE / max_exact)
                         * (N_BUCKETS - max_exact)).astype(jnp.int32)
    large = jnp.minimum(large, N_BUCKETS - 1)
    return jnp.where(n < max_exact, n, large)

def rel_bias_logits(dist, table):
    lq, lk = dist.shape
    b = table[t5_bucket(dist)].astype(jnp.float32)
    return jnp.transpose(b, (2, 0, 1)).reshape(ATT_KV_HEADS, ATT_GROUP, lq, lk)

def sink_attention(q, k, v, bias, mask, sinks):
    s = jnp.einsum('...qkgd,...skd->...kgqs', q, k).astype(jnp.float32) * (ATT_HEAD_DIM ** -0.5) + bias
    s = jnp.where(mask, s, -jnp.inf)
    sink = jnp.broadcast_to(sinks.astype(jnp.float32).reshape(ATT_KV_HEADS, ATT_GROUP, 1, 1),
                            s.shape[:-1] + (1,))
    p = jax.nn.softmax(jnp.concatenate([s, sink], axis=-1), axis=-1)[..., :-1]
    return jnp.einsum('...kgqs,...skd->...qkgd', p.astype(v.dtype), v)

def causal_dwconv(xpad, w, b):
    y = lax.conv_general_dilated(xpad, w[:, None, :].astype(xpad.dtype), window_strides=(1,),
                                 padding='VALID', dimension_numbers=('NWC', 'WIO', 'NWC'),
                                 feature_group_count=CONV_DIM)
    return jax.nn.silu(y + b)

def ssd_inputs(xbc, dt_raw, dt_bias):
    b, t, _ = xbc.shape
    xs, bs, cs = jnp.split(xbc, [SSD_WIDTH, SSD_WIDTH + SSD_GROUPS * D_STATE], axis=-1)
    dt = jax.nn.softplus((dt_raw + dt_bias).astype(jnp.float32))
    return (xs.reshape(b, t, SSD_HEADS, SSD_HEAD_DIM), dt,
            bs.reshape(b, t, SSD_GROUPS, D_STATE), cs.reshape(b, t, SSD_GROUPS, D_STATE))

def ssd_chunked(x, dt, A, Bm, Cm):
    b, s, _, _ = x.shape
    c, L = s // SSD_CHUNK, SSD_CHUNK
    xdt = (x.astype(jnp.float32) * dt[..., None]).reshape(b, c, L, SSD_GROUPS, SSD_HPG, SSD_HEAD_DIM)
    a = (dt * A).reshape(b, c, L, SSD_GROUPS, SSD_HPG).transpose(0, 1, 3, 4, 2)
    cs = jnp.cumsum(a, axis=-1)
    Bc = Bm.astype(jnp.float32).reshape(b, c, L, SSD_GROUPS, D_STATE)
    Cc = Cm.astype(jnp.float32).reshape(b, c, L, SSD_GROUPS, D_STATE)
    causal = jnp.tril(jnp.ones((L, L), dtype=bool))
    ldec = jnp.exp(jnp.where(causal, cs[..., :, None] - cs[..., None, :], -jnp.inf))
    cb = jnp.einsum('bclgn,bcsgn->bcgls', Cc, Bc)
    y_diag = jnp.einsum('bcgjls,bcsgjp->bclgjp', cb[:, :, :, None] * ldec, xdt)
    decay_to_end = jnp.exp(cs[..., -1:] - cs)
    chunk_states = jnp.einsum('bclgn,bcgjl,bclgjp->bcgjpn', Bc, decay_to_end, xdt)
    chunk_decay = jnp.exp(cs[..., -1])

    def step(h, inp):
        st, dec = inp
        return dec[..., None, None] * h + st, h

    h0 = jnp.zeros((b, SSD_GROUPS, SSD_HPG, SSD_HEAD_DIM, D_STATE), jnp.float32)
    h_final, prev = lax.scan(step, h0, (jnp.moveaxis(chunk_states, 1, 0), jnp.moveaxis(chunk_decay, 1, 0)))
    prev = jnp.moveaxis(prev, 0, 1)
    y_off = jnp.einsum('bclgn,bcgjpn,bcgjl->bclgjp', Cc, prev, jnp.exp(cs))
    y = (y_diag + y_off).reshape(b, s, SSD_HEADS, SSD_HEAD_DIM)
    return y.astype(x.dtype), h_final.reshape(b, SSD_HEADS, SSD_HEAD_DIM, D_STATE)

def ssd_recurrent(x, dt, A, Bm, Cm, h0):
    b = x.shape[0]
    Ag = A.reshape(SSD_GROUPS, SSD_HPG)

    def step(h, inp):
        xt, dtt, bt, ct = inp
        xt = xt.astype(jnp.float32).reshape(b, SSD_GROUPS, SSD_HPG, SSD_HEAD_DIM)
        dtt = dtt.reshape(b, SSD_GROUPS, SSD_HPG)
        h = jnp.exp(dtt * Ag)[..., None, None] * h + jnp.einsum('bgjp,bgn->bgjpn', xt * dtt[..., None],
                                                                  bt.astype(jnp.float32))
        y = jnp.einsum('bgjpn,bgn->bgjp', h, ct.astype(jnp.float32))
        return h, y.reshape(b, SSD_HEADS, SSD_HEAD_DIM)

    hs = h0.astype(jnp.float32).reshape(b, SSD_GROUPS, SSD_HPG, SSD_HEAD_DIM, D_STATE)
    h_final, ys = lax.scan(step, hs, (jnp.moveaxis(x, 1, 0), jnp.moveaxis(dt, 1, 0),
                                      jnp.moveaxis(Bm, 1, 0), jnp.moveaxis(Cm, 1, 0)))
    return jnp.moveaxis(ys, 0, 1).astype(x.dtype), h_final.reshape(b, SSD_HEADS, SSD_HEAD_DIM, D_STATE)

def merge_groups(o_att, y_ssd, z, lp):
    ya = rmsnorm(o_att, lp['attn_norm_w'])
    ys = rmsnorm(y_ssd * jax.nn.silu(z), lp['ssd_norm_w'])
    return jnp.concatenate([ya, ys], axis=-1) @ lp['w_out']

def memory_kv(mem, lp):
    b, m, _ = mem.shape
    mn = rmsnorm(mem, lp['mem_norm_w'])
    k = (mn @ lp['w_mk']).reshape(b, m, MEM_HEADS, MEM_HEAD_DIM)
    v = (mn @ lp['w_mv']).reshape(b, m, MEM_HEADS, MEM_HEAD_DIM)
    return k, v

def memory_attention(xn, mk, mv, lp):
    b, t, _ = xn.shape
    q = (xn @ lp['w_mq']).reshape(b, t, MEM_HEADS, MEM_HEAD_DIM)
    s = jnp.einsum('bthd,bmhd->bhtm', q, mk).astype(jnp.float32) * (MEM_HEAD_DIM ** -0.5)
    p = jax.nn.softmax(s, axis=-1).astype(mv.dtype)
    o = jnp.einsum('bhtm,bmhd->bthd', p, mv).reshape(b, t, D_MODEL)
    return o @ lp['w_mo']

def peer_ffn(xn, lp):
    b, t, _ = xn.shape
    xf = xn.reshape(b * t, D_MODEL)
    n = b * t
    q = (xf @ lp['peer_wq']).reshape(n, PEER_HEADS, 2, PEER_HALF)
    sub = jnp.einsum('nhpd,hpkd->nhpk', q, lp['peer_keys']).astype(jnp.float32)
    top_s, top_i = lax.top_k(sub, PEER_TOPK)
    cand_s = (top_s[:, :, 0, :, None] + top_s[:, :, 1, None, :]).reshape(n, PEER_HEADS, PEER_TOPK * PEER_TOPK)
    cand_i = (top_i[:, :, 0, :, None] * N_KEYS + top_i[:, :, 1, None, :]).reshape(n, PEER_HEADS, PEER_TOPK * PEER_TOPK)
    best_s, best_pos = lax.top_k(cand_s, PEER_TOPK)
    idx = jnp.take_along_axis(cand_i, best_pos, axis=-1).reshape(n, PEER_HEADS * PEER_TOPK)
    gate = jax.nn.softmax(best_s, axis=-1).reshape(n, PEER_HEADS * PEER_TOPK).astype(xn.dtype)
    n_pad = -(-n // PEER_BLOCK) * PEER_BLOCK
    pad = n_pad - n
    xp = jnp.pad(xf, ((0, pad), (0, 0))).reshape(-1, PEER_BLOCK, D_MODEL)
    ip = jnp.pad(idx, ((0, pad), (0, 0))).reshape(-1, PEER_BLOCK, PEER_HEADS * PEER_TOPK)
    gp = jnp.pad(gate, ((0, pad), (0, 0))).reshape(-1, PEER_BLOCK, PEER_HEADS * PEER_TOPK)

    def block(args):
        xb, ib, gb = args
        act = jax.nn.gelu(jnp.einsum('ted,td->te', lp['peer_u'][ib], xb), approximate=False)
        return jnp.einsum('te,ted->td', gb * act, lp['peer_v'][ib])

    out = lax.map(block, (xp, ip, gp)).reshape(n_pad, D_MODEL)[:n]
    return out.reshape(b, t, D_MODEL)

def layer_tail(x, mk, mv, lp):
    x = x + memory_attention(rmsnorm(x, lp['norm_mem_w']), mk, mv, lp)
    return x + peer_ffn(rmsnorm(x, lp['norm_ffn_w']), lp)

def prompt_layer(x, mem, lp, rel_bias):
    b, s, _ = x.shape
    h = rmsnorm(x, lp['norm_mix_w'])
    q, k, v, z, xbc, dt_raw = split_in(h @ lp['w_in'])
    nb = s // ATT_BLOCK
    qb = q.reshape(b, nb, ATT_BLOCK, ATT_KV_HEADS, ATT_GROUP, ATT_HEAD_DIM)
    kb = k.reshape(b, nb, ATT_BLOCK, ATT_KV_HEADS, ATT_HEAD_DIM)
    vb = v.reshape(b, nb, ATT_BLOCK, ATT_KV_HEADS, ATT_HEAD_DIM)
    kk = jnp.concatenate([jnp.concatenate([jnp.zeros_like(kb[:, :1]), kb[:, :-1]], axis=1), kb], axis=2)
    vv = jnp.concatenate([jnp.concatenate([jnp.zeros_like(vb[:, :1]), vb[:, :-1]], axis=1), vb], axis=2)
    kj = jnp.arange(2 * ATT_BLOCK)[None, :]
    dist = (jnp.arange(ATT_BLOCK)[:, None] + ATT_BLOCK) - kj
    in_window = (dist >= 0) & (dist <= WINDOW)
    key_exists = (jnp.arange(nb)[:, None] > 0) | (kj >= ATT_BLOCK)
    mask = in_window[None, None, None] & key_exists[:, None, None, None, :]
    o_att = sink_attention(qb, kk, vv, rel_bias_logits(dist, rel_bias), mask,
                           lp['attn_sinks']).reshape(b, s, ATT_WIDTH)
    swa_k = k.reshape(b, s, ATT_KV_HEADS, ATT_HEAD_DIM)[:, s - WINDOW:]
    swa_v = v.reshape(b, s, ATT_KV_HEADS, ATT_HEAD_DIM)[:, s - WINDOW:]
    xpad = jnp.concatenate([jnp.zeros((b, CONV_WIDTH - 1, CONV_DIM), xbc.dtype), xbc], axis=1)
    conv_state = xpad[:, -(CONV_WIDTH - 1):]
    xs, dt, bs, cs = ssd_inputs(causal_dwconv(xpad, lp['conv_w'], lp['conv_b']), dt_raw, lp['dt_bias'])
    A = -jnp.exp(lp['a_log'].astype(jnp.float32))
    y, ssm_state = ssd_chunked(xs, dt, A, bs, cs)
    y = (y + lp['d_skip'][:, None] * xs).reshape(b, s, SSD_WIDTH)
    x = x + merge_groups(o_att, y, z, lp)
    mk, mv = memory_kv(mem, lp)
    x = layer_tail(x, mk, mv, lp)
    return x, (swa_k, swa_v, ssm_state.astype(x.dtype), conv_state, mk, mv)

def sample_layer(x, cache_k, cache_v, ssm, conv, mk, mv, lp, rel_bias):
    b, t, _ = x.shape
    h = rmsnorm(x, lp['norm_mix_w'])
    q, k, v, z, xbc, dt_raw = split_in(h @ lp['w_in'])
    wc = cache_k.shape[1]
    qh = q.reshape(b, t, ATT_KV_HEADS, ATT_GROUP, ATT_HEAD_DIM)
    kk = jnp.concatenate([cache_k, k.reshape(b, t, ATT_KV_HEADS, ATT_HEAD_DIM)], axis=1)
    vv = jnp.concatenate([cache_v, v.reshape(b, t, ATT_KV_HEADS, ATT_HEAD_DIM)], axis=1)
    dist = (jnp.arange(t)[:, None] + wc) - jnp.arange(wc + t)[None, :]
    mask = (dist >= 0) & (dist <= WINDOW)
    o_att = sink_attention(qh, kk, vv, rel_bias_logits(dist, rel_bias), mask,
                           lp['attn_sinks']).reshape(b, t, ATT_WIDTH)
    new_k = kk[:, -wc:]
    new_v = vv[:, -wc:]
    xpad = jnp.concatenate([conv, xbc], axis=1)
    new_conv = xpad[:, -(CONV_WIDTH - 1):]
    xs, dt, bs, cs = ssd_inputs(causal_dwconv(xpad, lp['conv_w'], lp['conv_b']), dt_raw, lp['dt_bias'])
    A = -jnp.exp(lp['a_log'].astype(jnp.float32))
    y, new_ssm = ssd_recurrent(xs, dt, A, bs, cs, ssm)
    y = (y + lp['d_skip'][:, None] * xs).reshape(b, t, SSD_WIDTH)
    x = x + merge_groups(o_att, y, z, lp)
    x = layer_tail(x, mk, mv, lp)
    return x, (new_k, new_v, new_ssm.astype(ssm.dtype), new_conv)

def setup_inputs(seed: int = 0) -> dict:
    key = jax.random.key(seed)
    ks = iter(jax.random.split(key, 40))
    f32 = jnp.float32

    def nrm(shape, scale):
        return jax.random.normal(next(ks), shape, f32) * scale

    def gain(shape):
        return 1.0 + 0.02 * jax.random.normal(next(ks), shape, f32)

    win = min(WINDOW, PAST_LEN)
    x_prompt = nrm((BATCH, SEQ, D_MODEL), 1.0)
    x_sample = nrm((DEC_BATCH, DEC_SEQ, D_MODEL), 1.0)
    mem_prompt = nrm((BATCH, N_MEM, D_MODEL), 1.0)
    cache_swa_k = nrm((DEPTH, DEC_BATCH, win, ATT_KV_HEADS, ATT_HEAD_DIM), 1.0)
    cache_swa_v = nrm((DEPTH, DEC_BATCH, win, ATT_KV_HEADS, ATT_HEAD_DIM), 1.0)
    state_ssm = nrm((DEPTH, DEC_BATCH, SSD_HEADS, SSD_HEAD_DIM, D_STATE), 0.5)
    state_conv = nrm((DEPTH, DEC_BATCH, CONV_WIDTH - 1, CONV_DIM), 1.0)
    cache_mem_k = nrm((DEPTH, DEC_BATCH, N_MEM, MEM_HEADS, MEM_HEAD_DIM), 1.0)
    cache_mem_v = nrm((DEPTH, DEC_BATCH, N_MEM, MEM_HEADS, MEM_HEAD_DIM), 1.0)
    norm_mix_w = gain((DEPTH, D_MODEL))
    w_in = nrm((DEPTH, D_MODEL, IN_COLS), D_MODEL ** -0.5)
    attn_sinks = nrm((DEPTH, ATT_HEADS), 1.0)
    rel_bias = nrm((N_BUCKETS, ATT_HEADS), 0.5)
    attn_norm_w = gain((DEPTH, ATT_WIDTH))
    conv_w = nrm((DEPTH, CONV_WIDTH, CONV_DIM), CONV_WIDTH ** -0.5)
    conv_b = nrm((DEPTH, CONV_DIM), 0.02)
    dt0 = jnp.exp(jax.random.uniform(next(ks), (DEPTH, SSD_HEADS), f32, math.log(1e-3), math.log(1e-1)))
    dt_bias = dt0 + jnp.log(-jnp.expm1(-dt0))
    a_log = jnp.log(jax.random.uniform(next(ks), (DEPTH, SSD_HEADS), f32, 1.0, 16.0))
    d_skip = 1.0 + nrm((DEPTH, SSD_HEADS), 0.1)
    ssd_norm_w = gain((DEPTH, SSD_WIDTH))
    w_out = nrm((DEPTH, MIX_WIDTH, D_MODEL), MIX_WIDTH ** -0.5)
    norm_mem_w = gain((DEPTH, D_MODEL))
    mem_norm_w = gain((DEPTH, D_MODEL))
    w_mq = nrm((DEPTH, D_MODEL, D_MODEL), D_MODEL ** -0.5)
    w_mk = nrm((DEPTH, D_MODEL, D_MODEL), D_MODEL ** -0.5)
    w_mv = nrm((DEPTH, D_MODEL, D_MODEL), D_MODEL ** -0.5)
    w_mo = nrm((DEPTH, D_MODEL, D_MODEL), D_MODEL ** -0.5)
    norm_ffn_w = gain((DEPTH, D_MODEL))
    peer_wq = nrm((DEPTH, D_MODEL, PEER_HEADS * PEER_QDIM), D_MODEL ** -0.5)
    peer_keys = nrm((DEPTH, PEER_HEADS, 2, N_KEYS, PEER_HALF), PEER_HALF ** -0.5)
    peer_u = nrm((DEPTH, N_EXPERTS, D_MODEL), D_MODEL ** -0.5)
    peer_v = nrm((DEPTH, N_EXPERTS, D_MODEL), PEER_HEADS ** -0.5)
    final_norm_w = gain((D_MODEL,))
    return {'x_prompt': x_prompt, 'x_sample': x_sample, 'mem_prompt': mem_prompt,
            'cache_swa_k': cache_swa_k, 'cache_swa_v': cache_swa_v, 'state_ssm': state_ssm,
            'state_conv': state_conv, 'cache_mem_k': cache_mem_k, 'cache_mem_v': cache_mem_v,
            'norm_mix_w': norm_mix_w, 'w_in': w_in, 'attn_sinks': attn_sinks, 'rel_bias': rel_bias,
            'attn_norm_w': attn_norm_w, 'conv_w': conv_w, 'conv_b': conv_b, 'dt_bias': dt_bias,
            'a_log': a_log, 'd_skip': d_skip, 'ssd_norm_w': ssd_norm_w, 'w_out': w_out,
            'norm_mem_w': norm_mem_w, 'mem_norm_w': mem_norm_w, 'w_mq': w_mq, 'w_mk': w_mk,
            'w_mv': w_mv, 'w_mo': w_mo, 'norm_ffn_w': norm_ffn_w, 'peer_wq': peer_wq,
            'peer_keys': peer_keys, 'peer_u': peer_u, 'peer_v': peer_v, 'final_norm_w': final_norm_w}

def reference(x_prompt, x_sample, mem_prompt, cache_swa_k, cache_swa_v, state_ssm, state_conv,
              cache_mem_k, cache_mem_v, norm_mix_w, w_in, attn_sinks, rel_bias, attn_norm_w, conv_w,
              conv_b, dt_bias, a_log, d_skip, ssd_norm_w, w_out, norm_mem_w, mem_norm_w, w_mq, w_mk,
              w_mv, w_mo, norm_ffn_w, peer_wq, peer_keys, peer_u, peer_v, final_norm_w):
    yp, ys = x_prompt, x_sample
    p_states, s_states = [], []
    for l in range(DEPTH):
        lp = dict(norm_mix_w=norm_mix_w[l], w_in=w_in[l], attn_sinks=attn_sinks[l],
                  attn_norm_w=attn_norm_w[l], conv_w=conv_w[l], conv_b=conv_b[l], dt_bias=dt_bias[l],
                  a_log=a_log[l], d_skip=d_skip[l], ssd_norm_w=ssd_norm_w[l], w_out=w_out[l],
                  norm_mem_w=norm_mem_w[l], mem_norm_w=mem_norm_w[l], w_mq=w_mq[l], w_mk=w_mk[l],
                  w_mv=w_mv[l], w_mo=w_mo[l], norm_ffn_w=norm_ffn_w[l], peer_wq=peer_wq[l],
                  peer_keys=peer_keys[l], peer_u=peer_u[l], peer_v=peer_v[l])
        yp, ps = prompt_layer(yp, mem_prompt, lp, rel_bias)
        ys, ss = sample_layer(ys, cache_swa_k[l], cache_swa_v[l], state_ssm[l], state_conv[l],
                              cache_mem_k[l], cache_mem_v[l], lp, rel_bias)
        p_states.append(ps)
        s_states.append(ss)
    y_prompt = rmsnorm(yp, final_norm_w)
    y_sample = rmsnorm(ys, final_norm_w)

    def stack(states, i):
        return jnp.stack([st[i] for st in states])

    p_swa_k = stack(p_states, 0)
    p_swa_v = stack(p_states, 1)
    p_ssm = stack(p_states, 2)
    p_conv = stack(p_states, 3)
    p_mem_k = stack(p_states, 4)
    p_mem_v = stack(p_states, 5)
    s_swa_k = stack(s_states, 0)
    s_swa_v = stack(s_states, 1)
    s_ssm = stack(s_states, 2)
    s_conv = stack(s_states, 3)
    return (y_prompt, y_sample, p_swa_k, p_swa_v, p_ssm, p_conv, p_mem_k, p_mem_v, s_swa_k, s_swa_v, s_ssm, s_conv)


_drawn_inputs = setup_inputs


def setup_inputs(seed=0):
    import zlib

    import numpy as np

    out = dict(_drawn_inputs(seed))
    spreads = {}
    factors = {'attn_sinks': 3.402,
     'attn_norm_w': 3.327,
     'ssd_norm_w': 3.043,
     'norm_mem_w': 8.0,
     'mem_norm_w': 2.829,
     'norm_ffn_w': 11.296,
     'final_norm_w': 7.509}
    for name, (base, spread) in spreads.items():
        noise = np.random.default_rng([zlib.crc32(name.encode()), seed]).standard_normal(out[name].shape)
        drawn = base * np.exp(spread * noise) if base else spread * noise
        out[name] = jnp.asarray(drawn.astype(out[name].dtype))
    for name, factor in factors.items():
        out[name] = (out[name] * factor).astype(out[name].dtype)
    return out
```

```python
from contextlib import ExitStack

import numpy as np

import concourse.bass as bass
from concourse import mybir

F32 = mybir.dt.float32
U32 = mybir.dt.uint32
ALU = mybir.AluOpType
ACT = mybir.ActivationFunctionType
AX = mybir.AxisListType

P = 128
D = 1024
DB = D // P
SEQ = 1024
TILES = SEQ // P
DEC = 8
TOKENS = SEQ + DEC
HEADS, KV, HD = 16, 4, 64
GROUP = HEADS // KV
WINDOW = 128
BUCKETS = 32
SSD_HEADS, SSD_G, STATE = 16, 2, 128
SSD_HPG = SSD_HEADS // SSD_G
CONV = 4
CONV_DIM = 1536
CB = CONV_DIM // P
XBC0 = 2560
DT0 = XBC0 + CONV_DIM
IN_COLS = DT0 + SSD_HEADS
N_MEM = 256
MEM_HEADS, MEM_HD = 4, 256
PEER_HEADS, N_KEYS, TOPK = 8, 128, 16
SLOTS = PEER_HEADS * TOPK
EPS = 1e-6
FAR = -1e30
BANK = 512


class Event:

    def __init__(self, sem, per=1, unit=1):
        self.sem, self.per, self.unit = sem, per, unit

    def last(self, turn):
        return (turn * self.per + 1) * self.unit

    def this(self, turn, k=1):
        return (turn * self.per + 1 + k) * self.unit


class Fills:

    def __init__(self, sem, stage, order):
        self.place, count = {}, {}
        for name, b in order:
            count[b] = count.get(b, 0) + 1
            self.place[name] = (b, count[b])
        self.count = count
        self.full = {b: sem(f"{stage}_bank{b}_full") for b in count}
        self.free = {b: sem(f"{stage}_bank{b}_free") for b in count}

    def bank(self, name):
        return self.place[name][0]

    def at(self, name, turn):
        b, k = self.place[name]
        return turn * self.count[b] + k

    def prime(self, pe):
        for b in self.count:
            pe.sem_inc(self.free[b], 1)


class Stage:

    def __init__(self, nc):
        self.nc, self.scope, self.semaphores = nc, ExitStack(), []

    def __enter__(self):
        return self

    def buffer(self, name, shape, dt=F32):
        return self.scope.enter_context(self.nc.sbuf_tensor(name, shape, dt))

    def semaphore(self, name):
        self.semaphores.append(self.nc.alloc_semaphore(name))
        return self.semaphores[-1]

    def event(self, name, per=1, unit=1):
        return Event(self.semaphore(name), per, unit)

    def block(self):
        return self.scope.enter_context(self.nc.Block())

    def __exit__(self, kind, *rest):
        if kind is None:
            self.scope.close()
            self.nc.clear_and_free_semaphores(self.semaphores)
            self.nc.all_engine_barrier()


def flipped(ap):
    a = [list(x) for x in ap.ap]
    step, n = a[-1]
    return bass.AP(ap.tensor, ap.offset + (n - 1) * step, a[:-1] + [[-step, n]])


def attention_prompt(nc, io, psum, shared, w_qkv):
    ident, bias, sinks, gain = shared["ident"], shared["bias"], shared["sinks"], shared["gain_mix"]
    with Stage(nc) as stage:
        sb, sem, event = stage.buffer, stage.semaphore, stage.event

        x = sb("att_x", [P, D])
        junk = sb("att_junk", [P, D])
        ms = sb("att_ms", [P, 1])
        rstd = sb("att_rstd", [P, 1])
        half = sb("att_half", [P, 1])
        part = sb("att_part", [P, 1])
        hT = sb("att_hT", [P, DB, P])
        q = sb("att_q", [P, D])
        kv = sb("att_kv", [P, 512])
        v_old = sb("att_v_old", [P, 256])
        qT = sb("att_qT", [P, DB, P])
        kT = sb("att_kT", [P, 2, 2 * P])
        logits = sb("att_logits", [P, 2, GROUP, 2 * P])
        pT = sb("att_pT", [P, 2, GROUP, 2, P])
        top = sb("att_top", [P, HEADS])
        ntop = sb("att_ntop", [P, HEADS])
        total = sb("att_total", [P, HEADS])
        esink = sb("att_esink", [P, HEADS])
        rtotal = sb("att_rtotal", [P, HEADS])
        o = sb("att_o", [P, D])
        oms = sb("att_oms", [P, 1])
        orstd = sb("att_orstd", [P, 1])

        order = [("xT0", 0), ("xT1", 1), ("p0", 2), ("p1", 3), ("p2", 2),
                 ("qT0", 0), ("qT1", 1), ("kT", 0)]
        for g in range(KV):
            order += [(f"s{g}0", 4), (f"s{g}1", 5)]
        for g in range(KV):
            order += [(f"t{g}0", 1), (f"t{g}1", 0), (f"o{g}", 6 + g % 2)]
        fills = Fills(sem, "att", order)

        w_in = event("att_w", 1, 16)
        x_in = event("att_x_in", 1, 16)
        x_seen = event("att_x_seen", 2)
        ms_ready = event("att_ms_ready")
        rstd_ready = event("att_rstd_ready")
        hT_ready = event("att_hT_ready", 2)
        projected = event("att_projected")
        q_ready = event("att_q_ready")
        kv_ready = event("att_kv_ready")
        qT_ready = event("att_qT_ready")
        kT_ready = event("att_kT_ready")
        scored = event("att_scored")
        ntop_ready = event("att_ntop_ready", KV)
        p_ready = event("att_p_ready", KV)
        p_turned = event("att_p_turned", KV)
        pT_ready = event("att_pT_ready", KV)
        mixed = event("att_mixed", KV)
        o_ready = event("att_o_ready")
        oms_ready = event("att_oms_ready")
        orstd_ready = event("att_orstd_ready")
        out_ready = event("att_out_ready")
        stored = event("att_stored", 1, 16)
        tail_out = sem("att_tail_out")

        block = stage.block()

        @block.sync
        def _(sp):
            def turn(t):
                sp.wait_ge(x_seen.sem, x_seen.last(t))
                sp.dma_start(x[:], io["x_prompt"][bass.ds(t * P, P), :]).then_inc(x_in.sem, 16)
                sp.wait_ge(out_ready.sem, out_ready.this(t))
                sp.dma_start(io["mixed"][bass.ds(t * P, P), 0:D], o[:]).then_inc(stored.sem, 16)

            sp.sem_inc(x_in.sem, 16)
            sp.sem_inc(stored.sem, 16)
            sp.sem_inc(w_in.sem, 16)
            sp.dma_start(w_qkv[:], io["w_in"].rearrange("(b p) n -> p b n", p=P)[:, :, 0:1536]).then_inc(w_in.sem, 16)
            turn(0)
            with sp.Fori(1, TILES) as t:
                turn(t)
            sp.wait_ge(kv_ready.sem, kv_ready.this(TILES - 1))
            sp.dma_start(io["p_swa_k"], kv[:, 0:256]).then_inc(tail_out, 16)
            sp.dma_start(io["p_swa_v"], kv[:, 256:512]).then_inc(tail_out, 16)
            sp.wait_ge(tail_out, 32)
            sp.wait_ge(stored.sem, stored.this(TILES - 1))

        @block.tensor
        def _(pe):
            def turn(t, first):
                pe.wait_ge(x_in.sem, x_in.this(t))
                for h in range(2):
                    f = f"xT{h}"
                    pe.wait_ge(fills.free[fills.bank(f)], fills.at(f, t))
                    for j in range(4):
                        ins = nc.tensor.transpose(psum[fills.bank(f)][:, j * P:(j + 1) * P],
                                                  x[:, (4 * h + j) * P:(4 * h + j + 1) * P], ident[:])
                    ins.then_inc(fills.full[fills.bank(f)], 1)
                pe.drain()
                pe.sem_inc(x_seen.sem, 1)
                pe.wait_ge(hT_ready.sem, hT_ready.this(t, 2))
                for c in range(3):
                    f = f"p{c}"
                    pe.wait_ge(fills.free[fills.bank(f)], fills.at(f, t))
                    for b in range(DB):
                        ins = nc.tensor.matmul(psum[fills.bank(f)][:], hT[:, b, :],
                                               w_qkv[:, b, c * BANK:(c + 1) * BANK],
                                               start=(b == 0), stop=(b == DB - 1))
                    ins.then_inc(fills.full[fills.bank(f)], 1)
                pe.drain()
                pe.sem_inc(projected.sem, 1)
                pe.wait_ge(q_ready.sem, q_ready.this(t))
                for h in range(2):
                    f = f"qT{h}"
                    pe.wait_ge(fills.free[fills.bank(f)], fills.at(f, t))
                    for j in range(4):
                        ins = nc.tensor.transpose(psum[fills.bank(f)][:, j * P:(j + 1) * P],
                                                  q[:, (4 * h + j) * P:(4 * h + j + 1) * P], ident[:])
                    ins.then_inc(fills.full[fills.bank(f)], 1)
                pe.wait_ge(kv_ready.sem, kv_ready.this(t))
                pe.wait_ge(fills.free[fills.bank("kT")], fills.at("kT", t))
                for j in range(2):
                    ins = nc.tensor.transpose(psum[fills.bank("kT")][:, j * P:(j + 1) * P],
                                              kv[:, j * P:(j + 1) * P], ident[:])
                ins.then_inc(fills.full[fills.bank("kT")], 1)
                pe.wait_ge(qT_ready.sem, qT_ready.this(t))
                pe.wait_ge(kT_ready.sem, kT_ready.this(t))

                def scores(g):
                    lo, hi = (g % 2) * HD, (g % 2 + 1) * HD
                    for h in range(2):
                        f = f"s{g}{h}"
                        pe.wait_ge(fills.free[fills.bank(f)], fills.at(f, t))
                        for r in (2 * h, 2 * h + 1):
                            at = (r % 2) * 2 * P
                            off = P if first else 0
                            ins = nc.tensor.matmul(psum[fills.bank(f)][:, at + off:at + 2 * P],
                                                   qT[lo:hi, 4 * (g // 2) + r, :], kT[lo:hi, g // 2, off:2 * P],
                                                   start=True, stop=True)
                        ins.then_inc(fills.full[fills.bank(f)], 1)

                def values(g):
                    pe.wait_ge(p_ready.sem, p_ready.this(t, g + 1))
                    parts = (1,) if first else (0, 1)
                    for h in range(2):
                        f = f"t{g}{h}"
                        pe.wait_ge(fills.free[fills.bank(f)], fills.at(f, t))
                        for r in (2 * h, 2 * h + 1):
                            for part in parts:
                                at = ((r % 2) * 2 + part) * P
                                ins = nc.tensor.transpose(psum[fills.bank(f)][:, at:at + P],
                                                          logits[:, g % 2, r, part * P:(part + 1) * P], ident[:])
                        ins.then_inc(fills.full[fills.bank(f)], 1)
                    pe.drain()
                    pe.sem_inc(p_turned.sem, 1)
                    pe.wait_ge(pT_ready.sem, pT_ready.this(t, g + 1))
                    f = f"o{g}"
                    pe.wait_ge(fills.free[fills.bank(f)], fills.at(f, t))
                    for r in range(GROUP):
                        for part in parts:
                            v = kv[:, 256 + g * HD:256 + (g + 1) * HD] if part else v_old[:, g * HD:(g + 1) * HD]
                            ins = nc.tensor.matmul(psum[fills.bank(f)][:, r * HD:(r + 1) * HD],
                                                   pT[:, g % 2, r, part, :], v,
                                                   start=(part == parts[0]), stop=(part == 1))
                    ins.then_inc(fills.full[fills.bank(f)], 1)
                    pe.drain()
                    pe.sem_inc(mixed.sem, 1)

                scores(0)
                for g in range(KV):
                    if g + 1 < KV:
                        scores(g + 1)
                    else:
                        pe.drain()
                        pe.sem_inc(scored.sem, 1)
                    values(g)

            fills.prime(pe)
            pe.sem_inc(x_seen.sem, 1)
            for e in (projected, p_turned, mixed, scored):
                pe.sem_inc(e.sem, 1)
            pe.wait_ge(w_in.sem, w_in.this(0))
            turn(0, True)
            with pe.Fori(1, TILES) as t:
                turn(t, False)

        @block.scalar
        def _(act):
            def turn(t, first):
                act.wait_ge(x_in.sem, x_in.this(t))
                nc.scalar.activation(junk[:], x[:], ACT.Square, accum_out=ms[:])
                act.drain()
                act.sem_inc(ms_ready.sem, 1)
                act.sem_inc(x_seen.sem, 1)
                act.wait_ge(rstd_ready.sem, rstd_ready.this(t))
                for c in range(2):
                    f = f"p{c}"
                    act.wait_ge(fills.full[fills.bank(f)], fills.at(f, t))
                    out = q[:, c * BANK:(c + 1) * BANK].rearrange("p (r g d) -> p g r d", r=GROUP, g=2)
                    src = psum[fills.bank(f)][:].rearrange("p (g r d) -> p g r d", r=GROUP, g=2)
                    for gg in range(2):
                        nc.scalar.activation(out[:, gg], src[:, gg], ACT.Copy, scale=rstd[:])
                    act.drain()
                    act.sem_inc(fills.free[fills.bank(f)], 1)
                act.sem_inc(q_ready.sem, 1)
                act.wait_ge(scored.sem, scored.last(t))
                for h in range(2):
                    f = f"qT{h}"
                    act.wait_ge(fills.full[fills.bank(f)], fills.at(f, t))
                    nc.scalar.activation(qT[:, 4 * h:4 * h + 4, :], psum[fills.bank(f)][:].rearrange("p (b t) -> p b t", b=4),
                                         ACT.Copy, scale=HD ** -0.5).then_inc(fills.free[fills.bank(f)], 1)
                act.drain()
                act.sem_inc(qT_ready.sem, 1)
                off = P if first else 0
                for g in range(KV):
                    act.wait_ge(ntop_ready.sem, ntop_ready.this(t, g + 1))
                    for r in range(GROUP):
                        h = g * GROUP + r
                        nc.scalar.activation(logits[:, g % 2, r, off:2 * P], logits[:, g % 2, r, off:2 * P], ACT.Exp,
                                             bias=ntop[:, h:h + 1], accum_out=total[:, h:h + 1])
                    hs = slice(g * GROUP, (g + 1) * GROUP)
                    nc.scalar.activation(esink[:, hs], esink[:, hs], ACT.Exp)
                    act.drain()
                    act.sem_inc(p_ready.sem, 1)
                    for h in range(2):
                        f = f"t{g}{h}"
                        act.wait_ge(fills.full[fills.bank(f)], fills.at(f, t))
                        if h == 0:
                            act.wait_ge(mixed.sem, mixed.this(t, g - 1) if g >= 2 else mixed.last(t))
                        keys = slice(1, 2) if first else slice(0, 2)
                        nc.scalar.copy(pT[:, g % 2, 2 * h:2 * h + 2, keys, :],
                                       psum[fills.bank(f)][:].rearrange("p (r k t) -> p r k t", r=2, k=2)[:, :, keys, :]
                                       ).then_inc(fills.free[fills.bank(f)], 1)
                    act.drain()
                    act.sem_inc(pT_ready.sem, 1)
                act.wait_ge(o_ready.sem, o_ready.this(t))
                nc.scalar.activation(junk[:], o[:], ACT.Square, accum_out=oms[:])
                act.drain()
                act.sem_inc(oms_ready.sem, 1)

            for e in (ms_ready, q_ready, qT_ready, p_ready, pT_ready, oms_ready):
                act.sem_inc(e.sem, 1)
            turn(0, True)
            with act.Fori(1, TILES) as t:
                turn(t, False)

        @block.gpsimd
        def _(pool):
            def turn(t):
                for src, dst, ready, done in ((ms, rstd, ms_ready, rstd_ready), (oms, orstd, oms_ready, orstd_ready)):
                    pool.wait_ge(ready.sem, ready.this(t))
                    nc.gpsimd.tensor_tensor(src[:], src[:], part[:], ALU.mult)
                    pool.drain()
                    nc.gpsimd.tensor_scalar(src[:], src[:], EPS, None, ALU.add)
                    pool.drain()
                    nc.gpsimd.tensor_tensor(dst[:], src[:], half[:], ALU.pow)
                    pool.drain()
                    pool.sem_inc(done.sem, 1)

            nc.gpsimd.memset(half[:], -0.5)
            nc.gpsimd.memset(part[:], 1.0 / D)
            pool.drain()
            pool.sem_inc(rstd_ready.sem, 1)
            pool.sem_inc(orstd_ready.sem, 1)
            turn(0)
            with pool.Fori(1, TILES) as t:
                turn(t)

        @block.vector
        def _(dve):
            def turn(t, first):
                dve.wait_ge(projected.sem, projected.last(t))
                for h in range(2):
                    f = f"xT{h}"
                    dve.wait_ge(fills.full[fills.bank(f)], fills.at(f, t))
                    nc.vector.tensor_tensor(hT[:, 4 * h:4 * h + 4, :], psum[fills.bank(f)][:].rearrange("p (b t) -> p b t", b=4),
                                            gain[:, 4 * h:4 * h + 4, None].broadcast_to([P, 4, P]), ALU.mult
                                            ).then_inc(fills.free[fills.bank(f)], 1)
                    dve.drain()
                    dve.sem_inc(hT_ready.sem, 1)
                dve.wait_ge(mixed.sem, mixed.last(t))
                if not first:
                    nc.vector.tensor_copy(v_old[:], kv[:, 256:512])
                    nc.vector.tensor_copy(kT[:, :, 0:P], kT[:, :, P:2 * P])
                    dve.drain()
                dve.wait_ge(rstd_ready.sem, rstd_ready.this(t))
                f = "p2"
                dve.wait_ge(fills.full[fills.bank(f)], fills.at(f, t))
                nc.vector.tensor_scalar(kv[:], psum[fills.bank(f)][:], rstd[:], None, ALU.mult
                                        ).then_inc(fills.free[fills.bank(f)], 1)
                dve.drain()
                dve.sem_inc(kv_ready.sem, 1)
                f = "kT"
                dve.wait_ge(fills.full[fills.bank(f)], fills.at(f, t))
                nc.vector.tensor_copy(kT[:, :, P:2 * P], psum[fills.bank(f)][:, 0:256].rearrange("p (b t) -> p b t", b=2)
                                      ).then_inc(fills.free[fills.bank(f)], 1)
                dve.drain()
                dve.sem_inc(kT_ready.sem, 1)
                off = P if first else 0

                def softmax_top(g):
                    if g >= 2:
                        dve.wait_ge(p_turned.sem, p_turned.this(t, g - 1))
                    else:
                        dve.wait_ge(p_turned.sem, p_turned.last(t))
                    for h in range(2):
                        f = f"s{g}{h}"
                        dve.wait_ge(fills.full[fills.bank(f)], fills.at(f, t))
                        nc.vector.tensor_tensor(logits[:, g % 2, 2 * h:2 * h + 2, off:2 * P],
                                                psum[fills.bank(f)][:].rearrange("p (r k) -> p r k", r=2)[:, :, off:2 * P],
                                                bias[:, g * GROUP + 2 * h:g * GROUP + 2 * h + 2, off:2 * P], ALU.add
                                                ).then_inc(fills.free[fills.bank(f)], 1)
                    dve.drain()
                    hs = slice(g * GROUP, (g + 1) * GROUP)
                    nc.vector.tensor_reduce(top[:, hs], logits[:, g % 2, :, off:2 * P], AX.X, ALU.max)
                    dve.drain()
                    nc.vector.tensor_tensor(top[:, hs], top[:, hs], sinks[:, hs], ALU.max)
                    dve.drain()
                    nc.vector.tensor_scalar(ntop[:, hs], top[:, hs], -1.0, None, ALU.mult)
                    nc.vector.tensor_tensor(esink[:, hs], sinks[:, hs], top[:, hs], ALU.subtract)
                    dve.drain()
                    dve.sem_inc(ntop_ready.sem, 1)

                def outputs(g):
                    hs = slice(g * GROUP, (g + 1) * GROUP)
                    dve.wait_ge(p_ready.sem, p_ready.this(t, g + 1))
                    nc.vector.tensor_tensor(total[:, hs], total[:, hs], esink[:, hs], ALU.add)
                    dve.drain()
                    nc.vector.reciprocal(rtotal[:, hs], total[:, hs])
                    dve.drain()
                    f = f"o{g}"
                    dve.wait_ge(fills.full[fills.bank(f)], fills.at(f, t))
                    if g == 0:
                        dve.wait_ge(stored.sem, stored.last(t))
                    nc.vector.tensor_tensor(o[:, g * 256:(g + 1) * 256].rearrange("p (r d) -> p r d", r=GROUP),
                                            psum[fills.bank(f)][:, 0:256].rearrange("p (r d) -> p r d", r=GROUP),
                                            rtotal[:, hs, None].broadcast_to([P, GROUP, HD]), ALU.mult
                                            ).then_inc(fills.free[fills.bank(f)], 1)

                softmax_top(0)
                for g in range(KV):
                    if g + 1 < KV:
                        softmax_top(g + 1)
                    outputs(g)
                dve.drain()
                dve.sem_inc(o_ready.sem, 1)
                dve.wait_ge(orstd_ready.sem, orstd_ready.this(t))
                nc.vector.tensor_scalar(o[:], o[:], orstd[:], None, ALU.mult).then_inc(out_ready.sem, 1)

            for e in (hT_ready, kv_ready, kT_ready, ntop_ready, o_ready, out_ready):
                dve.sem_inc(e.sem, 1)
            turn(0, True)
            with dve.Fori(1, TILES) as t:
                turn(t, False)


def setup(nc, io, psum, shared):
    with Stage(nc) as stage:
        sb, sem = stage.buffer, stage.semaphore

        rows = sb("set_rows", [5 * DB, P])
        conv_rows = sb("set_conv_rows", [(CONV + 1) * CB, P])
        table = sb("set_table", [BUCKETS + 1, HEADS])
        onehot = sb("set_onehot", [BUCKETS + 1, 384])
        line = sb("set_line", [HEADS, 384])
        turned = sb("set_turned", [P, HEADS, 2 * P])
        loaded = sem("set_loaded")
        far_row = sem("set_far_row")
        multiplied = sem("set_multiplied")
        line_ready = sem("set_line_ready")
        line_stored = sem("set_line_stored")
        turned_loaded = sem("set_turned_loaded")
        block = stage.block()
        loads = [
            (shared["ident"][:], io["ident"]), (shared["tri"][:], io["tri"]),
            (shared["far"][:], io["far"]),
            (onehot[:], io["onehot"]), (table[0:BUCKETS, :], io["rel_bias"]),
            (shared["sinks"][:], io["attn_sinks"].rearrange("a h -> a h").broadcast_to([P, HEADS])),
            (shared["sink_col"][:], io["attn_sinks"].rearrange("a h -> h a")),
            (shared["head_mask"][:], io["head_mask"]),
        ]
        for i, name in enumerate(("norm_mix_w", "attn_norm_w", "ssd_norm_w", "norm_mem_w", "mem_norm_w")):
            loads.append((rows[i * DB:(i + 1) * DB, :], io[name].rearrange("a (b p) -> (a b) p", p=P)))
        loads.append((conv_rows[0:CONV * CB, :], io["conv_w"].rearrange("k (b p) -> (k b) p", p=P)))
        loads.append((conv_rows[CONV * CB:(CONV + 1) * CB, :], io["conv_b"].rearrange("a (b p) -> (a b) p", p=P)))

        @block.sync
        def _(sp):
            for dst, src in loads:
                sp.dma_start(dst, src).then_inc(loaded, 16)
            sp.wait_ge(line_ready, 1)
            sp.dma_start(io["bias_line"], line[:]).then_inc(line_stored, 16)
            sp.wait_ge(line_stored, 16)
            shifted = bass.AP(io["bias_line"].tensor, io["bias_line"].offset, [[1, P], [384, HEADS], [1, 2 * P]])
            sp.dma_start(turned[:], shifted).then_inc(turned_loaded, 16)

        @block.tensor
        def _(pe):
            pe.wait_ge(loaded, 16 * len(loads))
            pe.wait_ge(far_row, 1)
            nc.tensor.matmul(psum[0][0:HEADS, 0:384], table[:], onehot[:], start=True, stop=True).then_inc(multiplied, 1)
            nc.tensor.transpose(psum[1][:, 0:5 * DB], rows[:], shared["ident"][0:5 * DB, 0:5 * DB])
            n = (CONV + 1) * CB
            nc.tensor.transpose(psum[1][:, P:P + n], conv_rows[:], shared["ident"][0:n, 0:n]).then_inc(multiplied, 1)

        @block.vector
        def _(dve):
            nc.vector.memset(table[BUCKETS:BUCKETS + 1, :], FAR).then_inc(far_row, 1)
            nc.vector.memset(shared["ones"][:], 1.0)
            dve.wait_ge(multiplied, 2)
            nc.vector.tensor_copy(line[:], psum[0][0:HEADS, 0:384]).then_inc(line_ready, 1)
            nc.vector.tensor_copy(shared["gains"][:], psum[1][:, 0:5 * DB].rearrange("p (i b) -> p i b", b=DB))
            nc.vector.tensor_copy(shared["conv"][:], psum[1][:, P:P + (CONV + 1) * CB].rearrange("p (i b) -> p i b", b=CB))
            dve.drain()
            nc.vector.tensor_copy(shared["bias_row"][:], flipped(line[:, 127:256]))
            dve.wait_ge(turned_loaded, 16)
            nc.vector.tensor_copy(shared["bias"][:], flipped(turned[:]))
            dve.drain()


def attention_sample(nc, io, psum, shared, w_qkv):
    ident, sink, gain = shared["ident"], shared["sink_col"], shared["gain_mix"]
    KEYS = WINDOW + 1
    with Stage(nc) as stage:
        sb, sem = stage.buffer, stage.semaphore

        x = sb("sat_x", [DEC, D])
        junk = sb("sat_junk", [DEC, D])
        ms = sb("sat_ms", [DEC, 1])
        rstd = sb("sat_rstd", [DEC, 1])
        half = sb("sat_half", [DEC, 1])
        hT = sb("sat_hT", [P, DB, DEC])
        q = sb("sat_q", [DEC, D])
        kv = sb("sat_kv", [DEC, 512])
        k_cache = sb("sat_k_cache", [P, DEC, 256])
        v_cache = sb("sat_v_cache", [P, DEC, 256])
        q_heads = sb("sat_q_heads", [P, DEC, 2, HEADS])
        k_newT = sb("sat_k_newT", [P, 2, DEC])
        kT = sb("sat_kT", [P, DEC, 2, KEYS])
        p = sb("sat_p", [HEADS, DEC, KEYS])
        top = sb("sat_top", [HEADS, DEC])
        esink = sb("sat_esink", [HEADS, DEC])
        total = sb("sat_total", [HEADS, DEC])
        pT = sb("sat_pT", [P, DEC, HEADS])
        p_new = sb("sat_p_new", [DEC, HEADS])
        p_own = sb("sat_p_own", [DEC, DEC, HEADS])
        wide = sb("sat_wide", [HEADS, DEC, KV, HD])
        o_heads = sb("sat_o_heads", [HEADS, DEC, HD])
        o = sb("sat_o", [DEC, D])

        x_in, cache_in, copied = sem("sat_x_in"), sem("sat_cache_in"), sem("sat_copied")
        x_turned, ms_ready, rstd_ready = sem("sat_x_turned"), sem("sat_ms_ready"), sem("sat_rstd_ready")
        hT_ready, projected, q_ready, kv_ready = sem("sat_hT_ready"), sem("sat_projected"), sem("sat_q_ready"), sem("sat_kv_ready")
        qk_turned, q_heads_ready, k_newT_ready = sem("sat_qk_turned"), sem("sat_q_heads_ready"), sem("sat_k_newT_ready")
        cache_turned, kT_ready, scored = sem("sat_cache_turned"), sem("sat_kT_ready"), sem("sat_scored")
        shifted, esum, p_ready, p_turned = sem("sat_shifted"), sem("sat_esum"), sem("sat_p_ready"), sem("sat_p_turned")
        pT_ready, valued, o_heads_ready, o_in = sem("sat_pT_ready"), sem("sat_valued"), sem("sat_o_heads_ready"), sem("sat_o_in")
        oms_ready, orstd_ready, out_ready = sem("sat_oms_ready"), sem("sat_orstd_ready"), sem("sat_out_ready")
        stored = sem("sat_stored")
        block = stage.block()

        @block.sync
        def _(sp):
            sp.dma_start(x[:], io["x_sample"]).then_inc(x_in, 16)
            sp.dma_start(k_cache[:], io["cache_swa_k"].rearrange("b s n -> s b n")).then_inc(cache_in, 16)
            sp.dma_start(v_cache[:], io["cache_swa_v"].rearrange("b s n -> s b n")).then_inc(cache_in, 16)
            for new, old in (("s_swa_k", "cache_swa_k"), ("s_swa_v", "cache_swa_v")):
                sp.dma_start(io[new][:, 0:WINDOW - 1, :], io[old][:, 1:WINDOW, :]).then_inc(copied, 16)
            sp.wait_ge(kv_ready, 1)
            sp.dma_start(io["s_swa_k"][:, WINDOW - 1, :], kv[:, 0:256]).then_inc(copied, 16)
            sp.dma_start(io["s_swa_v"][:, WINDOW - 1, :], kv[:, 256:512]).then_inc(copied, 16)
            sp.wait_ge(o_heads_ready, 1)
            sp.dma_start(io["rows"].rearrange("b (h d) -> h b d", h=HEADS), o_heads[:]).then_inc(stored, 16)
            sp.wait_ge(stored, 16)
            sp.dma_start(o[:], io["rows"]).then_inc(o_in, 16)
            sp.wait_ge(o_in, 16)
            sp.wait_ge(out_ready, 1)
            sp.dma_start(io["mixed"][SEQ:TOKENS, 0:D], o[:]).then_inc(stored, 16)
            sp.wait_ge(stored, 32)
            sp.wait_ge(copied, 64)

        @block.tensor
        def _(pe):
            pe.wait_ge(x_in, 16)
            for b in range(DB):
                ins = nc.tensor.transpose(psum[0][:, b * DEC:(b + 1) * DEC], x[:, b * P:(b + 1) * P], ident[0:DEC, 0:DEC])
            ins.then_inc(x_turned, 1)
            pe.wait_ge(hT_ready, 1)
            for c in range(3):
                for b in range(DB):
                    ins = nc.tensor.matmul(psum[1 + c][0:DEC, :], hT[:, b, :], w_qkv[:, b, c * BANK:(c + 1) * BANK],
                                           start=(b == 0), stop=(b == DB - 1))
                ins.then_inc(projected, 1)
            pe.wait_ge(cache_in, 32)
            for n in range(4):
                for j in range(4):
                    b, half_k = (4 * n + j) // 2, j % 2
                    ins = nc.tensor.transpose(psum[4 + n][:, j * P:(j + 1) * P],
                                              k_cache[:, b, half_k * P:(half_k + 1) * P], ident[:])
                ins.then_inc(cache_turned, 1)
            pe.wait_ge(q_ready, 1)
            pe.wait_ge(kv_ready, 1)
            for b in range(DB):
                nc.tensor.transpose(psum[0][:, b * DEC:(b + 1) * DEC], q[:, b * P:(b + 1) * P], ident[0:DEC, 0:DEC])
            for b in range(2):
                ins = nc.tensor.transpose(psum[0][:, P + b * DEC:P + (b + 1) * DEC], kv[:, b * P:(b + 1) * P], ident[0:DEC, 0:DEC])
            ins.then_inc(qk_turned, 1)
            pe.wait_ge(q_heads_ready, 1)
            pe.wait_ge(kT_ready, 1)
            for b in range(DEC):
                for j in range(2):
                    ins = nc.tensor.matmul(psum[1 + b // 3][0:HEADS, (b % 3) * KEYS:(b % 3 + 1) * KEYS],
                                           q_heads[:, b, j, :], kT[:, b, j, :], start=(j == 0), stop=(j == 1))
            ins.then_inc(scored, 1)
            pe.wait_ge(p_ready, 1)
            for b in range(DEC):
                nc.tensor.transpose(psum[0][:, b * HEADS:(b + 1) * HEADS], p[:, b, 0:WINDOW], ident[0:HEADS, 0:HEADS])
            nc.tensor.transpose(psum[0][0:DEC, 256:256 + HEADS], p[:, :, WINDOW], ident[0:HEADS, 0:HEADS]).then_inc(p_turned, 1)
            pe.wait_ge(pT_ready, 1)
            for b in range(DEC):
                out = psum[4 + b // 2][0:HEADS, (b % 2) * 256:(b % 2 + 1) * 256]
                nc.tensor.matmul(out, pT[:, b, :], v_cache[:, b, :], start=True, stop=False)
                ins = nc.tensor.matmul(out, p_own[:, b, :], kv[:, 256:512], start=False, stop=True)
            ins.then_inc(valued, 1)

        @block.scalar
        def _(act):
            act.wait_ge(x_in, 16)
            nc.scalar.activation(junk[:], x[:], ACT.Square, accum_out=ms[:]).then_inc(ms_ready, 1)
            act.wait_ge(rstd_ready, 1)
            act.wait_ge(projected, 2)
            for c in range(2):
                out = q[:, c * BANK:(c + 1) * BANK].rearrange("p (r g d) -> p g r d", r=GROUP, g=2)
                src = psum[1 + c][0:DEC, :].rearrange("p (g r d) -> p g r d", r=GROUP, g=2)
                for gg in range(2):
                    nc.scalar.activation(out[:, gg], src[:, gg], ACT.Copy, scale=rstd[:])
            act.drain()
            act.sem_inc(q_ready, 1)
            act.wait_ge(shifted, 1)
            nc.scalar.activation(p[:], p[:], ACT.Exp)
            nc.scalar.activation(esink[:], esink[:], ACT.Exp).then_inc(esum, 1)
            act.wait_ge(o_in, 16)
            nc.scalar.activation(junk[:], o[:], ACT.Square, accum_out=ms[:]).then_inc(oms_ready, 1)

        @block.gpsimd
        def _(pool):
            nc.gpsimd.memset(half[:], -0.5)
            for ready, done in ((ms_ready, rstd_ready), (oms_ready, orstd_ready)):
                pool.wait_ge(ready, 1)
                nc.gpsimd.tensor_scalar(ms[:], ms[:], 1.0 / D, EPS, ALU.mult, ALU.add)
                pool.drain()
                nc.gpsimd.tensor_tensor(rstd[:], ms[:], half[:], ALU.pow).then_inc(done, 1)

        @block.vector
        def _(dve):
            nc.vector.memset(q_heads[:], 0.0)
            dve.wait_ge(x_turned, 1)
            nc.vector.tensor_tensor(hT[:], psum[0][:, 0:DB * DEC].rearrange("p (b t) -> p b t", b=DB),
                                    gain[:, :, None].broadcast_to([P, DB, DEC]), ALU.mult).then_inc(hT_ready, 1)
            dve.wait_ge(rstd_ready, 1)
            dve.wait_ge(projected, 3)
            nc.vector.tensor_scalar(kv[:], psum[3][0:DEC, :], rstd[:], None, ALU.mult).then_inc(kv_ready, 1)
            for n in range(4):
                dve.wait_ge(cache_turned, n + 1)
                nc.vector.tensor_copy(kT[:, 2 * n:2 * n + 2, :, 0:WINDOW],
                                      psum[4 + n][:].rearrange("p (b j k) -> p b j k", b=2, j=2))
            dve.wait_ge(qk_turned, 1)
            nc.vector.tensor_copy(k_newT[:], psum[0][:, P:P + 2 * DEC].rearrange("p (j b) -> p j b", j=2))
            for g in range(KV):
                lo, hi = (g % 2) * HD, (g % 2 + 1) * HD
                src = psum[0][lo:hi, (g // 2) * GROUP * DEC:(g // 2 + 1) * GROUP * DEC].rearrange("p (r b) -> p b r", r=GROUP)
                nc.vector.tensor_scalar(q_heads[lo:hi, :, g // 2, g * GROUP:(g + 1) * GROUP], src, HD ** -0.5, None, ALU.mult)
            dve.drain()
            dve.sem_inc(q_heads_ready, 1)
            for j in range(2):
                ins = nc.vector.tensor_copy(kT[:, :, j, WINDOW], k_newT[:, j, :])
            dve.drain()
            dve.sem_inc(kT_ready, 1)
            dve.wait_ge(scored, 1)
            for n, m in enumerate((3, 3, 2)):
                nc.vector.tensor_tensor(p[:, 3 * n:3 * n + m, :], psum[1 + n][0:HEADS, 0:m * KEYS].rearrange("p (b k) -> p b k", b=m),
                                        shared["bias_row"][:, None, :].broadcast_to([HEADS, m, KEYS]), ALU.add)
            dve.drain()
            nc.vector.tensor_reduce(top[:], p[:], AX.X, ALU.max)
            dve.drain()
            nc.vector.tensor_scalar(top[:], top[:], sink[:], None, ALU.max)
            dve.drain()
            nc.vector.tensor_tensor(p[:], p[:], top[:, :, None].broadcast_to([HEADS, DEC, KEYS]), ALU.subtract)
            nc.vector.tensor_scalar(esink[:], top[:], -1.0, sink[:], ALU.mult, ALU.add)
            dve.drain()
            dve.sem_inc(shifted, 1)
            dve.wait_ge(esum, 1)
            nc.vector.tensor_reduce(total[:], p[:], AX.X, ALU.add)
            dve.drain()
            nc.vector.tensor_tensor(total[:], total[:], esink[:], ALU.add)
            dve.drain()
            nc.vector.reciprocal(total[:], total[:])
            dve.drain()
            nc.vector.tensor_tensor(p[:], p[:], total[:, :, None].broadcast_to([HEADS, DEC, KEYS]), ALU.mult).then_inc(p_ready, 1)
            dve.wait_ge(p_turned, 1)
            nc.vector.tensor_copy(pT[:], psum[0][:, 0:P].rearrange("p (b h) -> p b h", b=DEC))
            nc.vector.tensor_copy(p_new[:], psum[0][0:DEC, 256:256 + HEADS])
            dve.drain()
            nc.vector.tensor_tensor(p_own[:], p_new[:, None, :].broadcast_to([DEC, DEC, HEADS]),
                                    ident[0:DEC, 0:DEC, None].broadcast_to([DEC, DEC, HEADS]), ALU.mult)
            dve.drain()
            dve.sem_inc(pT_ready, 1)
            dve.wait_ge(valued, 1)
            for b in range(DEC):
                nc.vector.tensor_tensor(wide[:, b], psum[4 + b // 2][0:HEADS, (b % 2) * 256:(b % 2 + 1) * 256].rearrange("p (g d) -> p g d", g=KV),
                                        shared["head_mask"][:, :, None].broadcast_to([HEADS, KV, HD]), ALU.mult)
            dve.drain()
            nc.vector.tensor_reduce(o_heads[:], wide[:].rearrange("p b g d -> p b d g"), AX.X, ALU.add).then_inc(o_heads_ready, 1)
            dve.wait_ge(orstd_ready, 1)
            nc.vector.tensor_scalar(o[:], o[:], rstd[:], None, ALU.mult).then_inc(out_ready, 1)




def ssd_prompt(nc, io, psum, shared, w_zx):
    ident, tri, far, ones, gain, conv = (shared[k] for k in ("ident", "tri", "far", "ones", "gain_mix", "conv"))
    NH = SSD_HEADS
    with Stage(nc) as stage:
        sb, sem, event = stage.buffer, stage.semaphore, stage.event

        x = sb("ssd_x", [P, D])
        junk = sb("ssd_junk", [P, D])
        ms, rstd, yms, yrstd = (sb("ssd_" + n, [P, 1]) for n in ("ms", "rstd", "yms", "yrstd"))
        half, part = sb("ssd_half", [P, 1]), sb("ssd_part", [P, 1])
        hT = sb("ssd_hT", [P, DB, P])
        zs = sb("ssd_zs", [P, D])
        xbc = sb("ssd_xbc", [P, CONV_DIM])
        xbcT = sb("ssd_xbcT", [P, CB, CONV - 1 + P])
        cv = sb("ssd_cv", [P, CB, P])
        tap = sb("ssd_tap", [P, CB, P])
        dt_raw, dt_neg, dt_exp, dt_u, dt_err, dt, decay = (sb("ssd_" + n, [P, NH]) for n in
                                                         ("dt_raw", "dt_neg", "dt_exp", "dt_u", "dt_err", "dt", "decay"))
        rate = sb("ssd_rate", [P, NH])
        dt_bias = sb("ssd_dt_bias", [P, NH])
        skip = sb("ssd_skip", [P, NH])
        sums = sb("ssd_sums", [P, 2, NH])
        esums = sb("ssd_esums", [P, 2, NH])
        nsum = sb("ssd_nsum", [P, NH])
        to_end = sb("ssd_to_end", [P, NH])
        xs = sb("ssd_xs", [P, D])
        bm = sb("ssd_bm", [P, SSD_G, STATE])
        xdt = sb("ssd_xdt", [P, D])
        xend = sb("ssd_xend", [P, D])
        cb = sb("ssd_cb", [P, SSD_G, P])
        dec = sb("ssd_dec", [P, 2, 4, P])
        y = sb("ssd_y", [P, D])
        xskip = sb("ssd_xskip", [P, D])
        state = sb("ssd_state", [P, D])

        def by_head(ap):
            return ap.rearrange("p (h d) -> p h d", d=HD)

        def per_head(ap, n=NH):
            return ap[:, :, None].broadcast_to([P, n, HD])

        order = [("xT0", 0), ("xT1", 1), ("z0", 2), ("z1", 3), ("x0", 2), ("x1", 3), ("x2", 2), ("dt", 3),
                 ("cT0", 0), ("cT1", 1), ("cT2", 0), ("sums", 1), ("xs0", 0), ("xs1", 1), ("bm", 0), ("cb", 1),
                 ("yo0", 2), ("yo1", 3), ("G0", 4), ("G1", 5), ("yd0", 6), ("G2", 4), ("G3", 5), ("yd1", 7),
                 ("st0", 2), ("st1", 3)]
        fills = Fills(sem, "ssd", order)
        chunks = {"z0": 0, "z1": 512, "x0": 1024, "x1": 1536, "x2": 2048, "dt": 2560}

        w_in = sem("ssd_w")
        x_in = event("ssd_x_in", 1, 16)
        x_seen = event("ssd_x_seen", 2)
        ms_ready, rstd_ready, yms_ready, yrstd_ready = (event("ssd_" + n) for n in ("ms_ready", "rstd_ready", "yms_ready", "yrstd_ready"))
        hT_ready = event("ssd_hT_ready")
        projected = event("ssd_projected")
        xbc_ready = event("ssd_xbc_ready", 2)
        xbcT_ready = event("ssd_xbcT_ready")
        taps_done = event("ssd_taps_done")
        cv_ready = event("ssd_cv_ready")
        dt_raw_ready, dt_exp_ready, dt_u_ready, dt_log_ready, decay_ready = (
            event("ssd_" + n) for n in ("dt_raw_ready", "dt_exp_ready", "dt_u_ready", "dt_log_ready", "decay_ready"))
        sums_ready, esums_ready = event("ssd_sums_ready"), event("ssd_esums_ready")
        xs_ready, bm_ready, xdt_ready, xend_ready, cb_ready = (
            event("ssd_" + n) for n in ("xs_ready", "bm_ready", "xdt_ready", "xend_ready", "cb_ready"))
        dec_ready, scan_ready, scanned = event("ssd_dec_ready", 4), event("ssd_scan_ready", 4), event("ssd_scanned", 4)
        y_ready, y_gated, out_ready = event("ssd_y_ready"), event("ssd_y_gated"), event("ssd_out_ready")
        state_ready = event("ssd_state_ready")
        pe_over = event("ssd_pe_over")
        stored = event("ssd_stored", 1, 16)
        loaded, rates_ready, consts_ready = sem("ssd_loaded"), sem("ssd_rates_ready"), sem("ssd_consts_ready")
        state_turned, state_copied, tail_out = sem("ssd_state_turned"), sem("ssd_state_copied"), sem("ssd_tail_out")

        block = stage.block()

        @block.sync
        def _(sp):
            def turn(t):
                sp.wait_ge(x_seen.sem, x_seen.last(t))
                sp.dma_start(x[:], io["x_prompt"][bass.ds(t * P, P), :]).then_inc(x_in.sem, 16)
                sp.wait_ge(out_ready.sem, out_ready.this(t))
                sp.dma_start(io["mixed"][bass.ds(t * P, P), D:2 * D], y[:]).then_inc(stored.sem, 16)

            sp.sem_inc(x_in.sem, 16)
            sp.sem_inc(stored.sem, 16)
            sp.dma_start(rate[:], io["a_log"].broadcast_to([P, NH])).then_inc(loaded, 16)
            sp.dma_start(dt_bias[:], io["dt_bias"].broadcast_to([P, NH])).then_inc(loaded, 16)
            sp.dma_start(skip[:], io["d_skip"].broadcast_to([P, NH])).then_inc(loaded, 16)
            sp.dma_start(w_zx[:], io["w_in"].rearrange("(b p) n -> p b n", p=P)[:, :, 1536:IN_COLS]).then_inc(w_in, 16)
            with sp.Fori(0, TILES) as t:
                turn(t)
            sp.dma_start(io["p_conv"], xbc[P - CONV + 1:P, :]).then_inc(tail_out, 16)
            sp.wait_ge(state_copied, 2)
            sp.dma_start(io["p_ssm"].rearrange("(j q) n -> q j n", q=P), y[:].rearrange("p (j n) -> p j n", j=DB)).then_inc(tail_out, 16)
            sp.wait_ge(tail_out, 32)

        @block.tensor
        def _(pe):
            def begin(f, t):
                pe.wait_ge(fills.free[fills.bank(f)], fills.at(f, t))
                return psum[fills.bank(f)]

            def turn(t):
                pe.wait_ge(x_in.sem, x_in.this(t))
                for h in range(2):
                    out = begin(f"xT{h}", t)
                    for j in range(4):
                        ins = nc.tensor.transpose(out[:, j * P:(j + 1) * P], x[:, (4 * h + j) * P:(4 * h + j + 1) * P], ident[:])
                    ins.then_inc(fills.full[h], 1)
                pe.drain()
                pe.sem_inc(x_seen.sem, 1)
                pe.wait_ge(hT_ready.sem, hT_ready.this(t))
                for f, col in chunks.items():
                    out = begin(f, t)
                    n = min(BANK, IN_COLS - 1536 - col)
                    for b in range(DB):
                        ins = nc.tensor.matmul(out[:, 0:n], hT[:, b, :], w_zx[:, b, col:col + n], start=(b == 0), stop=(b == DB - 1))
                    ins.then_inc(fills.full[fills.bank(f)], 1)
                pe.drain()
                pe.sem_inc(projected.sem, 1)
                pe.wait_ge(xbc_ready.sem, xbc_ready.this(t, 2))
                for n in range(3):
                    out = begin(f"cT{n}", t)
                    for j in range(4):
                        ins = nc.tensor.transpose(out[:, j * P:(j + 1) * P], xbc[:, (4 * n + j) * P:(4 * n + j + 1) * P], ident[:])
                    ins.then_inc(fills.full[fills.bank(f"cT{n}")], 1)
                pe.wait_ge(decay_ready.sem, decay_ready.this(t))
                out = begin("sums", t)
                nc.tensor.matmul(out[:, 0:NH], tri[:], decay[:], start=True, stop=True)
                nc.tensor.matmul(out[:, NH:2 * NH], ones[:], decay[:], start=True, stop=True).then_inc(fills.full[fills.bank("sums")], 1)
                pe.wait_ge(cv_ready.sem, cv_ready.this(t))
                for h in range(2):
                    out = begin(f"xs{h}", t)
                    for j in range(4):
                        ins = nc.tensor.transpose(out[:, j * P:(j + 1) * P], cv[:, 4 * h + j, :], ident[:])
                    ins.then_inc(fills.full[fills.bank(f"xs{h}")], 1)
                out = begin("bm", t)
                for g in range(SSD_G):
                    ins = nc.tensor.transpose(out[:, g * P:(g + 1) * P], cv[:, 8 + g, :], ident[:])
                ins.then_inc(fills.full[fills.bank("bm")], 1)
                out = begin("cb", t)
                for g in range(SSD_G):
                    ins = nc.tensor.matmul(out[:, g * P:(g + 1) * P], cv[:, 8 + g, :], cv[:, 10 + g, :], start=True, stop=True)
                ins.then_inc(fills.full[fills.bank("cb")], 1)
                pe.wait_ge(state_ready.sem, state_ready.last(t))
                for g in range(SSD_G):
                    out = begin(f"yo{g}", t)
                    nc.tensor.matmul(out[:], cv[:, 10 + g, :], state[:, g * BANK:(g + 1) * BANK], start=True, stop=True
                                     ).then_inc(fills.full[fills.bank(f"yo{g}")], 1)

                def decays(n):
                    out = begin(f"G{n}", t)
                    nc.tensor.matmul(out[:].rearrange("p (h l) -> p h l", h=4), ident[:],
                                     far[:, None, :].broadcast_to([P, 4, P]), start=True, stop=False)
                    for j in range(4):
                        ins = nc.tensor.matmul(out[:, j * P:(j + 1) * P], decay[:, 4 * n + j:4 * n + j + 1].broadcast_to([P, P]), tri[:],
                                               start=False, stop=(j == 3))
                    ins.then_inc(fills.full[fills.bank(f"G{n}")], 1)

                def scan(n):
                    pe.wait_ge(scan_ready.sem, scan_ready.this(t, n + 1))
                    f = f"yd{n // 2}"
                    if n % 2 == 0:
                        begin(f, t)
                    for j in range(4):
                        h = 4 * n + j
                        ins = nc.tensor.matmul(psum[fills.bank(f)][:, (h % 8) * HD:(h % 8 + 1) * HD], dec[:, n % 2, j, :],
                                               xdt[:, h * HD:(h + 1) * HD], start=True, stop=True)
                    pe.drain()
                    pe.sem_inc(scanned.sem, 1)
                    if n % 2:
                        pe.sem_inc(fills.full[fills.bank(f)], 1)

                decays(0)
                decays(1)
                pe.wait_ge(xdt_ready.sem, xdt_ready.this(t))
                scan(0)
                decays(2)
                scan(1)
                decays(3)
                scan(2)
                scan(3)
                pe.wait_ge(xend_ready.sem, xend_ready.this(t))
                for g in range(SSD_G):
                    out = begin(f"st{g}", t)
                    nc.tensor.matmul(out[:], bm[:, g, :], xend[:, g * BANK:(g + 1) * BANK], start=True, stop=True
                                     ).then_inc(fills.full[fills.bank(f"st{g}")], 1)
                pe.drain()
                pe.sem_inc(pe_over.sem, 1)

            fills.prime(pe)
            for e in (x_seen, projected, scanned, pe_over):
                pe.sem_inc(e.sem, 1)
            pe.wait_ge(w_in, 16)
            pe.wait_ge(consts_ready, 1)
            with pe.Fori(0, TILES) as t:
                turn(t)
            pe.wait_ge(state_ready.sem, state_ready.this(TILES - 1))
            for h in range(2):
                pe.wait_ge(fills.free[4 + h], 2 * TILES + 1)
                for j in range(4):
                    ins = nc.tensor.transpose(psum[4 + h][:, j * P:(j + 1) * P], state[:, (4 * h + j) * P:(4 * h + j + 1) * P], ident[:])
                ins.then_inc(state_turned, 1)

        @block.scalar
        def _(act):
            def full(f, t):
                act.wait_ge(fills.full[fills.bank(f)], fills.at(f, t))
                return psum[fills.bank(f)]

            def turn(t):
                act.wait_ge(x_in.sem, x_in.this(t))
                nc.scalar.activation(junk[:], x[:], ACT.Square, accum_out=ms[:])
                act.drain()
                act.sem_inc(ms_ready.sem, 1)
                act.sem_inc(x_seen.sem, 1)
                act.wait_ge(rstd_ready.sem, rstd_ready.this(t))
                act.wait_ge(y_gated.sem, y_gated.last(t))
                for h in range(2):
                    src = full(f"z{h}", t)
                    nc.scalar.activation(zs[:, h * BANK:(h + 1) * BANK], src[:], ACT.Silu, scale=rstd[:]
                                         ).then_inc(fills.free[fills.bank(f"z{h}")], 1)
                src = full("x1", t)
                nc.scalar.activation(xbc[:, BANK:2 * BANK], src[:], ACT.Copy, scale=rstd[:]).then_inc(fills.free[fills.bank("x1")], 1)
                act.drain()
                act.sem_inc(xbc_ready.sem, 1)
                act.wait_ge(dt_raw_ready.sem, dt_raw_ready.this(t))
                nc.scalar.activation(dt_exp[:], dt_neg[:], ACT.Exp)
                act.drain()
                act.sem_inc(dt_exp_ready.sem, 1)
                act.wait_ge(dt_u_ready.sem, dt_u_ready.this(t))
                nc.scalar.activation(dt_neg[:], dt_u[:], ACT.Ln)
                act.drain()
                act.sem_inc(dt_log_ready.sem, 1)
                act.wait_ge(taps_done.sem, taps_done.last(t))
                for n in range(3):
                    src = full(f"cT{n}", t)
                    nc.scalar.copy(xbcT[:, 4 * n:4 * n + 4, CONV - 1:], src[:].rearrange("p (b t) -> p b t", b=4)
                                   ).then_inc(fills.free[fills.bank(f"cT{n}")], 1)
                act.drain()
                act.sem_inc(xbcT_ready.sem, 1)
                act.wait_ge(sums_ready.sem, sums_ready.this(t))
                nc.scalar.activation(esums[:], sums[:], ACT.Exp)
                nc.scalar.activation(to_end[:], to_end[:], ACT.Exp)
                act.drain()
                act.sem_inc(esums_ready.sem, 1)
                act.wait_ge(taps_done.sem, taps_done.this(t))
                nc.scalar.activation(cv[:], cv[:], ACT.Silu)
                act.drain()
                act.sem_inc(cv_ready.sem, 1)
                for h in range(2):
                    src = full(f"xs{h}", t)
                    nc.scalar.copy(xs[:, h * BANK:(h + 1) * BANK], src[:]).then_inc(fills.free[fills.bank(f"xs{h}")], 1)
                act.drain()
                act.sem_inc(xs_ready.sem, 1)
                for n in range(4):
                    act.wait_ge(scanned.sem, scanned.this(t, n - 1) if n >= 2 else scanned.last(t))
                    src = full(f"G{n}", t)
                    for j in range(4):
                        ins = nc.scalar.activation(dec[:, n % 2, j, :], src[:, j * P:(j + 1) * P], ACT.Exp,
                                                   bias=nsum[:, 4 * n + j:4 * n + j + 1])
                    act.drain()
                    act.sem_inc(dec_ready.sem, 1)
                    act.sem_inc(fills.free[fills.bank(f"G{n}")], 1)
                act.wait_ge(y_gated.sem, y_gated.this(t))
                nc.scalar.activation(junk[:], y[:], ACT.Square, accum_out=yms[:])
                act.drain()
                act.sem_inc(yms_ready.sem, 1)

            for e in (ms_ready, dt_exp_ready, dt_log_ready, xbcT_ready, esums_ready, cv_ready, xs_ready, dec_ready, yms_ready):
                act.sem_inc(e.sem, 1)
            act.wait_ge(loaded, 48)
            nc.scalar.activation(rate[:], rate[:], ACT.Exp).then_inc(rates_ready, 1)
            with act.Fori(0, TILES) as t:
                turn(t)

        @block.gpsimd
        def _(pool):
            def factor(src, dst, ready, done, t):
                pool.wait_ge(ready.sem, ready.this(t))
                nc.gpsimd.tensor_tensor(src[:], src[:], part[:], ALU.mult)
                pool.drain()
                nc.gpsimd.tensor_scalar(src[:], src[:], EPS, None, ALU.add)
                pool.drain()
                nc.gpsimd.tensor_tensor(dst[:], src[:], half[:], ALU.pow)
                pool.drain()
                pool.sem_inc(done.sem, 1)

            def turn(t):
                factor(ms, rstd, ms_ready, rstd_ready, t)
                pool.wait_ge(xbcT_ready.sem, xbcT_ready.this(t))
                pool.wait_ge(pe_over.sem, pe_over.last(t))
                for k in range(CONV):
                    nc.gpsimd.tensor_tensor((tap if k else cv)[:], xbcT[:, :, k:k + P],
                                            conv[:, k, :, None].broadcast_to([P, CB, P]), ALU.mult)
                    pool.drain()
                    if k:
                        nc.gpsimd.tensor_tensor(cv[:], cv[:], tap[:], ALU.add)
                        pool.drain()
                nc.gpsimd.tensor_tensor(cv[:], cv[:], conv[:, CONV, :, None].broadcast_to([P, CB, P]), ALU.add)
                nc.gpsimd.tensor_copy(xbcT[:, :, 0:CONV - 1], xbcT[:, :, P:P + CONV - 1])
                pool.drain()
                pool.sem_inc(taps_done.sem, 1)
                pool.wait_ge(xs_ready.sem, xs_ready.this(t))
                nc.gpsimd.tensor_tensor(by_head(xskip[:]), by_head(xs[:]), per_head(skip), ALU.mult)
                pool.drain()
                pool.wait_ge(y_ready.sem, y_ready.this(t))
                nc.gpsimd.tensor_tensor(y[:], y[:], xskip[:], ALU.add)
                pool.drain()
                nc.gpsimd.tensor_tensor(y[:], y[:], zs[:], ALU.mult)
                pool.drain()
                pool.sem_inc(y_gated.sem, 1)
                factor(yms, yrstd, yms_ready, yrstd_ready, t)

            nc.gpsimd.memset(half[:], -0.5)
            nc.gpsimd.memset(part[:], 1.0 / D)
            nc.gpsimd.memset(xbcT[:, :, 0:CONV - 1], 0.0)
            pool.drain()
            for e in (rstd_ready, taps_done, y_gated, yrstd_ready):
                pool.sem_inc(e.sem, 1)
            pool.wait_ge(loaded, 48)
            with pool.Fori(0, TILES) as t:
                turn(t)

        @block.vector
        def _(dve):
            def full(f, t):
                dve.wait_ge(fills.full[fills.bank(f)], fills.at(f, t))
                return psum[fills.bank(f)]

            def turn(t):
                dve.wait_ge(projected.sem, projected.last(t))
                for h in range(2):
                    src = full(f"xT{h}", t)
                    nc.vector.tensor_tensor(hT[:, 4 * h:4 * h + 4, :], src[:].rearrange("p (b t) -> p b t", b=4),
                                            gain[:, 4 * h:4 * h + 4, None].broadcast_to([P, 4, P]), ALU.mult
                                            ).then_inc(fills.free[fills.bank(f"xT{h}")], 1)
                dve.drain()
                dve.sem_inc(hT_ready.sem, 1)
                dve.wait_ge(rstd_ready.sem, rstd_ready.this(t))
                for f, at in (("x0", 0), ("x2", 2)):
                    src = full(f, t)
                    nc.vector.tensor_scalar(xbc[:, at * BANK:(at + 1) * BANK], src[:], rstd[:], None, ALU.mult
                                            ).then_inc(fills.free[fills.bank(f)], 1)
                dve.drain()
                dve.sem_inc(xbc_ready.sem, 1)
                src = full("dt", t)
                nc.vector.scalar_tensor_tensor(dt_raw[:], src[:, 0:NH], rstd[:], dt_bias[:], ALU.mult, ALU.add
                                               ).then_inc(fills.free[fills.bank("dt")], 1)
                dve.drain()
                nc.vector.scalar_tensor_tensor(dt_neg[:], dt_raw[:], -1.0, dt_raw[:], ALU.mult, ALU.min)
                nc.vector.tensor_scalar(dt_raw[:], dt_raw[:], 0.0, None, ALU.max)
                dve.drain()
                dve.sem_inc(dt_raw_ready.sem, 1)
                dve.wait_ge(dt_exp_ready.sem, dt_exp_ready.this(t))
                nc.vector.tensor_scalar(dt_u[:], dt_exp[:], 1.0, None, ALU.add)
                dve.drain()
                dve.sem_inc(dt_u_ready.sem, 1)
                nc.vector.scalar_tensor_tensor(dt_err[:], dt_u[:], -1.0, dt_exp[:], ALU.add, ALU.subtract)
                nc.vector.reciprocal(dt[:], dt_u[:])
                dve.drain()
                nc.vector.tensor_tensor(dt_err[:], dt_err[:], dt[:], ALU.mult)
                dve.drain()
                nc.vector.tensor_tensor(dt_raw[:], dt_raw[:], dt_err[:], ALU.subtract)
                dve.drain()
                dve.wait_ge(dt_log_ready.sem, dt_log_ready.this(t))
                nc.vector.tensor_tensor(dt[:], dt_raw[:], dt_neg[:], ALU.add)
                dve.drain()
                dve.wait_ge(pe_over.sem, pe_over.last(t))
                nc.vector.tensor_tensor(decay[:], dt[:], rate[:], ALU.mult)
                dve.drain()
                dve.sem_inc(decay_ready.sem, 1)
                src = full("sums", t)
                nc.vector.tensor_copy(sums[:], src[:, 0:2 * NH].rearrange("p (k h) -> p k h", k=2)).then_inc(fills.free[fills.bank("sums")], 1)
                dve.drain()
                nc.vector.tensor_scalar(nsum[:], sums[:, 0, :], -1.0, None, ALU.mult)
                nc.vector.tensor_tensor(to_end[:], sums[:, 1, :], sums[:, 0, :], ALU.subtract)
                dve.drain()
                dve.sem_inc(sums_ready.sem, 1)
                dve.wait_ge(xs_ready.sem, xs_ready.this(t))
                nc.vector.tensor_tensor(by_head(xdt[:]), by_head(xs[:]), per_head(dt), ALU.mult)
                dve.drain()
                dve.sem_inc(xdt_ready.sem, 1)
                src = full("bm", t)
                nc.vector.tensor_copy(bm[:], src[:, 0:2 * P].rearrange("p (g n) -> p g n", g=2)).then_inc(fills.free[fills.bank("bm")], 1)
                src = full("cb", t)
                nc.vector.tensor_copy(cb[:], src[:, 0:2 * P].rearrange("p (g n) -> p g n", g=2)).then_inc(fills.free[fills.bank("cb")], 1)
                dve.wait_ge(esums_ready.sem, esums_ready.this(t))
                nc.vector.tensor_tensor(by_head(xend[:]), by_head(xdt[:]), per_head(to_end), ALU.mult)
                dve.drain()
                dve.sem_inc(xend_ready.sem, 1)
                dve.wait_ge(stored.sem, stored.last(t))
                for g in range(SSD_G):
                    src = full(f"yo{g}", t)
                    nc.vector.tensor_tensor(by_head(y[:, g * BANK:(g + 1) * BANK]), by_head(src[:]),
                                            per_head(esums[:, 0, g * SSD_HPG:(g + 1) * SSD_HPG], SSD_HPG), ALU.mult
                                            ).then_inc(fills.free[fills.bank(f"yo{g}")], 1)
                for n in range(4):
                    dve.wait_ge(dec_ready.sem, dec_ready.this(t, n + 1))
                    nc.vector.tensor_tensor(dec[:, n % 2], dec[:, n % 2], cb[:, n // 2, None, :].broadcast_to([P, 4, P]), ALU.mult)
                    dve.drain()
                    dve.sem_inc(scan_ready.sem, 1)
                for g in range(SSD_G):
                    src = full(f"yd{g}", t)
                    cols = slice(g * BANK, (g + 1) * BANK)
                    nc.vector.tensor_tensor(y[:, cols], y[:, cols], src[:], ALU.add).then_inc(fills.free[fills.bank(f"yd{g}")], 1)
                dve.drain()
                dve.sem_inc(y_ready.sem, 1)
                nc.vector.tensor_tensor(by_head(state[:]), by_head(state[:]), per_head(esums[:, 1, :]), ALU.mult)
                dve.drain()
                for g in range(SSD_G):
                    src = full(f"st{g}", t)
                    cols = slice(g * BANK, (g + 1) * BANK)
                    nc.vector.tensor_tensor(state[:, cols], state[:, cols], src[:], ALU.add).then_inc(fills.free[fills.bank(f"st{g}")], 1)
                dve.drain()
                dve.sem_inc(state_ready.sem, 1)
                dve.wait_ge(yrstd_ready.sem, yrstd_ready.this(t))
                nc.vector.tensor_scalar(y[:], y[:], yrstd[:], None, ALU.mult).then_inc(out_ready.sem, 1)

            nc.vector.memset(state[:], 0.0)
            dve.wait_ge(rates_ready, 1)
            nc.vector.tensor_scalar(rate[:], rate[:], -1.0, None, ALU.mult)
            dve.drain()
            dve.sem_inc(consts_ready, 1)
            for e in (hT_ready, xbc_ready, dt_raw_ready, dt_u_ready, decay_ready, sums_ready, bm_ready, xdt_ready, xend_ready,
                      cb_ready, scan_ready, y_ready, state_ready, out_ready):
                dve.sem_inc(e.sem, 1)
            with dve.Fori(0, TILES) as t:
                turn(t)
            dve.wait_ge(stored.sem, stored.this(TILES - 1))
            for h in range(2):
                dve.wait_ge(state_turned, h + 1)
                nc.vector.tensor_copy(y[:, h * BANK:(h + 1) * BANK], psum[4 + h][:]).then_inc(state_copied, 1)


def ssd_sample_inputs(nc, io, psum, shared, w_zx, keep):
    ident, gain = shared["ident"], shared["gain_mix"]
    NH = SSD_HEADS
    with Stage(nc) as stage:
        sb, sem = stage.buffer, stage.semaphore

        x, junk = sb("sin_x", [DEC, D]), sb("sin_junk", [DEC, D])
        ms, rstd, half = sb("sin_ms", [DEC, 1]), sb("sin_rstd", [DEC, 1]), sb("sin_half", [DEC, 1])
        hT = sb("sin_hT", [P, DB, DEC])
        past = sb("sin_past", [DEC, CONV, CONV_DIM])
        weights = sb("sin_weights", [DEC, CONV + 1, CONV_DIM])
        cv, tap = sb("sin_cv", [DEC, CONV_DIM]), sb("sin_tap", [DEC, CONV_DIM])
        dt_bias = sb("sin_dt_bias", [DEC, NH])
        raw, neg, e, u, err, dt = (sb("sin_" + n, [DEC, NH]) for n in ("raw", "neg", "e", "u", "err", "dt"))
        loaded, x_in, x_turned = sem("sin_loaded"), sem("sin_x_in"), sem("sin_x_turned")
        ms_ready, rstd_ready, hT_ready, projected = sem("sin_ms_ready"), sem("sin_rstd_ready"), sem("sin_hT_ready"), sem("sin_projected")
        new_ready, taps_done, cv_ready = sem("sin_new_ready"), sem("sin_taps_done"), sem("sin_cv_ready")
        neg_ready, e_ready, u_ready, log_ready, dt_ready = (sem("sin_" + n) for n in ("neg_ready", "e_ready", "u_ready", "log_ready", "dt_ready"))
        stored = sem("sin_stored")
        block = stage.block()

        @block.sync
        def _(sp):
            sp.dma_start(x[:], io["x_sample"]).then_inc(x_in, 16)
            sp.dma_start(past[:, 0:CONV - 1, :], io["state_conv"]).then_inc(loaded, 16)
            for k in range(CONV):
                sp.dma_start(weights[:, k, :], io["conv_w"][k:k + 1, :].broadcast_to([DEC, CONV_DIM])).then_inc(loaded, 16)
            sp.dma_start(weights[:, CONV, :], io["conv_b"].broadcast_to([DEC, CONV_DIM])).then_inc(loaded, 16)
            sp.dma_start(dt_bias[:], io["dt_bias"].broadcast_to([DEC, NH])).then_inc(loaded, 16)
            sp.wait_ge(new_ready, 1)
            sp.dma_start(io["s_conv"], past[:, 1:CONV, :]).then_inc(stored, 16)
            sp.wait_ge(dt_ready, 1)
            sp.dma_start(io["dts"], dt[:]).then_inc(stored, 16)
            sp.wait_ge(cv_ready, 1)
            sp.dma_start(io["rows2"], cv[:, 0:D]).then_inc(stored, 16)
            sp.dma_start(io["bcs"], cv[:, D:CONV_DIM]).then_inc(stored, 16)
            sp.wait_ge(stored, 64)

        @block.tensor
        def _(pe):
            pe.wait_ge(x_in, 16)
            for b in range(DB):
                ins = nc.tensor.transpose(psum[0][:, b * DEC:(b + 1) * DEC], x[:, b * P:(b + 1) * P], ident[0:DEC, 0:DEC])
            ins.then_inc(x_turned, 1)
            pe.wait_ge(hT_ready, 1)
            for c in range(6):
                n = min(BANK, IN_COLS - 1536 - c * BANK)
                for b in range(DB):
                    ins = nc.tensor.matmul(psum[1 + c][0:DEC, 0:n], hT[:, b, :], w_zx[:, b, c * BANK:c * BANK + n],
                                           start=(b == 0), stop=(b == DB - 1))
                ins.then_inc(projected, 1)

        @block.scalar
        def _(act):
            act.wait_ge(x_in, 16)
            nc.scalar.activation(junk[:], x[:], ACT.Square, accum_out=ms[:]).then_inc(ms_ready, 1)
            act.wait_ge(rstd_ready, 1)
            act.wait_ge(projected, 2)
            for h in range(2):
                nc.scalar.activation(keep["gate"][:, h * BANK:(h + 1) * BANK], psum[1 + h][0:DEC, :], ACT.Silu, scale=rstd[:])
            act.wait_ge(taps_done, 1)
            nc.scalar.activation(cv[:], cv[:], ACT.Silu)
            act.drain()
            act.sem_inc(cv_ready, 1)
            nc.scalar.copy(keep["xs"][:], cv[:, 0:D])
            act.wait_ge(neg_ready, 1)
            nc.scalar.activation(e[:], neg[:], ACT.Exp).then_inc(e_ready, 1)
            act.wait_ge(u_ready, 1)
            nc.scalar.activation(neg[:], u[:], ACT.Ln).then_inc(log_ready, 1)
            act.drain()

        @block.gpsimd
        def _(pool):
            nc.gpsimd.memset(half[:], -0.5)
            pool.wait_ge(ms_ready, 1)
            nc.gpsimd.tensor_scalar(ms[:], ms[:], 1.0 / D, EPS, ALU.mult, ALU.add)
            pool.drain()
            nc.gpsimd.tensor_tensor(rstd[:], ms[:], half[:], ALU.pow).then_inc(rstd_ready, 1)

        @block.vector
        def _(dve):
            dve.wait_ge(x_turned, 1)
            nc.vector.tensor_tensor(hT[:], psum[0][:, 0:DB * DEC].rearrange("p (b t) -> p b t", b=DB),
                                    gain[:, :, None].broadcast_to([P, DB, DEC]), ALU.mult).then_inc(hT_ready, 1)
            dve.wait_ge(rstd_ready, 1)
            dve.wait_ge(projected, 6)
            nc.vector.tensor_scalar(raw[:], psum[6][0:DEC, 0:NH], rstd[:], None, ALU.mult)
            for c in range(3):
                nc.vector.tensor_scalar(past[:, CONV - 1, c * BANK:(c + 1) * BANK], psum[3 + c][0:DEC, :], rstd[:], None, ALU.mult)
            dve.wait_ge(loaded, 16 * (CONV + 3))
            dve.drain()
            dve.sem_inc(new_ready, 1)
            nc.vector.tensor_tensor(raw[:], raw[:], dt_bias[:], ALU.add)
            dve.drain()
            nc.vector.scalar_tensor_tensor(neg[:], raw[:], -1.0, raw[:], ALU.mult, ALU.min)
            nc.vector.tensor_scalar(raw[:], raw[:], 0.0, None, ALU.max)
            dve.drain()
            dve.sem_inc(neg_ready, 1)
            for k in range(CONV):
                nc.vector.tensor_tensor((tap if k else cv)[:], past[:, k, :], weights[:, k, :], ALU.mult)
                dve.drain()
                if k:
                    nc.vector.tensor_tensor(cv[:], cv[:], tap[:], ALU.add)
                    dve.drain()
            nc.vector.tensor_tensor(cv[:], cv[:], weights[:, CONV, :], ALU.add).then_inc(taps_done, 1)
            dve.wait_ge(e_ready, 1)
            nc.vector.tensor_scalar(u[:], e[:], 1.0, None, ALU.add).then_inc(u_ready, 1)
            dve.drain()
            nc.vector.scalar_tensor_tensor(err[:], u[:], -1.0, e[:], ALU.add, ALU.subtract)
            nc.vector.reciprocal(dt[:], u[:])
            dve.drain()
            nc.vector.tensor_tensor(err[:], err[:], dt[:], ALU.mult)
            dve.drain()
            nc.vector.tensor_tensor(raw[:], raw[:], err[:], ALU.subtract)
            dve.drain()
            dve.wait_ge(log_ready, 1)
            nc.vector.tensor_tensor(dt[:], raw[:], neg[:], ALU.add).then_inc(dt_ready, 1)


def ssd_sample_step(nc, io, shared, keep):
    NH = SSD_HEADS
    with Stage(nc) as stage:
        sb, sem = stage.buffer, stage.semaphore

        state = sb("step_state", [P, HD, STATE])
        wide = sb("step_wide", [P, HD, STATE])
        x, dt, rate, dec = sb("step_x", [P, HD]), sb("step_dt", [P, 1]), sb("step_rate", [P, 1]), sb("step_dec", [P, 1])
        bc = sb("step_bc", [P, 2, STATE])
        y_pairs = sb("step_y_pairs", [P, HD])
        y, xskip, junk, skip = sb("step_y", [DEC, D]), sb("step_xskip", [DEC, D]), sb("step_junk", [DEC, D]), sb("step_skip", [DEC, NH])
        ms, rstd, half = sb("step_ms", [DEC, 1]), sb("step_rstd", [DEC, 1]), sb("step_half", [DEC, 1])
        loaded, state_in, rate_ready = sem("step_loaded"), sem("step_state_in"), sem("step_rate_ready")
        drate_ready, dec_ready, state_ready, y_ready = sem("step_drate_ready"), sem("step_dec_ready"), sem("step_state_ready"), sem("step_y_ready")
        stored, y_in, gated, ms_ready, rstd_ready, out_ready = (sem("step_" + n) for n in ("stored", "y_in", "gated", "ms_ready", "rstd_ready", "out_ready"))
        block = stage.block()

        @block.sync
        def _(sp):
            sp.dma_start(x[:], io["rows2"].rearrange("b (h d) -> (b h) d", h=NH)).then_inc(loaded, 16)
            sp.dma_start(dt[:], io["dts"].rearrange("b (h a) -> (b h) a", a=1)).then_inc(loaded, 16)
            al = io["a_log"]
            for b in range(DEC):
                sp.dma_start(rate[b * NH:(b + 1) * NH, :], al.rearrange("a h -> h a")).then_inc(loaded, 16)
                for g in range(SSD_G):
                    lo = b * NH + g * SSD_HPG
                    src = io["bcs"][b:b + 1, :].rearrange("a (k g n) -> a k g n", k=2, g=SSD_G)[:, :, g, :]
                    sp.dma_start(bc[lo:lo + SSD_HPG, :, :], src.broadcast_to([SSD_HPG, 2, STATE])).then_inc(loaded, 16)
            sp.dma_start(skip[:], io["d_skip"].broadcast_to([DEC, NH])).then_inc(loaded, 16)
            sp.dma_start(state[:], io["state_ssm"]).then_inc(state_in, 16)
            sp.wait_ge(state_ready, 1)
            sp.dma_start(io["s_ssm"], state[:]).then_inc(stored, 16)
            sp.wait_ge(y_ready, 1)
            sp.dma_start(io["rows3"].rearrange("b (h d) -> (b h) d", h=NH), y_pairs[:]).then_inc(y_in, 16)
            sp.wait_ge(y_in, 16)
            sp.dma_start(y[:], io["rows3"]).then_inc(y_in, 16)
            sp.wait_ge(y_in, 32)
            sp.wait_ge(out_ready, 1)
            sp.dma_start(io["mixed"][SEQ:TOKENS, D:2 * D], y[:]).then_inc(stored, 16)
            sp.wait_ge(stored, 32)

        @block.scalar
        def _(act):
            act.wait_ge(loaded, 16 * (3 + 3 * DEC))
            nc.scalar.activation(rate[:], rate[:], ACT.Exp).then_inc(rate_ready, 1)
            act.wait_ge(drate_ready, 1)
            nc.scalar.activation(dec[:], dec[:], ACT.Exp).then_inc(dec_ready, 1)
            act.wait_ge(gated, 1)
            nc.scalar.activation(junk[:], y[:], ACT.Square, accum_out=ms[:]).then_inc(ms_ready, 1)

        @block.gpsimd
        def _(pool):
            nc.gpsimd.memset(half[:], -0.5)
            pool.wait_ge(ms_ready, 1)
            nc.gpsimd.tensor_scalar(ms[:], ms[:], 1.0 / D, EPS, ALU.mult, ALU.add)
            pool.drain()
            nc.gpsimd.tensor_tensor(rstd[:], ms[:], half[:], ALU.pow).then_inc(rstd_ready, 1)

        @block.vector
        def _(dve):
            dve.wait_ge(rate_ready, 1)
            nc.vector.tensor_scalar(dec[:], dt[:], rate[:], -1.0, ALU.mult, ALU.mult).then_inc(drate_ready, 1)
            nc.vector.tensor_scalar(x[:], x[:], dt[:], None, ALU.mult)
            dve.drain()
            nc.vector.tensor_tensor(wide[:], x[:, :, None].broadcast_to([P, HD, STATE]),
                                    bc[:, 0, None, :].broadcast_to([P, HD, STATE]), ALU.mult)
            dve.drain()
            dve.wait_ge(state_in, 16)
            dve.wait_ge(dec_ready, 1)
            nc.vector.scalar_tensor_tensor(state[:].rearrange("p d n -> p (d n)"), state[:].rearrange("p d n -> p (d n)"), dec[:],
                                           wide[:].rearrange("p d n -> p (d n)"), ALU.mult, ALU.add)
            dve.drain()
            dve.sem_inc(state_ready, 1)
            nc.vector.tensor_tensor(wide[:], state[:], bc[:, 1, None, :].broadcast_to([P, HD, STATE]), ALU.mult)
            dve.drain()
            nc.vector.tensor_reduce(y_pairs[:], wide[:], AX.X, ALU.add).then_inc(y_ready, 1)
            nc.vector.tensor_tensor(xskip[:].rearrange("b (h d) -> b h d", h=NH), keep["xs"][:].rearrange("b (h d) -> b h d", h=NH),
                                    skip[:, :, None].broadcast_to([DEC, NH, HD]), ALU.mult)
            dve.wait_ge(y_in, 32)
            dve.drain()
            nc.vector.tensor_tensor(y[:], y[:], xskip[:], ALU.add)
            dve.drain()
            nc.vector.tensor_tensor(y[:], y[:], keep["gate"][:], ALU.mult).then_inc(gated, 1)
            dve.drain()
            dve.wait_ge(rstd_ready, 1)
            nc.vector.tensor_scalar(y[:], y[:], rstd[:], None, ALU.mult).then_inc(out_ready, 1)


def memory_kv(nc, io, psum, shared, mkT, mv):
    ident, gain = shared["ident"], shared["gain_mem"]
    MT = N_MEM // P
    with Stage(nc) as stage:
        sb, sem = stage.buffer, stage.semaphore

        w_mk, w_mv = sb("w_mk", [P, DB, D]), sb("w_mv", [P, DB, D])
        x, junk = sb("mem_x", [P, MT, D]), sb("mem_junk", [P, D])
        hT = sb("mem_hT", [P, MT, DB, P])
        mk = sb("mem_k", [P, MT, D])
        ms, rstd, half = sb("mem_ms", [P, MT]), sb("mem_rstd", [P, MT]), sb("mem_half", [P, MT])
        x_in, wk_in, wv_in = sem("mem_x_in"), sem("mem_wk_in"), sem("mem_wv_in")
        turned, hT_ready, ms_ready, rstd_ready = sem("mem_turned"), sem("mem_hT_ready"), sem("mem_ms_ready"), sem("mem_rstd_ready")
        projected, k_ready, v_ready, k_turned, stored = (sem("mem_" + n) for n in ("projected", "k_ready", "v_ready", "k_turned", "stored"))
        block = stage.block()

        @block.sync
        def _(sp):
            sp.dma_start(x[:], io["mem_prompt"].rearrange("(m p) n -> p m n", p=P)).then_inc(x_in, 16)
            sp.dma_start(w_mk[:], io["w_mk"].rearrange("(b p) n -> p b n", p=P)).then_inc(wk_in, 16)
            sp.dma_start(w_mv[:], io["w_mv"].rearrange("(b p) n -> p b n", p=P)).then_inc(wv_in, 16)
            sp.wait_ge(k_ready, MT)
            sp.dma_start(io["p_mem_k"].rearrange("(m p) n -> p m n", p=P), mk[:]).then_inc(stored, 16)
            sp.wait_ge(v_ready, MT)
            sp.dma_start(io["p_mem_v"].rearrange("(m p) n -> p m n", p=P), mv[:]).then_inc(stored, 16)
            sp.wait_ge(stored, 32)

        @block.tensor
        def _(pe):
            pe.wait_ge(x_in, 16)
            for m in range(MT):
                for h in range(2):
                    for j in range(4):
                        b = 4 * h + j
                        ins = nc.tensor.transpose(psum[2 * m + h][:, j * P:(j + 1) * P], x[:, m, b * P:(b + 1) * P], ident[:])
                    ins.then_inc(turned, 1)
            for w, arrived, first in ((w_mk, wk_in, 4), (w_mv, wv_in, 0)):
                pe.wait_ge(arrived, 16)
                pe.wait_ge(hT_ready, 4)
                for m in range(MT):
                    for c in range(2):
                        for b in range(DB):
                            ins = nc.tensor.matmul(psum[first + 2 * m + c][:], hT[:, m, b, :], w[:, b, c * BANK:(c + 1) * BANK],
                                                   start=(b == 0), stop=(b == DB - 1))
                        ins.then_inc(projected, 1)
            for m in range(MT):
                pe.wait_ge(k_ready, m + 1)
                for h in range(2):
                    for j in range(4):
                        b = 4 * h + j
                        ins = nc.tensor.transpose(psum[4 + 2 * m + h][:, j * P:(j + 1) * P], mk[:, m, b * P:(b + 1) * P], ident[:])
                    ins.then_inc(k_turned, 1)

        @block.scalar
        def _(act):
            act.wait_ge(x_in, 16)
            for m in range(MT):
                nc.scalar.activation(junk[:], x[:, m, :], ACT.Square, accum_out=ms[:, m:m + 1])
                act.drain()
            act.sem_inc(ms_ready, 1)
            act.wait_ge(rstd_ready, 1)
            for m in range(MT):
                act.wait_ge(projected, 2 * m + 2)
                for c in range(2):
                    nc.scalar.activation(mk[:, m, c * BANK:(c + 1) * BANK], psum[4 + 2 * m + c][:], ACT.Copy, scale=rstd[:, m:m + 1])
                act.drain()
                act.sem_inc(k_ready, 1)
            for m in range(MT):
                act.wait_ge(projected, 4 + 2 * m + 2)
                for c in range(2):
                    nc.scalar.activation(mv[:, m, c * BANK:(c + 1) * BANK], psum[2 * m + c][:], ACT.Copy, scale=rstd[:, m:m + 1])
                act.drain()
                act.sem_inc(v_ready, 1)

        @block.gpsimd
        def _(pool):
            nc.gpsimd.memset(half[:], -0.5)
            pool.wait_ge(ms_ready, 1)
            nc.gpsimd.tensor_scalar(ms[:], ms[:], 1.0 / D, EPS, ALU.mult, ALU.add)
            pool.drain()
            nc.gpsimd.tensor_tensor(rstd[:], ms[:], half[:], ALU.pow).then_inc(rstd_ready, 1)

        @block.vector
        def _(dve):
            for m in range(MT):
                for h in range(2):
                    dve.wait_ge(turned, 2 * m + h + 1)
                    nc.vector.tensor_tensor(hT[:, m, 4 * h:4 * h + 4, :], psum[2 * m + h][:].rearrange("p (b t) -> p b t", b=4),
                                            gain[:, 4 * h:4 * h + 4, None].broadcast_to([P, 4, P]), ALU.mult).then_inc(hT_ready, 1)
            for m in range(MT):
                for h in range(2):
                    dve.wait_ge(k_turned, 2 * m + h + 1)
                    nc.vector.tensor_copy(mkT[:, 4 * h:4 * h + 4, m * P:(m + 1) * P], psum[4 + 2 * m + h][:].rearrange("p (b t) -> p b t", b=4))
            dve.drain()


def memory_read(nc, io, psum, shared, w_out, w_mq, w_mo, mkT, mv):
    ident = shared["ident"]
    with Stage(nc) as stage:
        sb, sem, event = stage.buffer, stage.semaphore, stage.event

        mixed = sb("read_mixed", [P, 2 * D])
        x = sb("read_x", [P, D])
        mT = sb("read_mT", [P, 2 * DB, P])
        x1 = sb("read_x1", [P, D])
        hT = sb("read_hT", [P, DB, P])
        qT = sb("read_qT", [P, DB, P])
        p = sb("read_p", [P, MEM_HEADS, N_MEM])
        pT = sb("read_pT", [P, MEM_HEADS, 2, P])
        oT = sb("read_oT", [P, DB, P])
        ms, rstd, scale = sb("read_ms", [P, 1]), sb("read_rstd", [P, 1]), sb("read_scale", [P, 1])
        half, part = sb("read_half", [P, 1]), sb("read_part", [P, 1])
        top, total = sb("read_top", [P, MEM_HEADS]), sb("read_total", [P, MEM_HEADS])
        xn, gain_ffn = sb("read_xn", [P, D]), sb("read_gain_ffn", [P, D])
        o = p[:].rearrange("p h m -> p (h m)")

        order = [("m0", 0), ("m1", 1), ("m2", 0), ("m3", 1), ("r0", 2), ("r1", 3), ("h0", 0), ("h1", 1),
                 ("q0", 4), ("q1", 5), ("s0", 6), ("s1", 7), ("t0", 0), ("t1", 1), ("o0", 2), ("o1", 3),
                 ("u0", 0), ("u1", 1), ("y0", 4), ("y1", 5)]
        fills = Fills(sem, "read", order)
        w_out_in, w_mq_in, w_mo_in = sem("read_w_out"), sem("read_w_mq"), sem("read_w_mo")
        mixed_in, x_in = event("read_mixed_in", 1, 16), event("read_x_in", 1, 16)
        mixed_turned, x_added = event("read_mixed_turned"), event("read_x_added")
        mT_ready, mT_used = event("read_mT_ready", 4), event("read_mT_used")
        x1_ready = event("read_x1_ready", 2)
        ms_ready, rstd_ready, scale_ready = event("read_ms_ready"), event("read_rstd_ready"), event("read_scale_ready")
        hT_ready, hT_used, qT_ready = event("read_hT_ready"), event("read_hT_used"), event("read_qT_ready")
        ntop_ready, p_ready, p_turned, pT_ready, o_ready, oT_ready = (
            event("read_" + n) for n in ("ntop_ready", "p_ready", "p_turned", "pT_ready", "o_ready", "oT_ready"))
        x2_ready, stored = event("read_x2_ready"), event("read_stored", 1, 16)
        ms2_ready, rstd2_ready = event("read_ms2_ready"), event("read_rstd2_ready")
        xn_ready, xn_stored = event("read_xn_ready"), event("read_xn_stored", 1, 16)
        gain_in = sem("read_gain_in")
        block = stage.block()

        @block.sync
        def _(sp):
            for e in (mixed_in, x_in, stored, xn_stored):
                sp.sem_inc(e.sem, 16)
            sp.dma_start(gain_ffn[:], io["norm_ffn_w"].broadcast_to([P, D])).then_inc(gain_in, 16)
            sp.dma_start(w_out[:], io["w_out"].rearrange("(b p) n -> p b n", p=P)).then_inc(w_out_in, 16)
            sp.dma_start(w_mq[:], io["w_mq"].rearrange("(b p) n -> p b n", p=P)).then_inc(w_mq_in, 16)
            sp.dma_start(w_mo[:], io["w_mo"].rearrange("(b p) n -> p b n", p=P)).then_inc(w_mo_in, 16)
            with sp.Fori(0, TILES) as t:
                rows = bass.ds(t * P, P)
                sp.wait_ge(mixed_turned.sem, mixed_turned.last(t))
                sp.dma_start(mixed[:], io["mixed"][rows, :]).then_inc(mixed_in.sem, 16)
                sp.wait_ge(x_added.sem, x_added.last(t))
                sp.dma_start(x[:], io["x_prompt"][rows, :]).then_inc(x_in.sem, 16)
                sp.wait_ge(x2_ready.sem, x2_ready.this(t))
                sp.dma_start(io["x2"][rows, :], x1[:]).then_inc(stored.sem, 16)
                sp.wait_ge(xn_ready.sem, xn_ready.this(t))
                sp.dma_start(io["xn"][rows, :], xn[:]).then_inc(xn_stored.sem, 16)
            sp.wait_ge(stored.sem, stored.this(TILES - 1))
            sp.wait_ge(xn_stored.sem, xn_stored.this(TILES - 1))

        @block.tensor
        def _(pe):
            def begin(f, t):
                pe.wait_ge(fills.free[fills.bank(f)], fills.at(f, t))
                return psum[fills.bank(f)]

            def turn_blocks(prefix, src, t, n=2):
                for h in range(n):
                    out = begin(f"{prefix}{h}", t)
                    for j in range(4):
                        ins = nc.tensor.transpose(out[:, j * P:(j + 1) * P], src[:, (4 * h + j) * P:(4 * h + j + 1) * P], ident[:])
                    ins.then_inc(fills.full[fills.bank(f"{prefix}{h}")], 1)

            def turn(t):
                pe.wait_ge(mixed_in.sem, mixed_in.this(t))
                turn_blocks("m", mixed, t, 4)
                pe.drain()
                pe.sem_inc(mixed_turned.sem, 1)
                pe.wait_ge(mT_ready.sem, mT_ready.this(t, 4))
                for c in range(2):
                    out = begin(f"r{c}", t)
                    for b in range(2 * DB):
                        ins = nc.tensor.matmul(out[:], mT[:, b, :], w_out[:, b, c * BANK:(c + 1) * BANK],
                                               start=(b == 0), stop=(b == 2 * DB - 1))
                    ins.then_inc(fills.full[fills.bank(f"r{c}")], 1)
                pe.drain()
                pe.sem_inc(mT_used.sem, 1)
                pe.wait_ge(x1_ready.sem, x1_ready.this(t, 2))
                turn_blocks("h", x1, t)
                pe.wait_ge(hT_ready.sem, hT_ready.this(t))
                for h in range(2):
                    out = begin(f"q{h}", t)
                    for j in range(4):
                        d = 4 * h + j
                        for b in range(DB):
                            ins = nc.tensor.matmul(out[:, j * P:(j + 1) * P], w_mq[:, b, d * P:(d + 1) * P], hT[:, b, :],
                                                   start=(b == 0), stop=(b == DB - 1))
                    ins.then_inc(fills.full[fills.bank(f"q{h}")], 1)
                pe.wait_ge(qT_ready.sem, qT_ready.this(t))
                for n in range(2):
                    out = begin(f"s{n}", t)
                    for r in range(2):
                        for k in range(2):
                            d = 2 * (2 * n + r) + k
                            ins = nc.tensor.matmul(out[:, r * N_MEM:(r + 1) * N_MEM], qT[:, d, :], mkT[:, d, :], start=(k == 0), stop=(k == 1))
                    ins.then_inc(fills.full[fills.bank(f"s{n}")], 1)
                pe.wait_ge(p_ready.sem, p_ready.this(t))
                turn_blocks("t", o, t)
                pe.drain()
                pe.sem_inc(p_turned.sem, 1)
                pe.wait_ge(pT_ready.sem, pT_ready.this(t))
                for n in range(2):
                    out = begin(f"o{n}", t)
                    for r in range(2):
                        h = 2 * n + r
                        for k in range(2):
                            ins = nc.tensor.matmul(out[:, r * MEM_HD:(r + 1) * MEM_HD], pT[:, h, k, :], mv[:, k, h * MEM_HD:(h + 1) * MEM_HD],
                                                   start=(k == 0), stop=(k == 1))
                    ins.then_inc(fills.full[fills.bank(f"o{n}")], 1)
                pe.wait_ge(o_ready.sem, o_ready.this(t))
                turn_blocks("u", o, t)
                pe.wait_ge(oT_ready.sem, oT_ready.this(t))
                for c in range(2):
                    out = begin(f"y{c}", t)
                    for b in range(DB):
                        ins = nc.tensor.matmul(out[:], oT[:, b, :], w_mo[:, b, c * BANK:(c + 1) * BANK], start=(b == 0), stop=(b == DB - 1))
                    ins.then_inc(fills.full[fills.bank(f"y{c}")], 1)

            fills.prime(pe)
            for e in (mixed_turned, mT_used, p_turned):
                pe.sem_inc(e.sem, 1)
            for s in (w_out_in, w_mq_in, w_mo_in):
                pe.wait_ge(s, 16)
            with pe.Fori(0, TILES) as t:
                turn(t)

        @block.scalar
        def _(act):
            def full(f, t):
                act.wait_ge(fills.full[fills.bank(f)], fills.at(f, t))
                return psum[fills.bank(f)]

            def copy_blocks(prefix, dst, ready, t):
                for h in range(2):
                    src = full(f"{prefix}{h}", t)
                    nc.scalar.copy(dst[:, 4 * h:4 * h + 4, :], src[:].rearrange("p (b t) -> p b t", b=4)
                                   ).then_inc(fills.free[fills.bank(f"{prefix}{h}")], 1)
                act.drain()
                act.sem_inc(ready.sem, 1)

            def turn(t):
                act.wait_ge(x1_ready.sem, x1_ready.this(t, 2))
                nc.scalar.activation(p[:].rearrange("p h m -> p (h m)"), x1[:], ACT.Square, accum_out=ms[:])
                act.drain()
                act.sem_inc(ms_ready.sem, 1)
                copy_blocks("q", qT, qT_ready, t)
                act.wait_ge(ntop_ready.sem, ntop_ready.this(t))
                for h in range(MEM_HEADS):
                    if h % 2 == 0:
                        src = full(f"s{h // 2}", t)
                    ins = nc.scalar.activation(p[:, h, :], src[:, (h % 2) * N_MEM:(h % 2 + 1) * N_MEM], ACT.Exp,
                                               bias=top[:, h:h + 1], scale=scale[:], accum_out=total[:, h:h + 1])
                act.drain()
                act.sem_inc(p_ready.sem, 1)
                for n in range(2):
                    act.sem_inc(fills.free[fills.bank(f"s{n}")], 1)
                copy_blocks("t", pT[:].rearrange("p h k t -> p (h k) t"), pT_ready, t)
                copy_blocks("u", oT, oT_ready, t)
                act.wait_ge(x2_ready.sem, x2_ready.this(t))
                act.wait_ge(xn_stored.sem, xn_stored.last(t))
                nc.scalar.activation(xn[:], x1[:], ACT.Square, accum_out=ms[:])
                act.drain()
                act.sem_inc(ms2_ready.sem, 1)

            for e in (ms2_ready, ms_ready, qT_ready, p_ready, pT_ready, oT_ready):
                act.sem_inc(e.sem, 1)
            with act.Fori(0, TILES) as t:
                turn(t)

        @block.gpsimd
        def _(pool):
            nc.gpsimd.memset(half[:], -0.5)
            nc.gpsimd.memset(part[:], 1.0 / D)
            pool.drain()
            pool.sem_inc(rstd_ready.sem, 1)
            pool.sem_inc(rstd2_ready.sem, 1)
            with pool.Fori(0, TILES) as t:
                for ready, done in ((ms_ready, rstd_ready), (ms2_ready, rstd2_ready)):
                    pool.wait_ge(ready.sem, ready.this(t))
                    nc.gpsimd.tensor_tensor(ms[:], ms[:], part[:], ALU.mult)
                    pool.drain()
                    nc.gpsimd.tensor_scalar(ms[:], ms[:], EPS, None, ALU.add)
                    pool.drain()
                    nc.gpsimd.tensor_tensor(rstd[:], ms[:], half[:], ALU.pow)
                    pool.drain()
                    pool.sem_inc(done.sem, 1)

        @block.vector
        def _(dve):
            def full(f, t):
                dve.wait_ge(fills.full[fills.bank(f)], fills.at(f, t))
                return psum[fills.bank(f)]

            def with_gain(dst, gain, prefix, first, t, n):
                for h in range(n):
                    src = full(f"{prefix}{first + h}", t)
                    nc.vector.tensor_tensor(dst[:, 4 * h:4 * h + 4, :], src[:].rearrange("p (b t) -> p b t", b=4),
                                            gain[:, 4 * h:4 * h + 4, None].broadcast_to([P, 4, P]), ALU.mult
                                            ).then_inc(fills.free[fills.bank(f"{prefix}{first + h}")], 1)

            def turn(t):
                dve.wait_ge(mT_used.sem, mT_used.last(t))
                with_gain(mT[:, 0:DB], shared["gain_att"], "m", 0, t, 2)
                with_gain(mT[:, DB:2 * DB], shared["gain_ssd"], "m", 2, t, 2)
                dve.drain()
                dve.sem_inc(mT_ready.sem, 4)
                dve.wait_ge(x_in.sem, x_in.this(t))
                dve.wait_ge(stored.sem, stored.last(t))
                for c in range(2):
                    src = full(f"r{c}", t)
                    cols = slice(c * BANK, (c + 1) * BANK)
                    nc.vector.tensor_tensor(x1[:, cols], src[:], x[:, cols], ALU.add).then_inc(fills.free[fills.bank(f"r{c}")], 1)
                dve.drain()
                dve.sem_inc(x1_ready.sem, 2)
                dve.sem_inc(x_added.sem, 1)
                with_gain(hT, shared["gain_read"], "h", 0, t, 2)
                dve.drain()
                dve.sem_inc(hT_ready.sem, 1)
                dve.wait_ge(rstd_ready.sem, rstd_ready.this(t))
                nc.vector.tensor_scalar(scale[:], rstd[:], MEM_HD ** -0.5, None, ALU.mult)
                for n in range(2):
                    src = full(f"s{n}", t)
                    nc.vector.tensor_reduce(top[:, 2 * n:2 * n + 2], src[:].rearrange("p (r m) -> p r m", r=2), AX.X, ALU.max)
                dve.drain()
                nc.vector.tensor_scalar(top[:], top[:], scale[:], -1.0, ALU.mult, ALU.mult)
                dve.drain()
                dve.sem_inc(ntop_ready.sem, 1)
                dve.wait_ge(p_ready.sem, p_ready.this(t))
                nc.vector.reciprocal(total[:], total[:])
                dve.drain()
                dve.wait_ge(p_turned.sem, p_turned.this(t))
                for n in range(2):
                    src = full(f"o{n}", t)
                    nc.vector.tensor_tensor(p[:, 2 * n:2 * n + 2, :], src[:].rearrange("p (r m) -> p r m", r=2),
                                            total[:, 2 * n:2 * n + 2, None].broadcast_to([P, 2, MEM_HD]), ALU.mult
                                            ).then_inc(fills.free[fills.bank(f"o{n}")], 1)
                dve.drain()
                dve.sem_inc(o_ready.sem, 1)
                for c in range(2):
                    src = full(f"y{c}", t)
                    cols = slice(c * BANK, (c + 1) * BANK)
                    nc.vector.tensor_tensor(x1[:, cols], src[:], x1[:, cols], ALU.add).then_inc(fills.free[fills.bank(f"y{c}")], 1)
                dve.drain()
                dve.sem_inc(x2_ready.sem, 1)
                dve.wait_ge(rstd2_ready.sem, rstd2_ready.this(t))
                nc.vector.scalar_tensor_tensor(xn[:], x1[:], rstd[:], gain_ffn[:], ALU.mult, ALU.mult)
                dve.drain()
                dve.sem_inc(xn_ready.sem, 1)

            dve.wait_ge(gain_in, 16)
            for e in (xn_ready, mT_ready, x1_ready, x_added, hT_ready, ntop_ready, o_ready, x2_ready):
                dve.sem_inc(e.sem, 1)
            with dve.Fori(0, TILES) as t:
                turn(t)


def memory_read_sample_query(nc, io, psum, shared, w_out, w_mq, x1):
    ident = shared["ident"]
    with Stage(nc) as stage:
        sb, sem = stage.buffer, stage.semaphore

        mixed, x, junk, q = sb("rsq_mixed", [DEC, 2 * D]), sb("rsq_x", [DEC, D]), sb("rsq_junk", [DEC, D]), sb("rsq_q", [DEC, D])
        mT, hT = sb("rsq_mT", [P, 2 * DB, DEC]), sb("rsq_hT", [P, DB, DEC])
        ms, rstd, half = sb("rsq_ms", [DEC, 1]), sb("rsq_rstd", [DEC, 1]), sb("rsq_half", [DEC, 1])
        loaded, turned, mT_ready, summed, x1_ready = (sem("rsq_" + n) for n in ("loaded", "turned", "mT_ready", "summed", "x1_ready"))
        x1_turned, hT_ready, ms_ready, rstd_ready, projected, q_ready, stored = (
            sem("rsq_" + n) for n in ("x1_turned", "hT_ready", "ms_ready", "rstd_ready", "projected", "q_ready", "stored"))
        block = stage.block()

        @block.sync
        def _(sp):
            sp.dma_start(mixed[:], io["mixed"][SEQ:TOKENS, :]).then_inc(loaded, 16)
            sp.dma_start(x[:], io["x_sample"]).then_inc(loaded, 16)
            sp.wait_ge(q_ready, 1)
            sp.dma_start(io["rows"], q[:]).then_inc(stored, 16)
            sp.wait_ge(stored, 16)

        @block.tensor
        def _(pe):
            pe.wait_ge(loaded, 32)
            for b in range(2 * DB):
                ins = nc.tensor.transpose(psum[0][:, b * DEC:(b + 1) * DEC], mixed[:, b * P:(b + 1) * P], ident[0:DEC, 0:DEC])
            ins.then_inc(turned, 1)
            pe.wait_ge(mT_ready, 1)
            for c in range(2):
                for b in range(2 * DB):
                    ins = nc.tensor.matmul(psum[1 + c][0:DEC, :], mT[:, b, :], w_out[:, b, c * BANK:(c + 1) * BANK],
                                           start=(b == 0), stop=(b == 2 * DB - 1))
            ins.then_inc(summed, 1)
            pe.wait_ge(x1_ready, 1)
            for b in range(DB):
                ins = nc.tensor.transpose(psum[3][:, b * DEC:(b + 1) * DEC], x1[:, b * P:(b + 1) * P], ident[0:DEC, 0:DEC])
            ins.then_inc(x1_turned, 1)
            pe.wait_ge(hT_ready, 1)
            for c in range(2):
                for b in range(DB):
                    ins = nc.tensor.matmul(psum[4 + c][0:DEC, :], hT[:, b, :], w_mq[:, b, c * BANK:(c + 1) * BANK],
                                           start=(b == 0), stop=(b == DB - 1))
            ins.then_inc(projected, 1)

        @block.scalar
        def _(act):
            act.wait_ge(x1_ready, 1)
            nc.scalar.activation(junk[:], x1[:], ACT.Square, accum_out=ms[:]).then_inc(ms_ready, 1)

        @block.gpsimd
        def _(pool):
            nc.gpsimd.memset(half[:], -0.5)
            pool.wait_ge(ms_ready, 1)
            nc.gpsimd.tensor_scalar(ms[:], ms[:], 1.0 / D, EPS, ALU.mult, ALU.add)
            pool.drain()
            nc.gpsimd.tensor_tensor(rstd[:], ms[:], half[:], ALU.pow).then_inc(rstd_ready, 1)

        @block.vector
        def _(dve):
            dve.wait_ge(turned, 1)
            for i, gain in enumerate((shared["gain_att"], shared["gain_ssd"])):
                ins = nc.vector.tensor_tensor(mT[:, i * DB:(i + 1) * DB, :],
                                              psum[0][:, i * DB * DEC:(i + 1) * DB * DEC].rearrange("p (b t) -> p b t", b=DB),
                                              gain[:, :, None].broadcast_to([P, DB, DEC]), ALU.mult)
            ins.then_inc(mT_ready, 1)
            dve.wait_ge(summed, 1)
            for c in range(2):
                cols = slice(c * BANK, (c + 1) * BANK)
                ins = nc.vector.tensor_tensor(x1[:, cols], psum[1 + c][0:DEC, :], x[:, cols], ALU.add)
            ins.then_inc(x1_ready, 1)
            dve.wait_ge(x1_turned, 1)
            nc.vector.tensor_tensor(hT[:], psum[3][:, 0:DB * DEC].rearrange("p (b t) -> p b t", b=DB),
                                    shared["gain_read"][:, :, None].broadcast_to([P, DB, DEC]), ALU.mult).then_inc(hT_ready, 1)
            dve.wait_ge(rstd_ready, 1)
            dve.wait_ge(projected, 1)
            for c in range(2):
                ins = nc.vector.tensor_scalar(q[:, c * BANK:(c + 1) * BANK], psum[4 + c][0:DEC, :], rstd[:], MEM_HD ** -0.5, ALU.mult, ALU.mult)
            ins.then_inc(q_ready, 1)


def memory_read_sample(nc, io, psum, shared, w_mo, x1):
    ident = shared["ident"]
    ROWS = DEC * MEM_HEADS
    with Stage(nc) as stage:
        sb, sem = stage.buffer, stage.semaphore

        k = sb("rs_k", [P, 2, 2, D])
        v = sb("rs_v", [P, 3, 2, D])
        q = sb("rs_q", [P, DEC, D])
        prod = sb("rs_prod", [P, 2, 2 * MEM_HEADS, MEM_HD])
        sT = sb("rs_sT", [P, 2, DEC, MEM_HEADS])
        p = sb("rs_p", [ROWS, N_MEM])
        ntop, total = sb("rs_ntop", [ROWS, 1]), sb("rs_total", [ROWS, 1])
        pT = sb("rs_pT", [P, 2, ROWS])
        oT = sb("rs_oT", [P, DB, DEC])
        xn, gain_ffn = sb("rs_xn", [DEC, D]), sb("rs_gain_ffn", [DEC, D])
        ms, rstd, half = sb("rs_ms", [DEC, 1]), sb("rs_rstd", [DEC, 1]), sb("rs_half", [DEC, 1])
        blank = sb("rs_blank", [P - DEC, D])
        gain_in, blank_ready, ms_ready, rstd_ready, xn_ready = (sem("rs_" + n) for n in ("gain_in", "blank_ready", "ms_ready", "rstd_ready", "xn_ready"))
        q_in = sem("rs_q_in")
        k_in = [sem(f"rs_k_in{i}") for i in range(2)]
        v_in = [sem(f"rs_v_in{i}") for i in range(3)]
        multiplied, reduced = sem("rs_multiplied"), sem("rs_reduced")
        s_turned, ntop_ready, p_exp, p_ready, p_turned, pT_ready = (
            sem("rs_" + n) for n in ("s_turned", "ntop_ready", "p_exp", "p_ready", "p_turned", "pT_ready"))
        valued, oT_ready, projected, x2_ready, stored = (sem("rs_" + n) for n in ("valued", "oT_ready", "projected", "x2_ready", "stored"))
        block = stage.block()

        @block.sync
        def _(sp):
            sp.dma_start(gain_ffn[:], io["norm_ffn_w"].broadcast_to([DEC, D])).then_inc(gain_in, 16)
            for b in range(DEC):
                sp.dma_start(q[:, b, :], io["rows"][b:b + 1, :].broadcast_to([P, D])).then_inc(q_in, 16)
            for b in range(DEC):
                if b >= 2:
                    sp.wait_ge(multiplied, b - 1)
                sp.dma_start(k[:, b % 2], io["cache_mem_k"][b].rearrange("(m p) n -> p m n", p=P)).then_inc(k_in[b % 2], 16)
            for b in range(DEC):
                if b >= 3:
                    sp.wait_ge(valued, b - 2)
                sp.dma_start(v[:, b % 3], io["cache_mem_v"][b].rearrange("(m p) n -> p m n", p=P)).then_inc(v_in[b % 3], 16)
            sp.wait_ge(x2_ready, 1)
            sp.dma_start(io["x2"][SEQ:TOKENS, :], x1[:]).then_inc(stored, 16)
            sp.wait_ge(xn_ready, 1)
            sp.dma_start(io["xn"][SEQ:TOKENS, :], xn[:]).then_inc(stored, 16)
            sp.wait_ge(blank_ready, 1)
            for name in ("x2", "xn"):
                sp.dma_start(io[name][TOKENS:SEQ + P, :], blank[:]).then_inc(stored, 16)
            sp.wait_ge(stored, 64)

        @block.tensor
        def _(pe):
            pe.wait_ge(reduced, DEC)
            for m in range(2):
                ins = nc.tensor.transpose(psum[0][0:ROWS, m * P:(m + 1) * P], sT[:, m].rearrange("p b h -> p (b h)"), ident[:])
            ins.then_inc(s_turned, 1)
            pe.wait_ge(p_ready, 1)
            for m in range(2):
                ins = nc.tensor.transpose(psum[1][:, m * ROWS:(m + 1) * ROWS], p[:, m * P:(m + 1) * P], ident[0:ROWS, 0:ROWS])
            ins.then_inc(p_turned, 1)
            pe.wait_ge(pT_ready, 1)
            for b in range(DEC):
                pe.wait_ge(v_in[b % 3], 16 * (b // 3 + 1))
                for d in range(DB):
                    row = b * MEM_HEADS + d // 2
                    for m in range(2):
                        ins = nc.tensor.matmul(psum[2][:, d * DEC + b:d * DEC + b + 1], v[:, b % 3, m, d * P:(d + 1) * P],
                                               pT[:, m, row:row + 1], start=(m == 0), stop=(m == 1))
                ins.then_inc(valued, 1)
            pe.wait_ge(oT_ready, 1)
            for c in range(2):
                for b in range(DB):
                    ins = nc.tensor.matmul(psum[3 + c][0:DEC, :], oT[:, b, :], w_mo[:, b, c * BANK:(c + 1) * BANK],
                                           start=(b == 0), stop=(b == DB - 1))
            ins.then_inc(projected, 1)

        @block.scalar
        def _(act):
            act.wait_ge(ntop_ready, 1)
            nc.scalar.activation(p[:], psum[0][0:ROWS, 0:N_MEM], ACT.Exp, bias=ntop[:], accum_out=total[:])
            act.drain()
            act.sem_inc(p_exp, 1)
            act.wait_ge(x2_ready, 1)
            nc.scalar.activation(xn[:], x1[:], ACT.Square, accum_out=ms[:]).then_inc(ms_ready, 1)

        @block.gpsimd
        def _(pool):
            nc.gpsimd.memset(blank[:], 0.0).then_inc(blank_ready, 1)
            nc.gpsimd.memset(half[:], -0.5)
            pool.wait_ge(ms_ready, 1)
            nc.gpsimd.tensor_scalar(ms[:], ms[:], 1.0 / D, EPS, ALU.mult, ALU.add)
            pool.drain()
            nc.gpsimd.tensor_tensor(rstd[:], ms[:], half[:], ALU.pow).then_inc(rstd_ready, 1)

        @block.vector
        def _(dve):
            dve.wait_ge(q_in, 16 * DEC)
            for b in range(DEC):
                dve.wait_ge(k_in[b % 2], 16 * (b // 2 + 1))
                nc.vector.tensor_tensor(prod[:, b % 2].rearrange("p (m h) d -> p m (h d)", m=2), k[:, b % 2],
                                        q[:, b, None, :].broadcast_to([P, 2, D]), ALU.mult).then_inc(multiplied, 1)
                dve.drain()
                nc.vector.tensor_reduce(sT[:, :, b, :], prod[:, b % 2].rearrange("p (m h) d -> p m h d", m=2), AX.X, ALU.add).then_inc(reduced, 1)
            dve.wait_ge(s_turned, 1)
            nc.vector.tensor_reduce(ntop[:], psum[0][0:ROWS, 0:N_MEM], AX.X, ALU.max)
            dve.drain()
            nc.vector.tensor_scalar(ntop[:], ntop[:], -1.0, None, ALU.mult).then_inc(ntop_ready, 1)
            dve.wait_ge(p_exp, 1)
            nc.vector.reciprocal(total[:], total[:])
            dve.drain()
            nc.vector.tensor_scalar(p[:], p[:], total[:], None, ALU.mult).then_inc(p_ready, 1)
            dve.wait_ge(p_turned, 1)
            nc.vector.tensor_copy(pT[:], psum[1][:, 0:2 * ROWS].rearrange("p (m r) -> p m r", m=2)).then_inc(pT_ready, 1)
            dve.wait_ge(valued, DEC)
            nc.vector.tensor_copy(oT[:], psum[2][:, 0:DB * DEC].rearrange("p (d b) -> p d b", d=DB)).then_inc(oT_ready, 1)
            dve.wait_ge(projected, 1)
            for c in range(2):
                cols = slice(c * BANK, (c + 1) * BANK)
                ins = nc.vector.tensor_tensor(x1[:, cols], psum[3 + c][0:DEC, :], x1[:, cols], ALU.add)
            ins.then_inc(x2_ready, 1)
            dve.wait_ge(gain_in, 16)
            dve.wait_ge(rstd_ready, 1)
            nc.vector.scalar_tensor_tensor(xn[:], x1[:], rstd[:], gain_ffn[:], ALU.mult, ALU.mult).then_inc(xn_ready, 1)


def expert_mix(nc, io, psum, shared, idx, gate):
    ident = shared["ident"]
    PAIRS = PEER_HEADS // 2
    PER = 2 * TOPK
    RING = 8
    USES = PER // RING
    with Stage(nc) as stage:
        sb, sem, event = stage.buffer, stage.semaphore, stage.event
        w_pq = sb("w_pq", [P, DB, 2 * D])
        keysT = sb("ex_keysT", [P, 2 * PEER_HEADS * N_KEYS])
        rows = sb("ex_rows", [P, D])
        x_next = sb("ex_x_next", [P, D])
        x_cur = sb("ex_x_cur", [P, D])
        xT = sb("ex_xT", [P, DB, P])
        final_gain = sb("ex_final_gain", [P, D])
        total = sb("ex_total", [P, D])
        u_ring = sb("ex_u_ring", [P, RING, D])
        v_ring = sb("ex_v_ring", [P, RING, D])
        diag = sb("ex_diag", [P, 2, TOPK, P])
        slot_idx = sb("ex_slot_idx", [P, 2, TOPK], U32)
        slot_gate = sb("ex_slot_gate", [P, 2, TOPK])
        dots, weight = sb("ex_dots", [P, 2, TOPK]), sb("ex_weight", [P, 2, TOPK])
        q, qT = sb("ex_q", [P, 2 * P]), sb("ex_qT", [P, 2, P])
        sub, sub_less = sb("ex_sub", [P, 2, N_KEYS]), sb("ex_sub_less", [P, 2, N_KEYS])
        top, top_at, top_atf = sb("ex_top", [P, 2, TOPK]), sb("ex_top_at", [P, 2, TOPK], U32), sb("ex_top_atf", [P, 2, TOPK])
        cand, cand_less = sb("ex_cand", [P, TOPK * TOPK]), sb("ex_cand_less", [P, TOPK * TOPK])
        best, best_at = sb("ex_best", [P, TOPK]), sb("ex_best_at", [P, TOPK], U32)
        halves, halvesf = sb("ex_halves", [P, 2, TOPK], U32), sb("ex_halvesf", [P, 2, TOPK])
        match = sb("ex_match", [P, 2 * TOPK, TOPK])
        picked, joined = sb("ex_picked", [P, 2, TOPK]), sb("ex_joined", [P, TOPK])
        count16 = sb("ex_count16", [P, TOPK])
        nbest, esum = sb("ex_nbest", [P, 1]), sb("ex_esum", [P, 1])
        ms, root, rstd, err = (sb("ex_" + n, [P, 1]) for n in ("ms", "root", "rstd", "err"))
        squares = sb("ex_squares", [P, D])
        raw_keys = u_ring[:, 0:2, :].rearrange("p a (b d) -> p (a b) d", d=P)

        route_fills = Fills(sem, "route", [("q0", 0), ("qT0", 1), ("sub0", 2), ("q1", 0), ("qT1", 1), ("sub1", 2)])
        prep_fills = Fills(sem, "prep", [("xT0", 3), ("xT1", 4)])
        loaded, keys_in, keys_turned, keys_ready, w_in = (sem("ex_" + n) for n in ("loaded", "keys_in", "keys_turned", "keys_ready", "w_in"))
        x_in, x_turned, x_moved = event("ex_x_in", 1, 16), event("ex_x_turned"), event("ex_x_moved")
        rows_in, rows_used = event("ex_rows_in", 1, 16), event("ex_rows_used")
        xT_ready = event("ex_xT_ready")
        mix_over, mix_read = event("ex_mix_over"), event("ex_mix_read")
        var_ready, root_ready, out_ready, stored = event("ex_var_ready"), event("ex_root_ready"), event("ex_out_ready"), event("ex_stored", 1, 16)
        ms_ready = event("ex_ms_ready")
        routed_pe = event("ex_routed_pe", 2)
        q_ready, qT_ready, sub_ready = event("ex_q_ready", 2), event("ex_qT_ready", 2), event("ex_sub_ready", 2)
        best_ready, exp_ready = event("ex_best_ready", 2), event("ex_exp_ready", 2)
        idx_ready = event("ex_idx_ready", 2)
        dots_ready, gelu_ready, weight_ready, diag_ready, mixed = (
            event("ex_" + n, 2) for n in ("dots_ready", "gelu_ready", "weight_ready", "diag_ready", "mixed"))
        u_in = [sem(f"ex_u_in{r}") for r in range(RING)]
        v_in = [sem(f"ex_v_in{r}") for r in range(RING)]
        u_used, v_used = sem("ex_u_used"), sem("ex_v_used")
        gathers = sem("ex_gathers")
        block = stage.block()

        @block.sync
        def _(sp):
            def load_x(tile):
                sp.wait_ge(x_turned.sem, x_turned.last(tile))
                sp.wait_ge(x_moved.sem, x_moved.last(tile))
                sp.dma_start(x_next[:], io["xn"][bass.ds(tile * P, P), :]).then_inc(x_in.sem, 16)

            def load_rows(tile):
                sp.wait_ge(rows_used.sem, rows_used.last(tile))
                sp.dma_start(rows[:], io["x2"][bass.ds(tile * P, P), :]).then_inc(rows_in.sem, 16)

            for e in (x_in, rows_in, stored):
                sp.sem_inc(e.sem, 16)
            sp.dma_start(raw_keys, io["peer_keys"].rearrange("h k d -> k h d")).then_inc(keys_in, 16)
            load_x(0)
            sp.dma_start(w_pq[:], io["peer_wq"].rearrange("(b p) n -> p b n", p=P)).then_inc(w_in, 16)
            sp.dma_start(final_gain[:], io["final_norm_w"].broadcast_to([P, D])).then_inc(loaded, 16)
            load_rows(0)
            with sp.Fori(0, TILES) as t:
                load_x(t + 1)
                load_rows(t + 1)
                sp.wait_ge(out_ready.sem, out_ready.this(t))
                sp.dma_start(io["y_prompt"][bass.ds(t * P, P), :], total[:]).then_inc(stored.sem, 16)
            sp.wait_ge(stored.sem, stored.this(TILES - 1))
            sp.wait_ge(rows_in.sem, rows_in.this(TILES))

        @block.gpsimd
        def _(pool):
            def gather(table, ring, arrived, used, n, half, s):
                j = half * TOPK + s
                pool.wait_ge(used, n * PER + (j + 1))
                pool.sem_inc(gathers, 1)
                nc.gpsimd.indirect_dma_start(
                    out=ring[:, j % RING, :], out_offset=None, in_=io[table],
                    in_offset=bass.IndirectOffsetOnAxis(ap=slot_idx[:, half, s:s + 1], axis=0),
                ).then_inc(arrived[j % RING], 16)

            def pair(n):
                for half in range(2):
                    pool.wait_ge(idx_ready.sem, idx_ready.this(n, half + 1))
                    pool.sem_inc(gathers, 1)
                    for s in range(TOPK):
                        gather("peer_u", u_ring, u_in, u_used, n, half, s)
                        if half:
                            gather("peer_v", v_ring, v_in, v_used, n, 0, s)
                for s in range(TOPK):
                    gather("peer_v", v_ring, v_in, v_used, n, 1, s)

            nc.gpsimd.iota(count16[:], [[1, TOPK]], base=0, channel_multiplier=0, allow_small_or_imprecise_dtypes=True)
            pool.drain()
            pool.sem_inc(loaded, 16)
            pool.wait_ge(keys_ready, 2)
            with pool.Fori(0, TILES) as t:
                with pool.Fori(0, PAIRS) as i:
                    pair(t * PAIRS + i)

        @block.tensor
        def _(pe):
            def prepare(tile):
                pe.wait_ge(x_in.sem, x_in.this(tile))
                for h in range(2):
                    f = f"xT{h}"
                    bank = prep_fills.bank(f)
                    pe.wait_ge(prep_fills.free[bank], prep_fills.at(f, tile))
                    for j in range(4):
                        ins = nc.tensor.transpose(psum[bank][:, j * P:(j + 1) * P], x_next[:, (4 * h + j) * P:(4 * h + j + 1) * P], ident[:])
                    ins.then_inc(prep_fills.full[bank], 1)
                pe.drain()
                pe.sem_inc(x_turned.sem, 1)

            def route(m, tile, head, half):
                def begin(name):
                    pe.wait_ge(route_fills.free[route_fills.bank(name)], route_fills.at(name, m))
                    return psum[route_fills.bank(name)], route_fills.full[route_fills.bank(name)]

                out, full = begin(f"q{half}")
                if half == 0:
                    pe.wait_ge(xT_ready.sem, xT_ready.this(tile))
                for b in range(DB):
                    ins = nc.tensor.matmul(out[:, 0:2 * P], xT[:, b, :], w_pq[:, b, bass.ds(head * 2 * P, 2 * P)], start=(b == 0), stop=(b == DB - 1))
                ins.then_inc(full, 1)
                pe.wait_ge(q_ready.sem, q_ready.this(m, half + 1))
                out, full = begin(f"qT{half}")
                for p in range(2):
                    ins = nc.tensor.transpose(out[:, p * P:(p + 1) * P], q[:, p * P:(p + 1) * P], ident[:])
                ins.then_inc(full, 1)
                pe.wait_ge(qT_ready.sem, qT_ready.this(m, half + 1))
                out, full = begin(f"sub{half}")
                for p in range(2):
                    ins = nc.tensor.matmul(out[:, p * P:(p + 1) * P], qT[:, p, :], keysT[:, bass.ds((head * 2 + p) * P, P)], start=True, stop=True)
                ins.then_inc(full, 1)
                pe.drain()
                pe.sem_inc(routed_pe.sem, 1)

            def mix(n, half):
                pe.wait_ge(diag_ready.sem, diag_ready.this(n, half + 1))
                for s in range(TOPK):
                    j = half * TOPK + s
                    pe.wait_ge(v_in[j % RING], 16 * (n * USES + (j // RING + 1)))
                    for c in range(2):
                        ins = nc.tensor.matmul(psum[6 + c][:], diag[:, half, s, :], v_ring[:, j % RING, c * BANK:(c + 1) * BANK],
                                               start=False, stop=False, skip_group_check=True)
                    ins.then_inc(v_used, 1)
                pe.drain()
                pe.sem_inc(mixed.sem, 1)

            for f in (route_fills, prep_fills):
                f.prime(pe)
            for e in (x_turned, rows_used, routed_pe, mixed, mix_over):
                pe.sem_inc(e.sem, 1)
            pe.sem_inc(v_used, RING)
            pe.wait_ge(keys_in, 16)
            for n in range(4):
                for j in range(4):
                    ins = nc.tensor.transpose(psum[4 + n][:, j * P:(j + 1) * P], raw_keys[:, 4 * n + j, :], ident[:])
                ins.then_inc(keys_turned, 1)
            pe.wait_ge(keys_ready, 2)
            prepare(0)
            pe.wait_ge(w_in, 16)
            with pe.Fori(0, PAIRS) as i:
                for half in range(2):
                    route(i, 0, i * 2 + half, half)
            with pe.Fori(0, TILES) as t:
                pe.wait_ge(rows_in.sem, rows_in.this(t))
                pe.wait_ge(mix_read.sem, mix_read.last(t))
                for c in range(2):
                    nc.tensor.matmul(psum[6 + c][:], ident[:], rows[:, c * BANK:(c + 1) * BANK], start=True, stop=False, skip_group_check=True)
                pe.drain()
                pe.sem_inc(rows_used.sem, 1)
                prepare(t + 1)
                with pe.Fori(0, PAIRS) as i:
                    n = t * PAIRS + i
                    for half in range(2):
                        route(n + PAIRS, t + 1, i * 2 + half, half)
                        mix(n, half)
                pe.drain()
                pe.sem_inc(mix_over.sem, 1)

        @block.scalar
        def _(act):
            def prepare(tile):
                act.wait_ge(routed_pe.sem, routed_pe.last(tile * PAIRS))
                for h in range(2):
                    bank = prep_fills.bank(f"xT{h}")
                    act.wait_ge(prep_fills.full[bank], prep_fills.at(f"xT{h}", tile))
                    nc.scalar.copy(xT[:, 4 * h:4 * h + 4, :], psum[bank][:].rearrange("p (b t) -> p b t", b=4)).then_inc(prep_fills.free[bank], 1)
                act.drain()
                act.sem_inc(xT_ready.sem, 1)

            def queries(m, half):
                for name, dst, ready in ((f"q{half}", q[:], q_ready), (f"qT{half}", qT[:].rearrange("p a t -> p (a t)"), qT_ready)):
                    bank = route_fills.bank(name)
                    act.wait_ge(route_fills.full[bank], route_fills.at(name, m))
                    nc.scalar.copy(dst, psum[bank][:, 0:2 * P]).then_inc(route_fills.free[bank], 1)
                    act.drain()
                    act.sem_inc(ready.sem, 1)

            def exponentials(m, half):
                act.wait_ge(best_ready.sem, best_ready.this(m, half + 1))
                nc.scalar.activation(best[:], best[:], ACT.Exp, bias=nbest[:], accum_out=esum[:])
                act.drain()
                act.sem_inc(exp_ready.sem, 1)

            def weights(n, half):
                act.wait_ge(dots_ready.sem, dots_ready.this(n, half + 1))
                nc.scalar.activation(dots[:, half, :], dots[:, half, :], ACT.Gelu)
                act.drain()
                act.sem_inc(gelu_ready.sem, 1)
                act.wait_ge(weight_ready.sem, weight_ready.this(n, half + 1))
                act.wait_ge(mixed.sem, n * 2 + half + 1)
                for s in range(TOPK):
                    nc.scalar.activation(diag[:, half, s, :], ident[:], ACT.Copy, scale=weight[:, half, s:s + 1])
                act.drain()
                act.sem_inc(diag_ready.sem, 1)

            for e in (xT_ready, q_ready, qT_ready, exp_ready, gelu_ready, diag_ready, mix_read, ms_ready, root_ready):
                act.sem_inc(e.sem, 1)
            prepare(0)
            with act.Fori(0, PAIRS) as i:
                for half in range(2):
                    queries(i, half)
                    exponentials(i, half)
            with act.Fori(0, TILES) as t:
                prepare(t + 1)
                with act.Fori(0, PAIRS) as i:
                    n = t * PAIRS + i
                    for half in range(2):
                        queries(n + PAIRS, half)
                        weights(n, half)
                        exponentials(n + PAIRS, half)
                act.wait_ge(mix_over.sem, mix_over.this(t))
                act.wait_ge(stored.sem, stored.last(t))
                for c in range(2):
                    nc.scalar.copy(total[:, c * BANK:(c + 1) * BANK], psum[6 + c][:])
                act.drain()
                act.sem_inc(mix_read.sem, 1)
                nc.scalar.activation(squares[:], total[:], ACT.Square, accum_out=ms[:])
                act.drain()
                act.sem_inc(ms_ready.sem, 1)
                act.wait_ge(var_ready.sem, var_ready.this(t))
                nc.scalar.activation(root[:], ms[:], ACT.Sqrt)
                act.drain()
                act.sem_inc(root_ready.sem, 1)

        @block.vector
        def _(dve):
            def link(ins):
                dve.drain()

            def top16(values, less, out, at):
                link(nc.vector.max(out[:, 0:8], values))
                nc.vector.max_index(at[:, 0:8], out[:, 0:8], values)
                link(nc.vector.match_replace(less, out[:, 0:8], values, FAR))
                link(nc.vector.max(out[:, 8:16], less))
                link(nc.vector.max_index(at[:, 8:16], out[:, 8:16], less))

            def route(m, half, at):
                name = f"sub{half}"
                bank = route_fills.bank(name)
                dve.wait_ge(route_fills.full[bank], route_fills.at(name, m))
                link(nc.vector.tensor_copy(sub[:], psum[bank][:, 0:2 * P].rearrange("p (a k) -> p a k", a=2)).then_inc(route_fills.free[bank], 1))
                for a in range(2):
                    top16(sub[:, a, :], sub_less[:, a, :], top[:, a, :], top_at[:, a, :])
                nc.vector.tensor_copy(top_atf[:], top_at[:])
                link(nc.vector.tensor_tensor(cand[:].rearrange("p (i j) -> p i j", i=TOPK), top[:, 0, :, None].broadcast_to([P, TOPK, TOPK]),
                                             top[:, 1, None, :].broadcast_to([P, TOPK, TOPK]), ALU.add))
                top16(cand[:], cand_less[:], best, best_at)
                link(nc.vector.tensor_scalar(nbest[:], best[:, 0:1], -1.0, None, ALU.mult))
                dve.sem_inc(best_ready.sem, 1)
                nc.vector.tensor_scalar(halves[:, 0, :], best_at[:], 4, None, ALU.logical_shift_right)
                link(nc.vector.tensor_scalar(halves[:, 1, :], best_at[:], 15, None, ALU.bitwise_and))
                link(nc.vector.tensor_copy(halvesf[:], halves[:]))
                link(nc.vector.tensor_tensor(match[:], halvesf[:].rearrange("p a k -> p (a k)")[:, :, None].broadcast_to([P, 2 * TOPK, TOPK]),
                                             count16[:, None, :].broadcast_to([P, 2 * TOPK, TOPK]), ALU.is_equal))
                for a in range(2):
                    rows_a = slice(a * TOPK, (a + 1) * TOPK)
                    ins = nc.vector.tensor_tensor(match[:, rows_a, :], match[:, rows_a, :], top_atf[:, a, None, :].broadcast_to([P, TOPK, TOPK]), ALU.mult)
                link(ins)
                link(nc.vector.tensor_reduce(picked[:].rearrange("p a k -> p (a k)"), match[:], AX.X, ALU.add))
                link(nc.vector.scalar_tensor_tensor(joined[:], picked[:, 0, :], float(N_KEYS), picked[:, 1, :], ALU.mult, ALU.add))
                nc.vector.tensor_copy(idx[:, bass.ds(at, TOPK)], joined[:])
                dve.wait_ge(exp_ready.sem, exp_ready.this(m, half + 1))
                link(nc.vector.reciprocal(esum[:], esum[:]))
                link(nc.vector.tensor_scalar(gate[:, bass.ds(at, TOPK)], best[:], esum[:], None, ALU.mult))

            def take(n, half, at):
                nc.vector.tensor_copy(slot_idx[:, half, :], idx[:, bass.ds(at, TOPK)])
                link(nc.vector.tensor_copy(slot_gate[:, half, :], gate[:, bass.ds(at, TOPK)]))
                dve.sem_inc(idx_ready.sem, 1)

            def products(n, half):
                for s in range(TOPK):
                    j = half * TOPK + s
                    dve.wait_ge(u_in[j % RING], 16 * (n * USES + (j // RING + 1)))
                    nc.vector.tensor_tensor_reduce(u_ring[:, j % RING, :], u_ring[:, j % RING, :], x_cur[:], 1.0, 0.0, ALU.mult, ALU.add,
                                                   dots[:, half, s:s + 1]).then_inc(u_used, 1)
                dve.drain()
                dve.sem_inc(dots_ready.sem, 1)
                dve.wait_ge(gelu_ready.sem, gelu_ready.this(n, half + 1))
                nc.vector.tensor_tensor(weight[:, half, :], dots[:, half, :], slot_gate[:, half, :], ALU.mult)
                dve.drain()
                dve.sem_inc(weight_ready.sem, 1)

            for e in (x_moved, sub_ready, best_ready, idx_ready, dots_ready, weight_ready, var_ready, out_ready):
                dve.sem_inc(e.sem, 1)
            dve.sem_inc(u_used, RING)
            for n in range(4):
                dve.wait_ge(keys_turned, n + 1)
                ins = nc.vector.tensor_copy(keysT[:, n * BANK:(n + 1) * BANK], psum[4 + n][:])
            dve.drain()
            dve.sem_inc(keys_ready, 2)
            dve.wait_ge(loaded, 32)
            with dve.Fori(0, PAIRS) as i:
                for half in range(2):
                    route(i, half, (i * 2 + half) * TOPK)
            take(0, 0, 0)
            take(0, 1, TOPK)
            with dve.Fori(0, TILES) as t:
                dve.wait_ge(x_in.sem, x_in.this(t))
                nc.vector.tensor_copy(x_cur[:], x_next[:])
                dve.drain()
                dve.sem_inc(x_moved.sem, 1)
                with dve.Fori(0, PAIRS) as i:
                    n = t * PAIRS + i
                    routed = ((t + 1) * PEER_HEADS + i * 2) * TOPK
                    taken = (t * PEER_HEADS + i * 2 + 2) * TOPK
                    products(n, 0)
                    route(n + PAIRS, 0, routed)
                    products(n, 1)
                    route(n + PAIRS, 1, routed + TOPK)
                    for half in range(2):
                        dve.wait_ge(mixed.sem, mixed.this(n, half + 1))
                        take(n + 1, half, taken + half * TOPK)
                dve.wait_ge(ms_ready.sem, ms_ready.this(t))
                link(nc.vector.tensor_scalar(ms[:], ms[:], 1.0 / D, EPS, ALU.mult, ALU.add))
                dve.sem_inc(var_ready.sem, 1)
                dve.wait_ge(root_ready.sem, root_ready.this(t))
                link(nc.vector.reciprocal(rstd[:], root[:]))
                link(nc.vector.tensor_tensor(err[:], rstd[:], rstd[:], ALU.mult))
                link(nc.vector.tensor_tensor(err[:], err[:], ms[:], ALU.mult))
                link(nc.vector.tensor_scalar(err[:], err[:], -0.5, 1.5, ALU.mult, ALU.add))
                link(nc.vector.tensor_tensor(rstd[:], rstd[:], err[:], ALU.mult))
                nc.vector.scalar_tensor_tensor(total[:], total[:], rstd[:], final_gain[:], ALU.mult, ALU.mult)
                dve.drain()
                dve.sem_inc(out_ready.sem, 1)


def expert_mix_sample(nc, io, psum, shared, idx, gate):
    ident = shared["ident"]
    at = TILES * SLOTS
    with Stage(nc) as stage:
        sb, sem = stage.buffer, stage.semaphore
        x = sb("es_x", [P, DEC, D])
        u, v = sb("es_u", [P, DEC, D]), sb("es_v", [P, DEC, D])
        rows, gain = sb("es_rows", [DEC, D]), sb("es_gain", [DEC, D])
        junk = sb("es_junk", [DEC, D])
        idxf, idxT, gateT = sb("es_idxf", [DEC, SLOTS]), sb("es_idxT", [P, DEC], U32), sb("es_gateT", [P, DEC])
        dots, weight = sb("es_dots", [P, DEC]), sb("es_weight", [P, DEC])
        own = sb("es_own", [P, DEC, DEC])
        ms, rstd, half = sb("es_ms", [DEC, 1]), sb("es_rstd", [DEC, 1]), sb("es_half", [DEC, 1])
        loaded, idxf_ready, turned, idxT_ready = (sem("es_" + n) for n in ("loaded", "idxf_ready", "turned", "idxT_ready"))
        u_in = [sem(f"es_u_in{b}") for b in range(DEC)]
        v_in = [sem(f"es_v_in{b}") for b in range(DEC)]
        dots_ready, gelu_ready, own_ready, mixed, sum_ready, ms_ready, rstd_ready, out_ready, stored = (
            sem("es_" + n) for n in ("dots_ready", "gelu_ready", "own_ready", "mixed", "sum_ready", "ms_ready", "rstd_ready", "out_ready", "stored"))
        block = stage.block()

        @block.sync
        def _(sp):
            for b in range(DEC):
                sp.dma_start(x[:, b, :], io["xn"][SEQ + b:SEQ + b + 1, :].broadcast_to([P, D])).then_inc(loaded, 16)
            sp.dma_start(rows[:], io["x2"][SEQ:TOKENS, :]).then_inc(loaded, 16)
            sp.dma_start(gain[:], io["final_norm_w"].broadcast_to([DEC, D])).then_inc(loaded, 16)
            sp.wait_ge(out_ready, 1)
            sp.dma_start(io["y_sample"], rows[:]).then_inc(stored, 16)
            sp.wait_ge(stored, 16)

        @block.gpsimd
        def _(pool):
            nc.gpsimd.memset(half[:], -0.5)
            pool.wait_ge(idxT_ready, 1)
            for b in range(DEC):
                for table, rows_in, arrived in (("peer_u", u, u_in), ("peer_v", v, v_in)):
                    nc.gpsimd.indirect_dma_start(out=rows_in[:, b, :], out_offset=None, in_=io[table],
                                                 in_offset=bass.IndirectOffsetOnAxis(ap=idxT[:, b:b + 1], axis=0)).then_inc(arrived[b], 16)
            pool.wait_ge(ms_ready, 1)
            nc.gpsimd.tensor_scalar(ms[:], ms[:], 1.0 / D, EPS, ALU.mult, ALU.add)
            pool.drain()
            nc.gpsimd.tensor_tensor(rstd[:], ms[:], half[:], ALU.pow).then_inc(rstd_ready, 1)

        @block.tensor
        def _(pe):
            pe.wait_ge(idxf_ready, 1)
            nc.tensor.transpose(psum[0][:, 0:DEC], idxf[:], ident[0:DEC, 0:DEC])
            nc.tensor.transpose(psum[0][:, 32:32 + DEC], gate[0:DEC, at:at + SLOTS], ident[0:DEC, 0:DEC]).then_inc(turned, 1)
            pe.wait_ge(own_ready, 1)
            for b in range(DEC):
                pe.wait_ge(v_in[b], 16)
                for c in range(2):
                    ins = nc.tensor.matmul(psum[1 + c][0:DEC, :], own[:, b, :], v[:, b, c * BANK:(c + 1) * BANK], start=(b == 0), stop=(b == DEC - 1))
            ins.then_inc(mixed, 1)

        @block.scalar
        def _(act):
            act.wait_ge(dots_ready, 1)
            nc.scalar.activation(dots[:], dots[:], ACT.Gelu).then_inc(gelu_ready, 1)
            act.wait_ge(sum_ready, 1)
            nc.scalar.activation(junk[:], rows[:], ACT.Square, accum_out=ms[:]).then_inc(ms_ready, 1)

        @block.vector
        def _(dve):
            nc.vector.memset(own[:], 0.0)
            nc.vector.tensor_copy(idxf[:], idx[0:DEC, at:at + SLOTS]).then_inc(idxf_ready, 1)
            dve.wait_ge(turned, 1)
            nc.vector.tensor_copy(gateT[:], psum[0][:, 32:32 + DEC])
            nc.vector.tensor_copy(idxT[:], psum[0][:, 0:DEC]).then_inc(idxT_ready, 1)
            dve.wait_ge(loaded, 16 * (DEC + 2))
            for b in range(DEC):
                dve.wait_ge(u_in[b], 16)
                nc.vector.tensor_tensor_reduce(u[:, b, :], u[:, b, :], x[:, b, :], 1.0, 0.0, ALU.mult, ALU.add, dots[:, b:b + 1])
            dve.drain()
            dve.sem_inc(dots_ready, 1)
            dve.wait_ge(gelu_ready, 1)
            nc.vector.tensor_tensor(weight[:], dots[:], gateT[:], ALU.mult)
            dve.drain()
            diagonal = bass.AP(own[:].tensor, own[:].offset, [list(own[:].ap[0]), [DEC + 1, DEC]])
            nc.vector.tensor_copy(diagonal, weight[:]).then_inc(own_ready, 1)
            dve.wait_ge(mixed, 1)
            for c in range(2):
                cols = slice(c * BANK, (c + 1) * BANK)
                ins = nc.vector.tensor_tensor(rows[:, cols], psum[1 + c][0:DEC, :], rows[:, cols], ALU.add)
            ins.then_inc(sum_ready, 1)
            dve.wait_ge(rstd_ready, 1)
            nc.vector.scalar_tensor_tensor(rows[:], rows[:], rstd[:], gain[:], ALU.mult, ALU.mult).then_inc(out_ready, 1)


def buckets(distance):
    n = np.arange(distance + 1)
    large = BUCKETS // 2 + (np.log(np.maximum(n, 1).astype(np.float32) / np.float32(BUCKETS // 2)) / np.log(128 / (BUCKETS // 2))
                            * (BUCKETS - BUCKETS // 2)).astype(np.int32)
    return np.where(n < BUCKETS // 2, n, np.minimum(large, BUCKETS - 1))


def constants():
    onehot = np.zeros((BUCKETS + 1, 384), np.float32)
    onehot[BUCKETS] = 1
    onehot[BUCKETS, 127:127 + WINDOW + 1] = 0
    onehot[buckets(WINDOW), 127 + np.arange(WINDOW + 1)] = 1
    s, l = np.arange(P)[:, None], np.arange(P)[None, :]
    tri = (s <= l).astype(np.float32)
    return {
        "ident": np.eye(P, dtype=np.float32),
        "tri": tri,
        "far": ((1 - tri) * np.float32(FAR)).astype(np.float32),
        "onehot": onehot,
        "head_mask": np.kron(np.eye(KV), np.ones((GROUP, 1))).astype(np.float32),
    }


def program(nc, io):
    with ExitStack() as scope:
        def sb(name, shape, dt=F32):
            return scope.enter_context(nc.sbuf_tensor(name, shape, dt))

        psum = [scope.enter_context(nc.psum_tensor(f"psum{b}", [P, BANK], F32)) for b in range(8)]
        shared = {
            "ident": sb("ident", [P, P]), "tri": sb("tri", [P, P]), "far": sb("far", [P, P]), "ones": sb("ones", [P, P]),
            "sinks": sb("sinks", [P, HEADS]), "sink_col": sb("sink_col", [HEADS, 1]),
            "head_mask": sb("head_mask", [HEADS, KV]), "bias_row": sb("bias_row", [HEADS, WINDOW + 1]),
            "gains": sb("gains", [P, 5, DB]), "conv": sb("conv", [P, CONV + 1, CB]),
        }
        for i, name in enumerate(("mix", "att", "ssd", "read", "mem")):
            shared["gain_" + name] = shared["gains"][:, i, :]
        with ExitStack() as attention:
            shared["bias"] = attention.enter_context(nc.sbuf_tensor("bias", [P, HEADS, 2 * P], F32))
            w_qkv = attention.enter_context(nc.sbuf_tensor("w_qkv", [P, DB, 1536], F32))
            setup(nc, io, psum, shared)
            attention_prompt(nc, io, psum, shared, w_qkv)
            attention_sample(nc, io, psum, shared, w_qkv)
        with ExitStack() as states:
            keep = {name: states.enter_context(nc.sbuf_tensor("sample_" + name, [DEC, D], F32)) for name in ("gate", "xs")}
            with ExitStack() as ssd:
                w_zx = ssd.enter_context(nc.sbuf_tensor("w_zx", [P, DB, IN_COLS - 1536], F32))
                ssd_prompt(nc, io, psum, shared, w_zx)
                ssd_sample_inputs(nc, io, psum, shared, w_zx, keep)
            ssd_sample_step(nc, io, shared, keep)
        with ExitStack() as memory:
            mkT = memory.enter_context(nc.sbuf_tensor("mkT", [P, DB, N_MEM], F32))
            mv = memory.enter_context(nc.sbuf_tensor("mv", [P, N_MEM // P, D], F32))
            x1 = memory.enter_context(nc.sbuf_tensor("sample_x1", [DEC, D], F32))
            memory_kv(nc, io, psum, shared, mkT, mv)
            w_mo = memory.enter_context(nc.sbuf_tensor("w_mo", [P, DB, D], F32))
            with ExitStack() as outer:
                w_out = outer.enter_context(nc.sbuf_tensor("w_out", [P, 2 * DB, D], F32))
                w_mq = outer.enter_context(nc.sbuf_tensor("w_mq", [P, DB, D], F32))
                memory_read(nc, io, psum, shared, w_out, w_mq, w_mo, mkT, mv)
                memory_read_sample_query(nc, io, psum, shared, w_out, w_mq, x1)
            memory_read_sample(nc, io, psum, shared, w_mo, x1)
        with ExitStack() as experts:
            n = (TILES + 1) * SLOTS
            idx = experts.enter_context(nc.sbuf_tensor("expert_idx", [P, n + 2 * TOPK], U32))
            gate = experts.enter_context(nc.sbuf_tensor("expert_gate", [P, n + 2 * TOPK], F32))
            expert_mix(nc, io, psum, shared, idx, gate)
            expert_mix_sample(nc, io, psum, shared, idx, gate)


_VIEWS = {
    "x_prompt": (SEQ, D), "x_sample": (DEC, D), "mem_prompt": (N_MEM, D),
    "cache_swa_k": (DEC, WINDOW, KV * HD), "cache_swa_v": (DEC, WINDOW, KV * HD),
    "state_ssm": (DEC * SSD_HEADS, HD, STATE), "state_conv": (DEC, CONV - 1, CONV_DIM),
    "cache_mem_k": (DEC, N_MEM, D), "cache_mem_v": (DEC, N_MEM, D),
    "norm_mix_w": (1, D), "w_in": (D, IN_COLS), "attn_sinks": (1, HEADS), "rel_bias": (BUCKETS, HEADS),
    "attn_norm_w": (1, D), "conv_w": (CONV, CONV_DIM), "conv_b": (1, CONV_DIM), "dt_bias": (1, SSD_HEADS),
    "a_log": (1, SSD_HEADS), "d_skip": (1, SSD_HEADS), "ssd_norm_w": (1, D), "w_out": (2 * D, D),
    "norm_mem_w": (1, D), "mem_norm_w": (1, D), "w_mq": (D, D), "w_mk": (D, D), "w_mv": (D, D), "w_mo": (D, D),
    "norm_ffn_w": (1, D), "peer_wq": (D, 2 * D), "peer_keys": (2 * PEER_HEADS, N_KEYS, P),
    "peer_u": (N_KEYS * N_KEYS, D), "peer_v": (N_KEYS * N_KEYS, D), "final_norm_w": (1, D),
}
_OUTS = {
    "y_prompt": ((SEQ, D), (1, SEQ, D)), "y_sample": ((DEC, D), (DEC, 1, D)),
    "p_swa_k": ((WINDOW, KV * HD), (1, 1, WINDOW, KV, HD)), "p_swa_v": ((WINDOW, KV * HD), (1, 1, WINDOW, KV, HD)),
    "p_ssm": ((SSD_HEADS * HD, STATE), (1, 1, SSD_HEADS, HD, STATE)), "p_conv": ((CONV - 1, CONV_DIM), (1, 1, CONV - 1, CONV_DIM)),
    "p_mem_k": ((N_MEM, D), (1, 1, N_MEM, MEM_HEADS, MEM_HD)), "p_mem_v": ((N_MEM, D), (1, 1, N_MEM, MEM_HEADS, MEM_HD)),
    "s_swa_k": ((DEC, WINDOW, KV * HD), (1, DEC, WINDOW, KV, HD)), "s_swa_v": ((DEC, WINDOW, KV * HD), (1, DEC, WINDOW, KV, HD)),
    "s_ssm": ((DEC * SSD_HEADS, HD, STATE), (1, DEC, SSD_HEADS, HD, STATE)),
    "s_conv": ((DEC, CONV - 1, CONV_DIM), (1, DEC, CONV - 1, CONV_DIM)),
}
_SCRATCH = {
    "mixed": (TOKENS, 2 * D), "bias_line": (HEADS, 384), "rows": (DEC, D), "rows2": (DEC, D), "rows3": (DEC, D),
    "dts": (DEC, SSD_HEADS), "bcs": (DEC, 512), "x2": (SEQ + P, D), "xn": (SEQ + P, D),
}


def kernel(**inputs):
    import concourse.bacc as _bacc
    from concourse.bass_utils import run_bass_kernel_spmd as _run

    nc = _bacc.Bacc("TRN2", target_bir_lowering=False, num_devices=1)
    arrays, io = {}, {}
    laid = {name: np.ascontiguousarray(inputs[name]).reshape(shape) for name, shape in _VIEWS.items()}
    laid.update(constants())
    for name, a in laid.items():
        arrays[f"in_{name}"] = a
        io[name] = nc.dram_tensor(f"in_{name}", a.shape, mybir.dt.from_np(a.dtype), kind="ExternalInput").ap()
    for name, (shape, _) in _OUTS.items():
        io[name] = nc.dram_tensor(f"out_{name}", shape, F32, kind="ExternalOutput").ap()
    for name, shape in _SCRATCH.items():
        io[name] = nc.dram_tensor(f"scratch_{name}", shape, F32, kind="Internal").ap()
    program(nc, io)
    r = _run(nc, [arrays], core_ids=[0])
    return tuple(r.results[0][f"out_{name}"].reshape(shape) for name, (_, shape) in _OUTS.items())
```

```python
from contextlib import ExitStack

import numpy as np

import concourse.bass as bass
from concourse import mybir

F32 = mybir.dt.float32
U32 = mybir.dt.uint32
ALU = mybir.AluOpType
ACT = mybir.ActivationFunctionType
AX = mybir.AxisListType

P = 128
D = 1024
DB = D // P
SEQ = 1024
TILES = SEQ // P
DEC = 8
TOKENS = SEQ + DEC
HEADS, KV, HD = 16, 4, 64
GROUP = HEADS // KV
WINDOW = 128
BUCKETS = 32
SSD_HEADS, SSD_G, STATE = 16, 2, 128
SSD_HPG = SSD_HEADS // SSD_G
CONV = 4
CONV_DIM = 1536
CB = CONV_DIM // P
XBC0 = 2560
DT0 = XBC0 + CONV_DIM
IN_COLS = DT0 + SSD_HEADS
N_MEM = 256
MEM_HEADS, MEM_HD = 4, 256
PEER_HEADS, N_KEYS, TOPK = 8, 128, 16
SLOTS = PEER_HEADS * TOPK
EPS = 1e-6
FAR = -1e30
BANK = 512


class Event:

    def __init__(self, sem, per=1, unit=1):
        self.sem, self.per, self.unit = sem, per, unit

    def last(self, turn):
        return (turn * self.per + 1) * self.unit

    def this(self, turn, k=1):
        return (turn * self.per + 1 + k) * self.unit


class Fills:

    def __init__(self, sem, stage, order):
        self.place, count = {}, {}
        for name, b in order:
            count[b] = count.get(b, 0) + 1
            self.place[name] = (b, count[b])
        self.count = count
        self.full = {b: sem(f"{stage}_bank{b}_full") for b in count}
        self.free = {b: sem(f"{stage}_bank{b}_free") for b in count}

    def bank(self, name):
        return self.place[name][0]

    def at(self, name, turn):
        b, k = self.place[name]
        return turn * self.count[b] + k

    def prime(self, pe):
        for b in self.count:
            pe.sem_inc(self.free[b], 1)


class Stage:

    def __init__(self, nc):
        self.nc, self.scope, self.semaphores = nc, ExitStack(), []

    def __enter__(self):
        return self

    def buffer(self, name, shape, dt=F32):
        return self.scope.enter_context(self.nc.sbuf_tensor(name, shape, dt))

    def semaphore(self, name):
        self.semaphores.append(self.nc.alloc_semaphore(name))
        return self.semaphores[-1]

    def event(self, name, per=1, unit=1):
        return Event(self.semaphore(name), per, unit)

    def block(self):
        return self.scope.enter_context(self.nc.Block())

    def __exit__(self, kind, *rest):
        if kind is None:
            self.scope.close()
            self.nc.clear_and_free_semaphores(self.semaphores)
            self.nc.all_engine_barrier()


def flipped(ap):
    a = [list(x) for x in ap.ap]
    step, n = a[-1]
    return bass.AP(ap.tensor, ap.offset + (n - 1) * step, a[:-1] + [[-step, n]])


def attention_prompt(nc, io, psum, shared, w_qkv):
    ident, bias, sinks, gain = shared["ident"], shared["bias"], shared["sinks"], shared["gain_mix"]
    with Stage(nc) as stage:
        sb, sem, event = stage.buffer, stage.semaphore, stage.event

        x = sb("att_x", [P, D])
        junk = sb("att_junk", [P, D])
        ms = sb("att_ms", [P, 1])
        rstd = sb("att_rstd", [P, 1])
        half = sb("att_half", [P, 1])
        part = sb("att_part", [P, 1])
        hT = sb("att_hT", [P, DB, P])
        q = sb("att_q", [P, D])
        kv = sb("att_kv", [P, 512])
        v_old = sb("att_v_old", [P, 256])
        qT = sb("att_qT", [P, DB, P])
        kT = sb("att_kT", [P, 2, 2 * P])
        logits = sb("att_logits", [P, 2, GROUP, 2 * P])
        pT = sb("att_pT", [P, 2, GROUP, 2, P])
        top = sb("att_top", [P, HEADS])
        ntop = sb("att_ntop", [P, HEADS])
        total = sb("att_total", [P, HEADS])
        esink = sb("att_esink", [P, HEADS])
        rtotal = sb("att_rtotal", [P, HEADS])
        o = sb("att_o", [P, D])
        oms = sb("att_oms", [P, 1])
        orstd = sb("att_orstd", [P, 1])

        order = [("xT0", 0), ("xT1", 1), ("p0", 2), ("p1", 3), ("p2", 2),
                 ("qT0", 0), ("qT1", 1), ("kT", 0)]
        for g in range(KV):
            order += [(f"s{g}0", 4), (f"s{g}1", 5)]
        for g in range(KV):
            order += [(f"t{g}0", 1), (f"t{g}1", 0), (f"o{g}", 6 + g % 2)]
        fills = Fills(sem, "att", order)

        w_in = event("att_w", 1, 16)
        x_in = event("att_x_in", 1, 16)
        x_seen = event("att_x_seen", 2)
        ms_ready = event("att_ms_ready")
        rstd_ready = event("att_rstd_ready")
        hT_ready = event("att_hT_ready", 2)
        projected = event("att_projected")
        q_ready = event("att_q_ready")
        kv_ready = event("att_kv_ready")
        qT_ready = event("att_qT_ready")
        kT_ready = event("att_kT_ready")
        scored = event("att_scored")
        ntop_ready = event("att_ntop_ready", KV)
        p_ready = event("att_p_ready", KV)
        p_turned = event("att_p_turned", KV)
        pT_ready = event("att_pT_ready", KV)
        mixed = event("att_mixed", KV)
        o_ready = event("att_o_ready")
        oms_ready = event("att_oms_ready")
        orstd_ready = event("att_orstd_ready")
        out_ready = event("att_out_ready")
        stored = event("att_stored", 1, 16)
        tail_out = sem("att_tail_out")

        block = stage.block()

        @block.sync
        def _(sp):
            def turn(t):
                sp.wait_ge(x_seen.sem, x_seen.last(t))
                sp.dma_start(x[:], io["x_prompt"][bass.ds(t * P, P), :]).then_inc(x_in.sem, 16)
                sp.wait_ge(out_ready.sem, out_ready.this(t))
                sp.dma_start(io["mixed"][bass.ds(t * P, P), 0:D], o[:]).then_inc(stored.sem, 16)

            sp.sem_inc(x_in.sem, 16)
            sp.sem_inc(stored.sem, 16)
            sp.sem_inc(w_in.sem, 16)
            sp.dma_start(w_qkv[:], io["w_in"].rearrange("(b p) n -> p b n", p=P)[:, :, 0:1536]).then_inc(w_in.sem, 16)
            turn(0)
            with sp.Fori(1, TILES) as t:
                turn(t)
            sp.wait_ge(kv_ready.sem, kv_ready.this(TILES - 1))
            sp.dma_start(io["p_swa_k"], kv[:, 0:256]).then_inc(tail_out, 16)
            sp.dma_start(io["p_swa_v"], kv[:, 256:512]).then_inc(tail_out, 16)
            sp.wait_ge(tail_out, 32)
            sp.wait_ge(stored.sem, stored.this(TILES - 1))

        @block.tensor
        def _(pe):
            def turn(t, first):
                pe.wait_ge(x_in.sem, x_in.this(t))
                for h in range(2):
                    f = f"xT{h}"
                    pe.wait_ge(fills.free[fills.bank(f)], fills.at(f, t))
                    for j in range(4):
                        ins = nc.tensor.transpose(psum[fills.bank(f)][:, j * P:(j + 1) * P],
                                                  x[:, (4 * h + j) * P:(4 * h + j + 1) * P], ident[:])
                    ins.then_inc(fills.full[fills.bank(f)], 1)
                pe.drain()
                pe.sem_inc(x_seen.sem, 1)
                pe.wait_ge(hT_ready.sem, hT_ready.this(t, 2))
                for c in range(3):
                    f = f"p{c}"
                    pe.wait_ge(fills.free[fills.bank(f)], fills.at(f, t))
                    for b in range(DB):
                        ins = nc.tensor.matmul(psum[fills.bank(f)][:], hT[:, b, :],
                                               w_qkv[:, b, c * BANK:(c + 1) * BANK],
                                               start=(b == 0), stop=(b == DB - 1))
                    ins.then_inc(fills.full[fills.bank(f)], 1)
                pe.drain()
                pe.sem_inc(projected.sem, 1)
                pe.wait_ge(q_ready.sem, q_ready.this(t))
                for h in range(2):
                    f = f"qT{h}"
                    pe.wait_ge(fills.free[fills.bank(f)], fills.at(f, t))
                    for j in range(4):
                        ins = nc.tensor.transpose(psum[fills.bank(f)][:, j * P:(j + 1) * P],
                                                  q[:, (4 * h + j) * P:(4 * h + j + 1) * P], ident[:])
                    ins.then_inc(fills.full[fills.bank(f)], 1)
                pe.wait_ge(kv_ready.sem, kv_ready.this(t))
                pe.wait_ge(fills.free[fills.bank("kT")], fills.at("kT", t))
                for j in range(2):
                    ins = nc.tensor.transpose(psum[fills.bank("kT")][:, j * P:(j + 1) * P],
                                              kv[:, j * P:(j + 1) * P], ident[:])
                ins.then_inc(fills.full[fills.bank("kT")], 1)
                pe.wait_ge(qT_ready.sem, qT_ready.this(t))
                pe.wait_ge(kT_ready.sem, kT_ready.this(t))

                def scores(g):
                    lo, hi = (g % 2) * HD, (g % 2 + 1) * HD
                    for h in range(2):
                        f = f"s{g}{h}"
                        pe.wait_ge(fills.free[fills.bank(f)], fills.at(f, t))
                        for r in (2 * h, 2 * h + 1):
                            at = (r % 2) * 2 * P
                            off = P if first else 0
                            ins = nc.tensor.matmul(psum[fills.bank(f)][:, at + off:at + 2 * P],
                                                   qT[lo:hi, 4 * (g // 2) + r, :], kT[lo:hi, g // 2, off:2 * P],
                                                   start=True, stop=True)
                        ins.then_inc(fills.full[fills.bank(f)], 1)

                def values(g):
                    pe.wait_ge(p_ready.sem, p_ready.this(t, g + 1))
                    parts = (1,) if first else (0, 1)
                    for h in range(2):
                        f = f"t{g}{h}"
                        pe.wait_ge(fills.free[fills.bank(f)], fills.at(f, t))
                        for r in (2 * h, 2 * h + 1):
                            for part in parts:
                                at = ((r % 2) * 2 + part) * P
                                ins = nc.tensor.transpose(psum[fills.bank(f)][:, at:at + P],
                                                          logits[:, g % 2, r, part * P:(part + 1) * P], ident[:])
                        ins.then_inc(fills.full[fills.bank(f)], 1)
                    pe.drain()
                    pe.sem_inc(p_turned.sem, 1)
                    pe.wait_ge(pT_ready.sem, pT_ready.this(t, g + 1))
                    f = f"o{g}"
                    pe.wait_ge(fills.free[fills.bank(f)], fills.at(f, t))
                    for r in range(GROUP):
                        for part in parts:
                            v = kv[:, 256 + g * HD:256 + (g + 1) * HD] if part else v_old[:, g * HD:(g + 1) * HD]
                            ins = nc.tensor.matmul(psum[fills.bank(f)][:, r * HD:(r + 1) * HD],
                                                   pT[:, g % 2, r, part, :], v,
                                                   start=(part == parts[0]), stop=(part == 1))
                    ins.then_inc(fills.full[fills.bank(f)], 1)
                    pe.drain()
                    pe.sem_inc(mixed.sem, 1)

                scores(0)
                for g in range(KV):
                    if g + 1 < KV:
                        scores(g + 1)
                    else:
                        pe.drain()
                        pe.sem_inc(scored.sem, 1)
                    values(g)

            fills.prime(pe)
            pe.sem_inc(x_seen.sem, 1)
            for e in (projected, p_turned, mixed, scored):
                pe.sem_inc(e.sem, 1)
            pe.wait_ge(w_in.sem, w_in.this(0))
            turn(0, True)
            with pe.Fori(1, TILES) as t:
                turn(t, False)

        @block.scalar
        def _(act):
            def turn(t, first):
                act.wait_ge(x_in.sem, x_in.this(t))
                nc.scalar.activation(junk[:], x[:], ACT.Square, accum_out=ms[:])
                act.drain()
                act.sem_inc(ms_ready.sem, 1)
                act.sem_inc(x_seen.sem, 1)
                act.wait_ge(rstd_ready.sem, rstd_ready.this(t))
                for c in range(2):
                    f = f"p{c}"
                    act.wait_ge(fills.full[fills.bank(f)], fills.at(f, t))
                    out = q[:, c * BANK:(c + 1) * BANK].rearrange("p (r g d) -> p g r d", r=GROUP, g=2)
                    src = psum[fills.bank(f)][:].rearrange("p (g r d) -> p g r d", r=GROUP, g=2)
                    for gg in range(2):
                        nc.scalar.activation(out[:, gg], src[:, gg], ACT.Copy, scale=rstd[:])
                    act.drain()
                    act.sem_inc(fills.free[fills.bank(f)], 1)
                act.sem_inc(q_ready.sem, 1)
                act.wait_ge(scored.sem, scored.last(t))
                for h in range(2):
                    f = f"qT{h}"
                    act.wait_ge(fills.full[fills.bank(f)], fills.at(f, t))
                    nc.scalar.activation(qT[:, 4 * h:4 * h + 4, :], psum[fills.bank(f)][:].rearrange("p (b t) -> p b t", b=4),
                                         ACT.Copy, scale=HD ** -0.5).then_inc(fills.free[fills.bank(f)], 1)
                act.drain()
                act.sem_inc(qT_ready.sem, 1)
                off = P if first else 0
                for g in range(KV):
                    act.wait_ge(ntop_ready.sem, ntop_ready.this(t, g + 1))
                    for r in range(GROUP):
                        h = g * GROUP + r
                        nc.scalar.activation(logits[:, g % 2, r, off:2 * P], logits[:, g % 2, r, off:2 * P], ACT.Exp,
                                             bias=ntop[:, h:h + 1], accum_out=total[:, h:h + 1])
                    hs = slice(g * GROUP, (g + 1) * GROUP)
                    nc.scalar.activation(esink[:, hs], esink[:, hs], ACT.Exp)
                    act.drain()
                    act.sem_inc(p_ready.sem, 1)
                    for h in range(2):
                        f = f"t{g}{h}"
                        act.wait_ge(fills.full[fills.bank(f)], fills.at(f, t))
                        if h == 0:
                            act.wait_ge(mixed.sem, mixed.this(t, g - 1) if g >= 2 else mixed.last(t))
                        keys = slice(1, 2) if first else slice(0, 2)
                        nc.scalar.copy(pT[:, g % 2, 2 * h:2 * h + 2, keys, :],
                                       psum[fills.bank(f)][:].rearrange("p (r k t) -> p r k t", r=2, k=2)[:, :, keys, :]
                                       ).then_inc(fills.free[fills.bank(f)], 1)
                    act.drain()
                    act.sem_inc(pT_ready.sem, 1)
                act.wait_ge(o_ready.sem, o_ready.this(t))
                nc.scalar.activation(junk[:], o[:], ACT.Square, accum_out=oms[:])
                act.drain()
                act.sem_inc(oms_ready.sem, 1)

            for e in (ms_ready, q_ready, qT_ready, p_ready, pT_ready, oms_ready):
                act.sem_inc(e.sem, 1)
            turn(0, True)
            with act.Fori(1, TILES) as t:
                turn(t, False)

        @block.gpsimd
        def _(pool):
            def turn(t):
                for src, dst, ready, done in ((ms, rstd, ms_ready, rstd_ready), (oms, orstd, oms_ready, orstd_ready)):
                    pool.wait_ge(ready.sem, ready.this(t))
                    nc.gpsimd.tensor_tensor(src[:], src[:], part[:], ALU.mult)
                    pool.drain()
                    nc.gpsimd.tensor_scalar(src[:], src[:], EPS, None, ALU.add)
                    pool.drain()
                    nc.gpsimd.tensor_tensor(dst[:], src[:], half[:], ALU.pow)
                    pool.drain()
                    pool.sem_inc(done.sem, 1)

            nc.gpsimd.memset(half[:], -0.5)
            nc.gpsimd.memset(part[:], 1.0 / D)
            pool.drain()
            pool.sem_inc(rstd_ready.sem, 1)
            pool.sem_inc(orstd_ready.sem, 1)
            turn(0)
            with pool.Fori(1, TILES) as t:
                turn(t)

        @block.vector
        def _(dve):
            def turn(t, first):
                dve.wait_ge(projected.sem, projected.last(t))
                for h in range(2):
                    f = f"xT{h}"
                    dve.wait_ge(fills.full[fills.bank(f)], fills.at(f, t))
                    nc.vector.tensor_tensor(hT[:, 4 * h:4 * h + 4, :], psum[fills.bank(f)][:].rearrange("p (b t) -> p b t", b=4),
                                            gain[:, 4 * h:4 * h + 4, None].broadcast_to([P, 4, P]), ALU.mult
                                            ).then_inc(fills.free[fills.bank(f)], 1)
                    dve.drain()
                    dve.sem_inc(hT_ready.sem, 1)
                dve.wait_ge(mixed.sem, mixed.last(t))
                if not first:
                    nc.vector.tensor_copy(v_old[:], kv[:, 256:512])
                    nc.vector.tensor_copy(kT[:, :, 0:P], kT[:, :, P:2 * P])
                    dve.drain()
                dve.wait_ge(rstd_ready.sem, rstd_ready.this(t))
                f = "p2"
                dve.wait_ge(fills.full[fills.bank(f)], fills.at(f, t))
                nc.vector.tensor_scalar(kv[:], psum[fills.bank(f)][:], rstd[:], None, ALU.mult
                                        ).then_inc(fills.free[fills.bank(f)], 1)
                dve.drain()
                dve.sem_inc(kv_ready.sem, 1)
                f = "kT"
                dve.wait_ge(fills.full[fills.bank(f)], fills.at(f, t))
                nc.vector.tensor_copy(kT[:, :, P:2 * P], psum[fills.bank(f)][:, 0:256].rearrange("p (b t) -> p b t", b=2)
                                      ).then_inc(fills.free[fills.bank(f)], 1)
                dve.drain()
                dve.sem_inc(kT_ready.sem, 1)
                off = P if first else 0

                def softmax_top(g):
                    if g >= 2:
                        dve.wait_ge(p_turned.sem, p_turned.this(t, g - 1))
                    else:
                        dve.wait_ge(p_turned.sem, p_turned.last(t))
                    for h in range(2):
                        f = f"s{g}{h}"
                        dve.wait_ge(fills.full[fills.bank(f)], fills.at(f, t))
                        nc.vector.tensor_tensor(logits[:, g % 2, 2 * h:2 * h + 2, off:2 * P],
                                                psum[fills.bank(f)][:].rearrange("p (r k) -> p r k", r=2)[:, :, off:2 * P],
                                                bias[:, g * GROUP + 2 * h:g * GROUP + 2 * h + 2, off:2 * P], ALU.add
                                                ).then_inc(fills.free[fills.bank(f)], 1)
                    dve.drain()
                    hs = slice(g * GROUP, (g + 1) * GROUP)
                    nc.vector.tensor_reduce(top[:, hs], logits[:, g % 2, :, off:2 * P], AX.X, ALU.max)
                    dve.drain()
                    nc.vector.tensor_tensor(top[:, hs], top[:, hs], sinks[:, hs], ALU.max)
                    dve.drain()
                    nc.vector.tensor_scalar(ntop[:, hs], top[:, hs], -1.0, None, ALU.mult)
                    nc.vector.tensor_tensor(esink[:, hs], sinks[:, hs], top[:, hs], ALU.subtract)
                    dve.drain()
                    dve.sem_inc(ntop_ready.sem, 1)

                def outputs(g):
                    hs = slice(g * GROUP, (g + 1) * GROUP)
                    dve.wait_ge(p_ready.sem, p_ready.this(t, g + 1))
                    nc.vector.tensor_tensor(total[:, hs], total[:, hs], esink[:, hs], ALU.add)
                    dve.drain()
                    nc.vector.reciprocal(rtotal[:, hs], total[:, hs])
                    dve.drain()
                    f = f"o{g}"
                    dve.wait_ge(fills.full[fills.bank(f)], fills.at(f, t))
                    if g == 0:
                        dve.wait_ge(stored.sem, stored.last(t))
                    nc.vector.tensor_tensor(o[:, g * 256:(g + 1) * 256].rearrange("p (r d) -> p r d", r=GROUP),
                                            psum[fills.bank(f)][:, 0:256].rearrange("p (r d) -> p r d", r=GROUP),
                                            rtotal[:, hs, None].broadcast_to([P, GROUP, HD]), ALU.mult
                                            ).then_inc(fills.free[fills.bank(f)], 1)

                softmax_top(0)
                for g in range(KV):
                    if g + 1 < KV:
                        softmax_top(g + 1)
                    outputs(g)
                dve.drain()
                dve.sem_inc(o_ready.sem, 1)
                dve.wait_ge(orstd_ready.sem, orstd_ready.this(t))
                nc.vector.tensor_scalar(o[:], o[:], orstd[:], None, ALU.mult).then_inc(out_ready.sem, 1)

            for e in (hT_ready, kv_ready, kT_ready, ntop_ready, o_ready, out_ready):
                dve.sem_inc(e.sem, 1)
            turn(0, True)
            with dve.Fori(1, TILES) as t:
                turn(t, False)


def setup(nc, io, psum, shared):
    with Stage(nc) as stage:
        sb, sem = stage.buffer, stage.semaphore

        rows = sb("set_rows", [5 * DB, P])
        conv_rows = sb("set_conv_rows", [(CONV + 1) * CB, P])
        table = sb("set_table", [BUCKETS + 1, HEADS])
        onehot = sb("set_onehot", [BUCKETS + 1, 384])
        line = sb("set_line", [HEADS, 384])
        turned = sb("set_turned", [P, HEADS, 2 * P])
        loaded = sem("set_loaded")
        far_row = sem("set_far_row")
        multiplied = sem("set_multiplied")
        line_ready = sem("set_line_ready")
        line_stored = sem("set_line_stored")
        turned_loaded = sem("set_turned_loaded")
        block = stage.block()
        loads = [
            (shared["ident"][:], io["ident"]), (shared["tri"][:], io["tri"]),
            (shared["far"][:], io["far"]),
            (onehot[:], io["onehot"]), (table[0:BUCKETS, :], io["rel_bias"]),
            (shared["sinks"][:], io["attn_sinks"].rearrange("a h -> a h").broadcast_to([P, HEADS])),
            (shared["sink_col"][:], io["attn_sinks"].rearrange("a h -> h a")),
            (shared["head_mask"][:], io["head_mask"]),
        ]
        for i, name in enumerate(("norm_mix_w", "attn_norm_w", "ssd_norm_w", "norm_mem_w", "mem_norm_w")):
            loads.append((rows[i * DB:(i + 1) * DB, :], io[name].rearrange("a (b p) -> (a b) p", p=P)))
        loads.append((conv_rows[0:CONV * CB, :], io["conv_w"].rearrange("k (b p) -> (k b) p", p=P)))
        loads.append((conv_rows[CONV * CB:(CONV + 1) * CB, :], io["conv_b"].rearrange("a (b p) -> (a b) p", p=P)))

        @block.sync
        def _(sp):
            for dst, src in loads:
                sp.dma_start(dst, src).then_inc(loaded, 16)
            sp.wait_ge(line_ready, 1)
            sp.dma_start(io["bias_line"], line[:]).then_inc(line_stored, 16)
            sp.wait_ge(line_stored, 16)
            shifted = bass.AP(io["bias_line"].tensor, io["bias_line"].offset, [[1, P], [384, HEADS], [1, 2 * P]])
            sp.dma_start(turned[:], shifted).then_inc(turned_loaded, 16)

        @block.tensor
        def _(pe):
            pe.wait_ge(loaded, 16 * len(loads))
            pe.wait_ge(far_row, 1)
            nc.tensor.matmul(psum[0][0:HEADS, 0:384], table[:], onehot[:], start=True, stop=True).then_inc(multiplied, 1)
            nc.tensor.transpose(psum[1][:, 0:5 * DB], rows[:], shared["ident"][0:5 * DB, 0:5 * DB])
            n = (CONV + 1) * CB
            nc.tensor.transpose(psum[1][:, P:P + n], conv_rows[:], shared["ident"][0:n, 0:n]).then_inc(multiplied, 1)

        @block.vector
        def _(dve):
            nc.vector.memset(table[BUCKETS:BUCKETS + 1, :], FAR).then_inc(far_row, 1)
            nc.vector.memset(shared["ones"][:], 1.0)
            dve.wait_ge(multiplied, 2)
            nc.vector.tensor_copy(line[:], psum[0][0:HEADS, 0:384]).then_inc(line_ready, 1)
            nc.vector.tensor_copy(shared["gains"][:], psum[1][:, 0:5 * DB].rearrange("p (i b) -> p i b", b=DB))
            nc.vector.tensor_copy(shared["conv"][:], psum[1][:, P:P + (CONV + 1) * CB].rearrange("p (i b) -> p i b", b=CB))
            dve.drain()
            nc.vector.tensor_copy(shared["bias_row"][:], flipped(line[:, 127:256]))
            dve.wait_ge(turned_loaded, 16)
            nc.vector.tensor_copy(shared["bias"][:], flipped(turned[:]))
            dve.drain()


def attention_sample(nc, io, psum, shared, w_qkv):
    ident, sink, gain = shared["ident"], shared["sink_col"], shared["gain_mix"]
    KEYS = WINDOW + 1
    with Stage(nc) as stage:
        sb, sem = stage.buffer, stage.semaphore

        x = sb("sat_x", [DEC, D])
        junk = sb("sat_junk", [DEC, D])
        ms = sb("sat_ms", [DEC, 1])
        rstd = sb("sat_rstd", [DEC, 1])
        half = sb("sat_half", [DEC, 1])
        hT = sb("sat_hT", [P, DB, DEC])
        q = sb("sat_q", [DEC, D])
        kv = sb("sat_kv", [DEC, 512])
        k_cache = sb("sat_k_cache", [P, DEC, 256])
        v_cache = sb("sat_v_cache", [P, DEC, 256])
        q_heads = sb("sat_q_heads", [P, DEC, 2, HEADS])
        k_newT = sb("sat_k_newT", [P, 2, DEC])
        kT = sb("sat_kT", [P, DEC, 2, KEYS])
        p = sb("sat_p", [HEADS, DEC, KEYS])
        top = sb("sat_top", [HEADS, DEC])
        esink = sb("sat_esink", [HEADS, DEC])
        total = sb("sat_total", [HEADS, DEC])
        pT = sb("sat_pT", [P, DEC, HEADS])
        p_new = sb("sat_p_new", [DEC, HEADS])
        p_own = sb("sat_p_own", [DEC, DEC, HEADS])
        wide = sb("sat_wide", [HEADS, DEC, KV, HD])
        o_heads = sb("sat_o_heads", [HEADS, DEC, HD])
        o = sb("sat_o", [DEC, D])

        x_in, cache_in, copied = sem("sat_x_in"), sem("sat_cache_in"), sem("sat_copied")
        x_turned, ms_ready, rstd_ready = sem("sat_x_turned"), sem("sat_ms_ready"), sem("sat_rstd_ready")
        hT_ready, projected, q_ready, kv_ready = sem("sat_hT_ready"), sem("sat_projected"), sem("sat_q_ready"), sem("sat_kv_ready")
        qk_turned, q_heads_ready, k_newT_ready = sem("sat_qk_turned"), sem("sat_q_heads_ready"), sem("sat_k_newT_ready")
        cache_turned, kT_ready, scored = sem("sat_cache_turned"), sem("sat_kT_ready"), sem("sat_scored")
        shifted, esum, p_ready, p_turned = sem("sat_shifted"), sem("sat_esum"), sem("sat_p_ready"), sem("sat_p_turned")
        pT_ready, valued, o_heads_ready, o_in = sem("sat_pT_ready"), sem("sat_valued"), sem("sat_o_heads_ready"), sem("sat_o_in")
        oms_ready, orstd_ready, out_ready = sem("sat_oms_ready"), sem("sat_orstd_ready"), sem("sat_out_ready")
        stored = sem("sat_stored")
        block = stage.block()

        @block.sync
        def _(sp):
            sp.dma_start(x[:], io["x_sample"]).then_inc(x_in, 16)
            sp.dma_start(k_cache[:], io["cache_swa_k"].rearrange("b s n -> s b n")).then_inc(cache_in, 16)
            sp.dma_start(v_cache[:], io["cache_swa_v"].rearrange("b s n -> s b n")).then_inc(cache_in, 16)
            for new, old in (("s_swa_k", "cache_swa_k"), ("s_swa_v", "cache_swa_v")):
                sp.dma_start(io[new][:, 0:WINDOW - 1, :], io[old][:, 1:WINDOW, :]).then_inc(copied, 16)
            sp.wait_ge(kv_ready, 1)
            sp.dma_start(io["s_swa_k"][:, WINDOW - 1, :], kv[:, 0:256]).then_inc(copied, 16)
            sp.dma_start(io["s_swa_v"][:, WINDOW - 1, :], kv[:, 256:512]).then_inc(copied, 16)
            sp.wait_ge(o_heads_ready, 1)
            sp.dma_start(io["rows"].rearrange("b (h d) -> h b d", h=HEADS), o_heads[:]).then_inc(stored, 16)
            sp.wait_ge(stored, 16)
            sp.dma_start(o[:], io["rows"]).then_inc(o_in, 16)
            sp.wait_ge(o_in, 16)
            sp.wait_ge(out_ready, 1)
            sp.dma_start(io["mixed"][SEQ:TOKENS, 0:D], o[:]).then_inc(stored, 16)
            sp.wait_ge(stored, 32)
            sp.wait_ge(copied, 64)

        @block.tensor
        def _(pe):
            pe.wait_ge(x_in, 16)
            for b in range(DB):
                ins = nc.tensor.transpose(psum[0][:, b * DEC:(b + 1) * DEC], x[:, b * P:(b + 1) * P], ident[0:DEC, 0:DEC])
            ins.then_inc(x_turned, 1)
            pe.wait_ge(hT_ready, 1)
            for c in range(3):
                for b in range(DB):
                    ins = nc.tensor.matmul(psum[1 + c][0:DEC, :], hT[:, b, :], w_qkv[:, b, c * BANK:(c + 1) * BANK],
                                           start=(b == 0), stop=(b == DB - 1))
                ins.then_inc(projected, 1)
            pe.wait_ge(cache_in, 32)
            for n in range(4):
                for j in range(4):
                    b, half_k = (4 * n + j) // 2, j % 2
                    ins = nc.tensor.transpose(psum[4 + n][:, j * P:(j + 1) * P],
                                              k_cache[:, b, half_k * P:(half_k + 1) * P], ident[:])
                ins.then_inc(cache_turned, 1)
            pe.wait_ge(q_ready, 1)
            pe.wait_ge(kv_ready, 1)
            for b in range(DB):
                nc.tensor.transpose(psum[0][:, b * DEC:(b + 1) * DEC], q[:, b * P:(b + 1) * P], ident[0:DEC, 0:DEC])
            for b in range(2):
                ins = nc.tensor.transpose(psum[0][:, P + b * DEC:P + (b + 1) * DEC], kv[:, b * P:(b + 1) * P], ident[0:DEC, 0:DEC])
            ins.then_inc(qk_turned, 1)
            pe.wait_ge(q_heads_ready, 1)
            pe.wait_ge(kT_ready, 1)
            for b in range(DEC):
                for j in range(2):
                    ins = nc.tensor.matmul(psum[1 + b // 3][0:HEADS, (b % 3) * KEYS:(b % 3 + 1) * KEYS],
                                           q_heads[:, b, j, :], kT[:, b, j, :], start=(j == 0), stop=(j == 1))
            ins.then_inc(scored, 1)
            pe.wait_ge(p_ready, 1)
            for b in range(DEC):
                nc.tensor.transpose(psum[0][:, b * HEADS:(b + 1) * HEADS], p[:, b, 0:WINDOW], ident[0:HEADS, 0:HEADS])
            nc.tensor.transpose(psum[0][0:DEC, 256:256 + HEADS], p[:, :, WINDOW], ident[0:HEADS, 0:HEADS]).then_inc(p_turned, 1)
            pe.wait_ge(pT_ready, 1)
            for b in range(DEC):
                out = psum[4 + b // 2][0:HEADS, (b % 2) * 256:(b % 2 + 1) * 256]
                nc.tensor.matmul(out, pT[:, b, :], v_cache[:, b, :], start=True, stop=False)
                ins = nc.tensor.matmul(out, p_own[:, b, :], kv[:, 256:512], start=False, stop=True)
            ins.then_inc(valued, 1)

        @block.scalar
        def _(act):
            act.wait_ge(x_in, 16)
            nc.scalar.activation(junk[:], x[:], ACT.Square, accum_out=ms[:]).then_inc(ms_ready, 1)
            act.wait_ge(rstd_ready, 1)
            act.wait_ge(projected, 2)
            for c in range(2):
                out = q[:, c * BANK:(c + 1) * BANK].rearrange("p (r g d) -> p g r d", r=GROUP, g=2)
                src = psum[1 + c][0:DEC, :].rearrange("p (g r d) -> p g r d", r=GROUP, g=2)
                for gg in range(2):
                    nc.scalar.activation(out[:, gg], src[:, gg], ACT.Copy, scale=rstd[:])
            act.drain()
            act.sem_inc(q_ready, 1)
            act.wait_ge(shifted, 1)
            nc.scalar.activation(p[:], p[:], ACT.Exp)
            nc.scalar.activation(esink[:], esink[:], ACT.Exp).then_inc(esum, 1)
            act.wait_ge(o_in, 16)
            nc.scalar.activation(junk[:], o[:], ACT.Square, accum_out=ms[:]).then_inc(oms_ready, 1)

        @block.gpsimd
        def _(pool):
            nc.gpsimd.memset(half[:], -0.5)
            for ready, done in ((ms_ready, rstd_ready), (oms_ready, orstd_ready)):
                pool.wait_ge(ready, 1)
                nc.gpsimd.tensor_scalar(ms[:], ms[:], 1.0 / D, EPS, ALU.mult, ALU.add)
                pool.drain()
                nc.gpsimd.tensor_tensor(rstd[:], ms[:], half[:], ALU.pow).then_inc(done, 1)

        @block.vector
        def _(dve):
            nc.vector.memset(q_heads[:], 0.0)
            dve.wait_ge(x_turned, 1)
            nc.vector.tensor_tensor(hT[:], psum[0][:, 0:DB * DEC].rearrange("p (b t) -> p b t", b=DB),
                                    gain[:, :, None].broadcast_to([P, DB, DEC]), ALU.mult).then_inc(hT_ready, 1)
            dve.wait_ge(rstd_ready, 1)
            dve.wait_ge(projected, 3)
            nc.vector.tensor_scalar(kv[:], psum[3][0:DEC, :], rstd[:], None, ALU.mult).then_inc(kv_ready, 1)
            for n in range(4):
                dve.wait_ge(cache_turned, n + 1)
                nc.vector.tensor_copy(kT[:, 2 * n:2 * n + 2, :, 0:WINDOW],
                                      psum[4 + n][:].rearrange("p (b j k) -> p b j k", b=2, j=2))
            dve.wait_ge(qk_turned, 1)
            nc.vector.tensor_copy(k_newT[:], psum[0][:, P:P + 2 * DEC].rearrange("p (j b) -> p j b", j=2))
            for g in range(KV):
                lo, hi = (g % 2) * HD, (g % 2 + 1) * HD
                src = psum[0][lo:hi, (g // 2) * GROUP * DEC:(g // 2 + 1) * GROUP * DEC].rearrange("p (r b) -> p b r", r=GROUP)
                nc.vector.tensor_scalar(q_heads[lo:hi, :, g // 2, g * GROUP:(g + 1) * GROUP], src, HD ** -0.5, None, ALU.mult)
            dve.drain()
            dve.sem_inc(q_heads_ready, 1)
            for j in range(2):
                ins = nc.vector.tensor_copy(kT[:, :, j, WINDOW], k_newT[:, j, :])
            dve.drain()
            dve.sem_inc(kT_ready, 1)
            dve.wait_ge(scored, 1)
            for n, m in enumerate((3, 3, 2)):
                nc.vector.tensor_tensor(p[:, 3 * n:3 * n + m, :], psum[1 + n][0:HEADS, 0:m * KEYS].rearrange("p (b k) -> p b k", b=m),
                                        shared["bias_row"][:, None, :].broadcast_to([HEADS, m, KEYS]), ALU.add)
            dve.drain()
            nc.vector.tensor_reduce(top[:], p[:], AX.X, ALU.max)
            dve.drain()
            nc.vector.tensor_scalar(top[:], top[:], sink[:], None, ALU.max)
            dve.drain()
            nc.vector.tensor_tensor(p[:], p[:], top[:, :, None].broadcast_to([HEADS, DEC, KEYS]), ALU.subtract)
            nc.vector.tensor_scalar(esink[:], top[:], -1.0, sink[:], ALU.mult, ALU.add)
            dve.drain()
            dve.sem_inc(shifted, 1)
            dve.wait_ge(esum, 1)
            nc.vector.tensor_reduce(total[:], p[:], AX.X, ALU.add)
            dve.drain()
            nc.vector.tensor_tensor(total[:], total[:], esink[:], ALU.add)
            dve.drain()
            nc.vector.reciprocal(total[:], total[:])
            dve.drain()
            nc.vector.tensor_tensor(p[:], p[:], total[:, :, None].broadcast_to([HEADS, DEC, KEYS]), ALU.mult).then_inc(p_ready, 1)
            dve.wait_ge(p_turned, 1)
            nc.vector.tensor_copy(pT[:], psum[0][:, 0:P].rearrange("p (b h) -> p b h", b=DEC))
            nc.vector.tensor_copy(p_new[:], psum[0][0:DEC, 256:256 + HEADS])
            dve.drain()
            nc.vector.tensor_tensor(p_own[:], p_new[:, None, :].broadcast_to([DEC, DEC, HEADS]),
                                    ident[0:DEC, 0:DEC, None].broadcast_to([DEC, DEC, HEADS]), ALU.mult)
            dve.drain()
            dve.sem_inc(pT_ready, 1)
            dve.wait_ge(valued, 1)
            for b in range(DEC):
                nc.vector.tensor_tensor(wide[:, b], psum[4 + b // 2][0:HEADS, (b % 2) * 256:(b % 2 + 1) * 256].rearrange("p (g d) -> p g d", g=KV),
                                        shared["head_mask"][:, :, None].broadcast_to([HEADS, KV, HD]), ALU.mult)
            dve.drain()
            nc.vector.tensor_reduce(o_heads[:], wide[:].rearrange("p b g d -> p b d g"), AX.X, ALU.add).then_inc(o_heads_ready, 1)
            dve.wait_ge(orstd_ready, 1)
            nc.vector.tensor_scalar(o[:], o[:], rstd[:], None, ALU.mult).then_inc(out_ready, 1)




def ssd_prompt(nc, io, psum, shared, w_zx):
    ident, tri, far, ones, gain, conv = (shared[k] for k in ("ident", "tri", "far", "ones", "gain_mix", "conv"))
    NH = SSD_HEADS
    with Stage(nc) as stage:
        sb, sem, event = stage.buffer, stage.semaphore, stage.event

        x = sb("ssd_x", [P, D])
        junk = sb("ssd_junk", [P, D])
        ms, rstd, yms, yrstd = (sb("ssd_" + n, [P, 1]) for n in ("ms", "rstd", "yms", "yrstd"))
        half, part = sb("ssd_half", [P, 1]), sb("ssd_part", [P, 1])
        hT = sb("ssd_hT", [P, DB, P])
        zs = sb("ssd_zs", [P, D])
        xbc = sb("ssd_xbc", [P, CONV_DIM])
        xbcT = sb("ssd_xbcT", [P, CB, CONV - 1 + P])
        cv = sb("ssd_cv", [P, CB, P])
        tap = sb("ssd_tap", [P, CB, P])
        dt_raw, dt_neg, dt_exp, dt_u, dt_err, dt, decay = (sb("ssd_" + n, [P, NH]) for n in
                                                         ("dt_raw", "dt_neg", "dt_exp", "dt_u", "dt_err", "dt", "decay"))
        rate = sb("ssd_rate", [P, NH])
        dt_bias = sb("ssd_dt_bias", [P, NH])
        skip = sb("ssd_skip", [P, NH])
        sums = sb("ssd_sums", [P, 2, NH])
        esums = sb("ssd_esums", [P, 2, NH])
        nsum = sb("ssd_nsum", [P, NH])
        to_end = sb("ssd_to_end", [P, NH])
        xs = sb("ssd_xs", [P, D])
        bm = sb("ssd_bm", [P, SSD_G, STATE])
        xdt = sb("ssd_xdt", [P, D])
        xend = sb("ssd_xend", [P, D])
        cb = sb("ssd_cb", [P, SSD_G, P])
        dec = sb("ssd_dec", [P, 2, 4, P])
        y = sb("ssd_y", [P, D])
        out_rows = sb("ssd_out", [P, D])
        xskip = sb("ssd_xskip", [P, D])
        state = sb("ssd_state", [P, D])

        def by_head(ap):
            return ap.rearrange("p (h d) -> p h d", d=HD)

        def per_head(ap, n=NH):
            return ap[:, :, None].broadcast_to([P, n, HD])

        front_fills = Fills(sem, "ssd_front", [
            ("xT0", 0), ("xT1", 1), ("x0", 2), ("x1", 3), ("x2", 0), ("dt", 1),
            ("cT0", 2), ("cT1", 3), ("cT2", 0), ("z0", 1), ("z1", 2), ("sums", 3)])
        back_fills = Fills(sem, "ssd_back", [
            ("xs0", 4), ("xs1", 5), ("bc", 6), ("yo0", 7), ("yo1", 4), ("G0", 5), ("G1", 6),
            ("yd0", 7), ("G2", 5), ("G3", 6), ("yd1", 4), ("st0", 5), ("st1", 6)])

        def fill(name):
            f = front_fills if name in front_fills.place else back_fills
            return f, f.bank(name), psum[f.bank(name)]

        chunks = {"z0": 0, "z1": 512, "x0": 1024, "x1": 1536, "x2": 2048, "dt": 2560}

        w_in = sem("ssd_w")
        x_in = event("ssd_x_in", 1, 16)
        x_seen = event("ssd_x_seen", 2)
        ms_ready, rstd_ready, yms_ready, yrstd_ready = (event("ssd_" + n) for n in ("ms_ready", "rstd_ready", "yms_ready", "yrstd_ready"))
        hT_ready = event("ssd_hT_ready")
        projected = event("ssd_projected")
        xbc_ready = event("ssd_xbc_ready", 2)
        xbcT_ready = event("ssd_xbcT_ready")
        taps_done = event("ssd_taps_done", 2)
        cv_ready, cv_used = event("ssd_cv_ready"), event("ssd_cv_used")
        decays_over, xskip_ready = event("ssd_decays_over"), event("ssd_xskip_ready")
        dt_raw_ready, dt_exp_ready, dt_u_ready, dt_log_ready, decay_ready = (
            event("ssd_" + n) for n in ("dt_raw_ready", "dt_exp_ready", "dt_u_ready", "dt_log_ready", "decay_ready"))
        sums_ready, esums_ready = event("ssd_sums_ready"), event("ssd_esums_ready")
        xs_ready, bm_ready, xdt_ready, xend_ready, cb_ready = (
            event("ssd_" + n) for n in ("xs_ready", "bm_ready", "xdt_ready", "xend_ready", "cb_ready"))
        dec_ready, scan_ready, scanned = event("ssd_dec_ready", 4), event("ssd_scan_ready", 4), event("ssd_scanned", 4)
        y_ready, y_gated, out_ready = event("ssd_y_ready"), event("ssd_y_gated"), event("ssd_out_ready")
        state_ready = event("ssd_state_ready")
        stored = event("ssd_stored", 1, 16)
        loaded, rates_ready, consts_ready = sem("ssd_loaded"), sem("ssd_rates_ready"), sem("ssd_consts_ready")
        state_turned, state_copied, tail_out = sem("ssd_state_turned"), sem("ssd_state_copied"), sem("ssd_tail_out")

        HALF = CB // 2

        def convolve(eng, engine, lo, hi, chunk):
            engine.wait_ge(xbcT_ready.sem, xbcT_ready.this(chunk))
            engine.wait_ge(cv_used.sem, cv_used.last(chunk))
            n, c, x = hi - lo, cv[:, lo:hi, :], xbcT[:, lo:hi, :]
            for k in range(CONV):
                eng.tensor_tensor(tap[:, lo:hi, :] if k else c, x[:, :, k:k + P],
                                  conv[:, k, lo:hi, None].broadcast_to([P, n, P]), ALU.mult)
                engine.drain()
                if k:
                    eng.tensor_tensor(c, c, tap[:, lo:hi, :], ALU.add)
                    engine.drain()
            eng.tensor_tensor(c, c, conv[:, CONV, lo:hi, None].broadcast_to([P, n, P]), ALU.add)
            eng.tensor_copy(x[:, :, 0:CONV - 1], x[:, :, P:P + CONV - 1])
            engine.drain()
            engine.sem_inc(taps_done.sem, 1)

        block = stage.block()

        @block.sync
        def _(sp):
            def load(t):
                sp.wait_ge(x_seen.sem, x_seen.last(t))
                sp.dma_start(x[:], io["x_prompt"][bass.ds(t * P, P), :]).then_inc(x_in.sem, 16)

            def store(t):
                sp.wait_ge(out_ready.sem, out_ready.this(t))
                sp.dma_start(io["mixed"][bass.ds(t * P, P), D:2 * D], out_rows[:]).then_inc(stored.sem, 16)

            sp.sem_inc(x_in.sem, 16)
            sp.sem_inc(stored.sem, 16)
            sp.dma_start(rate[:], io["a_log"].broadcast_to([P, NH])).then_inc(loaded, 16)
            sp.dma_start(dt_bias[:], io["dt_bias"].broadcast_to([P, NH])).then_inc(loaded, 16)
            sp.dma_start(skip[:], io["d_skip"].broadcast_to([P, NH])).then_inc(loaded, 16)
            sp.dma_start(w_zx[:], io["w_in"].rearrange("(b p) n -> p b n", p=P)[:, :, 1536:IN_COLS]).then_inc(w_in, 16)
            for t in range(3):
                load(t)
            with sp.Fori(0, TILES - 3) as t:
                store(t)
                load(t + 3)
            with sp.Fori(TILES - 3, TILES) as t:
                store(t)
            sp.dma_start(io["p_conv"], xbc[P - CONV + 1:P, :]).then_inc(tail_out, 16)
            sp.wait_ge(state_copied, 2)
            sp.dma_start(io["p_ssm"].rearrange("(j q) n -> q j n", q=P), y[:].rearrange("p (j n) -> p j n", j=DB)).then_inc(tail_out, 16)
            sp.wait_ge(tail_out, 32)
            sp.wait_ge(stored.sem, stored.this(TILES - 1))

        @block.tensor
        def _(pe):
            def begin(name, t):
                f, bank, out = fill(name)
                pe.wait_ge(f.free[bank], f.at(name, t))
                return out, f.full[bank]

            def turned(name, t, blocks):
                out, full = begin(name, t)
                for j, block_in in enumerate(blocks):
                    ins = nc.tensor.transpose(out[:, j * P:(j + 1) * P], block_in, ident[:])
                ins.then_inc(full, 1)

            def rows(u):
                pe.wait_ge(x_in.sem, x_in.this(u))
                for h in range(2):
                    turned(f"xT{h}", u, [x[:, (4 * h + j) * P:(4 * h + j + 1) * P] for j in range(4)])
                pe.drain()
                pe.sem_inc(x_seen.sem, 1)

            def project(name, u):
                col = chunks[name]
                n = min(BANK, IN_COLS - 1536 - col)
                out, full = begin(name, u)
                for b in range(DB):
                    ins = nc.tensor.matmul(out[:, 0:n], hT[:, b, :], w_zx[:, b, col:col + n], start=(b == 0), stop=(b == DB - 1))
                ins.then_inc(full, 1)

            def channels(u):
                pe.wait_ge(xbc_ready.sem, xbc_ready.this(u, 2))
                for n in range(3):
                    turned(f"cT{n}", u, [xbc[:, (4 * n + j) * P:(4 * n + j + 1) * P] for j in range(4)])

            def summed(u):
                pe.wait_ge(decay_ready.sem, decay_ready.this(u))
                out, full = begin("sums", u)
                nc.tensor.matmul(out[:, 0:NH], tri[:], decay[:], start=True, stop=True)
                nc.tensor.matmul(out[:, NH:2 * NH], ones[:], decay[:], start=True, stop=True).then_inc(full, 1)

            def tokens(t):
                pe.wait_ge(cv_ready.sem, cv_ready.this(t))
                for h in range(2):
                    turned(f"xs{h}", t, [cv[:, 4 * h + j, :] for j in range(4)])
                out, full = begin("bc", t)
                for g in range(SSD_G):
                    nc.tensor.transpose(out[:, g * P:(g + 1) * P], cv[:, 8 + g, :], ident[:])
                for g in range(SSD_G):
                    ins = nc.tensor.matmul(out[:, (2 + g) * P:(3 + g) * P], cv[:, 8 + g, :], cv[:, 10 + g, :], start=True, stop=True)
                ins.then_inc(full, 1)
                pe.wait_ge(state_ready.sem, state_ready.last(t))
                for g in range(SSD_G):
                    out, full = begin(f"yo{g}", t)
                    nc.tensor.matmul(out[:], cv[:, 10 + g, :], state[:, g * BANK:(g + 1) * BANK], start=True, stop=True).then_inc(full, 1)
                pe.drain()
                pe.sem_inc(cv_used.sem, 1)

            def decays(t, n):
                out, full = begin(f"G{n}", t)
                nc.tensor.matmul(out[:].rearrange("p (h l) -> p h l", h=4), ident[:],
                                 far[:, None, :].broadcast_to([P, 4, P]), start=True, stop=False)
                for j in range(4):
                    ins = nc.tensor.matmul(out[:, j * P:(j + 1) * P], decay[:, 4 * n + j:4 * n + j + 1].broadcast_to([P, P]), tri[:],
                                           start=False, stop=(j == 3))
                ins.then_inc(full, 1)
                if n == 3:
                    pe.drain()
                    pe.sem_inc(decays_over.sem, 1)

            def scan(t, n):
                if n == 0:
                    pe.wait_ge(xdt_ready.sem, xdt_ready.this(t))
                pe.wait_ge(scan_ready.sem, scan_ready.this(t, n + 1))
                f, bank, out = fill(f"yd{n // 2}")
                if n % 2 == 0:
                    begin(f"yd{n // 2}", t)
                for j in range(4):
                    h = 4 * n + j
                    nc.tensor.matmul(out[:, (h % 8) * HD:(h % 8 + 1) * HD], dec[:, n % 2, j, :],
                                     xdt[:, h * HD:(h + 1) * HD], start=True, stop=True)
                pe.drain()
                pe.sem_inc(scanned.sem, 1)
                if n % 2:
                    pe.sem_inc(f.full[bank], 1)

            def grown(t):
                pe.wait_ge(xend_ready.sem, xend_ready.this(t))
                for g in range(SSD_G):
                    out, full = begin(f"st{g}", t)
                    nc.tensor.matmul(out[:], bm[:, g, :], xend[:, g * BANK:(g + 1) * BANK], start=True, stop=True).then_inc(full, 1)

            def turn(t, u):
                back, front = t is not None, u is not None
                if front:
                    rows(u)
                if back:
                    tokens(t)
                if front:
                    pe.wait_ge(hT_ready.sem, hT_ready.this(u))
                    project("x0", u)
                    project("x1", u)
                if back:
                    decays(t, 0)
                if front:
                    project("x2", u)
                    project("dt", u)
                if back:
                    decays(t, 1)
                if front:
                    channels(u)
                if back:
                    scan(t, 0)
                    decays(t, 2)
                    scan(t, 1)
                    decays(t, 3)
                if front:
                    project("z0", u)
                if back:
                    scan(t, 2)
                    scan(t, 3)
                    grown(t)
                if front:
                    project("z1", u)
                    pe.drain()
                    pe.sem_inc(projected.sem, 1)
                    summed(u)

            front_fills.prime(pe)
            back_fills.prime(pe)
            for e in (x_seen, projected, scanned, cv_used, decays_over):
                pe.sem_inc(e.sem, 1)
            pe.wait_ge(w_in, 16)
            pe.wait_ge(consts_ready, 1)
            turn(None, 0)
            with pe.Fori(0, TILES - 1) as t:
                turn(t, t + 1)
            turn(TILES - 1, None)
            pe.wait_ge(state_ready.sem, state_ready.this(TILES - 1))
            for h in range(2):
                pe.wait_ge(back_fills.free[4 + h], TILES * back_fills.count[4 + h] + 1)
                for j in range(4):
                    ins = nc.tensor.transpose(psum[4 + h][:, j * P:(j + 1) * P], state[:, (4 * h + j) * P:(4 * h + j + 1) * P], ident[:])
                ins.then_inc(state_turned, 1)

        @block.scalar
        def _(act):
            def take(name, t, dst, func=ACT.Copy, **how):
                f, bank, src = fill(name)
                act.wait_ge(f.full[bank], f.at(name, t))
                nc.scalar.activation(dst, src[:], func, **how).then_inc(f.free[bank], 1)

            def squares(u):
                act.wait_ge(x_in.sem, x_in.this(u))
                nc.scalar.activation(junk[:], x[:], ACT.Square, accum_out=ms[:])
                act.drain()
                act.sem_inc(ms_ready.sem, 1)
                act.sem_inc(x_seen.sem, 1)

            def tokens(t):
                act.wait_ge(taps_done.sem, taps_done.this(t, 2))
                nc.scalar.activation(cv[:], cv[:], ACT.Silu)
                act.drain()
                act.sem_inc(cv_ready.sem, 1)
                for h in range(2):
                    take(f"xs{h}", t, xs[:, h * BANK:(h + 1) * BANK])
                act.drain()
                act.sem_inc(xs_ready.sem, 1)

            def middle(u):
                act.wait_ge(rstd_ready.sem, rstd_ready.this(u))
                take("x1", u, xbc[:, BANK:2 * BANK], scale=rstd[:])
                act.drain()
                act.sem_inc(xbc_ready.sem, 1)

            def channels(u):
                act.wait_ge(taps_done.sem, taps_done.last(u))
                for n in range(3):
                    f, bank, src = fill(f"cT{n}")
                    act.wait_ge(f.full[bank], f.at(f"cT{n}", u))
                    nc.scalar.copy(xbcT[:, 4 * n:4 * n + 4, CONV - 1:], src[:].rearrange("p (b t) -> p b t", b=4)
                                   ).then_inc(f.free[bank], 1)
                act.drain()
                act.sem_inc(xbcT_ready.sem, 1)

            def softplus_exp(u):
                act.wait_ge(dt_raw_ready.sem, dt_raw_ready.this(u))
                nc.scalar.activation(dt_exp[:], dt_neg[:], ACT.Exp)
                act.drain()
                act.sem_inc(dt_exp_ready.sem, 1)

            def softplus_log(u):
                act.wait_ge(dt_u_ready.sem, dt_u_ready.this(u))
                nc.scalar.activation(dt_neg[:], dt_u[:], ACT.Ln)
                act.drain()
                act.sem_inc(dt_log_ready.sem, 1)

            def decays(t, n):
                act.wait_ge(scanned.sem, scanned.this(t, n - 1) if n >= 2 else scanned.last(t))
                f, bank, src = fill(f"G{n}")
                act.wait_ge(f.full[bank], f.at(f"G{n}", t))
                for j in range(4):
                    nc.scalar.activation(dec[:, n % 2, j, :], src[:, j * P:(j + 1) * P], ACT.Exp,
                                         bias=nsum[:, 4 * n + j:4 * n + j + 1])
                act.drain()
                act.sem_inc(dec_ready.sem, 1)
                act.sem_inc(f.free[bank], 1)

            def gated(t):
                act.wait_ge(y_gated.sem, y_gated.this(t))
                nc.scalar.activation(junk[:], y[:], ACT.Square, accum_out=yms[:])
                act.drain()
                act.sem_inc(yms_ready.sem, 1)

            def gates(u):
                act.wait_ge(y_gated.sem, y_gated.last(u))
                for h in range(2):
                    take(f"z{h}", u, zs[:, h * BANK:(h + 1) * BANK], ACT.Silu, scale=rstd[:])

            def summed(u):
                act.wait_ge(sums_ready.sem, sums_ready.this(u))
                nc.scalar.activation(esums[:], sums[:], ACT.Exp)
                nc.scalar.activation(to_end[:], to_end[:], ACT.Exp)
                act.drain()
                act.sem_inc(esums_ready.sem, 1)

            def turn(t, u):
                back, front = t is not None, u is not None
                if front:
                    squares(u)
                if back:
                    tokens(t)
                if front:
                    middle(u)
                if back:
                    decays(t, 0)
                if front:
                    softplus_exp(u)
                if back:
                    decays(t, 1)
                if front:
                    channels(u)
                    softplus_log(u)
                if back:
                    decays(t, 2)
                    decays(t, 3)
                    gated(t)
                if front:
                    gates(u)
                    summed(u)

            for e in (ms_ready, dt_exp_ready, dt_log_ready, xbcT_ready, esums_ready, cv_ready, xs_ready, dec_ready, yms_ready):
                act.sem_inc(e.sem, 1)
            act.wait_ge(loaded, 48)
            nc.scalar.activation(rate[:], rate[:], ACT.Exp).then_inc(rates_ready, 1)
            turn(None, 0)
            with act.Fori(0, TILES - 1) as t:
                turn(t, t + 1)
            turn(TILES - 1, None)

        @block.gpsimd
        def _(pool):
            def factor(src, dst, ready, done, t):
                pool.wait_ge(ready.sem, ready.this(t))
                nc.gpsimd.tensor_tensor(src[:], src[:], part[:], ALU.mult)
                pool.drain()
                nc.gpsimd.tensor_scalar(src[:], src[:], EPS, None, ALU.add)
                pool.drain()
                nc.gpsimd.tensor_tensor(dst[:], src[:], half[:], ALU.pow)
                pool.drain()
                pool.sem_inc(done.sem, 1)

            def turn(t, u):
                if u is not None:
                    factor(ms, rstd, ms_ready, rstd_ready, u)
                if t is not None:
                    pool.wait_ge(xs_ready.sem, xs_ready.this(t))
                    nc.gpsimd.tensor_tensor(by_head(xskip[:]), by_head(xs[:]), per_head(skip), ALU.mult)
                    pool.drain()
                    pool.sem_inc(xskip_ready.sem, 1)
                if u is not None:
                    convolve(nc.gpsimd, pool, 0, HALF, u)
                if t is not None:
                    factor(yms, yrstd, yms_ready, yrstd_ready, t)

            nc.gpsimd.memset(half[:], -0.5)
            nc.gpsimd.memset(part[:], 1.0 / D)
            nc.gpsimd.memset(xbcT[:, :, 0:CONV - 1], 0.0)
            pool.drain()
            for e in (rstd_ready, taps_done, xskip_ready, yrstd_ready):
                pool.sem_inc(e.sem, 1)
            pool.wait_ge(loaded, 48)
            turn(None, 0)
            with pool.Fori(0, TILES - 1) as t:
                turn(t, t + 1)
            turn(TILES - 1, None)

        @block.vector
        def _(dve):
            def full(name, t):
                f, bank, src = fill(name)
                dve.wait_ge(f.full[bank], f.at(name, t))
                return src, f.free[bank]

            def rows(u):
                dve.wait_ge(projected.sem, projected.last(u))
                for h in range(2):
                    src, free = full(f"xT{h}", u)
                    nc.vector.tensor_tensor(hT[:, 4 * h:4 * h + 4, :], src[:].rearrange("p (b t) -> p b t", b=4),
                                            gain[:, 4 * h:4 * h + 4, None].broadcast_to([P, 4, P]), ALU.mult).then_inc(free, 1)
                dve.drain()
                dve.sem_inc(hT_ready.sem, 1)

            def tokens(t):
                dve.wait_ge(xs_ready.sem, xs_ready.this(t))
                nc.vector.tensor_tensor(by_head(xdt[:]), by_head(xs[:]), per_head(dt), ALU.mult)
                dve.drain()
                dve.sem_inc(xdt_ready.sem, 1)
                src, free = full("bc", t)
                nc.vector.tensor_copy(bm[:], src[:, 0:2 * P].rearrange("p (g n) -> p g n", g=2))
                nc.vector.tensor_copy(cb[:], src[:, 2 * P:4 * P].rearrange("p (g n) -> p g n", g=2)).then_inc(free, 1)
                dve.wait_ge(esums_ready.sem, esums_ready.this(t))
                nc.vector.tensor_tensor(by_head(xend[:]), by_head(xdt[:]), per_head(to_end), ALU.mult)
                dve.drain()
                dve.sem_inc(xend_ready.sem, 1)

            def scaled(t):
                dve.wait_ge(stored.sem, stored.last(t))
                dve.wait_ge(yrstd_ready.sem, yrstd_ready.this(t))
                nc.vector.tensor_scalar(out_rows[:], y[:], yrstd[:], None, ALU.mult)
                dve.drain()
                dve.sem_inc(out_ready.sem, 1)

            def begin_y(t):
                for g in range(SSD_G):
                    src, free = full(f"yo{g}", t)
                    nc.vector.tensor_tensor(by_head(y[:, g * BANK:(g + 1) * BANK]), by_head(src[:]),
                                            per_head(esums[:, 0, g * SSD_HPG:(g + 1) * SSD_HPG], SSD_HPG), ALU.mult).then_inc(free, 1)

            def middle(u):
                dve.wait_ge(rstd_ready.sem, rstd_ready.this(u))
                for name, at in (("x0", 0), ("x2", 2)):
                    src, free = full(name, u)
                    nc.vector.tensor_scalar(xbc[:, at * BANK:(at + 1) * BANK], src[:], rstd[:], None, ALU.mult).then_inc(free, 1)
                dve.drain()
                dve.sem_inc(xbc_ready.sem, 1)
                src, free = full("dt", u)
                nc.vector.scalar_tensor_tensor(dt_raw[:], src[:, 0:NH], rstd[:], dt_bias[:], ALU.mult, ALU.add).then_inc(free, 1)
                dve.drain()
                nc.vector.scalar_tensor_tensor(dt_neg[:], dt_raw[:], -1.0, dt_raw[:], ALU.mult, ALU.min)
                nc.vector.tensor_scalar(dt_raw[:], dt_raw[:], 0.0, None, ALU.max)
                dve.drain()
                dve.sem_inc(dt_raw_ready.sem, 1)

            def softplus(u):
                dve.wait_ge(dt_exp_ready.sem, dt_exp_ready.this(u))
                nc.vector.tensor_scalar(dt_u[:], dt_exp[:], 1.0, None, ALU.add)
                dve.drain()
                dve.sem_inc(dt_u_ready.sem, 1)
                nc.vector.scalar_tensor_tensor(dt_err[:], dt_u[:], -1.0, dt_exp[:], ALU.add, ALU.subtract)
                nc.vector.reciprocal(dt[:], dt_u[:])
                dve.drain()
                nc.vector.tensor_tensor(dt_err[:], dt_err[:], dt[:], ALU.mult)
                dve.drain()
                nc.vector.tensor_tensor(dt_raw[:], dt_raw[:], dt_err[:], ALU.subtract)
                dve.drain()

            def rates(u):
                dve.wait_ge(dt_log_ready.sem, dt_log_ready.this(u))
                nc.vector.tensor_tensor(dt[:], dt_raw[:], dt_neg[:], ALU.add)
                dve.drain()
                dve.wait_ge(decays_over.sem, decays_over.last(u))
                nc.vector.tensor_tensor(decay[:], dt[:], rate[:], ALU.mult)
                dve.drain()
                dve.sem_inc(decay_ready.sem, 1)

            def decays(t, n):
                dve.wait_ge(dec_ready.sem, dec_ready.this(t, n + 1))
                nc.vector.tensor_tensor(dec[:, n % 2], dec[:, n % 2], cb[:, n // 2, None, :].broadcast_to([P, 4, P]), ALU.mult)
                dve.drain()
                dve.sem_inc(scan_ready.sem, 1)

            def finish(t):
                for g in range(SSD_G):
                    src, free = full(f"yd{g}", t)
                    cols = slice(g * BANK, (g + 1) * BANK)
                    nc.vector.tensor_tensor(y[:, cols], y[:, cols], src[:], ALU.add).then_inc(free, 1)
                dve.drain()
                dve.wait_ge(xskip_ready.sem, xskip_ready.this(t))
                nc.vector.tensor_tensor(y[:], y[:], xskip[:], ALU.add)
                dve.drain()
                nc.vector.tensor_tensor(y[:], y[:], zs[:], ALU.mult)
                dve.drain()
                dve.sem_inc(y_gated.sem, 1)
                nc.vector.tensor_tensor(by_head(state[:]), by_head(state[:]), per_head(esums[:, 1, :]), ALU.mult)
                dve.drain()
                for g in range(SSD_G):
                    src, free = full(f"st{g}", t)
                    cols = slice(g * BANK, (g + 1) * BANK)
                    nc.vector.tensor_tensor(state[:, cols], state[:, cols], src[:], ALU.add).then_inc(free, 1)
                dve.drain()
                dve.sem_inc(state_ready.sem, 1)

            def summed(u):
                src, free = full("sums", u)
                nc.vector.tensor_copy(sums[:], src[:, 0:2 * NH].rearrange("p (k h) -> p k h", k=2)).then_inc(free, 1)
                dve.drain()
                nc.vector.tensor_scalar(nsum[:], sums[:, 0, :], -1.0, None, ALU.mult)
                nc.vector.tensor_tensor(to_end[:], sums[:, 1, :], sums[:, 0, :], ALU.subtract)
                dve.drain()
                dve.sem_inc(sums_ready.sem, 1)

            def turn(t, u, first=False):
                back, front = t is not None, u is not None
                if front:
                    rows(u)
                if back:
                    tokens(t)
                    if not first:
                        scaled(t - 1)
                    begin_y(t)
                if front:
                    middle(u)
                if back:
                    decays(t, 0)
                    decays(t, 1)
                if front:
                    softplus(u)
                    convolve(nc.vector, dve, HALF, CB, u)
                if back:
                    decays(t, 2)
                    decays(t, 3)
                if front:
                    rates(u)
                if back:
                    finish(t)
                if front:
                    summed(u)

            nc.vector.memset(state[:], 0.0)
            dve.wait_ge(rates_ready, 1)
            nc.vector.tensor_scalar(rate[:], rate[:], -1.0, None, ALU.mult)
            dve.drain()
            dve.sem_inc(consts_ready, 1)
            for e in (hT_ready, xbc_ready, dt_raw_ready, dt_u_ready, decay_ready, sums_ready, bm_ready, xdt_ready, xend_ready,
                      scan_ready, y_gated, state_ready, out_ready):
                dve.sem_inc(e.sem, 1)
            turn(None, 0)
            turn(0, 1, first=True)
            with dve.Fori(1, TILES - 1) as t:
                turn(t, t + 1)
            turn(TILES - 1, None)
            scaled(TILES - 1)
            for h in range(2):
                dve.wait_ge(state_turned, h + 1)
                nc.vector.tensor_copy(y[:, h * BANK:(h + 1) * BANK], psum[4 + h][:]).then_inc(state_copied, 1)


def ssd_sample_inputs(nc, io, psum, shared, w_zx, keep):
    ident, gain = shared["ident"], shared["gain_mix"]
    NH = SSD_HEADS
    with Stage(nc) as stage:
        sb, sem = stage.buffer, stage.semaphore

        x, junk = sb("sin_x", [DEC, D]), sb("sin_junk", [DEC, D])
        ms, rstd, half = sb("sin_ms", [DEC, 1]), sb("sin_rstd", [DEC, 1]), sb("sin_half", [DEC, 1])
        hT = sb("sin_hT", [P, DB, DEC])
        past = sb("sin_past", [DEC, CONV, CONV_DIM])
        weights = sb("sin_weights", [DEC, CONV + 1, CONV_DIM])
        cv, tap = sb("sin_cv", [DEC, CONV_DIM]), sb("sin_tap", [DEC, CONV_DIM])
        dt_bias = sb("sin_dt_bias", [DEC, NH])
        raw, neg, e, u, err, dt = (sb("sin_" + n, [DEC, NH]) for n in ("raw", "neg", "e", "u", "err", "dt"))
        loaded, x_in, x_turned = sem("sin_loaded"), sem("sin_x_in"), sem("sin_x_turned")
        ms_ready, rstd_ready, hT_ready, projected = sem("sin_ms_ready"), sem("sin_rstd_ready"), sem("sin_hT_ready"), sem("sin_projected")
        new_ready, taps_done, cv_ready = sem("sin_new_ready"), sem("sin_taps_done"), sem("sin_cv_ready")
        neg_ready, e_ready, u_ready, log_ready, dt_ready = (sem("sin_" + n) for n in ("neg_ready", "e_ready", "u_ready", "log_ready", "dt_ready"))
        stored = sem("sin_stored")
        block = stage.block()

        @block.sync
        def _(sp):
            sp.dma_start(x[:], io["x_sample"]).then_inc(x_in, 16)
            sp.dma_start(past[:, 0:CONV - 1, :], io["state_conv"]).then_inc(loaded, 16)
            for k in range(CONV):
                sp.dma_start(weights[:, k, :], io["conv_w"][k:k + 1, :].broadcast_to([DEC, CONV_DIM])).then_inc(loaded, 16)
            sp.dma_start(weights[:, CONV, :], io["conv_b"].broadcast_to([DEC, CONV_DIM])).then_inc(loaded, 16)
            sp.dma_start(dt_bias[:], io["dt_bias"].broadcast_to([DEC, NH])).then_inc(loaded, 16)
            sp.wait_ge(new_ready, 1)
            sp.dma_start(io["s_conv"], past[:, 1:CONV, :]).then_inc(stored, 16)
            sp.wait_ge(dt_ready, 1)
            sp.dma_start(io["dts"], dt[:]).then_inc(stored, 16)
            sp.wait_ge(cv_ready, 1)
            sp.dma_start(io["rows2"], cv[:, 0:D]).then_inc(stored, 16)
            sp.dma_start(io["bcs"], cv[:, D:CONV_DIM]).then_inc(stored, 16)
            sp.wait_ge(stored, 64)

        @block.tensor
        def _(pe):
            pe.wait_ge(x_in, 16)
            for b in range(DB):
                ins = nc.tensor.transpose(psum[0][:, b * DEC:(b + 1) * DEC], x[:, b * P:(b + 1) * P], ident[0:DEC, 0:DEC])
            ins.then_inc(x_turned, 1)
            pe.wait_ge(hT_ready, 1)
            for c in range(6):
                n = min(BANK, IN_COLS - 1536 - c * BANK)
                for b in range(DB):
                    ins = nc.tensor.matmul(psum[1 + c][0:DEC, 0:n], hT[:, b, :], w_zx[:, b, c * BANK:c * BANK + n],
                                           start=(b == 0), stop=(b == DB - 1))
                ins.then_inc(projected, 1)

        @block.scalar
        def _(act):
            act.wait_ge(x_in, 16)
            nc.scalar.activation(junk[:], x[:], ACT.Square, accum_out=ms[:]).then_inc(ms_ready, 1)
            act.wait_ge(rstd_ready, 1)
            act.wait_ge(projected, 2)
            for h in range(2):
                nc.scalar.activation(keep["gate"][:, h * BANK:(h + 1) * BANK], psum[1 + h][0:DEC, :], ACT.Silu, scale=rstd[:])
            act.wait_ge(taps_done, 1)
            nc.scalar.activation(cv[:], cv[:], ACT.Silu)
            act.drain()
            act.sem_inc(cv_ready, 1)
            nc.scalar.copy(keep["xs"][:], cv[:, 0:D])
            act.wait_ge(neg_ready, 1)
            nc.scalar.activation(e[:], neg[:], ACT.Exp).then_inc(e_ready, 1)
            act.wait_ge(u_ready, 1)
            nc.scalar.activation(neg[:], u[:], ACT.Ln).then_inc(log_ready, 1)
            act.drain()

        @block.gpsimd
        def _(pool):
            nc.gpsimd.memset(half[:], -0.5)
            pool.wait_ge(ms_ready, 1)
            nc.gpsimd.tensor_scalar(ms[:], ms[:], 1.0 / D, EPS, ALU.mult, ALU.add)
            pool.drain()
            nc.gpsimd.tensor_tensor(rstd[:], ms[:], half[:], ALU.pow).then_inc(rstd_ready, 1)

        @block.vector
        def _(dve):
            dve.wait_ge(x_turned, 1)
            nc.vector.tensor_tensor(hT[:], psum[0][:, 0:DB * DEC].rearrange("p (b t) -> p b t", b=DB),
                                    gain[:, :, None].broadcast_to([P, DB, DEC]), ALU.mult).then_inc(hT_ready, 1)
            dve.wait_ge(rstd_ready, 1)
            dve.wait_ge(projected, 6)
            nc.vector.tensor_scalar(raw[:], psum[6][0:DEC, 0:NH], rstd[:], None, ALU.mult)
            for c in range(3):
                nc.vector.tensor_scalar(past[:, CONV - 1, c * BANK:(c + 1) * BANK], psum[3 + c][0:DEC, :], rstd[:], None, ALU.mult)
            dve.wait_ge(loaded, 16 * (CONV + 3))
            dve.drain()
            dve.sem_inc(new_ready, 1)
            nc.vector.tensor_tensor(raw[:], raw[:], dt_bias[:], ALU.add)
            dve.drain()
            nc.vector.scalar_tensor_tensor(neg[:], raw[:], -1.0, raw[:], ALU.mult, ALU.min)
            nc.vector.tensor_scalar(raw[:], raw[:], 0.0, None, ALU.max)
            dve.drain()
            dve.sem_inc(neg_ready, 1)
            for k in range(CONV):
                nc.vector.tensor_tensor((tap if k else cv)[:], past[:, k, :], weights[:, k, :], ALU.mult)
                dve.drain()
                if k:
                    nc.vector.tensor_tensor(cv[:], cv[:], tap[:], ALU.add)
                    dve.drain()
            nc.vector.tensor_tensor(cv[:], cv[:], weights[:, CONV, :], ALU.add).then_inc(taps_done, 1)
            dve.wait_ge(e_ready, 1)
            nc.vector.tensor_scalar(u[:], e[:], 1.0, None, ALU.add).then_inc(u_ready, 1)
            dve.drain()
            nc.vector.scalar_tensor_tensor(err[:], u[:], -1.0, e[:], ALU.add, ALU.subtract)
            nc.vector.reciprocal(dt[:], u[:])
            dve.drain()
            nc.vector.tensor_tensor(err[:], err[:], dt[:], ALU.mult)
            dve.drain()
            nc.vector.tensor_tensor(raw[:], raw[:], err[:], ALU.subtract)
            dve.drain()
            dve.wait_ge(log_ready, 1)
            nc.vector.tensor_tensor(dt[:], raw[:], neg[:], ALU.add).then_inc(dt_ready, 1)


def ssd_sample_step(nc, io, shared, keep):
    NH = SSD_HEADS
    with Stage(nc) as stage:
        sb, sem = stage.buffer, stage.semaphore

        state = sb("step_state", [P, HD, STATE])
        wide = sb("step_wide", [P, HD, STATE])
        x, dt, rate, dec = sb("step_x", [P, HD]), sb("step_dt", [P, 1]), sb("step_rate", [P, 1]), sb("step_dec", [P, 1])
        bc = sb("step_bc", [P, 2, STATE])
        y_pairs = sb("step_y_pairs", [P, HD])
        y, xskip, junk, skip = sb("step_y", [DEC, D]), sb("step_xskip", [DEC, D]), sb("step_junk", [DEC, D]), sb("step_skip", [DEC, NH])
        ms, rstd, half = sb("step_ms", [DEC, 1]), sb("step_rstd", [DEC, 1]), sb("step_half", [DEC, 1])
        loaded, state_in, rate_ready = sem("step_loaded"), sem("step_state_in"), sem("step_rate_ready")
        drate_ready, dec_ready, state_ready, y_ready = sem("step_drate_ready"), sem("step_dec_ready"), sem("step_state_ready"), sem("step_y_ready")
        stored, y_in, gated, ms_ready, rstd_ready, out_ready = (sem("step_" + n) for n in ("stored", "y_in", "gated", "ms_ready", "rstd_ready", "out_ready"))
        block = stage.block()

        @block.sync
        def _(sp):
            sp.dma_start(x[:], io["rows2"].rearrange("b (h d) -> (b h) d", h=NH)).then_inc(loaded, 16)
            sp.dma_start(dt[:], io["dts"].rearrange("b (h a) -> (b h) a", a=1)).then_inc(loaded, 16)
            al = io["a_log"]
            for b in range(DEC):
                sp.dma_start(rate[b * NH:(b + 1) * NH, :], al.rearrange("a h -> h a")).then_inc(loaded, 16)
                for g in range(SSD_G):
                    lo = b * NH + g * SSD_HPG
                    src = io["bcs"][b:b + 1, :].rearrange("a (k g n) -> a k g n", k=2, g=SSD_G)[:, :, g, :]
                    sp.dma_start(bc[lo:lo + SSD_HPG, :, :], src.broadcast_to([SSD_HPG, 2, STATE])).then_inc(loaded, 16)
            sp.dma_start(skip[:], io["d_skip"].broadcast_to([DEC, NH])).then_inc(loaded, 16)
            sp.dma_start(state[:], io["state_ssm"]).then_inc(state_in, 16)
            sp.wait_ge(state_ready, 1)
            sp.dma_start(io["s_ssm"], state[:]).then_inc(stored, 16)
            sp.wait_ge(y_ready, 1)
            sp.dma_start(io["rows3"].rearrange("b (h d) -> (b h) d", h=NH), y_pairs[:]).then_inc(y_in, 16)
            sp.wait_ge(y_in, 16)
            sp.dma_start(y[:], io["rows3"]).then_inc(y_in, 16)
            sp.wait_ge(y_in, 32)
            sp.wait_ge(out_ready, 1)
            sp.dma_start(io["mixed"][SEQ:TOKENS, D:2 * D], y[:]).then_inc(stored, 16)
            sp.wait_ge(stored, 32)

        @block.scalar
        def _(act):
            act.wait_ge(loaded, 16 * (3 + 3 * DEC))
            nc.scalar.activation(rate[:], rate[:], ACT.Exp).then_inc(rate_ready, 1)
            act.wait_ge(drate_ready, 1)
            nc.scalar.activation(dec[:], dec[:], ACT.Exp).then_inc(dec_ready, 1)
            act.wait_ge(gated, 1)
            nc.scalar.activation(junk[:], y[:], ACT.Square, accum_out=ms[:]).then_inc(ms_ready, 1)

        @block.gpsimd
        def _(pool):
            nc.gpsimd.memset(half[:], -0.5)
            pool.wait_ge(ms_ready, 1)
            nc.gpsimd.tensor_scalar(ms[:], ms[:], 1.0 / D, EPS, ALU.mult, ALU.add)
            pool.drain()
            nc.gpsimd.tensor_tensor(rstd[:], ms[:], half[:], ALU.pow).then_inc(rstd_ready, 1)

        @block.vector
        def _(dve):
            dve.wait_ge(rate_ready, 1)
            nc.vector.tensor_scalar(dec[:], dt[:], rate[:], -1.0, ALU.mult, ALU.mult).then_inc(drate_ready, 1)
            nc.vector.tensor_scalar(x[:], x[:], dt[:], None, ALU.mult)
            dve.drain()
            nc.vector.tensor_tensor(wide[:], x[:, :, None].broadcast_to([P, HD, STATE]),
                                    bc[:, 0, None, :].broadcast_to([P, HD, STATE]), ALU.mult)
            dve.drain()
            dve.wait_ge(state_in, 16)
            dve.wait_ge(dec_ready, 1)
            nc.vector.scalar_tensor_tensor(state[:].rearrange("p d n -> p (d n)"), state[:].rearrange("p d n -> p (d n)"), dec[:],
                                           wide[:].rearrange("p d n -> p (d n)"), ALU.mult, ALU.add)
            dve.drain()
            dve.sem_inc(state_ready, 1)
            nc.vector.tensor_tensor(wide[:], state[:], bc[:, 1, None, :].broadcast_to([P, HD, STATE]), ALU.mult)
            dve.drain()
            nc.vector.tensor_reduce(y_pairs[:], wide[:], AX.X, ALU.add).then_inc(y_ready, 1)
            nc.vector.tensor_tensor(xskip[:].rearrange("b (h d) -> b h d", h=NH), keep["xs"][:].rearrange("b (h d) -> b h d", h=NH),
                                    skip[:, :, None].broadcast_to([DEC, NH, HD]), ALU.mult)
            dve.wait_ge(y_in, 32)
            dve.drain()
            nc.vector.tensor_tensor(y[:], y[:], xskip[:], ALU.add)
            dve.drain()
            nc.vector.tensor_tensor(y[:], y[:], keep["gate"][:], ALU.mult).then_inc(gated, 1)
            dve.drain()
            dve.wait_ge(rstd_ready, 1)
            nc.vector.tensor_scalar(y[:], y[:], rstd[:], None, ALU.mult).then_inc(out_ready, 1)


def memory_kv(nc, io, psum, shared, mkT, mv):
    ident, gain = shared["ident"], shared["gain_mem"]
    MT = N_MEM // P
    with Stage(nc) as stage:
        sb, sem = stage.buffer, stage.semaphore

        w_mk, w_mv = sb("w_mk", [P, DB, D]), sb("w_mv", [P, DB, D])
        x, junk = sb("mem_x", [P, MT, D]), sb("mem_junk", [P, D])
        hT = sb("mem_hT", [P, MT, DB, P])
        mk = sb("mem_k", [P, MT, D])
        ms, rstd, half = sb("mem_ms", [P, MT]), sb("mem_rstd", [P, MT]), sb("mem_half", [P, MT])
        x_in, wk_in, wv_in = sem("mem_x_in"), sem("mem_wk_in"), sem("mem_wv_in")
        turned, hT_ready, ms_ready, rstd_ready = sem("mem_turned"), sem("mem_hT_ready"), sem("mem_ms_ready"), sem("mem_rstd_ready")
        projected, k_ready, v_ready, k_turned, stored = (sem("mem_" + n) for n in ("projected", "k_ready", "v_ready", "k_turned", "stored"))
        block = stage.block()

        @block.sync
        def _(sp):
            sp.dma_start(x[:], io["mem_prompt"].rearrange("(m p) n -> p m n", p=P)).then_inc(x_in, 16)
            sp.dma_start(w_mk[:], io["w_mk"].rearrange("(b p) n -> p b n", p=P)).then_inc(wk_in, 16)
            sp.dma_start(w_mv[:], io["w_mv"].rearrange("(b p) n -> p b n", p=P)).then_inc(wv_in, 16)
            sp.wait_ge(k_ready, MT)
            sp.dma_start(io["p_mem_k"].rearrange("(m p) n -> p m n", p=P), mk[:]).then_inc(stored, 16)
            sp.wait_ge(v_ready, MT)
            sp.dma_start(io["p_mem_v"].rearrange("(m p) n -> p m n", p=P), mv[:]).then_inc(stored, 16)
            sp.wait_ge(stored, 32)

        @block.tensor
        def _(pe):
            pe.wait_ge(x_in, 16)
            for m in range(MT):
                for h in range(2):
                    for j in range(4):
                        b = 4 * h + j
                        ins = nc.tensor.transpose(psum[2 * m + h][:, j * P:(j + 1) * P], x[:, m, b * P:(b + 1) * P], ident[:])
                    ins.then_inc(turned, 1)
            for w, arrived, first in ((w_mk, wk_in, 4), (w_mv, wv_in, 0)):
                pe.wait_ge(arrived, 16)
                pe.wait_ge(hT_ready, 4)
                for m in range(MT):
                    for c in range(2):
                        for b in range(DB):
                            ins = nc.tensor.matmul(psum[first + 2 * m + c][:], hT[:, m, b, :], w[:, b, c * BANK:(c + 1) * BANK],
                                                   start=(b == 0), stop=(b == DB - 1))
                        ins.then_inc(projected, 1)
            for m in range(MT):
                pe.wait_ge(k_ready, m + 1)
                for h in range(2):
                    for j in range(4):
                        b = 4 * h + j
                        ins = nc.tensor.transpose(psum[4 + 2 * m + h][:, j * P:(j + 1) * P], mk[:, m, b * P:(b + 1) * P], ident[:])
                    ins.then_inc(k_turned, 1)

        @block.scalar
        def _(act):
            act.wait_ge(x_in, 16)
            for m in range(MT):
                nc.scalar.activation(junk[:], x[:, m, :], ACT.Square, accum_out=ms[:, m:m + 1])
                act.drain()
            act.sem_inc(ms_ready, 1)
            act.wait_ge(rstd_ready, 1)
            for m in range(MT):
                act.wait_ge(projected, 2 * m + 2)
                for c in range(2):
                    nc.scalar.activation(mk[:, m, c * BANK:(c + 1) * BANK], psum[4 + 2 * m + c][:], ACT.Copy, scale=rstd[:, m:m + 1])
                act.drain()
                act.sem_inc(k_ready, 1)
            for m in range(MT):
                act.wait_ge(projected, 4 + 2 * m + 2)
                for c in range(2):
                    nc.scalar.activation(mv[:, m, c * BANK:(c + 1) * BANK], psum[2 * m + c][:], ACT.Copy, scale=rstd[:, m:m + 1])
                act.drain()
                act.sem_inc(v_ready, 1)

        @block.gpsimd
        def _(pool):
            nc.gpsimd.memset(half[:], -0.5)
            pool.wait_ge(ms_ready, 1)
            nc.gpsimd.tensor_scalar(ms[:], ms[:], 1.0 / D, EPS, ALU.mult, ALU.add)
            pool.drain()
            nc.gpsimd.tensor_tensor(rstd[:], ms[:], half[:], ALU.pow).then_inc(rstd_ready, 1)

        @block.vector
        def _(dve):
            for m in range(MT):
                for h in range(2):
                    dve.wait_ge(turned, 2 * m + h + 1)
                    nc.vector.tensor_tensor(hT[:, m, 4 * h:4 * h + 4, :], psum[2 * m + h][:].rearrange("p (b t) -> p b t", b=4),
                                            gain[:, 4 * h:4 * h + 4, None].broadcast_to([P, 4, P]), ALU.mult).then_inc(hT_ready, 1)
            for m in range(MT):
                for h in range(2):
                    dve.wait_ge(k_turned, 2 * m + h + 1)
                    nc.vector.tensor_copy(mkT[:, 4 * h:4 * h + 4, m * P:(m + 1) * P], psum[4 + 2 * m + h][:].rearrange("p (b t) -> p b t", b=4))
            dve.drain()


def memory_read(nc, io, psum, shared, w_out, w_mq, w_mo, mkT, mv):
    ident = shared["ident"]
    with Stage(nc) as stage:
        sb, sem, event = stage.buffer, stage.semaphore, stage.event

        mixed = sb("read_mixed", [P, 2 * D])
        x = sb("read_x", [P, D])
        mT = sb("read_mT", [P, 2 * DB, P])
        x1 = sb("read_x1", [P, D])
        hT = sb("read_hT", [P, DB, P])
        qT = sb("read_qT", [P, DB, P])
        p = sb("read_p", [P, MEM_HEADS, N_MEM])
        pT = sb("read_pT", [P, MEM_HEADS, 2, P])
        oT = sb("read_oT", [P, DB, P])
        ms, rstd, scale = sb("read_ms", [P, 1]), sb("read_rstd", [P, 1]), sb("read_scale", [P, 1])
        half, part = sb("read_half", [P, 1]), sb("read_part", [P, 1])
        top, total = sb("read_top", [P, MEM_HEADS]), sb("read_total", [P, MEM_HEADS])
        xn, gain_ffn = sb("read_xn", [P, D]), sb("read_gain_ffn", [P, D])
        o = p[:].rearrange("p h m -> p (h m)")

        order = [("m0", 0), ("m1", 1), ("m2", 0), ("m3", 1), ("r0", 2), ("r1", 3), ("h0", 0), ("h1", 1),
                 ("q0", 4), ("q1", 5), ("s0", 6), ("s1", 7), ("t0", 0), ("t1", 1), ("o0", 2), ("o1", 3),
                 ("u0", 0), ("u1", 1), ("y0", 4), ("y1", 5)]
        fills = Fills(sem, "read", order)
        w_out_in, w_mq_in, w_mo_in = sem("read_w_out"), sem("read_w_mq"), sem("read_w_mo")
        mixed_in, x_in = event("read_mixed_in", 1, 16), event("read_x_in", 1, 16)
        mixed_turned, x_added = event("read_mixed_turned"), event("read_x_added")
        mT_ready, mT_used = event("read_mT_ready", 4), event("read_mT_used")
        x1_ready = event("read_x1_ready", 2)
        ms_ready, rstd_ready, scale_ready = event("read_ms_ready"), event("read_rstd_ready"), event("read_scale_ready")
        hT_ready, hT_used, qT_ready = event("read_hT_ready"), event("read_hT_used"), event("read_qT_ready")
        ntop_ready, p_ready, p_turned, pT_ready, o_ready, oT_ready = (
            event("read_" + n) for n in ("ntop_ready", "p_ready", "p_turned", "pT_ready", "o_ready", "oT_ready"))
        x2_ready, stored = event("read_x2_ready"), event("read_stored", 1, 16)
        ms2_ready, rstd2_ready = event("read_ms2_ready"), event("read_rstd2_ready")
        xn_ready, xn_stored = event("read_xn_ready"), event("read_xn_stored", 1, 16)
        gain_in = sem("read_gain_in")
        block = stage.block()

        @block.sync
        def _(sp):
            for e in (mixed_in, x_in, stored, xn_stored):
                sp.sem_inc(e.sem, 16)
            sp.dma_start(gain_ffn[:], io["norm_ffn_w"].broadcast_to([P, D])).then_inc(gain_in, 16)
            sp.dma_start(w_out[:], io["w_out"].rearrange("(b p) n -> p b n", p=P)).then_inc(w_out_in, 16)
            sp.dma_start(w_mq[:], io["w_mq"].rearrange("(b p) n -> p b n", p=P)).then_inc(w_mq_in, 16)
            sp.dma_start(w_mo[:], io["w_mo"].rearrange("(b p) n -> p b n", p=P)).then_inc(w_mo_in, 16)
            with sp.Fori(0, TILES) as t:
                rows = bass.ds(t * P, P)
                sp.wait_ge(mixed_turned.sem, mixed_turned.last(t))
                sp.dma_start(mixed[:], io["mixed"][rows, :]).then_inc(mixed_in.sem, 16)
                sp.wait_ge(x_added.sem, x_added.last(t))
                sp.dma_start(x[:], io["x_prompt"][rows, :]).then_inc(x_in.sem, 16)
                sp.wait_ge(x2_ready.sem, x2_ready.this(t))
                sp.dma_start(io["x2"][rows, :], x1[:]).then_inc(stored.sem, 16)
                sp.wait_ge(xn_ready.sem, xn_ready.this(t))
                sp.dma_start(io["xn"][rows, :], xn[:]).then_inc(xn_stored.sem, 16)
            sp.wait_ge(stored.sem, stored.this(TILES - 1))
            sp.wait_ge(xn_stored.sem, xn_stored.this(TILES - 1))

        @block.tensor
        def _(pe):
            def begin(f, t):
                pe.wait_ge(fills.free[fills.bank(f)], fills.at(f, t))
                return psum[fills.bank(f)]

            def turn_blocks(prefix, src, t, n=2):
                for h in range(n):
                    out = begin(f"{prefix}{h}", t)
                    for j in range(4):
                        ins = nc.tensor.transpose(out[:, j * P:(j + 1) * P], src[:, (4 * h + j) * P:(4 * h + j + 1) * P], ident[:])
                    ins.then_inc(fills.full[fills.bank(f"{prefix}{h}")], 1)

            def turn(t):
                pe.wait_ge(mixed_in.sem, mixed_in.this(t))
                turn_blocks("m", mixed, t, 4)
                pe.drain()
                pe.sem_inc(mixed_turned.sem, 1)
                pe.wait_ge(mT_ready.sem, mT_ready.this(t, 4))
                for c in range(2):
                    out = begin(f"r{c}", t)
                    for b in range(2 * DB):
                        ins = nc.tensor.matmul(out[:], mT[:, b, :], w_out[:, b, c * BANK:(c + 1) * BANK],
                                               start=(b == 0), stop=(b == 2 * DB - 1))
                    ins.then_inc(fills.full[fills.bank(f"r{c}")], 1)
                pe.drain()
                pe.sem_inc(mT_used.sem, 1)
                pe.wait_ge(x1_ready.sem, x1_ready.this(t, 2))
                turn_blocks("h", x1, t)
                pe.wait_ge(hT_ready.sem, hT_ready.this(t))
                for h in range(2):
                    out = begin(f"q{h}", t)
                    for j in range(4):
                        d = 4 * h + j
                        for b in range(DB):
                            ins = nc.tensor.matmul(out[:, j * P:(j + 1) * P], w_mq[:, b, d * P:(d + 1) * P], hT[:, b, :],
                                                   start=(b == 0), stop=(b == DB - 1))
                    ins.then_inc(fills.full[fills.bank(f"q{h}")], 1)
                pe.wait_ge(qT_ready.sem, qT_ready.this(t))
                for n in range(2):
                    out = begin(f"s{n}", t)
                    for r in range(2):
                        for k in range(2):
                            d = 2 * (2 * n + r) + k
                            ins = nc.tensor.matmul(out[:, r * N_MEM:(r + 1) * N_MEM], qT[:, d, :], mkT[:, d, :], start=(k == 0), stop=(k == 1))
                    ins.then_inc(fills.full[fills.bank(f"s{n}")], 1)
                pe.wait_ge(p_ready.sem, p_ready.this(t))
                turn_blocks("t", o, t)
                pe.drain()
                pe.sem_inc(p_turned.sem, 1)
                pe.wait_ge(pT_ready.sem, pT_ready.this(t))
                for n in range(2):
                    out = begin(f"o{n}", t)
                    for r in range(2):
                        h = 2 * n + r
                        for k in range(2):
                            ins = nc.tensor.matmul(out[:, r * MEM_HD:(r + 1) * MEM_HD], pT[:, h, k, :], mv[:, k, h * MEM_HD:(h + 1) * MEM_HD],
                                                   start=(k == 0), stop=(k == 1))
                    ins.then_inc(fills.full[fills.bank(f"o{n}")], 1)
                pe.wait_ge(o_ready.sem, o_ready.this(t))
                turn_blocks("u", o, t)
                pe.wait_ge(oT_ready.sem, oT_ready.this(t))
                for c in range(2):
                    out = begin(f"y{c}", t)
                    for b in range(DB):
                        ins = nc.tensor.matmul(out[:], oT[:, b, :], w_mo[:, b, c * BANK:(c + 1) * BANK], start=(b == 0), stop=(b == DB - 1))
                    ins.then_inc(fills.full[fills.bank(f"y{c}")], 1)

            fills.prime(pe)
            for e in (mixed_turned, mT_used, p_turned):
                pe.sem_inc(e.sem, 1)
            for s in (w_out_in, w_mq_in, w_mo_in):
                pe.wait_ge(s, 16)
            with pe.Fori(0, TILES) as t:
                turn(t)

        @block.scalar
        def _(act):
            def full(f, t):
                act.wait_ge(fills.full[fills.bank(f)], fills.at(f, t))
                return psum[fills.bank(f)]

            def copy_blocks(prefix, dst, ready, t):
                for h in range(2):
                    src = full(f"{prefix}{h}", t)
                    nc.scalar.copy(dst[:, 4 * h:4 * h + 4, :], src[:].rearrange("p (b t) -> p b t", b=4)
                                   ).then_inc(fills.free[fills.bank(f"{prefix}{h}")], 1)
                act.drain()
                act.sem_inc(ready.sem, 1)

            def turn(t):
                act.wait_ge(x1_ready.sem, x1_ready.this(t, 2))
                nc.scalar.activation(p[:].rearrange("p h m -> p (h m)"), x1[:], ACT.Square, accum_out=ms[:])
                act.drain()
                act.sem_inc(ms_ready.sem, 1)
                copy_blocks("q", qT, qT_ready, t)
                act.wait_ge(ntop_ready.sem, ntop_ready.this(t))
                for h in range(MEM_HEADS):
                    if h % 2 == 0:
                        src = full(f"s{h // 2}", t)
                    ins = nc.scalar.activation(p[:, h, :], src[:, (h % 2) * N_MEM:(h % 2 + 1) * N_MEM], ACT.Exp,
                                               bias=top[:, h:h + 1], scale=scale[:], accum_out=total[:, h:h + 1])
                act.drain()
                act.sem_inc(p_ready.sem, 1)
                for n in range(2):
                    act.sem_inc(fills.free[fills.bank(f"s{n}")], 1)
                copy_blocks("t", pT[:].rearrange("p h k t -> p (h k) t"), pT_ready, t)
                copy_blocks("u", oT, oT_ready, t)
                act.wait_ge(x2_ready.sem, x2_ready.this(t))
                act.wait_ge(xn_stored.sem, xn_stored.last(t))
                nc.scalar.activation(xn[:], x1[:], ACT.Square, accum_out=ms[:])
                act.drain()
                act.sem_inc(ms2_ready.sem, 1)

            for e in (ms2_ready, ms_ready, qT_ready, p_ready, pT_ready, oT_ready):
                act.sem_inc(e.sem, 1)
            with act.Fori(0, TILES) as t:
                turn(t)

        @block.gpsimd
        def _(pool):
            nc.gpsimd.memset(half[:], -0.5)
            nc.gpsimd.memset(part[:], 1.0 / D)
            pool.drain()
            pool.sem_inc(rstd_ready.sem, 1)
            pool.sem_inc(rstd2_ready.sem, 1)
            with pool.Fori(0, TILES) as t:
                for ready, done in ((ms_ready, rstd_ready), (ms2_ready, rstd2_ready)):
                    pool.wait_ge(ready.sem, ready.this(t))
                    nc.gpsimd.tensor_tensor(ms[:], ms[:], part[:], ALU.mult)
                    pool.drain()
                    nc.gpsimd.tensor_scalar(ms[:], ms[:], EPS, None, ALU.add)
                    pool.drain()
                    nc.gpsimd.tensor_tensor(rstd[:], ms[:], half[:], ALU.pow)
                    pool.drain()
                    pool.sem_inc(done.sem, 1)

        @block.vector
        def _(dve):
            def full(f, t):
                dve.wait_ge(fills.full[fills.bank(f)], fills.at(f, t))
                return psum[fills.bank(f)]

            def with_gain(dst, gain, prefix, first, t, n):
                for h in range(n):
                    src = full(f"{prefix}{first + h}", t)
                    nc.vector.tensor_tensor(dst[:, 4 * h:4 * h + 4, :], src[:].rearrange("p (b t) -> p b t", b=4),
                                            gain[:, 4 * h:4 * h + 4, None].broadcast_to([P, 4, P]), ALU.mult
                                            ).then_inc(fills.free[fills.bank(f"{prefix}{first + h}")], 1)

            def turn(t):
                dve.wait_ge(mT_used.sem, mT_used.last(t))
                with_gain(mT[:, 0:DB], shared["gain_att"], "m", 0, t, 2)
                with_gain(mT[:, DB:2 * DB], shared["gain_ssd"], "m", 2, t, 2)
                dve.drain()
                dve.sem_inc(mT_ready.sem, 4)
                dve.wait_ge(x_in.sem, x_in.this(t))
                dve.wait_ge(stored.sem, stored.last(t))
                for c in range(2):
                    src = full(f"r{c}", t)
                    cols = slice(c * BANK, (c + 1) * BANK)
                    nc.vector.tensor_tensor(x1[:, cols], src[:], x[:, cols], ALU.add).then_inc(fills.free[fills.bank(f"r{c}")], 1)
                dve.drain()
                dve.sem_inc(x1_ready.sem, 2)
                dve.sem_inc(x_added.sem, 1)
                with_gain(hT, shared["gain_read"], "h", 0, t, 2)
                dve.drain()
                dve.sem_inc(hT_ready.sem, 1)
                dve.wait_ge(rstd_ready.sem, rstd_ready.this(t))
                nc.vector.tensor_scalar(scale[:], rstd[:], MEM_HD ** -0.5, None, ALU.mult)
                for n in range(2):
                    src = full(f"s{n}", t)
                    nc.vector.tensor_reduce(top[:, 2 * n:2 * n + 2], src[:].rearrange("p (r m) -> p r m", r=2), AX.X, ALU.max)
                dve.drain()
                nc.vector.tensor_scalar(top[:], top[:], scale[:], -1.0, ALU.mult, ALU.mult)
                dve.drain()
                dve.sem_inc(ntop_ready.sem, 1)
                dve.wait_ge(p_ready.sem, p_ready.this(t))
                nc.vector.reciprocal(total[:], total[:])
                dve.drain()
                dve.wait_ge(p_turned.sem, p_turned.this(t))
                for n in range(2):
                    src = full(f"o{n}", t)
                    nc.vector.tensor_tensor(p[:, 2 * n:2 * n + 2, :], src[:].rearrange("p (r m) -> p r m", r=2),
                                            total[:, 2 * n:2 * n + 2, None].broadcast_to([P, 2, MEM_HD]), ALU.mult
                                            ).then_inc(fills.free[fills.bank(f"o{n}")], 1)
                dve.drain()
                dve.sem_inc(o_ready.sem, 1)
                for c in range(2):
                    src = full(f"y{c}", t)
                    cols = slice(c * BANK, (c + 1) * BANK)
                    nc.vector.tensor_tensor(x1[:, cols], src[:], x1[:, cols], ALU.add).then_inc(fills.free[fills.bank(f"y{c}")], 1)
                dve.drain()
                dve.sem_inc(x2_ready.sem, 1)
                dve.wait_ge(rstd2_ready.sem, rstd2_ready.this(t))
                nc.vector.scalar_tensor_tensor(xn[:], x1[:], rstd[:], gain_ffn[:], ALU.mult, ALU.mult)
                dve.drain()
                dve.sem_inc(xn_ready.sem, 1)

            dve.wait_ge(gain_in, 16)
            for e in (xn_ready, mT_ready, x1_ready, x_added, hT_ready, ntop_ready, o_ready, x2_ready):
                dve.sem_inc(e.sem, 1)
            with dve.Fori(0, TILES) as t:
                turn(t)


def memory_read_sample_query(nc, io, psum, shared, w_out, w_mq, x1):
    ident = shared["ident"]
    with Stage(nc) as stage:
        sb, sem = stage.buffer, stage.semaphore

        mixed, x, junk, q = sb("rsq_mixed", [DEC, 2 * D]), sb("rsq_x", [DEC, D]), sb("rsq_junk", [DEC, D]), sb("rsq_q", [DEC, D])
        mT, hT = sb("rsq_mT", [P, 2 * DB, DEC]), sb("rsq_hT", [P, DB, DEC])
        ms, rstd, half = sb("rsq_ms", [DEC, 1]), sb("rsq_rstd", [DEC, 1]), sb("rsq_half", [DEC, 1])
        loaded, turned, mT_ready, summed, x1_ready = (sem("rsq_" + n) for n in ("loaded", "turned", "mT_ready", "summed", "x1_ready"))
        x1_turned, hT_ready, ms_ready, rstd_ready, projected, q_ready, stored = (
            sem("rsq_" + n) for n in ("x1_turned", "hT_ready", "ms_ready", "rstd_ready", "projected", "q_ready", "stored"))
        block = stage.block()

        @block.sync
        def _(sp):
            sp.dma_start(mixed[:], io["mixed"][SEQ:TOKENS, :]).then_inc(loaded, 16)
            sp.dma_start(x[:], io["x_sample"]).then_inc(loaded, 16)
            sp.wait_ge(q_ready, 1)
            sp.dma_start(io["rows"], q[:]).then_inc(stored, 16)
            sp.wait_ge(stored, 16)

        @block.tensor
        def _(pe):
            pe.wait_ge(loaded, 32)
            for b in range(2 * DB):
                ins = nc.tensor.transpose(psum[0][:, b * DEC:(b + 1) * DEC], mixed[:, b * P:(b + 1) * P], ident[0:DEC, 0:DEC])
            ins.then_inc(turned, 1)
            pe.wait_ge(mT_ready, 1)
            for c in range(2):
                for b in range(2 * DB):
                    ins = nc.tensor.matmul(psum[1 + c][0:DEC, :], mT[:, b, :], w_out[:, b, c * BANK:(c + 1) * BANK],
                                           start=(b == 0), stop=(b == 2 * DB - 1))
            ins.then_inc(summed, 1)
            pe.wait_ge(x1_ready, 1)
            for b in range(DB):
                ins = nc.tensor.transpose(psum[3][:, b * DEC:(b + 1) * DEC], x1[:, b * P:(b + 1) * P], ident[0:DEC, 0:DEC])
            ins.then_inc(x1_turned, 1)
            pe.wait_ge(hT_ready, 1)
            for c in range(2):
                for b in range(DB):
                    ins = nc.tensor.matmul(psum[4 + c][0:DEC, :], hT[:, b, :], w_mq[:, b, c * BANK:(c + 1) * BANK],
                                           start=(b == 0), stop=(b == DB - 1))
            ins.then_inc(projected, 1)

        @block.scalar
        def _(act):
            act.wait_ge(x1_ready, 1)
            nc.scalar.activation(junk[:], x1[:], ACT.Square, accum_out=ms[:]).then_inc(ms_ready, 1)

        @block.gpsimd
        def _(pool):
            nc.gpsimd.memset(half[:], -0.5)
            pool.wait_ge(ms_ready, 1)
            nc.gpsimd.tensor_scalar(ms[:], ms[:], 1.0 / D, EPS, ALU.mult, ALU.add)
            pool.drain()
            nc.gpsimd.tensor_tensor(rstd[:], ms[:], half[:], ALU.pow).then_inc(rstd_ready, 1)

        @block.vector
        def _(dve):
            dve.wait_ge(turned, 1)
            for i, gain in enumerate((shared["gain_att"], shared["gain_ssd"])):
                ins = nc.vector.tensor_tensor(mT[:, i * DB:(i + 1) * DB, :],
                                              psum[0][:, i * DB * DEC:(i + 1) * DB * DEC].rearrange("p (b t) -> p b t", b=DB),
                                              gain[:, :, None].broadcast_to([P, DB, DEC]), ALU.mult)
            ins.then_inc(mT_ready, 1)
            dve.wait_ge(summed, 1)
            for c in range(2):
                cols = slice(c * BANK, (c + 1) * BANK)
                ins = nc.vector.tensor_tensor(x1[:, cols], psum[1 + c][0:DEC, :], x[:, cols], ALU.add)
            ins.then_inc(x1_ready, 1)
            dve.wait_ge(x1_turned, 1)
            nc.vector.tensor_tensor(hT[:], psum[3][:, 0:DB * DEC].rearrange("p (b t) -> p b t", b=DB),
                                    shared["gain_read"][:, :, None].broadcast_to([P, DB, DEC]), ALU.mult).then_inc(hT_ready, 1)
            dve.wait_ge(rstd_ready, 1)
            dve.wait_ge(projected, 1)
            for c in range(2):
                ins = nc.vector.tensor_scalar(q[:, c * BANK:(c + 1) * BANK], psum[4 + c][0:DEC, :], rstd[:], MEM_HD ** -0.5, ALU.mult, ALU.mult)
            ins.then_inc(q_ready, 1)


def memory_read_sample(nc, io, psum, shared, w_mo, x1):
    ident = shared["ident"]
    ROWS = DEC * MEM_HEADS
    with Stage(nc) as stage:
        sb, sem = stage.buffer, stage.semaphore

        k = sb("rs_k", [P, 2, 2, D])
        v = sb("rs_v", [P, 3, 2, D])
        q = sb("rs_q", [P, DEC, D])
        prod = sb("rs_prod", [P, 2, 2 * MEM_HEADS, MEM_HD])
        sT = sb("rs_sT", [P, 2, DEC, MEM_HEADS])
        p = sb("rs_p", [ROWS, N_MEM])
        ntop, total = sb("rs_ntop", [ROWS, 1]), sb("rs_total", [ROWS, 1])
        pT = sb("rs_pT", [P, 2, ROWS])
        oT = sb("rs_oT", [P, DB, DEC])
        xn, gain_ffn = sb("rs_xn", [DEC, D]), sb("rs_gain_ffn", [DEC, D])
        ms, rstd, half = sb("rs_ms", [DEC, 1]), sb("rs_rstd", [DEC, 1]), sb("rs_half", [DEC, 1])
        blank = sb("rs_blank", [P - DEC, D])
        gain_in, blank_ready, ms_ready, rstd_ready, xn_ready = (sem("rs_" + n) for n in ("gain_in", "blank_ready", "ms_ready", "rstd_ready", "xn_ready"))
        q_in = sem("rs_q_in")
        k_in = [sem(f"rs_k_in{i}") for i in range(2)]
        v_in = [sem(f"rs_v_in{i}") for i in range(3)]
        multiplied, reduced = sem("rs_multiplied"), sem("rs_reduced")
        s_turned, ntop_ready, p_exp, p_ready, p_turned, pT_ready = (
            sem("rs_" + n) for n in ("s_turned", "ntop_ready", "p_exp", "p_ready", "p_turned", "pT_ready"))
        valued, oT_ready, projected, x2_ready, stored = (sem("rs_" + n) for n in ("valued", "oT_ready", "projected", "x2_ready", "stored"))
        block = stage.block()

        @block.sync
        def _(sp):
            sp.dma_start(gain_ffn[:], io["norm_ffn_w"].broadcast_to([DEC, D])).then_inc(gain_in, 16)
            for b in range(DEC):
                sp.dma_start(q[:, b, :], io["rows"][b:b + 1, :].broadcast_to([P, D])).then_inc(q_in, 16)
            for b in range(DEC):
                if b >= 2:
                    sp.wait_ge(multiplied, b - 1)
                sp.dma_start(k[:, b % 2], io["cache_mem_k"][b].rearrange("(m p) n -> p m n", p=P)).then_inc(k_in[b % 2], 16)
            for b in range(DEC):
                if b >= 3:
                    sp.wait_ge(valued, b - 2)
                sp.dma_start(v[:, b % 3], io["cache_mem_v"][b].rearrange("(m p) n -> p m n", p=P)).then_inc(v_in[b % 3], 16)
            sp.wait_ge(x2_ready, 1)
            sp.dma_start(io["x2"][SEQ:TOKENS, :], x1[:]).then_inc(stored, 16)
            sp.wait_ge(xn_ready, 1)
            sp.dma_start(io["xn"][SEQ:TOKENS, :], xn[:]).then_inc(stored, 16)
            sp.wait_ge(blank_ready, 1)
            for name in ("x2", "xn"):
                sp.dma_start(io[name][TOKENS:SEQ + P, :], blank[:]).then_inc(stored, 16)
            sp.wait_ge(stored, 64)

        @block.tensor
        def _(pe):
            pe.wait_ge(reduced, DEC)
            for m in range(2):
                ins = nc.tensor.transpose(psum[0][0:ROWS, m * P:(m + 1) * P], sT[:, m].rearrange("p b h -> p (b h)"), ident[:])
            ins.then_inc(s_turned, 1)
            pe.wait_ge(p_ready, 1)
            for m in range(2):
                ins = nc.tensor.transpose(psum[1][:, m * ROWS:(m + 1) * ROWS], p[:, m * P:(m + 1) * P], ident[0:ROWS, 0:ROWS])
            ins.then_inc(p_turned, 1)
            pe.wait_ge(pT_ready, 1)
            for b in range(DEC):
                pe.wait_ge(v_in[b % 3], 16 * (b // 3 + 1))
                for d in range(DB):
                    row = b * MEM_HEADS + d // 2
                    for m in range(2):
                        ins = nc.tensor.matmul(psum[2][:, d * DEC + b:d * DEC + b + 1], v[:, b % 3, m, d * P:(d + 1) * P],
                                               pT[:, m, row:row + 1], start=(m == 0), stop=(m == 1))
                ins.then_inc(valued, 1)
            pe.wait_ge(oT_ready, 1)
            for c in range(2):
                for b in range(DB):
                    ins = nc.tensor.matmul(psum[3 + c][0:DEC, :], oT[:, b, :], w_mo[:, b, c * BANK:(c + 1) * BANK],
                                           start=(b == 0), stop=(b == DB - 1))
            ins.then_inc(projected, 1)

        @block.scalar
        def _(act):
            act.wait_ge(ntop_ready, 1)
            nc.scalar.activation(p[:], psum[0][0:ROWS, 0:N_MEM], ACT.Exp, bias=ntop[:], accum_out=total[:])
            act.drain()
            act.sem_inc(p_exp, 1)
            act.wait_ge(x2_ready, 1)
            nc.scalar.activation(xn[:], x1[:], ACT.Square, accum_out=ms[:]).then_inc(ms_ready, 1)

        @block.gpsimd
        def _(pool):
            nc.gpsimd.memset(blank[:], 0.0).then_inc(blank_ready, 1)
            nc.gpsimd.memset(half[:], -0.5)
            pool.wait_ge(ms_ready, 1)
            nc.gpsimd.tensor_scalar(ms[:], ms[:], 1.0 / D, EPS, ALU.mult, ALU.add)
            pool.drain()
            nc.gpsimd.tensor_tensor(rstd[:], ms[:], half[:], ALU.pow).then_inc(rstd_ready, 1)

        @block.vector
        def _(dve):
            dve.wait_ge(q_in, 16 * DEC)
            for b in range(DEC):
                dve.wait_ge(k_in[b % 2], 16 * (b // 2 + 1))
                nc.vector.tensor_tensor(prod[:, b % 2].rearrange("p (m h) d -> p m (h d)", m=2), k[:, b % 2],
                                        q[:, b, None, :].broadcast_to([P, 2, D]), ALU.mult).then_inc(multiplied, 1)
                dve.drain()
                nc.vector.tensor_reduce(sT[:, :, b, :], prod[:, b % 2].rearrange("p (m h) d -> p m h d", m=2), AX.X, ALU.add).then_inc(reduced, 1)
            dve.wait_ge(s_turned, 1)
            nc.vector.tensor_reduce(ntop[:], psum[0][0:ROWS, 0:N_MEM], AX.X, ALU.max)
            dve.drain()
            nc.vector.tensor_scalar(ntop[:], ntop[:], -1.0, None, ALU.mult).then_inc(ntop_ready, 1)
            dve.wait_ge(p_exp, 1)
            nc.vector.reciprocal(total[:], total[:])
            dve.drain()
            nc.vector.tensor_scalar(p[:], p[:], total[:], None, ALU.mult).then_inc(p_ready, 1)
            dve.wait_ge(p_turned, 1)
            nc.vector.tensor_copy(pT[:], psum[1][:, 0:2 * ROWS].rearrange("p (m r) -> p m r", m=2)).then_inc(pT_ready, 1)
            dve.wait_ge(valued, DEC)
            nc.vector.tensor_copy(oT[:], psum[2][:, 0:DB * DEC].rearrange("p (d b) -> p d b", d=DB)).then_inc(oT_ready, 1)
            dve.wait_ge(projected, 1)
            for c in range(2):
                cols = slice(c * BANK, (c + 1) * BANK)
                ins = nc.vector.tensor_tensor(x1[:, cols], psum[3 + c][0:DEC, :], x1[:, cols], ALU.add)
            ins.then_inc(x2_ready, 1)
            dve.wait_ge(gain_in, 16)
            dve.wait_ge(rstd_ready, 1)
            nc.vector.scalar_tensor_tensor(xn[:], x1[:], rstd[:], gain_ffn[:], ALU.mult, ALU.mult).then_inc(xn_ready, 1)


def expert_mix(nc, io, psum, shared, idx, gate):
    ident = shared["ident"]
    PAIRS = PEER_HEADS // 2
    PER = 2 * TOPK
    RING = 8
    USES = PER // RING
    with Stage(nc) as stage:
        sb, sem, event = stage.buffer, stage.semaphore, stage.event
        w_pq = sb("w_pq", [P, DB, 2 * D])
        keysT = sb("ex_keysT", [P, 2 * PEER_HEADS * N_KEYS])
        rows = sb("ex_rows", [P, D])
        x_next = sb("ex_x_next", [P, D])
        x_cur = sb("ex_x_cur", [P, D])
        xT = sb("ex_xT", [P, DB, P])
        final_gain = sb("ex_final_gain", [P, D])
        total = sb("ex_total", [P, D])
        u_ring = sb("ex_u_ring", [P, RING, D])
        v_ring = sb("ex_v_ring", [P, RING, D])
        diag = sb("ex_diag", [P, 2, TOPK, P])
        u_idx, v_idx = sb("ex_u_idx", [P, 2, TOPK], U32), sb("ex_v_idx", [P, 2, TOPK], U32)
        dots, weight = sb("ex_dots", [P, 2, TOPK]), sb("ex_weight", [P, 2, TOPK])
        q, qT = sb("ex_q", [P, 2 * P]), sb("ex_qT", [P, 2, P])
        sub, sub_less = sb("ex_sub", [P, 2, N_KEYS]), sb("ex_sub_less", [P, 2, N_KEYS])
        top, top_at, top_atf = sb("ex_top", [P, 2, TOPK]), sb("ex_top_at", [P, 2, TOPK], U32), sb("ex_top_atf", [P, 2, TOPK])
        cand, cand_less = sb("ex_cand", [P, TOPK * TOPK]), sb("ex_cand_less", [P, TOPK * TOPK])
        best, best_at = sb("ex_best", [P, TOPK]), sb("ex_best_at", [P, TOPK], U32)
        halves, halvesf = sb("ex_halves", [P, 2, TOPK], U32), sb("ex_halvesf", [P, 2, TOPK])
        match = sb("ex_match", [P, 2 * TOPK, TOPK])
        picked, joined = sb("ex_picked", [P, 2, TOPK]), sb("ex_joined", [P, TOPK])
        count16 = sb("ex_count16", [P, TOPK])
        nbest, esum = sb("ex_nbest", [P, 1]), sb("ex_esum", [P, 1])
        ms, root, rstd, err = (sb("ex_" + n, [P, 1]) for n in ("ms", "root", "rstd", "err"))
        squares = sb("ex_squares", [P, D])
        raw_keys = u_ring[:, 0:2, :].rearrange("p a (b d) -> p (a b) d", d=P)

        route_fills = Fills(sem, "route", [("q0", 0), ("qT0", 1), ("sub0", 2), ("q1", 0), ("qT1", 1), ("sub1", 2)])
        prep_fills = Fills(sem, "prep", [("xT0", 3), ("xT1", 4)])
        loaded, keys_in, keys_turned, keys_ready, w_in = (sem("ex_" + n) for n in ("loaded", "keys_in", "keys_turned", "keys_ready", "w_in"))
        x_in, x_turned, x_moved = event("ex_x_in", 1, 16), event("ex_x_turned"), event("ex_x_moved")
        rows_in, rows_used = event("ex_rows_in", 1, 16), event("ex_rows_used")
        xT_ready = event("ex_xT_ready")
        mix_over, mix_read = event("ex_mix_over"), event("ex_mix_read")
        var_ready, root_ready, out_ready, stored = event("ex_var_ready"), event("ex_root_ready"), event("ex_out_ready"), event("ex_stored", 1, 16)
        ms_ready = event("ex_ms_ready")
        routed_pe = event("ex_routed_pe", 2)
        q_ready, qT_ready, sub_ready = event("ex_q_ready", 2), event("ex_qT_ready", 2), event("ex_sub_ready", 2)
        best_ready, exp_ready = event("ex_best_ready", 2), event("ex_exp_ready", 2)
        u_idx_ready = event("ex_u_idx_ready", 2)
        v_idx_ready = [event(f"ex_v_idx_ready{half}") for half in range(2)]
        dots_ready, gelu_ready, weight_ready, diag_ready = (
            event("ex_" + n, 2) for n in ("dots_ready", "gelu_ready", "weight_ready", "diag_ready"))
        mixed = [event(f"ex_mixed{half}") for half in range(2)]
        u_in = [sem(f"ex_u_in{r}") for r in range(RING)]
        v_in = [sem(f"ex_v_in{r}") for r in range(RING)]
        u_used, v_used = sem("ex_u_used"), sem("ex_v_used")
        gathers = sem("ex_gathers")
        block = stage.block()

        @block.sync
        def _(sp):
            def load_x(tile):
                sp.wait_ge(x_turned.sem, x_turned.last(tile))
                sp.wait_ge(x_moved.sem, x_moved.last(tile))
                sp.dma_start(x_next[:], io["xn"][bass.ds(tile * P, P), :]).then_inc(x_in.sem, 16)

            def load_rows(tile):
                sp.wait_ge(rows_used.sem, rows_used.last(tile))
                sp.dma_start(rows[:], io["x2"][bass.ds(tile * P, P), :]).then_inc(rows_in.sem, 16)

            for e in (x_in, rows_in, stored):
                sp.sem_inc(e.sem, 16)
            sp.dma_start(raw_keys, io["peer_keys"].rearrange("h k d -> k h d")).then_inc(keys_in, 16)
            load_x(0)
            sp.dma_start(w_pq[:], io["peer_wq"].rearrange("(b p) n -> p b n", p=P)).then_inc(w_in, 16)
            sp.dma_start(final_gain[:], io["final_norm_w"].broadcast_to([P, D])).then_inc(loaded, 16)
            load_rows(0)
            with sp.Fori(0, TILES) as t:
                load_x(t + 1)
                load_rows(t + 1)
                sp.wait_ge(out_ready.sem, out_ready.this(t))
                sp.dma_start(io["y_prompt"][bass.ds(t * P, P), :], total[:]).then_inc(stored.sem, 16)
            sp.wait_ge(stored.sem, stored.this(TILES - 1))
            sp.wait_ge(rows_in.sem, rows_in.this(TILES))

        @block.gpsimd
        def _(pool):
            def gather(table, ring, places, arrived, used, n, half, s):
                j = half * TOPK + s
                pool.wait_ge(used, n * PER + (j + 1))
                pool.sem_inc(gathers, 1)
                nc.gpsimd.indirect_dma_start(
                    out=ring[:, j % RING, :], out_offset=None, in_=io[table],
                    in_offset=bass.IndirectOffsetOnAxis(ap=places[:, half, s:s + 1], axis=0),
                ).then_inc(arrived[j % RING], 16)

            def rows_u(n, half, s):
                gather("peer_u", u_ring, u_idx, u_in, u_used, n, half, s)

            def rows_v(n, half, s):
                gather("peer_v", v_ring, v_idx, v_in, v_used, n, half, s)

            def pair(n, first=False):
                pool.wait_ge(u_idx_ready.sem, u_idx_ready.this(n, 1))
                pool.sem_inc(gathers, 1)
                if not first:
                    pool.wait_ge(v_idx_ready[1].sem, v_idx_ready[1].last(n))
                    pool.sem_inc(gathers, 1)
                for s in range(TOPK):
                    rows_u(n, 0, s)
                    if not first:
                        rows_v(n - 1, 1, s)
                pool.wait_ge(u_idx_ready.sem, u_idx_ready.this(n, 2))
                pool.sem_inc(gathers, 1)
                pool.wait_ge(v_idx_ready[0].sem, v_idx_ready[0].this(n))
                pool.sem_inc(gathers, 1)
                for s in range(TOPK):
                    rows_u(n, 1, s)
                    rows_v(n, 0, s)

            nc.gpsimd.iota(count16[:], [[1, TOPK]], base=0, channel_multiplier=0, allow_small_or_imprecise_dtypes=True)
            pool.drain()
            pool.sem_inc(loaded, 16)
            pool.wait_ge(keys_ready, 2)
            pair(0, first=True)
            with pool.Fori(1, TILES * PAIRS) as n:
                pair(n)
            pool.wait_ge(v_idx_ready[1].sem, v_idx_ready[1].last(TILES * PAIRS))
            for s in range(TOPK):
                rows_v(TILES * PAIRS - 1, 1, s)

        @block.tensor
        def _(pe):
            def prepare(tile):
                pe.wait_ge(x_in.sem, x_in.this(tile))
                for h in range(2):
                    f = f"xT{h}"
                    bank = prep_fills.bank(f)
                    pe.wait_ge(prep_fills.free[bank], prep_fills.at(f, tile))
                    for j in range(4):
                        ins = nc.tensor.transpose(psum[bank][:, j * P:(j + 1) * P], x_next[:, (4 * h + j) * P:(4 * h + j + 1) * P], ident[:])
                    ins.then_inc(prep_fills.full[bank], 1)
                pe.drain()
                pe.sem_inc(x_turned.sem, 1)

            def route(m, tile, head, half):
                def begin(name):
                    pe.wait_ge(route_fills.free[route_fills.bank(name)], route_fills.at(name, m))
                    return psum[route_fills.bank(name)], route_fills.full[route_fills.bank(name)]

                out, full = begin(f"q{half}")
                if half == 0:
                    pe.wait_ge(xT_ready.sem, xT_ready.this(tile))
                for b in range(DB):
                    ins = nc.tensor.matmul(out[:, 0:2 * P], xT[:, b, :], w_pq[:, b, bass.ds(head * 2 * P, 2 * P)], start=(b == 0), stop=(b == DB - 1))
                ins.then_inc(full, 1)
                pe.wait_ge(q_ready.sem, q_ready.this(m, half + 1))
                out, full = begin(f"qT{half}")
                for p in range(2):
                    ins = nc.tensor.transpose(out[:, p * P:(p + 1) * P], q[:, p * P:(p + 1) * P], ident[:])
                ins.then_inc(full, 1)
                pe.wait_ge(qT_ready.sem, qT_ready.this(m, half + 1))
                out, full = begin(f"sub{half}")
                for p in range(2):
                    ins = nc.tensor.matmul(out[:, p * P:(p + 1) * P], qT[:, p, :], keysT[:, bass.ds((head * 2 + p) * P, P)], start=True, stop=True)
                ins.then_inc(full, 1)
                pe.drain()
                pe.sem_inc(routed_pe.sem, 1)

            def mix(n, half):
                pe.wait_ge(diag_ready.sem, diag_ready.this(n, half + 1))
                for s in range(TOPK):
                    j = half * TOPK + s
                    pe.wait_ge(v_in[j % RING], 16 * (n * USES + (j // RING + 1)))
                    for c in range(2):
                        ins = nc.tensor.matmul(psum[6 + c][:], diag[:, half, s, :], v_ring[:, j % RING, c * BANK:(c + 1) * BANK],
                                               start=False, stop=False, skip_group_check=True)
                    ins.then_inc(v_used, 1)
                pe.drain()
                pe.sem_inc(mixed[half].sem, 1)

            def begin_sum(t):
                pe.wait_ge(rows_in.sem, rows_in.this(t))
                pe.wait_ge(mix_read.sem, mix_read.last(t))
                for c in range(2):
                    nc.tensor.matmul(psum[6 + c][:], ident[:], rows[:, c * BANK:(c + 1) * BANK], start=True, stop=False, skip_group_check=True)
                pe.drain()
                pe.sem_inc(rows_used.sem, 1)

            def pair(n, tile, i, boundary=False, first=False):
                route(n + 1, tile, i * 2, 0)
                if not first:
                    mix(n - 1, 1)
                if boundary:
                    pe.sem_inc(mix_over.sem, 1)
                if boundary or first:
                    begin_sum(tile)
                route(n + 1, tile, i * 2 + 1, 1)
                mix(n, 0)

            def turn(t, first=False):
                n = t * PAIRS
                pair(n, t, 1, boundary=not first, first=first)
                with pe.Fori(1, PAIRS - 1) as i:
                    pair(n + i, t, i + 1)
                prepare(t + 1)
                pair(n + PAIRS - 1, t + 1, 0)

            for f in (route_fills, prep_fills):
                f.prime(pe)
            for e in (x_turned, rows_used, routed_pe, mixed[0], mixed[1], mix_over):
                pe.sem_inc(e.sem, 1)
            pe.sem_inc(v_used, RING)
            pe.wait_ge(keys_in, 16)
            for n in range(4):
                for j in range(4):
                    ins = nc.tensor.transpose(psum[4 + n][:, j * P:(j + 1) * P], raw_keys[:, 4 * n + j, :], ident[:])
                ins.then_inc(keys_turned, 1)
            pe.wait_ge(keys_ready, 2)
            prepare(0)
            pe.wait_ge(w_in, 16)
            for half in range(2):
                route(0, 0, half, half)
            turn(0, first=True)
            with pe.Fori(1, TILES) as t:
                turn(t)
            mix(TILES * PAIRS - 1, 1)
            pe.sem_inc(mix_over.sem, 1)
            with pe.Fori(1, PAIRS) as i:
                for half in range(2):
                    route(i + TILES * PAIRS, TILES, i * 2 + half, half)

        @block.scalar
        def _(act):
            def prepare(tile):
                act.wait_ge(routed_pe.sem, routed_pe.last(tile * PAIRS))
                for h in range(2):
                    bank = prep_fills.bank(f"xT{h}")
                    act.wait_ge(prep_fills.full[bank], prep_fills.at(f"xT{h}", tile))
                    nc.scalar.copy(xT[:, 4 * h:4 * h + 4, :], psum[bank][:].rearrange("p (b t) -> p b t", b=4)).then_inc(prep_fills.free[bank], 1)
                act.drain()
                act.sem_inc(xT_ready.sem, 1)

            def queries(m, half):
                for name, dst, ready in ((f"q{half}", q[:], q_ready), (f"qT{half}", qT[:].rearrange("p a t -> p (a t)"), qT_ready)):
                    bank = route_fills.bank(name)
                    act.wait_ge(route_fills.full[bank], route_fills.at(name, m))
                    nc.scalar.copy(dst, psum[bank][:, 0:2 * P]).then_inc(route_fills.free[bank], 1)
                    act.drain()
                    act.sem_inc(ready.sem, 1)

            def exponentials(m, half):
                act.wait_ge(best_ready.sem, best_ready.this(m, half + 1))
                nc.scalar.activation(best[:], best[:], ACT.Exp, bias=nbest[:], accum_out=esum[:])
                act.drain()
                act.sem_inc(exp_ready.sem, 1)

            def weights(n, half):
                act.wait_ge(dots_ready.sem, dots_ready.this(n, half + 1))
                nc.scalar.activation(dots[:, half, :], dots[:, half, :], ACT.Gelu)
                act.drain()
                act.sem_inc(gelu_ready.sem, 1)
                act.wait_ge(weight_ready.sem, weight_ready.this(n, half + 1))
                act.wait_ge(mixed[half].sem, mixed[half].last(n))
                for s in range(TOPK):
                    nc.scalar.activation(diag[:, half, s, :], ident[:], ACT.Copy, scale=weight[:, half, s:s + 1])
                act.drain()
                act.sem_inc(diag_ready.sem, 1)

            def finish(t):
                act.wait_ge(mix_over.sem, mix_over.this(t))
                act.wait_ge(stored.sem, stored.last(t))
                for c in range(2):
                    nc.scalar.copy(total[:, c * BANK:(c + 1) * BANK], psum[6 + c][:])
                act.drain()
                act.sem_inc(mix_read.sem, 1)
                nc.scalar.activation(squares[:], total[:], ACT.Square, accum_out=ms[:])
                act.drain()
                act.sem_inc(ms_ready.sem, 1)
                act.wait_ge(var_ready.sem, var_ready.this(t))
                nc.scalar.activation(root[:], ms[:], ACT.Sqrt)
                act.drain()
                act.sem_inc(root_ready.sem, 1)

            def pair(n, boundary=None):
                for half in range(2):
                    queries(n + 1, half)
                    weights(n, half)
                    exponentials(n + 1, half)
                    if boundary is not None and half == 0:
                        finish(boundary)

            def turn(t, first=False):
                n = t * PAIRS
                pair(n, boundary=None if first else t - 1)
                with act.Fori(1, PAIRS - 1) as i:
                    pair(n + i)
                prepare(t + 1)
                pair(n + PAIRS - 1)

            for e in (xT_ready, q_ready, qT_ready, exp_ready, gelu_ready, diag_ready, mix_read, ms_ready, root_ready):
                act.sem_inc(e.sem, 1)
            prepare(0)
            for half in range(2):
                queries(0, half)
                exponentials(0, half)
            turn(0, first=True)
            with act.Fori(1, TILES) as t:
                turn(t)
            finish(TILES - 1)
            with act.Fori(1, PAIRS) as i:
                for half in range(2):
                    queries(i + TILES * PAIRS, half)
                    exponentials(i + TILES * PAIRS, half)

        @block.vector
        def _(dve):
            def link(ins):
                dve.drain()

            def top16(values, less, out, at):
                link(nc.vector.max(out[:, 0:8], values))
                nc.vector.max_index(at[:, 0:8], out[:, 0:8], values)
                link(nc.vector.match_replace(less, out[:, 0:8], values, FAR))
                link(nc.vector.max(out[:, 8:16], less))
                link(nc.vector.max_index(at[:, 8:16], out[:, 8:16], less))

            def route(m, half, at):
                name = f"sub{half}"
                bank = route_fills.bank(name)
                dve.wait_ge(route_fills.full[bank], route_fills.at(name, m))
                link(nc.vector.tensor_copy(sub[:], psum[bank][:, 0:2 * P].rearrange("p (a k) -> p a k", a=2)).then_inc(route_fills.free[bank], 1))
                for a in range(2):
                    top16(sub[:, a, :], sub_less[:, a, :], top[:, a, :], top_at[:, a, :])
                nc.vector.tensor_copy(top_atf[:], top_at[:])
                link(nc.vector.tensor_tensor(cand[:].rearrange("p (i j) -> p i j", i=TOPK), top[:, 0, :, None].broadcast_to([P, TOPK, TOPK]),
                                             top[:, 1, None, :].broadcast_to([P, TOPK, TOPK]), ALU.add))
                top16(cand[:], cand_less[:], best, best_at)
                link(nc.vector.tensor_scalar(nbest[:], best[:, 0:1], -1.0, None, ALU.mult))
                dve.sem_inc(best_ready.sem, 1)
                nc.vector.tensor_scalar(halves[:, 0, :], best_at[:], 4, None, ALU.logical_shift_right)
                link(nc.vector.tensor_scalar(halves[:, 1, :], best_at[:], 15, None, ALU.bitwise_and))
                link(nc.vector.tensor_copy(halvesf[:], halves[:]))
                link(nc.vector.tensor_tensor(match[:], halvesf[:].rearrange("p a k -> p (a k)")[:, :, None].broadcast_to([P, 2 * TOPK, TOPK]),
                                             count16[:, None, :].broadcast_to([P, 2 * TOPK, TOPK]), ALU.is_equal))
                for a in range(2):
                    rows_a = slice(a * TOPK, (a + 1) * TOPK)
                    ins = nc.vector.tensor_tensor(match[:, rows_a, :], match[:, rows_a, :], top_atf[:, a, None, :].broadcast_to([P, TOPK, TOPK]), ALU.mult)
                link(ins)
                link(nc.vector.tensor_reduce(picked[:].rearrange("p a k -> p (a k)"), match[:], AX.X, ALU.add))
                link(nc.vector.scalar_tensor_tensor(joined[:], picked[:, 0, :], float(N_KEYS), picked[:, 1, :], ALU.mult, ALU.add))
                nc.vector.tensor_copy(idx[:, bass.ds(at, TOPK)], joined[:])
                dve.wait_ge(exp_ready.sem, exp_ready.this(m, half + 1))
                link(nc.vector.reciprocal(esum[:], esum[:]))
                link(nc.vector.tensor_scalar(gate[:, bass.ds(at, TOPK)], best[:], esum[:], None, ALU.mult))

            def take_u(half, at):
                link(nc.vector.tensor_copy(u_idx[:, half, :], idx[:, bass.ds(at, TOPK)]))
                dve.sem_inc(u_idx_ready.sem, 1)

            def take_v(n, half, at):
                dve.wait_ge(mixed[half].sem, mixed[half].last(n))
                link(nc.vector.tensor_copy(v_idx[:, half, :], idx[:, bass.ds(at, TOPK)]))
                dve.sem_inc(v_idx_ready[half].sem, 1)

            def products(n, half, at):
                for s in range(TOPK):
                    j = half * TOPK + s
                    dve.wait_ge(u_in[j % RING], 16 * (n * USES + (j // RING + 1)))
                    nc.vector.tensor_tensor_reduce(u_ring[:, j % RING, :], u_ring[:, j % RING, :], x_cur[:], 1.0, 0.0, ALU.mult, ALU.add,
                                                   dots[:, half, s:s + 1]).then_inc(u_used, 1)
                dve.drain()
                dve.sem_inc(dots_ready.sem, 1)
                dve.wait_ge(gelu_ready.sem, gelu_ready.this(n, half + 1))
                nc.vector.tensor_tensor(weight[:, half, :], dots[:, half, :], gate[:, bass.ds(at, TOPK)], ALU.mult)
                dve.drain()
                dve.sem_inc(weight_ready.sem, 1)

            def finish(t):
                dve.wait_ge(ms_ready.sem, ms_ready.this(t))
                link(nc.vector.tensor_scalar(ms[:], ms[:], 1.0 / D, EPS, ALU.mult, ALU.add))
                dve.sem_inc(var_ready.sem, 1)
                dve.wait_ge(root_ready.sem, root_ready.this(t))
                link(nc.vector.reciprocal(rstd[:], root[:]))
                link(nc.vector.tensor_tensor(err[:], rstd[:], rstd[:], ALU.mult))
                link(nc.vector.tensor_tensor(err[:], err[:], ms[:], ALU.mult))
                link(nc.vector.tensor_scalar(err[:], err[:], -0.5, 1.5, ALU.mult, ALU.add))
                link(nc.vector.tensor_tensor(rstd[:], rstd[:], err[:], ALU.mult))
                nc.vector.scalar_tensor_tensor(total[:], total[:], rstd[:], final_gain[:], ALU.mult, ALU.mult)
                dve.drain()
                dve.sem_inc(out_ready.sem, 1)

            def pair(n, boundary=None):
                at = n * PER
                take_v(n, 0, at)
                for half in range(2):
                    products(n, half, at + half * TOPK)
                    route(n + 1, half, at + PER + half * TOPK)
                    take_u(half, at + PER + half * TOPK)
                    if boundary is not None and half == 0:
                        finish(boundary)
                take_v(n, 1, at + TOPK)

            def turn(t, first=False):
                n = t * PAIRS
                dve.wait_ge(x_in.sem, x_in.this(t))
                nc.vector.tensor_copy(x_cur[:], x_next[:])
                dve.drain()
                dve.sem_inc(x_moved.sem, 1)
                pair(n, boundary=None if first else t - 1)
                with dve.Fori(1, PAIRS) as i:
                    pair(n + i)

            for e in (x_moved, sub_ready, best_ready, u_idx_ready, v_idx_ready[0], v_idx_ready[1], dots_ready, weight_ready, var_ready, out_ready):
                dve.sem_inc(e.sem, 1)
            dve.sem_inc(u_used, RING)
            for n in range(4):
                dve.wait_ge(keys_turned, n + 1)
                ins = nc.vector.tensor_copy(keysT[:, n * BANK:(n + 1) * BANK], psum[4 + n][:])
            dve.drain()
            dve.sem_inc(keys_ready, 2)
            dve.wait_ge(loaded, 32)
            for half in range(2):
                route(0, half, half * TOPK)
                take_u(half, half * TOPK)
            turn(0, first=True)
            with dve.Fori(1, TILES) as t:
                turn(t)
            finish(TILES - 1)
            with dve.Fori(1, PAIRS) as i:
                for half in range(2):
                    route(i + TILES * PAIRS, half, (TILES * PAIRS + i) * PER + half * TOPK)


def expert_mix_sample(nc, io, psum, shared, idx, gate):
    ident = shared["ident"]
    at = TILES * SLOTS
    with Stage(nc) as stage:
        sb, sem = stage.buffer, stage.semaphore
        x = sb("es_x", [P, DEC, D])
        u, v = sb("es_u", [P, DEC, D]), sb("es_v", [P, DEC, D])
        rows, gain = sb("es_rows", [DEC, D]), sb("es_gain", [DEC, D])
        junk = sb("es_junk", [DEC, D])
        idxf, idxT, gateT = sb("es_idxf", [DEC, SLOTS]), sb("es_idxT", [P, DEC], U32), sb("es_gateT", [P, DEC])
        dots, weight = sb("es_dots", [P, DEC]), sb("es_weight", [P, DEC])
        own = sb("es_own", [P, DEC, DEC])
        ms, rstd, half = sb("es_ms", [DEC, 1]), sb("es_rstd", [DEC, 1]), sb("es_half", [DEC, 1])
        loaded, idxf_ready, turned, idxT_ready = (sem("es_" + n) for n in ("loaded", "idxf_ready", "turned", "idxT_ready"))
        u_in = [sem(f"es_u_in{b}") for b in range(DEC)]
        v_in = [sem(f"es_v_in{b}") for b in range(DEC)]
        dots_ready, gelu_ready, own_ready, mixed, sum_ready, ms_ready, rstd_ready, out_ready, stored = (
            sem("es_" + n) for n in ("dots_ready", "gelu_ready", "own_ready", "mixed", "sum_ready", "ms_ready", "rstd_ready", "out_ready", "stored"))
        block = stage.block()

        @block.sync
        def _(sp):
            for b in range(DEC):
                sp.dma_start(x[:, b, :], io["xn"][SEQ + b:SEQ + b + 1, :].broadcast_to([P, D])).then_inc(loaded, 16)
            sp.dma_start(rows[:], io["x2"][SEQ:TOKENS, :]).then_inc(loaded, 16)
            sp.dma_start(gain[:], io["final_norm_w"].broadcast_to([DEC, D])).then_inc(loaded, 16)
            sp.wait_ge(out_ready, 1)
            sp.dma_start(io["y_sample"], rows[:]).then_inc(stored, 16)
            sp.wait_ge(stored, 16)

        @block.gpsimd
        def _(pool):
            nc.gpsimd.memset(half[:], -0.5)
            pool.wait_ge(idxT_ready, 1)
            for b in range(DEC):
                for table, rows_in, arrived in (("peer_u", u, u_in), ("peer_v", v, v_in)):
                    nc.gpsimd.indirect_dma_start(out=rows_in[:, b, :], out_offset=None, in_=io[table],
                                                 in_offset=bass.IndirectOffsetOnAxis(ap=idxT[:, b:b + 1], axis=0)).then_inc(arrived[b], 16)
            pool.wait_ge(ms_ready, 1)
            nc.gpsimd.tensor_scalar(ms[:], ms[:], 1.0 / D, EPS, ALU.mult, ALU.add)
            pool.drain()
            nc.gpsimd.tensor_tensor(rstd[:], ms[:], half[:], ALU.pow).then_inc(rstd_ready, 1)

        @block.tensor
        def _(pe):
            pe.wait_ge(idxf_ready, 1)
            nc.tensor.transpose(psum[0][:, 0:DEC], idxf[:], ident[0:DEC, 0:DEC])
            nc.tensor.transpose(psum[0][:, 32:32 + DEC], gate[0:DEC, at:at + SLOTS], ident[0:DEC, 0:DEC]).then_inc(turned, 1)
            pe.wait_ge(own_ready, 1)
            for b in range(DEC):
                pe.wait_ge(v_in[b], 16)
                for c in range(2):
                    ins = nc.tensor.matmul(psum[1 + c][0:DEC, :], own[:, b, :], v[:, b, c * BANK:(c + 1) * BANK], start=(b == 0), stop=(b == DEC - 1))
            ins.then_inc(mixed, 1)

        @block.scalar
        def _(act):
            act.wait_ge(dots_ready, 1)
            nc.scalar.activation(dots[:], dots[:], ACT.Gelu).then_inc(gelu_ready, 1)
            act.wait_ge(sum_ready, 1)
            nc.scalar.activation(junk[:], rows[:], ACT.Square, accum_out=ms[:]).then_inc(ms_ready, 1)

        @block.vector
        def _(dve):
            nc.vector.memset(own[:], 0.0)
            nc.vector.tensor_copy(idxf[:], idx[0:DEC, at:at + SLOTS]).then_inc(idxf_ready, 1)
            dve.wait_ge(turned, 1)
            nc.vector.tensor_copy(gateT[:], psum[0][:, 32:32 + DEC])
            nc.vector.tensor_copy(idxT[:], psum[0][:, 0:DEC]).then_inc(idxT_ready, 1)
            dve.wait_ge(loaded, 16 * (DEC + 2))
            for b in range(DEC):
                dve.wait_ge(u_in[b], 16)
                nc.vector.tensor_tensor_reduce(u[:, b, :], u[:, b, :], x[:, b, :], 1.0, 0.0, ALU.mult, ALU.add, dots[:, b:b + 1])
            dve.drain()
            dve.sem_inc(dots_ready, 1)
            dve.wait_ge(gelu_ready, 1)
            nc.vector.tensor_tensor(weight[:], dots[:], gateT[:], ALU.mult)
            dve.drain()
            diagonal = bass.AP(own[:].tensor, own[:].offset, [list(own[:].ap[0]), [DEC + 1, DEC]])
            nc.vector.tensor_copy(diagonal, weight[:]).then_inc(own_ready, 1)
            dve.wait_ge(mixed, 1)
            for c in range(2):
                cols = slice(c * BANK, (c + 1) * BANK)
                ins = nc.vector.tensor_tensor(rows[:, cols], psum[1 + c][0:DEC, :], rows[:, cols], ALU.add)
            ins.then_inc(sum_ready, 1)
            dve.wait_ge(rstd_ready, 1)
            nc.vector.scalar_tensor_tensor(rows[:], rows[:], rstd[:], gain[:], ALU.mult, ALU.mult).then_inc(out_ready, 1)


def buckets(distance):
    n = np.arange(distance + 1)
    large = BUCKETS // 2 + (np.log(np.maximum(n, 1).astype(np.float32) / np.float32(BUCKETS // 2)) / np.log(128 / (BUCKETS // 2))
                            * (BUCKETS - BUCKETS // 2)).astype(np.int32)
    return np.where(n < BUCKETS // 2, n, np.minimum(large, BUCKETS - 1))


def constants():
    onehot = np.zeros((BUCKETS + 1, 384), np.float32)
    onehot[BUCKETS] = 1
    onehot[BUCKETS, 127:127 + WINDOW + 1] = 0
    onehot[buckets(WINDOW), 127 + np.arange(WINDOW + 1)] = 1
    s, l = np.arange(P)[:, None], np.arange(P)[None, :]
    tri = (s <= l).astype(np.float32)
    return {
        "ident": np.eye(P, dtype=np.float32),
        "tri": tri,
        "far": ((1 - tri) * np.float32(FAR)).astype(np.float32),
        "onehot": onehot,
        "head_mask": np.kron(np.eye(KV), np.ones((GROUP, 1))).astype(np.float32),
    }


def program(nc, io):
    with ExitStack() as scope:
        def sb(name, shape, dt=F32):
            return scope.enter_context(nc.sbuf_tensor(name, shape, dt))

        psum = [scope.enter_context(nc.psum_tensor(f"psum{b}", [P, BANK], F32)) for b in range(8)]
        shared = {
            "ident": sb("ident", [P, P]), "tri": sb("tri", [P, P]), "far": sb("far", [P, P]), "ones": sb("ones", [P, P]),
            "sinks": sb("sinks", [P, HEADS]), "sink_col": sb("sink_col", [HEADS, 1]),
            "head_mask": sb("head_mask", [HEADS, KV]), "bias_row": sb("bias_row", [HEADS, WINDOW + 1]),
            "gains": sb("gains", [P, 5, DB]), "conv": sb("conv", [P, CONV + 1, CB]),
        }
        for i, name in enumerate(("mix", "att", "ssd", "read", "mem")):
            shared["gain_" + name] = shared["gains"][:, i, :]
        with ExitStack() as attention:
            shared["bias"] = attention.enter_context(nc.sbuf_tensor("bias", [P, HEADS, 2 * P], F32))
            w_qkv = attention.enter_context(nc.sbuf_tensor("w_qkv", [P, DB, 1536], F32))
            setup(nc, io, psum, shared)
            attention_prompt(nc, io, psum, shared, w_qkv)
            attention_sample(nc, io, psum, shared, w_qkv)
        with ExitStack() as states:
            keep = {name: states.enter_context(nc.sbuf_tensor("sample_" + name, [DEC, D], F32)) for name in ("gate", "xs")}
            with ExitStack() as ssd:
                w_zx = ssd.enter_context(nc.sbuf_tensor("w_zx", [P, DB, IN_COLS - 1536], F32))
                ssd_prompt(nc, io, psum, shared, w_zx)
                ssd_sample_inputs(nc, io, psum, shared, w_zx, keep)
            ssd_sample_step(nc, io, shared, keep)
        with ExitStack() as memory:
            mkT = memory.enter_context(nc.sbuf_tensor("mkT", [P, DB, N_MEM], F32))
            mv = memory.enter_context(nc.sbuf_tensor("mv", [P, N_MEM // P, D], F32))
            x1 = memory.enter_context(nc.sbuf_tensor("sample_x1", [DEC, D], F32))
            memory_kv(nc, io, psum, shared, mkT, mv)
            w_mo = memory.enter_context(nc.sbuf_tensor("w_mo", [P, DB, D], F32))
            with ExitStack() as outer:
                w_out = outer.enter_context(nc.sbuf_tensor("w_out", [P, 2 * DB, D], F32))
                w_mq = outer.enter_context(nc.sbuf_tensor("w_mq", [P, DB, D], F32))
                memory_read(nc, io, psum, shared, w_out, w_mq, w_mo, mkT, mv)
                memory_read_sample_query(nc, io, psum, shared, w_out, w_mq, x1)
            memory_read_sample(nc, io, psum, shared, w_mo, x1)
        with ExitStack() as experts:
            n = (TILES + 1) * SLOTS
            idx = experts.enter_context(nc.sbuf_tensor("expert_idx", [P, n + 2 * TOPK], U32))
            gate = experts.enter_context(nc.sbuf_tensor("expert_gate", [P, n + 2 * TOPK], F32))
            expert_mix(nc, io, psum, shared, idx, gate)
            expert_mix_sample(nc, io, psum, shared, idx, gate)


_VIEWS = {
    "x_prompt": (SEQ, D), "x_sample": (DEC, D), "mem_prompt": (N_MEM, D),
    "cache_swa_k": (DEC, WINDOW, KV * HD), "cache_swa_v": (DEC, WINDOW, KV * HD),
    "state_ssm": (DEC * SSD_HEADS, HD, STATE), "state_conv": (DEC, CONV - 1, CONV_DIM),
    "cache_mem_k": (DEC, N_MEM, D), "cache_mem_v": (DEC, N_MEM, D),
    "norm_mix_w": (1, D), "w_in": (D, IN_COLS), "attn_sinks": (1, HEADS), "rel_bias": (BUCKETS, HEADS),
    "attn_norm_w": (1, D), "conv_w": (CONV, CONV_DIM), "conv_b": (1, CONV_DIM), "dt_bias": (1, SSD_HEADS),
    "a_log": (1, SSD_HEADS), "d_skip": (1, SSD_HEADS), "ssd_norm_w": (1, D), "w_out": (2 * D, D),
    "norm_mem_w": (1, D), "mem_norm_w": (1, D), "w_mq": (D, D), "w_mk": (D, D), "w_mv": (D, D), "w_mo": (D, D),
    "norm_ffn_w": (1, D), "peer_wq": (D, 2 * D), "peer_keys": (2 * PEER_HEADS, N_KEYS, P),
    "peer_u": (N_KEYS * N_KEYS, D), "peer_v": (N_KEYS * N_KEYS, D), "final_norm_w": (1, D),
}
_OUTS = {
    "y_prompt": ((SEQ, D), (1, SEQ, D)), "y_sample": ((DEC, D), (DEC, 1, D)),
    "p_swa_k": ((WINDOW, KV * HD), (1, 1, WINDOW, KV, HD)), "p_swa_v": ((WINDOW, KV * HD), (1, 1, WINDOW, KV, HD)),
    "p_ssm": ((SSD_HEADS * HD, STATE), (1, 1, SSD_HEADS, HD, STATE)), "p_conv": ((CONV - 1, CONV_DIM), (1, 1, CONV - 1, CONV_DIM)),
    "p_mem_k": ((N_MEM, D), (1, 1, N_MEM, MEM_HEADS, MEM_HD)), "p_mem_v": ((N_MEM, D), (1, 1, N_MEM, MEM_HEADS, MEM_HD)),
    "s_swa_k": ((DEC, WINDOW, KV * HD), (1, DEC, WINDOW, KV, HD)), "s_swa_v": ((DEC, WINDOW, KV * HD), (1, DEC, WINDOW, KV, HD)),
    "s_ssm": ((DEC * SSD_HEADS, HD, STATE), (1, DEC, SSD_HEADS, HD, STATE)),
    "s_conv": ((DEC, CONV - 1, CONV_DIM), (1, DEC, CONV - 1, CONV_DIM)),
}
_SCRATCH = {
    "mixed": (TOKENS, 2 * D), "bias_line": (HEADS, 384), "rows": (DEC, D), "rows2": (DEC, D), "rows3": (DEC, D),
    "dts": (DEC, SSD_HEADS), "bcs": (DEC, 512), "x2": (SEQ + P, D), "xn": (SEQ + P, D),
}


def kernel(**inputs):
    import concourse.bacc as _bacc
    from concourse.bass_utils import run_bass_kernel_spmd as _run

    nc = _bacc.Bacc("TRN2", target_bir_lowering=False, num_devices=1)
    arrays, io = {}, {}
    laid = {name: np.ascontiguousarray(inputs[name]).reshape(shape) for name, shape in _VIEWS.items()}
    laid.update(constants())
    for name, a in laid.items():
        arrays[f"in_{name}"] = a
        io[name] = nc.dram_tensor(f"in_{name}", a.shape, mybir.dt.from_np(a.dtype), kind="ExternalInput").ap()
    for name, (shape, _) in _OUTS.items():
        io[name] = nc.dram_tensor(f"out_{name}", shape, F32, kind="ExternalOutput").ap()
    for name, shape in _SCRATCH.items():
        io[name] = nc.dram_tensor(f"scratch_{name}", shape, F32, kind="Internal").ap()
    program(nc, io)
    r = _run(nc, [arrays], core_ids=[0])
    return tuple(r.results[0][f"out_{name}"].reshape(shape) for name, (_, shape) in _OUTS.items())
```

```python
from contextlib import ExitStack

import numpy as np

import concourse.bass as bass
from concourse import mybir

F32 = mybir.dt.float32
U32 = mybir.dt.uint32
ALU = mybir.AluOpType
ACT = mybir.ActivationFunctionType
AX = mybir.AxisListType

P = 128
D = 1024
DB = D // P
SEQ = 1024
TILES = SEQ // P
DEC = 8
TOKENS = SEQ + DEC
HEADS, KV, HD = 16, 4, 64
GROUP = HEADS // KV
WINDOW = 128
BUCKETS = 32
SSD_HEADS, SSD_G, STATE = 16, 2, 128
SSD_HPG = SSD_HEADS // SSD_G
CONV = 4
CONV_DIM = 1536
CB = CONV_DIM // P
XBC0 = 2560
DT0 = XBC0 + CONV_DIM
IN_COLS = DT0 + SSD_HEADS
N_MEM = 256
MEM_HEADS, MEM_HD = 4, 256
PEER_HEADS, N_KEYS, TOPK = 8, 128, 16
SLOTS = PEER_HEADS * TOPK
EPS = 1e-6
FAR = -1e30
BANK = 512


class Event:

    def __init__(self, sem, per=1, unit=1):
        self.sem, self.per, self.unit = sem, per, unit

    def last(self, turn):
        return (turn * self.per + 1) * self.unit

    def this(self, turn, k=1):
        return (turn * self.per + 1 + k) * self.unit


class Fills:

    def __init__(self, sem, stage, order):
        self.place, count = {}, {}
        for name, b in order:
            count[b] = count.get(b, 0) + 1
            self.place[name] = (b, count[b])
        self.count = count
        self.full = {b: sem(f"{stage}_bank{b}_full") for b in count}
        self.free = {b: sem(f"{stage}_bank{b}_free") for b in count}

    def bank(self, name):
        return self.place[name][0]

    def at(self, name, turn):
        b, k = self.place[name]
        return turn * self.count[b] + k

    def prime(self, pe):
        for b in self.count:
            pe.sem_inc(self.free[b], 1)


class Stage:

    def __init__(self, nc):
        self.nc, self.scope, self.semaphores = nc, ExitStack(), []

    def __enter__(self):
        return self

    def buffer(self, name, shape, dt=F32):
        return self.scope.enter_context(self.nc.sbuf_tensor(name, shape, dt))

    def semaphore(self, name):
        self.semaphores.append(self.nc.alloc_semaphore(name))
        return self.semaphores[-1]

    def event(self, name, per=1, unit=1):
        return Event(self.semaphore(name), per, unit)

    def block(self):
        return self.scope.enter_context(self.nc.Block())

    def __exit__(self, kind, *rest):
        if kind is None:
            self.scope.close()
            self.nc.clear_and_free_semaphores(self.semaphores)
            self.nc.all_engine_barrier()


def flipped(ap):
    a = [list(x) for x in ap.ap]
    step, n = a[-1]
    return bass.AP(ap.tensor, ap.offset + (n - 1) * step, a[:-1] + [[-step, n]])


def attention_prompt(nc, io, psum, shared, w_qkv, w_zx):
    ident, bias, sinks, gain = shared["ident"], shared["bias"], shared["sinks"], shared["gain_mix"]
    with Stage(nc) as stage:
        sb, sem, event = stage.buffer, stage.semaphore, stage.event

        x = sb("att_x", [P, D])
        junk = sb("att_junk", [P, D])
        ms = sb("att_ms", [P, 1])
        rstd = sb("att_rstd", [P, 1])
        half = sb("att_half", [P, 1])
        part = sb("att_part", [P, 1])
        hT = sb("att_hT", [P, DB, P])
        q = sb("att_q", [P, D])
        kv = sb("att_kv", [P, 512])
        values = sb("att_values", [P, 2, 256])
        out_rows = sb("att_out", [P, D])
        qT = sb("att_qT", [P, DB, P])
        kT = sb("att_kT", [P, 2, 2 * P])
        logits = sb("att_logits", [P, 2, GROUP, 2 * P])
        pT = sb("att_pT", [P, 2, GROUP, 2, P])
        top = sb("att_top", [P, HEADS])
        ntop = sb("att_ntop", [P, HEADS])
        total = sb("att_total", [P, HEADS])
        esink = sb("att_esink", [P, HEADS])
        rtotal = sb("att_rtotal", [P, HEADS])
        o = sb("att_o", [P, D])
        oms = sb("att_oms", [P, 1])
        orstd = sb("att_orstd", [P, 1])

        front_fills = Fills(sem, "att_front", [
            ("xT0", 0), ("xT1", 1), ("p0", 2), ("p1", 0), ("p2", 1), ("qT0", 2), ("qT1", 0), ("kT", 1)])
        order = []
        for g in range(KV):
            order += [(f"s{g}0", 3), (f"s{g}1", 4)]
        for g in range(KV):
            order += [(f"t{g}0", 5), (f"t{g}1", 6), (f"o{g}", 7)]
        back_fills = Fills(sem, "att_back", order)

        def fill(name):
            f = front_fills if name in front_fills.place else back_fills
            return f, f.bank(name), psum[f.bank(name)]

        w_in = [sem(f"att_w{c}") for c in range(3)]
        zx_in = sem("att_w_zx")
        x_in = event("att_x_in", 1, 16)
        x_seen = event("att_x_seen", 2)
        ms_ready = event("att_ms_ready")
        rstd_ready = event("att_rstd_ready")
        hT_ready = event("att_hT_ready", 2)
        projected = event("att_projected")
        q_ready = event("att_q_ready")
        kv_ready = event("att_kv_ready")
        qT_ready = event("att_qT_ready")
        kT_ready, v_ready = event("att_kT_ready"), event("att_v_ready")
        scored = event("att_scored")
        ntop_ready = event("att_ntop_ready", KV)
        p_ready = event("att_p_ready", KV)
        p_turned = event("att_p_turned", KV)
        pT_ready = event("att_pT_ready", KV)
        mixed = event("att_mixed", KV)
        o_ready = event("att_o_ready")
        oms_ready = event("att_oms_ready")
        orstd_ready = event("att_orstd_ready")
        out_ready = event("att_out_ready")
        stored = event("att_stored", 1, 16)
        tail_out = sem("att_tail_out")

        block = stage.block()

        @block.sync
        def _(sp):
            def load(t):
                sp.wait_ge(x_seen.sem, x_seen.last(t))
                sp.dma_start(x[:], io["x_prompt"][bass.ds(t * P, P), :]).then_inc(x_in.sem, 16)

            def store(t):
                sp.wait_ge(out_ready.sem, out_ready.this(t))
                sp.dma_start(io["mixed"][bass.ds(t * P, P), 0:D], out_rows[:]).then_inc(stored.sem, 16)

            sp.sem_inc(x_in.sem, 16)
            sp.sem_inc(stored.sem, 16)
            weights = io["w_in"].rearrange("(b p) n -> p b n", p=P)
            load(0)
            for c in range(3):
                cols = slice(c * BANK, (c + 1) * BANK)
                sp.dma_start(w_qkv[:, :, cols], weights[:, :, cols]).then_inc(w_in[c], 16)
            load(1)
            load(2)
            sp.dma_start(w_zx[:], weights[:, :, 1536:IN_COLS]).then_inc(zx_in, 16)
            with sp.Fori(0, TILES - 3) as t:
                store(t)
                load(t + 3)
            with sp.Fori(TILES - 3, TILES) as t:
                store(t)
            sp.wait_ge(kv_ready.sem, kv_ready.this(TILES - 1))
            sp.dma_start(io["p_swa_k"], kv[:, 0:256]).then_inc(tail_out, 16)
            sp.dma_start(io["p_swa_v"], kv[:, 256:512]).then_inc(tail_out, 16)
            sp.wait_ge(tail_out, 32)
            sp.wait_ge(stored.sem, stored.this(TILES - 1))
            sp.wait_ge(zx_in, 16)

        @block.tensor
        def _(pe):
            def begin(name, t):
                f, bank, out = fill(name)
                pe.wait_ge(f.free[bank], f.at(name, t))
                return out, f.full[bank]

            def turned(name, t, blocks):
                out, full = begin(name, t)
                for j, block_in in enumerate(blocks):
                    ins = nc.tensor.transpose(out[:, j * P:(j + 1) * P], block_in, ident[:])
                ins.then_inc(full, 1)

            def rows(u):
                pe.wait_ge(x_in.sem, x_in.this(u))
                for h in range(2):
                    turned(f"xT{h}", u, [x[:, (4 * h + j) * P:(4 * h + j + 1) * P] for j in range(4)])
                pe.drain()
                pe.sem_inc(x_seen.sem, 1)

            def project(c, u, first_use=False):
                if first_use:
                    pe.wait_ge(w_in[c], 16)
                if c == 0:
                    pe.wait_ge(hT_ready.sem, hT_ready.this(u, 2))
                out, full = begin(f"p{c}", u)
                for b in range(DB):
                    ins = nc.tensor.matmul(out[:], hT[:, b, :], w_qkv[:, b, c * BANK:(c + 1) * BANK], start=(b == 0), stop=(b == DB - 1))
                ins.then_inc(full, 1)
                if c == 2:
                    pe.drain()
                    pe.sem_inc(projected.sem, 1)

            def turn_q(u):
                pe.wait_ge(q_ready.sem, q_ready.this(u))
                for h in range(2):
                    turned(f"qT{h}", u, [q[:, (4 * h + j) * P:(4 * h + j + 1) * P] for j in range(4)])

            def turn_k(u):
                pe.wait_ge(kv_ready.sem, kv_ready.this(u))
                turned("kT", u, [kv[:, j * P:(j + 1) * P] for j in range(2)])

            def scores(t, g, first):
                if g == 0:
                    pe.wait_ge(qT_ready.sem, qT_ready.this(t))
                    pe.wait_ge(kT_ready.sem, kT_ready.this(t))
                lo, hi = (g % 2) * HD, (g % 2 + 1) * HD
                off = P if first else 0
                for h in range(2):
                    out, full = begin(f"s{g}{h}", t)
                    for r in (2 * h, 2 * h + 1):
                        at = (r % 2) * 2 * P
                        ins = nc.tensor.matmul(out[:, at + off:at + 2 * P], qT[lo:hi, 4 * (g // 2) + r, :], kT[lo:hi, g // 2, off:2 * P],
                                               start=True, stop=True)
                    ins.then_inc(full, 1)
                if g == KV - 1:
                    pe.drain()
                    pe.sem_inc(scored.sem, 1)

            def turn_p(t, g, first):
                pe.wait_ge(p_ready.sem, p_ready.this(t, g + 1))
                for h in range(2):
                    out, full = begin(f"t{g}{h}", t)
                    for r in (2 * h, 2 * h + 1):
                        for part in (1,) if first else (0, 1):
                            at = ((r % 2) * 2 + part) * P
                            ins = nc.tensor.transpose(out[:, at:at + P], logits[:, g % 2, r, part * P:(part + 1) * P], ident[:])
                    ins.then_inc(full, 1)
                pe.drain()
                pe.sem_inc(p_turned.sem, 1)

            def mix(t, g, first):
                if g == 0:
                    pe.wait_ge(v_ready.sem, v_ready.this(t))
                pe.wait_ge(pT_ready.sem, pT_ready.this(t, g + 1))
                out, full = begin(f"o{g}", t)
                parts = (1,) if first else (0, 1)
                for r in range(GROUP):
                    for part in parts:
                        ins = nc.tensor.matmul(out[:, r * HD:(r + 1) * HD], pT[:, g % 2, r, part, :], values[:, part, g * HD:(g + 1) * HD],
                                               start=(part == parts[0]), stop=(part == 1))
                ins.then_inc(full, 1)
                pe.drain()
                pe.sem_inc(mixed.sem, 1)

            def turn(t, u, first=False):
                front = u is not None
                if front:
                    rows(u)
                scores(t, 0, first)
                scores(t, 1, first)
                for g in range(KV):
                    if front and g < 3:
                        project(g, u)
                    if front and g == 3:
                        turn_q(u)
                    if g > 0:
                        mix(t, g - 1, first)
                    turn_p(t, g, first)
                    if g + 2 < KV:
                        scores(t, g + 2, first)
                if front:
                    turn_k(u)
                mix(t, KV - 1, first)

            front_fills.prime(pe)
            back_fills.prime(pe)
            pe.sem_inc(x_seen.sem, 1)
            for e in (projected, p_turned, mixed, scored):
                pe.sem_inc(e.sem, 1)
            rows(0)
            for c in range(3):
                project(c, 0, first_use=True)
            turn_q(0)
            turn_k(0)
            turn(0, 1, first=True)
            with pe.Fori(1, TILES - 1) as t:
                turn(t, t + 1)
            turn(TILES - 1, None)

        @block.scalar
        def _(act):
            def squares(u):
                act.wait_ge(x_in.sem, x_in.this(u))
                nc.scalar.activation(junk[:], x[:], ACT.Square, accum_out=ms[:])
                act.drain()
                act.sem_inc(ms_ready.sem, 1)
                act.sem_inc(x_seen.sem, 1)

            def queries(c, u):
                if c == 0:
                    act.wait_ge(rstd_ready.sem, rstd_ready.this(u))
                f, bank, src = fill(f"p{c}")
                act.wait_ge(f.full[bank], f.at(f"p{c}", u))
                out = q[:, c * BANK:(c + 1) * BANK].rearrange("p (r g d) -> p g r d", r=GROUP, g=2)
                src = src[:].rearrange("p (g r d) -> p g r d", r=GROUP, g=2)
                for gg in range(2):
                    nc.scalar.activation(out[:, gg], src[:, gg], ACT.Copy, scale=rstd[:])
                act.drain()
                act.sem_inc(f.free[bank], 1)
                if c == 1:
                    act.sem_inc(q_ready.sem, 1)

            def turned_q(u):
                act.wait_ge(scored.sem, scored.last(u))
                for h in range(2):
                    f, bank, src = fill(f"qT{h}")
                    act.wait_ge(f.full[bank], f.at(f"qT{h}", u))
                    nc.scalar.activation(qT[:, 4 * h:4 * h + 4, :], src[:].rearrange("p (b t) -> p b t", b=4),
                                         ACT.Copy, scale=HD ** -0.5).then_inc(f.free[bank], 1)
                act.drain()
                act.sem_inc(qT_ready.sem, 1)

            def exponentials(t, g, first):
                off = P if first else 0
                act.wait_ge(ntop_ready.sem, ntop_ready.this(t, g + 1))
                for r in range(GROUP):
                    h = g * GROUP + r
                    nc.scalar.activation(logits[:, g % 2, r, off:2 * P], logits[:, g % 2, r, off:2 * P], ACT.Exp,
                                         bias=ntop[:, h:h + 1], accum_out=total[:, h:h + 1])
                hs = slice(g * GROUP, (g + 1) * GROUP)
                nc.scalar.activation(esink[:, hs], esink[:, hs], ACT.Exp)
                act.drain()
                act.sem_inc(p_ready.sem, 1)

            def turned_p(t, g, first):
                act.wait_ge(mixed.sem, mixed.this(t, g - 1) if g >= 2 else mixed.last(t))
                for h in range(2):
                    f, bank, src = fill(f"t{g}{h}")
                    act.wait_ge(f.full[bank], f.at(f"t{g}{h}", t))
                    keys = slice(1, 2) if first else slice(0, 2)
                    nc.scalar.copy(pT[:, g % 2, 2 * h:2 * h + 2, keys, :],
                                   src[:].rearrange("p (r k t) -> p r k t", r=2, k=2)[:, :, keys, :]).then_inc(f.free[bank], 1)
                act.drain()
                act.sem_inc(pT_ready.sem, 1)

            def turn(t, u, first=False):
                front = u is not None
                if front:
                    squares(u)
                for g in range(KV):
                    exponentials(t, g, first)
                    if front and g < 2:
                        queries(g, u)
                    turned_p(t, g, first)
                    if front and g == 2:
                        turned_q(u)
                act.wait_ge(o_ready.sem, o_ready.this(t))
                nc.scalar.activation(junk[:], o[:], ACT.Square, accum_out=oms[:])
                act.drain()
                act.sem_inc(oms_ready.sem, 1)

            for e in (ms_ready, q_ready, qT_ready, p_ready, pT_ready, oms_ready):
                act.sem_inc(e.sem, 1)
            squares(0)
            for c in range(2):
                queries(c, 0)
            turned_q(0)
            turn(0, 1, first=True)
            with act.Fori(1, TILES - 1) as t:
                turn(t, t + 1)
            turn(TILES - 1, None)

        @block.gpsimd
        def _(pool):
            def factor(src, dst, ready, done, t):
                pool.wait_ge(ready.sem, ready.this(t))
                nc.gpsimd.tensor_tensor(src[:], src[:], part[:], ALU.mult)
                pool.drain()
                nc.gpsimd.tensor_scalar(src[:], src[:], EPS, None, ALU.add)
                pool.drain()
                nc.gpsimd.tensor_tensor(dst[:], src[:], half[:], ALU.pow)
                pool.drain()
                pool.sem_inc(done.sem, 1)

            nc.gpsimd.memset(half[:], -0.5)
            nc.gpsimd.memset(part[:], 1.0 / D)
            pool.drain()
            pool.sem_inc(rstd_ready.sem, 1)
            pool.sem_inc(orstd_ready.sem, 1)
            factor(ms, rstd, ms_ready, rstd_ready, 0)
            with pool.Fori(0, TILES - 1) as t:
                pool.wait_ge(kv_ready.sem, kv_ready.this(t))
                factor(ms, rstd, ms_ready, rstd_ready, t + 1)
                factor(oms, orstd, oms_ready, orstd_ready, t)
            factor(oms, orstd, oms_ready, orstd_ready, TILES - 1)

        @block.vector
        def _(dve):
            def full(name, t):
                f, bank, src = fill(name)
                dve.wait_ge(f.full[bank], f.at(name, t))
                return src, f.free[bank]

            def rows(u):
                dve.wait_ge(projected.sem, projected.last(u))
                for h in range(2):
                    src, free = full(f"xT{h}", u)
                    nc.vector.tensor_tensor(hT[:, 4 * h:4 * h + 4, :], src[:].rearrange("p (b t) -> p b t", b=4),
                                            gain[:, 4 * h:4 * h + 4, None].broadcast_to([P, 4, P]), ALU.mult).then_inc(free, 1)
                    dve.drain()
                    dve.sem_inc(hT_ready.sem, 1)

            def keys_values(u):
                dve.wait_ge(rstd_ready.sem, rstd_ready.this(u))
                src, free = full("p2", u)
                nc.vector.tensor_scalar(kv[:], src[:], rstd[:], None, ALU.mult).then_inc(free, 1)
                dve.drain()
                dve.sem_inc(kv_ready.sem, 1)

            def next_keys(u, first=False):
                dve.wait_ge(scored.sem, scored.last(u))
                if not first:
                    nc.vector.tensor_copy(kT[:, :, 0:P], kT[:, :, P:2 * P])
                    dve.drain()
                src, free = full("kT", u)
                nc.vector.tensor_copy(kT[:, :, P:2 * P], src[:, 0:256].rearrange("p (b t) -> p b t", b=2)).then_inc(free, 1)
                dve.drain()
                dve.sem_inc(kT_ready.sem, 1)

            def next_values(u, first=False):
                dve.wait_ge(mixed.sem, mixed.last(u))
                if not first:
                    nc.vector.tensor_copy(values[:, 0, :], values[:, 1, :])
                    dve.drain()
                nc.vector.tensor_copy(values[:, 1, :], kv[:, 256:512])
                dve.drain()
                dve.sem_inc(v_ready.sem, 1)

            def softmax_top(t, g, first):
                off = P if first else 0
                dve.wait_ge(p_turned.sem, p_turned.this(t, g - 1) if g >= 2 else p_turned.last(t))
                for h in range(2):
                    src, free = full(f"s{g}{h}", t)
                    nc.vector.tensor_tensor(logits[:, g % 2, 2 * h:2 * h + 2, off:2 * P],
                                            src[:].rearrange("p (r k) -> p r k", r=2)[:, :, off:2 * P],
                                            bias[:, g * GROUP + 2 * h:g * GROUP + 2 * h + 2, off:2 * P], ALU.add).then_inc(free, 1)
                dve.drain()
                hs = slice(g * GROUP, (g + 1) * GROUP)
                nc.vector.tensor_reduce(top[:, hs], logits[:, g % 2, :, off:2 * P], AX.X, ALU.max)
                dve.drain()
                nc.vector.tensor_tensor(top[:, hs], top[:, hs], sinks[:, hs], ALU.max)
                dve.drain()
                nc.vector.tensor_scalar(ntop[:, hs], top[:, hs], -1.0, None, ALU.mult)
                nc.vector.tensor_tensor(esink[:, hs], sinks[:, hs], top[:, hs], ALU.subtract)
                dve.drain()
                dve.sem_inc(ntop_ready.sem, 1)

            def outputs(t, g):
                hs = slice(g * GROUP, (g + 1) * GROUP)
                dve.wait_ge(p_ready.sem, p_ready.this(t, g + 1))
                nc.vector.tensor_tensor(total[:, hs], total[:, hs], esink[:, hs], ALU.add)
                dve.drain()
                nc.vector.reciprocal(rtotal[:, hs], total[:, hs])
                dve.drain()
                src, free = full(f"o{g}", t)
                nc.vector.tensor_tensor(o[:, g * 256:(g + 1) * 256].rearrange("p (r d) -> p r d", r=GROUP),
                                        src[:, 0:256].rearrange("p (r d) -> p r d", r=GROUP),
                                        rtotal[:, hs, None].broadcast_to([P, GROUP, HD]), ALU.mult).then_inc(free, 1)

            def scaled(t):
                dve.wait_ge(orstd_ready.sem, orstd_ready.this(t))
                dve.wait_ge(stored.sem, stored.last(t))
                nc.vector.tensor_scalar(out_rows[:], o[:], orstd[:], None, ALU.mult)
                dve.drain()
                dve.sem_inc(out_ready.sem, 1)

            def turn(t, u, first=False):
                front = u is not None
                if front:
                    rows(u)
                softmax_top(t, 0, first)
                softmax_top(t, 1, first)
                if not first:
                    scaled(t - 1)
                softmax_top(t, 2, first)
                outputs(t, 0)
                softmax_top(t, 3, first)
                outputs(t, 1)
                if front:
                    keys_values(u)
                outputs(t, 2)
                if front:
                    next_keys(u)
                outputs(t, 3)
                dve.drain()
                dve.sem_inc(o_ready.sem, 1)
                if front:
                    next_values(u)

            for e in (hT_ready, kv_ready, kT_ready, v_ready, ntop_ready, o_ready, out_ready):
                dve.sem_inc(e.sem, 1)
            rows(0)
            keys_values(0)
            next_keys(0, first=True)
            next_values(0, first=True)
            turn(0, 1, first=True)
            with dve.Fori(1, TILES - 1) as t:
                turn(t, t + 1)
            turn(TILES - 1, None)
            scaled(TILES - 1)


def setup(nc, io, psum, shared):
    with Stage(nc) as stage:
        sb, sem = stage.buffer, stage.semaphore

        rows = sb("set_rows", [5 * DB, P])
        conv_rows = sb("set_conv_rows", [(CONV + 1) * CB, P])
        table = sb("set_table", [BUCKETS + 1, HEADS])
        onehot = sb("set_onehot", [BUCKETS + 1, 384])
        line = sb("set_line", [HEADS, 384])
        turned = sb("set_turned", [P, HEADS, 2 * P])
        loaded = sem("set_loaded")
        far_row = sem("set_far_row")
        multiplied = sem("set_multiplied")
        line_ready = sem("set_line_ready")
        line_stored = sem("set_line_stored")
        turned_loaded = sem("set_turned_loaded")
        block = stage.block()
        loads = [
            (shared["ident"][:], io["ident"]), (shared["tri"][:], io["tri"]),
            (shared["far"][:], io["far"]),
            (onehot[:], io["onehot"]), (table[0:BUCKETS, :], io["rel_bias"]),
            (shared["sinks"][:], io["attn_sinks"].rearrange("a h -> a h").broadcast_to([P, HEADS])),
            (shared["sink_col"][:], io["attn_sinks"].rearrange("a h -> h a")),
            (shared["head_mask"][:], io["head_mask"]),
        ]
        for i, name in enumerate(("norm_mix_w", "attn_norm_w", "ssd_norm_w", "norm_mem_w", "mem_norm_w")):
            loads.append((rows[i * DB:(i + 1) * DB, :], io[name].rearrange("a (b p) -> (a b) p", p=P)))
        loads.append((conv_rows[0:CONV * CB, :], io["conv_w"].rearrange("k (b p) -> (k b) p", p=P)))
        loads.append((conv_rows[CONV * CB:(CONV + 1) * CB, :], io["conv_b"].rearrange("a (b p) -> (a b) p", p=P)))

        @block.sync
        def _(sp):
            for dst, src in loads:
                sp.dma_start(dst, src).then_inc(loaded, 16)
            sp.wait_ge(line_ready, 1)
            sp.dma_start(io["bias_line"], line[:]).then_inc(line_stored, 16)
            sp.wait_ge(line_stored, 16)
            shifted = bass.AP(io["bias_line"].tensor, io["bias_line"].offset, [[1, P], [384, HEADS], [1, 2 * P]])
            sp.dma_start(turned[:], shifted).then_inc(turned_loaded, 16)

        @block.tensor
        def _(pe):
            pe.wait_ge(loaded, 16 * len(loads))
            pe.wait_ge(far_row, 1)
            nc.tensor.matmul(psum[0][0:HEADS, 0:384], table[:], onehot[:], start=True, stop=True).then_inc(multiplied, 1)
            nc.tensor.transpose(psum[1][:, 0:5 * DB], rows[:], shared["ident"][0:5 * DB, 0:5 * DB])
            n = (CONV + 1) * CB
            nc.tensor.transpose(psum[1][:, P:P + n], conv_rows[:], shared["ident"][0:n, 0:n]).then_inc(multiplied, 1)

        @block.vector
        def _(dve):
            nc.vector.memset(table[BUCKETS:BUCKETS + 1, :], FAR).then_inc(far_row, 1)
            nc.vector.memset(shared["ones"][:], 1.0)
            dve.wait_ge(multiplied, 2)
            nc.vector.tensor_copy(line[:], psum[0][0:HEADS, 0:384]).then_inc(line_ready, 1)
            nc.vector.tensor_copy(shared["gains"][:], psum[1][:, 0:5 * DB].rearrange("p (i b) -> p i b", b=DB))
            nc.vector.tensor_copy(shared["conv"][:], psum[1][:, P:P + (CONV + 1) * CB].rearrange("p (i b) -> p i b", b=CB))
            dve.drain()
            nc.vector.tensor_copy(shared["bias_row"][:], flipped(line[:, 127:256]))
            dve.wait_ge(turned_loaded, 16)
            nc.vector.tensor_copy(shared["bias"][:], flipped(turned[:]))
            dve.drain()


def attention_sample(nc, io, psum, shared, w_qkv):
    ident, sink, gain = shared["ident"], shared["sink_col"], shared["gain_mix"]
    KEYS = WINDOW + 1
    with Stage(nc) as stage:
        sb, sem = stage.buffer, stage.semaphore

        x = sb("sat_x", [DEC, D])
        junk = sb("sat_junk", [DEC, D])
        ms = sb("sat_ms", [DEC, 1])
        rstd = sb("sat_rstd", [DEC, 1])
        half = sb("sat_half", [DEC, 1])
        hT = sb("sat_hT", [P, DB, DEC])
        q = sb("sat_q", [DEC, D])
        kv = sb("sat_kv", [DEC, 512])
        k_cache = sb("sat_k_cache", [P, DEC, 256])
        v_cache = sb("sat_v_cache", [P, DEC, 256])
        q_heads = sb("sat_q_heads", [P, DEC, 2, HEADS])
        k_newT = sb("sat_k_newT", [P, 2, DEC])
        kT = sb("sat_kT", [P, DEC, 2, KEYS])
        p = sb("sat_p", [HEADS, DEC, KEYS])
        top = sb("sat_top", [HEADS, DEC])
        esink = sb("sat_esink", [HEADS, DEC])
        total = sb("sat_total", [HEADS, DEC])
        pT = sb("sat_pT", [P, DEC, HEADS])
        p_new = sb("sat_p_new", [DEC, HEADS])
        p_own = sb("sat_p_own", [DEC, DEC, HEADS])
        wide = sb("sat_wide", [HEADS, DEC, KV, HD])
        o_heads = sb("sat_o_heads", [HEADS, DEC, HD])
        o = sb("sat_o", [DEC, D])

        x_in, cache_in, copied = sem("sat_x_in"), sem("sat_cache_in"), sem("sat_copied")
        x_turned, ms_ready, rstd_ready = sem("sat_x_turned"), sem("sat_ms_ready"), sem("sat_rstd_ready")
        hT_ready, projected, q_ready, kv_ready = sem("sat_hT_ready"), sem("sat_projected"), sem("sat_q_ready"), sem("sat_kv_ready")
        qk_turned, q_heads_ready, k_newT_ready = sem("sat_qk_turned"), sem("sat_q_heads_ready"), sem("sat_k_newT_ready")
        cache_turned, kT_ready, scored = sem("sat_cache_turned"), sem("sat_kT_ready"), sem("sat_scored")
        shifted, esum, p_ready, p_turned = sem("sat_shifted"), sem("sat_esum"), sem("sat_p_ready"), sem("sat_p_turned")
        pT_ready, valued, o_heads_ready, o_in = sem("sat_pT_ready"), sem("sat_valued"), sem("sat_o_heads_ready"), sem("sat_o_in")
        oms_ready, orstd_ready, out_ready = sem("sat_oms_ready"), sem("sat_orstd_ready"), sem("sat_out_ready")
        stored = sem("sat_stored")
        block = stage.block()

        @block.sync
        def _(sp):
            sp.dma_start(x[:], io["x_sample"]).then_inc(x_in, 16)
            sp.dma_start(k_cache[:], io["cache_swa_k"].rearrange("b s n -> s b n")).then_inc(cache_in, 16)
            sp.dma_start(v_cache[:], io["cache_swa_v"].rearrange("b s n -> s b n")).then_inc(cache_in, 16)
            for new, old in (("s_swa_k", "cache_swa_k"), ("s_swa_v", "cache_swa_v")):
                sp.dma_start(io[new][:, 0:WINDOW - 1, :], io[old][:, 1:WINDOW, :]).then_inc(copied, 16)
            sp.wait_ge(kv_ready, 1)
            sp.dma_start(io["s_swa_k"][:, WINDOW - 1, :], kv[:, 0:256]).then_inc(copied, 16)
            sp.dma_start(io["s_swa_v"][:, WINDOW - 1, :], kv[:, 256:512]).then_inc(copied, 16)
            sp.wait_ge(o_heads_ready, 1)
            sp.dma_start(io["rows"].rearrange("b (h d) -> h b d", h=HEADS), o_heads[:]).then_inc(stored, 16)
            sp.wait_ge(stored, 16)
            sp.dma_start(o[:], io["rows"]).then_inc(o_in, 16)
            sp.wait_ge(o_in, 16)
            sp.wait_ge(out_ready, 1)
            sp.dma_start(io["mixed"][SEQ:TOKENS, 0:D], o[:]).then_inc(stored, 16)
            sp.wait_ge(stored, 32)
            sp.wait_ge(copied, 64)

        @block.tensor
        def _(pe):
            pe.wait_ge(x_in, 16)
            for b in range(DB):
                ins = nc.tensor.transpose(psum[0][:, b * DEC:(b + 1) * DEC], x[:, b * P:(b + 1) * P], ident[0:DEC, 0:DEC])
            ins.then_inc(x_turned, 1)
            pe.wait_ge(hT_ready, 1)
            for c in range(3):
                for b in range(DB):
                    ins = nc.tensor.matmul(psum[1 + c][0:DEC, :], hT[:, b, :], w_qkv[:, b, c * BANK:(c + 1) * BANK],
                                           start=(b == 0), stop=(b == DB - 1))
                ins.then_inc(projected, 1)
            pe.wait_ge(cache_in, 32)
            for n in range(4):
                for j in range(4):
                    b, half_k = (4 * n + j) // 2, j % 2
                    ins = nc.tensor.transpose(psum[4 + n][:, j * P:(j + 1) * P],
                                              k_cache[:, b, half_k * P:(half_k + 1) * P], ident[:])
                ins.then_inc(cache_turned, 1)
            pe.wait_ge(q_ready, 1)
            pe.wait_ge(kv_ready, 1)
            for b in range(DB):
                nc.tensor.transpose(psum[0][:, b * DEC:(b + 1) * DEC], q[:, b * P:(b + 1) * P], ident[0:DEC, 0:DEC])
            for b in range(2):
                ins = nc.tensor.transpose(psum[0][:, P + b * DEC:P + (b + 1) * DEC], kv[:, b * P:(b + 1) * P], ident[0:DEC, 0:DEC])
            ins.then_inc(qk_turned, 1)
            pe.wait_ge(q_heads_ready, 1)
            pe.wait_ge(kT_ready, 1)
            for b in range(DEC):
                for j in range(2):
                    ins = nc.tensor.matmul(psum[1 + b // 3][0:HEADS, (b % 3) * KEYS:(b % 3 + 1) * KEYS],
                                           q_heads[:, b, j, :], kT[:, b, j, :], start=(j == 0), stop=(j == 1))
            ins.then_inc(scored, 1)
            pe.wait_ge(p_ready, 1)
            for b in range(DEC):
                nc.tensor.transpose(psum[0][:, b * HEADS:(b + 1) * HEADS], p[:, b, 0:WINDOW], ident[0:HEADS, 0:HEADS])
            nc.tensor.transpose(psum[0][0:DEC, 256:256 + HEADS], p[:, :, WINDOW], ident[0:HEADS, 0:HEADS]).then_inc(p_turned, 1)
            pe.wait_ge(pT_ready, 1)
            for b in range(DEC):
                out = psum[4 + b // 2][0:HEADS, (b % 2) * 256:(b % 2 + 1) * 256]
                nc.tensor.matmul(out, pT[:, b, :], v_cache[:, b, :], start=True, stop=False)
                ins = nc.tensor.matmul(out, p_own[:, b, :], kv[:, 256:512], start=False, stop=True)
            ins.then_inc(valued, 1)

        @block.scalar
        def _(act):
            act.wait_ge(x_in, 16)
            nc.scalar.activation(junk[:], x[:], ACT.Square, accum_out=ms[:]).then_inc(ms_ready, 1)
            act.wait_ge(rstd_ready, 1)
            act.wait_ge(projected, 2)
            for c in range(2):
                out = q[:, c * BANK:(c + 1) * BANK].rearrange("p (r g d) -> p g r d", r=GROUP, g=2)
                src = psum[1 + c][0:DEC, :].rearrange("p (g r d) -> p g r d", r=GROUP, g=2)
                for gg in range(2):
                    nc.scalar.activation(out[:, gg], src[:, gg], ACT.Copy, scale=rstd[:])
            act.drain()
            act.sem_inc(q_ready, 1)
            act.wait_ge(shifted, 1)
            nc.scalar.activation(p[:], p[:], ACT.Exp)
            nc.scalar.activation(esink[:], esink[:], ACT.Exp).then_inc(esum, 1)
            act.wait_ge(o_in, 16)
            nc.scalar.activation(junk[:], o[:], ACT.Square, accum_out=ms[:]).then_inc(oms_ready, 1)

        @block.gpsimd
        def _(pool):
            nc.gpsimd.memset(half[:], -0.5)
            for ready, done in ((ms_ready, rstd_ready), (oms_ready, orstd_ready)):
                pool.wait_ge(ready, 1)
                nc.gpsimd.tensor_scalar(ms[:], ms[:], 1.0 / D, EPS, ALU.mult, ALU.add)
                pool.drain()
                nc.gpsimd.tensor_tensor(rstd[:], ms[:], half[:], ALU.pow).then_inc(done, 1)

        @block.vector
        def _(dve):
            nc.vector.memset(q_heads[:], 0.0)
            dve.wait_ge(x_turned, 1)
            nc.vector.tensor_tensor(hT[:], psum[0][:, 0:DB * DEC].rearrange("p (b t) -> p b t", b=DB),
                                    gain[:, :, None].broadcast_to([P, DB, DEC]), ALU.mult).then_inc(hT_ready, 1)
            dve.wait_ge(rstd_ready, 1)
            dve.wait_ge(projected, 3)
            nc.vector.tensor_scalar(kv[:], psum[3][0:DEC, :], rstd[:], None, ALU.mult).then_inc(kv_ready, 1)
            for n in range(4):
                dve.wait_ge(cache_turned, n + 1)
                nc.vector.tensor_copy(kT[:, 2 * n:2 * n + 2, :, 0:WINDOW],
                                      psum[4 + n][:].rearrange("p (b j k) -> p b j k", b=2, j=2))
            dve.wait_ge(qk_turned, 1)
            nc.vector.tensor_copy(k_newT[:], psum[0][:, P:P + 2 * DEC].rearrange("p (j b) -> p j b", j=2))
            for g in range(KV):
                lo, hi = (g % 2) * HD, (g % 2 + 1) * HD
                src = psum[0][lo:hi, (g // 2) * GROUP * DEC:(g // 2 + 1) * GROUP * DEC].rearrange("p (r b) -> p b r", r=GROUP)
                nc.vector.tensor_scalar(q_heads[lo:hi, :, g // 2, g * GROUP:(g + 1) * GROUP], src, HD ** -0.5, None, ALU.mult)
            dve.drain()
            dve.sem_inc(q_heads_ready, 1)
            for j in range(2):
                ins = nc.vector.tensor_copy(kT[:, :, j, WINDOW], k_newT[:, j, :])
            dve.drain()
            dve.sem_inc(kT_ready, 1)
            dve.wait_ge(scored, 1)
            for n, m in enumerate((3, 3, 2)):
                nc.vector.tensor_tensor(p[:, 3 * n:3 * n + m, :], psum[1 + n][0:HEADS, 0:m * KEYS].rearrange("p (b k) -> p b k", b=m),
                                        shared["bias_row"][:, None, :].broadcast_to([HEADS, m, KEYS]), ALU.add)
            dve.drain()
            nc.vector.tensor_reduce(top[:], p[:], AX.X, ALU.max)
            dve.drain()
            nc.vector.tensor_scalar(top[:], top[:], sink[:], None, ALU.max)
            dve.drain()
            nc.vector.tensor_tensor(p[:], p[:], top[:, :, None].broadcast_to([HEADS, DEC, KEYS]), ALU.subtract)
            nc.vector.tensor_scalar(esink[:], top[:], -1.0, sink[:], ALU.mult, ALU.add)
            dve.drain()
            dve.sem_inc(shifted, 1)
            dve.wait_ge(esum, 1)
            nc.vector.tensor_reduce(total[:], p[:], AX.X, ALU.add)
            dve.drain()
            nc.vector.tensor_tensor(total[:], total[:], esink[:], ALU.add)
            dve.drain()
            nc.vector.reciprocal(total[:], total[:])
            dve.drain()
            nc.vector.tensor_tensor(p[:], p[:], total[:, :, None].broadcast_to([HEADS, DEC, KEYS]), ALU.mult).then_inc(p_ready, 1)
            dve.wait_ge(p_turned, 1)
            nc.vector.tensor_copy(pT[:], psum[0][:, 0:P].rearrange("p (b h) -> p b h", b=DEC))
            nc.vector.tensor_copy(p_new[:], psum[0][0:DEC, 256:256 + HEADS])
            dve.drain()
            nc.vector.tensor_tensor(p_own[:], p_new[:, None, :].broadcast_to([DEC, DEC, HEADS]),
                                    ident[0:DEC, 0:DEC, None].broadcast_to([DEC, DEC, HEADS]), ALU.mult)
            dve.drain()
            dve.sem_inc(pT_ready, 1)
            dve.wait_ge(valued, 1)
            for b in range(DEC):
                nc.vector.tensor_tensor(wide[:, b], psum[4 + b // 2][0:HEADS, (b % 2) * 256:(b % 2 + 1) * 256].rearrange("p (g d) -> p g d", g=KV),
                                        shared["head_mask"][:, :, None].broadcast_to([HEADS, KV, HD]), ALU.mult)
            dve.drain()
            nc.vector.tensor_reduce(o_heads[:], wide[:].rearrange("p b g d -> p b d g"), AX.X, ALU.add).then_inc(o_heads_ready, 1)
            dve.wait_ge(orstd_ready, 1)
            nc.vector.tensor_scalar(o[:], o[:], rstd[:], None, ALU.mult).then_inc(out_ready, 1)




def ssd_prompt(nc, io, psum, shared, w_zx):
    ident, tri, far, ones, gain, conv = (shared[k] for k in ("ident", "tri", "far", "ones", "gain_mix", "conv"))
    NH = SSD_HEADS
    with Stage(nc) as stage:
        sb, sem, event = stage.buffer, stage.semaphore, stage.event

        x = sb("ssd_x", [P, D])
        junk = sb("ssd_junk", [P, D])
        ms, rstd, yms, yrstd = (sb("ssd_" + n, [P, 1]) for n in ("ms", "rstd", "yms", "yrstd"))
        half, part = sb("ssd_half", [P, 1]), sb("ssd_part", [P, 1])
        hT = sb("ssd_hT", [P, DB, P])
        zs = sb("ssd_zs", [P, D])
        xbc = sb("ssd_xbc", [P, CONV_DIM])
        xbcT = sb("ssd_xbcT", [P, CB, CONV - 1 + P])
        cv = sb("ssd_cv", [P, CB, P])
        tap = sb("ssd_tap", [P, CB, P])
        dt_raw, dt_neg, dt_exp, dt_u, dt_err, dt, decay = (sb("ssd_" + n, [P, NH]) for n in
                                                         ("dt_raw", "dt_neg", "dt_exp", "dt_u", "dt_err", "dt", "decay"))
        rate = sb("ssd_rate", [P, NH])
        dt_bias = sb("ssd_dt_bias", [P, NH])
        skip = sb("ssd_skip", [P, NH])
        sums = sb("ssd_sums", [P, 2, NH])
        esums = sb("ssd_esums", [P, 2, NH])
        nsum = sb("ssd_nsum", [P, NH])
        to_end = sb("ssd_to_end", [P, NH])
        xs = sb("ssd_xs", [P, D])
        bm = sb("ssd_bm", [P, SSD_G, STATE])
        xdt = sb("ssd_xdt", [P, D])
        xend = sb("ssd_xend", [P, D])
        cb = sb("ssd_cb", [P, SSD_G, P])
        dec = sb("ssd_dec", [P, 2, 4, P])
        y = sb("ssd_y", [P, D])
        out_rows = sb("ssd_out", [P, D])
        xskip = sb("ssd_xskip", [P, D])
        state = sb("ssd_state", [P, D])

        def by_head(ap):
            return ap.rearrange("p (h d) -> p h d", d=HD)

        def per_head(ap, n=NH):
            return ap[:, :, None].broadcast_to([P, n, HD])

        front_fills = Fills(sem, "ssd_front", [
            ("xT0", 0), ("xT1", 1), ("x0", 2), ("x1", 3), ("x2", 0), ("dt", 1),
            ("cT0", 2), ("cT1", 3), ("cT2", 0), ("z0", 1), ("z1", 2), ("sums", 3)])
        back_fills = Fills(sem, "ssd_back", [
            ("xs0", 4), ("xs1", 5), ("bc", 6), ("yo0", 7), ("yo1", 4), ("G0", 5), ("G1", 6),
            ("yd0", 7), ("G2", 5), ("G3", 6), ("yd1", 4), ("st0", 5), ("st1", 6)])

        def fill(name):
            f = front_fills if name in front_fills.place else back_fills
            return f, f.bank(name), psum[f.bank(name)]

        chunks = {"z0": 0, "z1": 512, "x0": 1024, "x1": 1536, "x2": 2048, "dt": 2560}

        x_in = event("ssd_x_in", 1, 16)
        x_seen = event("ssd_x_seen", 2)
        ms_ready, rstd_ready, yms_ready, yrstd_ready = (event("ssd_" + n) for n in ("ms_ready", "rstd_ready", "yms_ready", "yrstd_ready"))
        hT_ready = event("ssd_hT_ready")
        projected = event("ssd_projected")
        xbc_ready = event("ssd_xbc_ready", 2)
        xbcT_ready = event("ssd_xbcT_ready")
        taps_done = event("ssd_taps_done", 2)
        cv_ready, cv_used = event("ssd_cv_ready"), event("ssd_cv_used")
        decays_over, xskip_ready = event("ssd_decays_over"), event("ssd_xskip_ready")
        dt_raw_ready, dt_exp_ready, dt_u_ready, dt_log_ready, decay_ready = (
            event("ssd_" + n) for n in ("dt_raw_ready", "dt_exp_ready", "dt_u_ready", "dt_log_ready", "decay_ready"))
        sums_ready, esums_ready = event("ssd_sums_ready"), event("ssd_esums_ready")
        xs_ready, xdt_ready, xend_ready = event("ssd_xs_ready"), event("ssd_xdt_ready"), event("ssd_xend_ready")
        dec_ready, scan_ready, scanned = event("ssd_dec_ready", 4), event("ssd_scan_ready", 4), event("ssd_scanned", 4)
        y_gated, out_ready = event("ssd_y_gated"), event("ssd_out_ready")
        state_ready = event("ssd_state_ready")
        stored = event("ssd_stored", 1, 16)
        loaded, rates_ready, consts_ready = sem("ssd_loaded"), sem("ssd_rates_ready"), sem("ssd_consts_ready")
        state_turned, state_copied, tail_out = sem("ssd_state_turned"), sem("ssd_state_copied"), sem("ssd_tail_out")

        HALF = CB // 2

        def convolve(eng, engine, lo, hi, chunk):
            engine.wait_ge(xbcT_ready.sem, xbcT_ready.this(chunk))
            engine.wait_ge(cv_used.sem, cv_used.last(chunk))
            n, c, x = hi - lo, cv[:, lo:hi, :], xbcT[:, lo:hi, :]
            for k in range(CONV):
                eng.tensor_tensor(tap[:, lo:hi, :] if k else c, x[:, :, k:k + P],
                                  conv[:, k, lo:hi, None].broadcast_to([P, n, P]), ALU.mult)
                engine.drain()
                if k:
                    eng.tensor_tensor(c, c, tap[:, lo:hi, :], ALU.add)
                    engine.drain()
            eng.tensor_tensor(c, c, conv[:, CONV, lo:hi, None].broadcast_to([P, n, P]), ALU.add)
            eng.tensor_copy(x[:, :, 0:CONV - 1], x[:, :, P:P + CONV - 1])
            engine.drain()
            engine.sem_inc(taps_done.sem, 1)

        block = stage.block()

        @block.sync
        def _(sp):
            def load(t):
                sp.wait_ge(x_seen.sem, x_seen.last(t))
                sp.dma_start(x[:], io["x_prompt"][bass.ds(t * P, P), :]).then_inc(x_in.sem, 16)

            def store(t):
                sp.wait_ge(out_ready.sem, out_ready.this(t))
                sp.dma_start(io["mixed"][bass.ds(t * P, P), D:2 * D], out_rows[:]).then_inc(stored.sem, 16)

            sp.sem_inc(x_in.sem, 16)
            sp.sem_inc(stored.sem, 16)
            sp.dma_start(rate[:], io["a_log"].broadcast_to([P, NH])).then_inc(loaded, 16)
            sp.dma_start(dt_bias[:], io["dt_bias"].broadcast_to([P, NH])).then_inc(loaded, 16)
            sp.dma_start(skip[:], io["d_skip"].broadcast_to([P, NH])).then_inc(loaded, 16)
            for t in range(3):
                load(t)
            with sp.Fori(0, TILES - 3) as t:
                store(t)
                load(t + 3)
            with sp.Fori(TILES - 3, TILES) as t:
                store(t)
            sp.dma_start(io["p_conv"], xbc[P - CONV + 1:P, :]).then_inc(tail_out, 16)
            sp.wait_ge(state_copied, 2)
            sp.dma_start(io["p_ssm"].rearrange("(j q) n -> q j n", q=P), y[:].rearrange("p (j n) -> p j n", j=DB)).then_inc(tail_out, 16)
            sp.wait_ge(tail_out, 32)
            sp.wait_ge(stored.sem, stored.this(TILES - 1))

        @block.tensor
        def _(pe):
            def begin(name, t):
                f, bank, out = fill(name)
                pe.wait_ge(f.free[bank], f.at(name, t))
                return out, f.full[bank]

            def turned(name, t, blocks):
                out, full = begin(name, t)
                for j, block_in in enumerate(blocks):
                    ins = nc.tensor.transpose(out[:, j * P:(j + 1) * P], block_in, ident[:])
                ins.then_inc(full, 1)

            def rows(u):
                pe.wait_ge(x_in.sem, x_in.this(u))
                for h in range(2):
                    turned(f"xT{h}", u, [x[:, (4 * h + j) * P:(4 * h + j + 1) * P] for j in range(4)])
                pe.drain()
                pe.sem_inc(x_seen.sem, 1)

            def project(name, u):
                col = chunks[name]
                n = min(BANK, IN_COLS - 1536 - col)
                out, full = begin(name, u)
                for b in range(DB):
                    ins = nc.tensor.matmul(out[:, 0:n], hT[:, b, :], w_zx[:, b, col:col + n], start=(b == 0), stop=(b == DB - 1))
                ins.then_inc(full, 1)

            def channels(u):
                pe.wait_ge(xbc_ready.sem, xbc_ready.this(u, 2))
                for n in range(3):
                    turned(f"cT{n}", u, [xbc[:, (4 * n + j) * P:(4 * n + j + 1) * P] for j in range(4)])

            def summed(u):
                pe.wait_ge(decay_ready.sem, decay_ready.this(u))
                out, full = begin("sums", u)
                nc.tensor.matmul(out[:, 0:NH], tri[:], decay[:], start=True, stop=True)
                nc.tensor.matmul(out[:, NH:2 * NH], ones[:], decay[:], start=True, stop=True).then_inc(full, 1)

            def tokens(t):
                pe.wait_ge(cv_ready.sem, cv_ready.this(t))
                for h in range(2):
                    turned(f"xs{h}", t, [cv[:, 4 * h + j, :] for j in range(4)])
                out, full = begin("bc", t)
                for g in range(SSD_G):
                    nc.tensor.transpose(out[:, g * P:(g + 1) * P], cv[:, 8 + g, :], ident[:])
                for g in range(SSD_G):
                    ins = nc.tensor.matmul(out[:, (2 + g) * P:(3 + g) * P], cv[:, 8 + g, :], cv[:, 10 + g, :], start=True, stop=True)
                ins.then_inc(full, 1)
                pe.wait_ge(state_ready.sem, state_ready.last(t))
                for g in range(SSD_G):
                    out, full = begin(f"yo{g}", t)
                    nc.tensor.matmul(out[:], cv[:, 10 + g, :], state[:, g * BANK:(g + 1) * BANK], start=True, stop=True).then_inc(full, 1)
                pe.drain()
                pe.sem_inc(cv_used.sem, 1)

            def decays(t, n):
                out, full = begin(f"G{n}", t)
                nc.tensor.matmul(out[:].rearrange("p (h l) -> p h l", h=4), ident[:],
                                 far[:, None, :].broadcast_to([P, 4, P]), start=True, stop=False)
                for j in range(4):
                    ins = nc.tensor.matmul(out[:, j * P:(j + 1) * P], decay[:, 4 * n + j:4 * n + j + 1].broadcast_to([P, P]), tri[:],
                                           start=False, stop=(j == 3))
                ins.then_inc(full, 1)
                if n == 3:
                    pe.drain()
                    pe.sem_inc(decays_over.sem, 1)

            def scan(t, n):
                if n == 0:
                    pe.wait_ge(xdt_ready.sem, xdt_ready.this(t))
                pe.wait_ge(scan_ready.sem, scan_ready.this(t, n + 1))
                f, bank, out = fill(f"yd{n // 2}")
                if n % 2 == 0:
                    begin(f"yd{n // 2}", t)
                for j in range(4):
                    h = 4 * n + j
                    nc.tensor.matmul(out[:, (h % 8) * HD:(h % 8 + 1) * HD], dec[:, n % 2, j, :],
                                     xdt[:, h * HD:(h + 1) * HD], start=True, stop=True)
                pe.drain()
                pe.sem_inc(scanned.sem, 1)
                if n % 2:
                    pe.sem_inc(f.full[bank], 1)

            def grown(t):
                pe.wait_ge(xend_ready.sem, xend_ready.this(t))
                for g in range(SSD_G):
                    out, full = begin(f"st{g}", t)
                    nc.tensor.matmul(out[:], bm[:, g, :], xend[:, g * BANK:(g + 1) * BANK], start=True, stop=True).then_inc(full, 1)

            def turn(t, u):
                back, front = t is not None, u is not None
                if front:
                    rows(u)
                if back:
                    tokens(t)
                if front:
                    pe.wait_ge(hT_ready.sem, hT_ready.this(u))
                    project("x0", u)
                    project("x1", u)
                if back:
                    decays(t, 0)
                if front:
                    project("x2", u)
                    project("dt", u)
                if back:
                    decays(t, 1)
                if front:
                    channels(u)
                if back:
                    scan(t, 0)
                    decays(t, 2)
                    scan(t, 1)
                    decays(t, 3)
                if front:
                    project("z0", u)
                if back:
                    scan(t, 2)
                    scan(t, 3)
                    grown(t)
                if front:
                    project("z1", u)
                    pe.drain()
                    pe.sem_inc(projected.sem, 1)
                    summed(u)

            front_fills.prime(pe)
            back_fills.prime(pe)
            for e in (x_seen, projected, scanned, cv_used, decays_over):
                pe.sem_inc(e.sem, 1)
            pe.wait_ge(consts_ready, 1)
            turn(None, 0)
            with pe.Fori(0, TILES - 1) as t:
                turn(t, t + 1)
            turn(TILES - 1, None)
            pe.wait_ge(state_ready.sem, state_ready.this(TILES - 1))
            for h in range(2):
                pe.wait_ge(back_fills.free[4 + h], TILES * back_fills.count[4 + h] + 1)
                for j in range(4):
                    ins = nc.tensor.transpose(psum[4 + h][:, j * P:(j + 1) * P], state[:, (4 * h + j) * P:(4 * h + j + 1) * P], ident[:])
                ins.then_inc(state_turned, 1)

        @block.scalar
        def _(act):
            def take(name, t, dst, func=ACT.Copy, **how):
                f, bank, src = fill(name)
                act.wait_ge(f.full[bank], f.at(name, t))
                nc.scalar.activation(dst, src[:], func, **how).then_inc(f.free[bank], 1)

            def squares(u):
                act.wait_ge(x_in.sem, x_in.this(u))
                nc.scalar.activation(junk[:], x[:], ACT.Square, accum_out=ms[:])
                act.drain()
                act.sem_inc(ms_ready.sem, 1)
                act.sem_inc(x_seen.sem, 1)

            def convolved(u):
                act.wait_ge(taps_done.sem, taps_done.this(u, 2))
                nc.scalar.activation(cv[:], cv[:], ACT.Silu)
                act.drain()
                act.sem_inc(cv_ready.sem, 1)

            def tokens(t):
                for h in range(2):
                    take(f"xs{h}", t, xs[:, h * BANK:(h + 1) * BANK])
                act.drain()
                act.sem_inc(xs_ready.sem, 1)

            def middle(u):
                act.wait_ge(rstd_ready.sem, rstd_ready.this(u))
                take("x1", u, xbc[:, BANK:2 * BANK], scale=rstd[:])
                act.drain()
                act.sem_inc(xbc_ready.sem, 1)

            def channels(u):
                act.wait_ge(taps_done.sem, taps_done.last(u))
                for n in range(3):
                    f, bank, src = fill(f"cT{n}")
                    act.wait_ge(f.full[bank], f.at(f"cT{n}", u))
                    nc.scalar.copy(xbcT[:, 4 * n:4 * n + 4, CONV - 1:], src[:].rearrange("p (b t) -> p b t", b=4)
                                   ).then_inc(f.free[bank], 1)
                act.drain()
                act.sem_inc(xbcT_ready.sem, 1)

            def softplus_exp(u):
                act.wait_ge(dt_raw_ready.sem, dt_raw_ready.this(u))
                nc.scalar.activation(dt_exp[:], dt_neg[:], ACT.Exp)
                act.drain()
                act.sem_inc(dt_exp_ready.sem, 1)

            def softplus_log(u):
                act.wait_ge(dt_u_ready.sem, dt_u_ready.this(u))
                nc.scalar.activation(dt_neg[:], dt_u[:], ACT.Ln)
                act.drain()
                act.sem_inc(dt_log_ready.sem, 1)

            def decays(t, n):
                act.wait_ge(scanned.sem, scanned.this(t, n - 1) if n >= 2 else scanned.last(t))
                f, bank, src = fill(f"G{n}")
                act.wait_ge(f.full[bank], f.at(f"G{n}", t))
                for j in range(4):
                    nc.scalar.activation(dec[:, n % 2, j, :], src[:, j * P:(j + 1) * P], ACT.Exp,
                                         bias=nsum[:, 4 * n + j:4 * n + j + 1])
                act.drain()
                act.sem_inc(dec_ready.sem, 1)
                act.sem_inc(f.free[bank], 1)

            def gated(t):
                act.wait_ge(y_gated.sem, y_gated.this(t))
                nc.scalar.activation(junk[:], y[:], ACT.Square, accum_out=yms[:])
                act.drain()
                act.sem_inc(yms_ready.sem, 1)

            def gates(u):
                act.wait_ge(y_gated.sem, y_gated.last(u))
                for h in range(2):
                    take(f"z{h}", u, zs[:, h * BANK:(h + 1) * BANK], ACT.Silu, scale=rstd[:])

            def summed(u):
                act.wait_ge(sums_ready.sem, sums_ready.this(u))
                nc.scalar.activation(esums[:], sums[:], ACT.Exp)
                nc.scalar.activation(to_end[:], to_end[:], ACT.Exp)
                act.drain()
                act.sem_inc(esums_ready.sem, 1)

            def turn(t, u):
                back, front = t is not None, u is not None
                if front:
                    squares(u)
                if back:
                    tokens(t)
                if front:
                    middle(u)
                if back:
                    decays(t, 0)
                if front:
                    softplus_exp(u)
                if back:
                    decays(t, 1)
                if front:
                    channels(u)
                    softplus_log(u)
                if back:
                    decays(t, 2)
                    decays(t, 3)
                    gated(t)
                if front:
                    gates(u)
                    convolved(u)
                    summed(u)

            for e in (ms_ready, dt_exp_ready, dt_log_ready, xbcT_ready, esums_ready, cv_ready, xs_ready, dec_ready, yms_ready):
                act.sem_inc(e.sem, 1)
            act.wait_ge(loaded, 48)
            nc.scalar.activation(rate[:], rate[:], ACT.Exp).then_inc(rates_ready, 1)
            turn(None, 0)
            with act.Fori(0, TILES - 1) as t:
                turn(t, t + 1)
            turn(TILES - 1, None)

        @block.gpsimd
        def _(pool):
            def factor(src, dst, ready, done, t):
                pool.wait_ge(ready.sem, ready.this(t))
                nc.gpsimd.tensor_tensor(src[:], src[:], part[:], ALU.mult)
                pool.drain()
                nc.gpsimd.tensor_scalar(src[:], src[:], EPS, None, ALU.add)
                pool.drain()
                nc.gpsimd.tensor_tensor(dst[:], src[:], half[:], ALU.pow)
                pool.drain()
                pool.sem_inc(done.sem, 1)

            def turn(t, u):
                if u is not None:
                    factor(ms, rstd, ms_ready, rstd_ready, u)
                if t is not None:
                    pool.wait_ge(xs_ready.sem, xs_ready.this(t))
                    nc.gpsimd.tensor_tensor(by_head(xskip[:]), by_head(xs[:]), per_head(skip), ALU.mult)
                    pool.drain()
                    pool.sem_inc(xskip_ready.sem, 1)
                if u is not None:
                    convolve(nc.gpsimd, pool, 0, HALF, u)
                if t is not None:
                    factor(yms, yrstd, yms_ready, yrstd_ready, t)

            nc.gpsimd.memset(half[:], -0.5)
            nc.gpsimd.memset(part[:], 1.0 / D)
            nc.gpsimd.memset(xbcT[:, :, 0:CONV - 1], 0.0)
            pool.drain()
            for e in (rstd_ready, taps_done, xskip_ready, yrstd_ready):
                pool.sem_inc(e.sem, 1)
            pool.wait_ge(loaded, 48)
            turn(None, 0)
            with pool.Fori(0, TILES - 1) as t:
                turn(t, t + 1)
            turn(TILES - 1, None)

        @block.vector
        def _(dve):
            def full(name, t):
                f, bank, src = fill(name)
                dve.wait_ge(f.full[bank], f.at(name, t))
                return src, f.free[bank]

            def rows(u):
                dve.wait_ge(projected.sem, projected.last(u))
                for h in range(2):
                    src, free = full(f"xT{h}", u)
                    nc.vector.tensor_tensor(hT[:, 4 * h:4 * h + 4, :], src[:].rearrange("p (b t) -> p b t", b=4),
                                            gain[:, 4 * h:4 * h + 4, None].broadcast_to([P, 4, P]), ALU.mult).then_inc(free, 1)
                dve.drain()
                dve.sem_inc(hT_ready.sem, 1)

            def tokens(t):
                dve.wait_ge(xs_ready.sem, xs_ready.this(t))
                nc.vector.tensor_tensor(by_head(xdt[:]), by_head(xs[:]), per_head(dt), ALU.mult)
                dve.drain()
                dve.sem_inc(xdt_ready.sem, 1)
                src, free = full("bc", t)
                nc.vector.tensor_copy(bm[:], src[:, 0:2 * P].rearrange("p (g n) -> p g n", g=2))
                nc.vector.tensor_copy(cb[:], src[:, 2 * P:4 * P].rearrange("p (g n) -> p g n", g=2)).then_inc(free, 1)
                dve.wait_ge(esums_ready.sem, esums_ready.this(t))
                nc.vector.tensor_tensor(by_head(xend[:]), by_head(xdt[:]), per_head(to_end), ALU.mult)
                dve.drain()
                dve.sem_inc(xend_ready.sem, 1)

            def scaled(t):
                dve.wait_ge(stored.sem, stored.last(t))
                dve.wait_ge(yrstd_ready.sem, yrstd_ready.this(t))
                nc.vector.tensor_scalar(out_rows[:], y[:], yrstd[:], None, ALU.mult)
                dve.drain()
                dve.sem_inc(out_ready.sem, 1)

            def begin_y(t):
                for g in range(SSD_G):
                    src, free = full(f"yo{g}", t)
                    nc.vector.tensor_tensor(by_head(y[:, g * BANK:(g + 1) * BANK]), by_head(src[:]),
                                            per_head(esums[:, 0, g * SSD_HPG:(g + 1) * SSD_HPG], SSD_HPG), ALU.mult).then_inc(free, 1)

            def middle(u):
                dve.wait_ge(rstd_ready.sem, rstd_ready.this(u))
                for name, at in (("x0", 0), ("x2", 2)):
                    src, free = full(name, u)
                    nc.vector.tensor_scalar(xbc[:, at * BANK:(at + 1) * BANK], src[:], rstd[:], None, ALU.mult).then_inc(free, 1)
                dve.drain()
                dve.sem_inc(xbc_ready.sem, 1)
                src, free = full("dt", u)
                nc.vector.scalar_tensor_tensor(dt_raw[:], src[:, 0:NH], rstd[:], dt_bias[:], ALU.mult, ALU.add).then_inc(free, 1)
                dve.drain()
                nc.vector.scalar_tensor_tensor(dt_neg[:], dt_raw[:], -1.0, dt_raw[:], ALU.mult, ALU.min)
                nc.vector.tensor_scalar(dt_raw[:], dt_raw[:], 0.0, None, ALU.max)
                dve.drain()
                dve.sem_inc(dt_raw_ready.sem, 1)

            def softplus(u):
                dve.wait_ge(dt_exp_ready.sem, dt_exp_ready.this(u))
                nc.vector.tensor_scalar(dt_u[:], dt_exp[:], 1.0, None, ALU.add)
                dve.drain()
                dve.sem_inc(dt_u_ready.sem, 1)
                nc.vector.scalar_tensor_tensor(dt_err[:], dt_u[:], -1.0, dt_exp[:], ALU.add, ALU.subtract)
                nc.vector.reciprocal(dt[:], dt_u[:])
                dve.drain()
                nc.vector.tensor_tensor(dt_err[:], dt_err[:], dt[:], ALU.mult)
                dve.drain()
                nc.vector.tensor_tensor(dt_raw[:], dt_raw[:], dt_err[:], ALU.subtract)
                dve.drain()

            def rates(u):
                dve.wait_ge(dt_log_ready.sem, dt_log_ready.this(u))
                nc.vector.tensor_tensor(dt[:], dt_raw[:], dt_neg[:], ALU.add)
                dve.drain()
                dve.wait_ge(decays_over.sem, decays_over.last(u))
                nc.vector.tensor_tensor(decay[:], dt[:], rate[:], ALU.mult)
                dve.drain()
                dve.sem_inc(decay_ready.sem, 1)

            def decays(t, n):
                dve.wait_ge(dec_ready.sem, dec_ready.this(t, n + 1))
                nc.vector.tensor_tensor(dec[:, n % 2], dec[:, n % 2], cb[:, n // 2, None, :].broadcast_to([P, 4, P]), ALU.mult)
                dve.drain()
                dve.sem_inc(scan_ready.sem, 1)

            def finish(t):
                for g in range(SSD_G):
                    src, free = full(f"yd{g}", t)
                    cols = slice(g * BANK, (g + 1) * BANK)
                    nc.vector.tensor_tensor(y[:, cols], y[:, cols], src[:], ALU.add).then_inc(free, 1)
                dve.drain()
                dve.wait_ge(xskip_ready.sem, xskip_ready.this(t))
                nc.vector.tensor_tensor(y[:], y[:], xskip[:], ALU.add)
                dve.drain()
                nc.vector.tensor_tensor(y[:], y[:], zs[:], ALU.mult)
                dve.drain()
                dve.sem_inc(y_gated.sem, 1)
                nc.vector.tensor_tensor(by_head(state[:]), by_head(state[:]), per_head(esums[:, 1, :]), ALU.mult)
                dve.drain()
                for g in range(SSD_G):
                    src, free = full(f"st{g}", t)
                    cols = slice(g * BANK, (g + 1) * BANK)
                    nc.vector.tensor_tensor(state[:, cols], state[:, cols], src[:], ALU.add).then_inc(free, 1)
                dve.drain()
                dve.sem_inc(state_ready.sem, 1)

            def summed(u):
                src, free = full("sums", u)
                nc.vector.tensor_copy(sums[:], src[:, 0:2 * NH].rearrange("p (k h) -> p k h", k=2)).then_inc(free, 1)
                dve.drain()
                nc.vector.tensor_scalar(nsum[:], sums[:, 0, :], -1.0, None, ALU.mult)
                nc.vector.tensor_tensor(to_end[:], sums[:, 1, :], sums[:, 0, :], ALU.subtract)
                dve.drain()
                dve.sem_inc(sums_ready.sem, 1)

            def turn(t, u, first=False):
                back, front = t is not None, u is not None
                if front:
                    rows(u)
                if back:
                    tokens(t)
                    if not first:
                        scaled(t - 1)
                    begin_y(t)
                if front:
                    middle(u)
                if back:
                    decays(t, 0)
                    decays(t, 1)
                if front:
                    softplus(u)
                    convolve(nc.vector, dve, HALF, CB, u)
                if back:
                    decays(t, 2)
                    decays(t, 3)
                if front:
                    rates(u)
                if back:
                    finish(t)
                if front:
                    summed(u)

            nc.vector.memset(state[:], 0.0)
            dve.wait_ge(rates_ready, 1)
            nc.vector.tensor_scalar(rate[:], rate[:], -1.0, None, ALU.mult)
            dve.drain()
            dve.sem_inc(consts_ready, 1)
            for e in (hT_ready, xbc_ready, dt_raw_ready, dt_u_ready, decay_ready, sums_ready, xdt_ready, xend_ready,
                      scan_ready, y_gated, state_ready, out_ready):
                dve.sem_inc(e.sem, 1)
            turn(None, 0)
            turn(0, 1, first=True)
            with dve.Fori(1, TILES - 1) as t:
                turn(t, t + 1)
            turn(TILES - 1, None)
            scaled(TILES - 1)
            for h in range(2):
                dve.wait_ge(state_turned, h + 1)
                nc.vector.tensor_copy(y[:, h * BANK:(h + 1) * BANK], psum[4 + h][:]).then_inc(state_copied, 1)


def ssd_sample_inputs(nc, io, psum, shared, w_zx):
    ident, gain = shared["ident"], shared["gain_mix"]
    NH = SSD_HEADS
    with Stage(nc) as stage:
        sb, sem = stage.buffer, stage.semaphore

        x, junk, gates = sb("sin_x", [DEC, D]), sb("sin_junk", [DEC, D]), sb("sin_gates", [DEC, D])
        ms, rstd, half = sb("sin_ms", [DEC, 1]), sb("sin_rstd", [DEC, 1]), sb("sin_half", [DEC, 1])
        hT = sb("sin_hT", [P, DB, DEC])
        past = sb("sin_past", [DEC, CONV, CONV_DIM])
        weights = sb("sin_weights", [DEC, CONV + 1, CONV_DIM])
        cv, tap = sb("sin_cv", [DEC, CONV_DIM]), sb("sin_tap", [DEC, CONV_DIM])
        dt_bias = sb("sin_dt_bias", [DEC, NH])
        raw, neg, e, u, err, dt = (sb("sin_" + n, [DEC, NH]) for n in ("raw", "neg", "e", "u", "err", "dt"))
        loaded, x_in, x_turned = sem("sin_loaded"), sem("sin_x_in"), sem("sin_x_turned")
        ms_ready, rstd_ready, hT_ready, projected = sem("sin_ms_ready"), sem("sin_rstd_ready"), sem("sin_hT_ready"), sem("sin_projected")
        new_ready, taps_done, cv_ready = sem("sin_new_ready"), sem("sin_taps_done"), sem("sin_cv_ready")
        neg_ready, e_ready, u_ready, log_ready, dt_ready = (sem("sin_" + n) for n in ("neg_ready", "e_ready", "u_ready", "log_ready", "dt_ready"))
        gates_ready, stored = sem("sin_gates_ready"), sem("sin_stored")
        block = stage.block()

        @block.sync
        def _(sp):
            sp.dma_start(x[:], io["x_sample"]).then_inc(x_in, 16)
            sp.dma_start(past[:, 0:CONV - 1, :], io["state_conv"]).then_inc(loaded, 16)
            for k in range(CONV):
                sp.dma_start(weights[:, k, :], io["conv_w"][k:k + 1, :].broadcast_to([DEC, CONV_DIM])).then_inc(loaded, 16)
            sp.dma_start(weights[:, CONV, :], io["conv_b"].broadcast_to([DEC, CONV_DIM])).then_inc(loaded, 16)
            sp.dma_start(dt_bias[:], io["dt_bias"].broadcast_to([DEC, NH])).then_inc(loaded, 16)
            sp.wait_ge(new_ready, 1)
            sp.dma_start(io["s_conv"], past[:, 1:CONV, :]).then_inc(stored, 16)
            sp.wait_ge(cv_ready, 1)
            sp.dma_start(io["rows2"], cv[:, 0:D]).then_inc(stored, 16)
            sp.dma_start(io["bcs"], cv[:, D:CONV_DIM]).then_inc(stored, 16)
            sp.wait_ge(dt_ready, 1)
            sp.dma_start(io["dts"], dt[:]).then_inc(stored, 16)
            sp.wait_ge(gates_ready, 1)
            sp.dma_start(io["gates"], gates[:]).then_inc(stored, 16)
            sp.wait_ge(stored, 80)

        @block.tensor
        def _(pe):
            pe.wait_ge(x_in, 16)
            for b in range(DB):
                ins = nc.tensor.transpose(psum[0][:, b * DEC:(b + 1) * DEC], x[:, b * P:(b + 1) * P], ident[0:DEC, 0:DEC])
            ins.then_inc(x_turned, 1)
            pe.wait_ge(hT_ready, 1)
            for c in (2, 3, 4, 5, 0, 1):
                n = min(BANK, IN_COLS - 1536 - c * BANK)
                for b in range(DB):
                    ins = nc.tensor.matmul(psum[1 + c][0:DEC, 0:n], hT[:, b, :], w_zx[:, b, c * BANK:c * BANK + n],
                                           start=(b == 0), stop=(b == DB - 1))
                ins.then_inc(projected, 1)

        @block.scalar
        def _(act):
            act.wait_ge(x_in, 16)
            nc.scalar.activation(junk[:], x[:], ACT.Square, accum_out=ms[:]).then_inc(ms_ready, 1)
            act.wait_ge(neg_ready, 1)
            nc.scalar.activation(e[:], neg[:], ACT.Exp).then_inc(e_ready, 1)
            act.wait_ge(taps_done, 1)
            nc.scalar.activation(cv[:], cv[:], ACT.Silu).then_inc(cv_ready, 1)
            act.wait_ge(u_ready, 1)
            nc.scalar.activation(neg[:], u[:], ACT.Ln).then_inc(log_ready, 1)
            act.wait_ge(rstd_ready, 1)
            act.wait_ge(projected, 6)
            for h in range(2):
                ins = nc.scalar.activation(gates[:, h * BANK:(h + 1) * BANK], psum[1 + h][0:DEC, :], ACT.Silu, scale=rstd[:])
            ins.then_inc(gates_ready, 1)

        @block.gpsimd
        def _(pool):
            nc.gpsimd.memset(half[:], -0.5)
            pool.wait_ge(ms_ready, 1)
            nc.gpsimd.tensor_scalar(ms[:], ms[:], 1.0 / D, EPS, ALU.mult, ALU.add)
            pool.drain()
            nc.gpsimd.tensor_tensor(rstd[:], ms[:], half[:], ALU.pow).then_inc(rstd_ready, 1)

        @block.vector
        def _(dve):
            dve.wait_ge(x_turned, 1)
            nc.vector.tensor_tensor(hT[:], psum[0][:, 0:DB * DEC].rearrange("p (b t) -> p b t", b=DB),
                                    gain[:, :, None].broadcast_to([P, DB, DEC]), ALU.mult).then_inc(hT_ready, 1)

            def tap_of(k):
                nc.vector.tensor_tensor((tap if k else cv)[:], past[:, k, :], weights[:, k, :], ALU.mult)
                dve.drain()
                if k:
                    nc.vector.tensor_tensor(cv[:], cv[:], tap[:], ALU.add)
                    dve.drain()

            dve.wait_ge(loaded, 16 * (CONV + 3))
            for k in range(CONV - 1):
                tap_of(k)
            dve.wait_ge(rstd_ready, 1)
            dve.wait_ge(projected, 4)
            nc.vector.tensor_scalar(raw[:], psum[6][0:DEC, 0:NH], rstd[:], None, ALU.mult)
            for c in range(3):
                nc.vector.tensor_scalar(past[:, CONV - 1, c * BANK:(c + 1) * BANK], psum[3 + c][0:DEC, :], rstd[:], None, ALU.mult)
            dve.drain()
            dve.sem_inc(new_ready, 1)
            nc.vector.tensor_tensor(raw[:], raw[:], dt_bias[:], ALU.add)
            dve.drain()
            nc.vector.scalar_tensor_tensor(neg[:], raw[:], -1.0, raw[:], ALU.mult, ALU.min)
            nc.vector.tensor_scalar(raw[:], raw[:], 0.0, None, ALU.max)
            dve.drain()
            dve.sem_inc(neg_ready, 1)
            tap_of(CONV - 1)
            nc.vector.tensor_tensor(cv[:], cv[:], weights[:, CONV, :], ALU.add).then_inc(taps_done, 1)
            dve.wait_ge(e_ready, 1)
            nc.vector.tensor_scalar(u[:], e[:], 1.0, None, ALU.add).then_inc(u_ready, 1)
            dve.drain()
            nc.vector.scalar_tensor_tensor(err[:], u[:], -1.0, e[:], ALU.add, ALU.subtract)
            nc.vector.reciprocal(dt[:], u[:])
            dve.drain()
            nc.vector.tensor_tensor(err[:], err[:], dt[:], ALU.mult)
            dve.drain()
            nc.vector.tensor_tensor(raw[:], raw[:], err[:], ALU.subtract)
            dve.drain()
            dve.wait_ge(log_ready, 1)
            nc.vector.tensor_tensor(dt[:], raw[:], neg[:], ALU.add).then_inc(dt_ready, 1)


def memory_kv_and_sample_step(nc, io, psum, shared, mkT, mv, w_out, w_mo, w_out_in):
    ident, gain = shared["ident"], shared["gain_mem"]
    MT = N_MEM // P
    NH = SSD_HEADS
    with Stage(nc) as stage:
        sb, sem = stage.buffer, stage.semaphore

        w_mk, w_mv = w_mo, sb("w_mv", [P, DB, D])
        x, junk = sb("mem_x", [P, MT, D]), sb("mem_junk", [P, D])
        hT = sb("mem_hT", [P, MT, DB, P])
        mk = sb("mem_k", [P, MT, D])
        ms, rstd, half = sb("mem_ms", [P, MT]), sb("mem_rstd", [P, MT]), sb("mem_half", [P, MT])
        x_in, wk_in, wv_in = sem("mem_x_in"), sem("mem_wk_in"), sem("mem_wv_in")
        turned, hT_ready, ms_ready, rstd_ready = sem("mem_turned"), sem("mem_hT_ready"), sem("mem_ms_ready"), sem("mem_rstd_ready")
        projected, k_ready, v_ready, k_turned, stored = (sem("mem_" + n) for n in ("projected", "k_ready", "v_ready", "k_turned", "stored"))

        state, wide = (w_out[:, i * DB:(i + 1) * DB, :].rearrange("p b n -> p (b n)").rearrange("p (d n) -> p d n", n=STATE) for i in range(2))
        step_x, dt, rate, dec = sb("step_x", [P, HD]), sb("step_dt", [P, 1]), sb("step_rate", [P, 1]), sb("step_dec", [P, 1])
        bc = sb("step_bc", [P, 2, STATE])
        y_pairs = sb("step_y_pairs", [P, HD])
        y, xs, gates, skip = sb("step_y", [DEC, D]), sb("step_xs", [DEC, D]), sb("step_gates", [DEC, D]), sb("step_skip", [DEC, NH])
        yms, yrstd = sb("step_yms", [DEC, 1]), sb("step_yrstd", [DEC, 1])
        loaded, state_in, rate_ready = sem("step_loaded"), sem("step_state_in"), sem("step_rate_ready")
        drate_ready, dec_ready, state_ready, y_ready = sem("step_drate_ready"), sem("step_dec_ready"), sem("step_state_ready"), sem("step_y_ready")
        state_stored, pairs_stored, y_in, gated, yms_ready, yrstd_ready, out_ready, out_stored = (
            sem("step_" + n) for n in ("state_stored", "pairs_stored", "y_in", "gated", "yms_ready", "yrstd_ready", "out_ready", "out_stored"))
        states_used = sem("step_states_used")
        LOADS = 5 + 3 * DEC
        block = stage.block()

        @block.sync
        def _(sp):
            sp.dma_start(x[:], io["mem_prompt"].rearrange("(m p) n -> p m n", p=P)).then_inc(x_in, 16)
            sp.dma_start(w_mk[:], io["w_mk"].rearrange("(b p) n -> p b n", p=P)).then_inc(wk_in, 16)
            sp.dma_start(step_x[:], io["rows2"].rearrange("b (h d) -> (b h) d", h=NH)).then_inc(loaded, 16)
            sp.dma_start(dt[:], io["dts"].rearrange("b (h a) -> (b h) a", a=1)).then_inc(loaded, 16)
            for b in range(DEC):
                sp.dma_start(rate[b * NH:(b + 1) * NH, :], io["a_log"].rearrange("a h -> h a")).then_inc(loaded, 16)
                for g in range(SSD_G):
                    lo = b * NH + g * SSD_HPG
                    src = io["bcs"][b:b + 1, :].rearrange("a (k g n) -> a k g n", k=2, g=SSD_G)[:, :, g, :]
                    sp.dma_start(bc[lo:lo + SSD_HPG, :, :], src.broadcast_to([SSD_HPG, 2, STATE])).then_inc(loaded, 16)
            sp.dma_start(state, io["state_ssm"]).then_inc(state_in, 16)
            sp.dma_start(skip[:], io["d_skip"].broadcast_to([DEC, NH])).then_inc(loaded, 16)
            sp.dma_start(xs[:], io["rows2"]).then_inc(loaded, 16)
            sp.dma_start(gates[:], io["gates"]).then_inc(loaded, 16)
            sp.dma_start(w_mv[:], io["w_mv"].rearrange("(b p) n -> p b n", p=P)).then_inc(wv_in, 16)
            sp.wait_ge(state_ready, 1)
            sp.dma_start(io["s_ssm"], state).then_inc(state_stored, 16)
            w_out_rows = io["w_out"].rearrange("(b p) n -> p b n", p=P)
            sp.wait_ge(state_stored, 16)
            sp.wait_ge(states_used, 1)
            sp.dma_start(w_out[:, 0:DB, :], w_out_rows[:, 0:DB, :]).then_inc(w_out_in, 16)
            sp.wait_ge(y_ready, 1)
            sp.dma_start(io["rows3"].rearrange("b (h d) -> (b h) d", h=NH), y_pairs[:]).then_inc(pairs_stored, 16)
            sp.dma_start(w_out[:, DB:2 * DB, :], w_out_rows[:, DB:2 * DB, :]).then_inc(w_out_in, 16)
            sp.wait_ge(pairs_stored, 16)
            sp.dma_start(y[:], io["rows3"]).then_inc(y_in, 16)
            sp.wait_ge(k_ready, MT)
            sp.dma_start(io["p_mem_k"].rearrange("(m p) n -> p m n", p=P), mk[:]).then_inc(stored, 16)
            sp.wait_ge(v_ready, MT)
            sp.dma_start(io["p_mem_v"].rearrange("(m p) n -> p m n", p=P), mv[:]).then_inc(stored, 16)
            sp.wait_ge(out_ready, 1)
            sp.dma_start(io["mixed"][SEQ:TOKENS, D:2 * D], y[:]).then_inc(out_stored, 16)
            sp.wait_ge(stored, 32)
            sp.wait_ge(out_stored, 16)

        @block.tensor
        def _(pe):
            pe.wait_ge(x_in, 16)
            for m in range(MT):
                for h in range(2):
                    for j in range(4):
                        b = 4 * h + j
                        ins = nc.tensor.transpose(psum[2 * m + h][:, j * P:(j + 1) * P], x[:, m, b * P:(b + 1) * P], ident[:])
                    ins.then_inc(turned, 1)
            for w, arrived, first in ((w_mk, wk_in, 4), (w_mv, wv_in, 0)):
                pe.wait_ge(arrived, 16)
                pe.wait_ge(hT_ready, 4)
                for m in range(MT):
                    for c in range(2):
                        for b in range(DB):
                            ins = nc.tensor.matmul(psum[first + 2 * m + c][:], hT[:, m, b, :], w[:, b, c * BANK:(c + 1) * BANK],
                                                   start=(b == 0), stop=(b == DB - 1))
                        ins.then_inc(projected, 1)
            for m in range(MT):
                pe.wait_ge(k_ready, m + 1)
                for h in range(2):
                    for j in range(4):
                        b = 4 * h + j
                        ins = nc.tensor.transpose(psum[4 + 2 * m + h][:, j * P:(j + 1) * P], mk[:, m, b * P:(b + 1) * P], ident[:])
                    ins.then_inc(k_turned, 1)

        @block.scalar
        def _(act):
            act.wait_ge(x_in, 16)
            for m in range(MT):
                nc.scalar.activation(junk[:], x[:, m, :], ACT.Square, accum_out=ms[:, m:m + 1])
                act.drain()
            act.sem_inc(ms_ready, 1)
            act.wait_ge(loaded, 16 * LOADS)
            nc.scalar.activation(rate[:], rate[:], ACT.Exp).then_inc(rate_ready, 1)
            act.wait_ge(drate_ready, 1)
            nc.scalar.activation(dec[:], dec[:], ACT.Exp).then_inc(dec_ready, 1)
            act.wait_ge(rstd_ready, 1)
            for m in range(MT):
                act.wait_ge(projected, 2 * m + 2)
                for c in range(2):
                    nc.scalar.activation(mk[:, m, c * BANK:(c + 1) * BANK], psum[4 + 2 * m + c][:], ACT.Copy, scale=rstd[:, m:m + 1])
                act.drain()
                act.sem_inc(k_ready, 1)
            for m in range(MT):
                act.wait_ge(projected, 4 + 2 * m + 2)
                for c in range(2):
                    nc.scalar.activation(mv[:, m, c * BANK:(c + 1) * BANK], psum[2 * m + c][:], ACT.Copy, scale=rstd[:, m:m + 1])
                act.drain()
                act.sem_inc(v_ready, 1)
            act.wait_ge(gated, 1)
            nc.scalar.activation(junk[0:DEC, :], y[:], ACT.Square, accum_out=yms[:]).then_inc(yms_ready, 1)

        @block.gpsimd
        def _(pool):
            nc.gpsimd.memset(half[:], -0.5)
            for src, dst, ready, done, n in ((ms, rstd, ms_ready, rstd_ready, P), (yms, yrstd, yms_ready, yrstd_ready, DEC)):
                pool.wait_ge(ready, 1)
                nc.gpsimd.tensor_scalar(src[:], src[:], 1.0 / D, EPS, ALU.mult, ALU.add)
                pool.drain()
                nc.gpsimd.tensor_tensor(dst[:], src[:], half[0:n, 0:src.shape[-1]], ALU.pow).then_inc(done, 1)

        @block.vector
        def _(dve):
            for m in range(MT):
                for h in range(2):
                    dve.wait_ge(turned, 2 * m + h + 1)
                    nc.vector.tensor_tensor(hT[:, m, 4 * h:4 * h + 4, :], psum[2 * m + h][:].rearrange("p (b t) -> p b t", b=4),
                                            gain[:, 4 * h:4 * h + 4, None].broadcast_to([P, 4, P]), ALU.mult).then_inc(hT_ready, 1)
            dve.wait_ge(rate_ready, 1)
            nc.vector.tensor_scalar(dec[:], dt[:], rate[:], -1.0, ALU.mult, ALU.mult).then_inc(drate_ready, 1)
            nc.vector.tensor_scalar(step_x[:], step_x[:], dt[:], None, ALU.mult)
            dve.drain()
            nc.vector.tensor_tensor(wide, step_x[:, :, None].broadcast_to([P, HD, STATE]),
                                    bc[:, 0, None, :].broadcast_to([P, HD, STATE]), ALU.mult)
            dve.drain()
            dve.wait_ge(state_in, 16)
            dve.wait_ge(dec_ready, 1)
            nc.vector.scalar_tensor_tensor(state.rearrange("p d n -> p (d n)"), state.rearrange("p d n -> p (d n)"), dec[:],
                                           wide.rearrange("p d n -> p (d n)"), ALU.mult, ALU.add)
            dve.drain()
            dve.sem_inc(state_ready, 1)
            nc.vector.tensor_tensor(wide, state, bc[:, 1, None, :].broadcast_to([P, HD, STATE]), ALU.mult).then_inc(states_used, 1)
            dve.drain()
            nc.vector.tensor_reduce(y_pairs[:], wide, AX.X, ALU.add).then_inc(y_ready, 1)
            nc.vector.tensor_tensor(xs[:].rearrange("b (h d) -> b h d", h=NH), xs[:].rearrange("b (h d) -> b h d", h=NH),
                                    skip[:, :, None].broadcast_to([DEC, NH, HD]), ALU.mult)
            dve.drain()
            dve.wait_ge(y_in, 16)
            nc.vector.tensor_tensor(y[:], y[:], xs[:], ALU.add)
            dve.drain()
            nc.vector.tensor_tensor(y[:], y[:], gates[:], ALU.mult).then_inc(gated, 1)
            for m in range(MT):
                for h in range(2):
                    dve.wait_ge(k_turned, 2 * m + h + 1)
                    nc.vector.tensor_copy(mkT[:, 4 * h:4 * h + 4, m * P:(m + 1) * P], psum[4 + 2 * m + h][:].rearrange("p (b t) -> p b t", b=4))
            dve.drain()
            dve.wait_ge(yrstd_ready, 1)
            nc.vector.tensor_scalar(y[:], y[:], yrstd[:], None, ALU.mult).then_inc(out_ready, 1)


def memory_read(nc, io, psum, shared, w_out, w_mq, w_mo, mkT, mv, w_out_in):
    ident = shared["ident"]
    with Stage(nc) as stage:
        sb, sem, event = stage.buffer, stage.semaphore, stage.event

        mixed = sb("read_mixed", [P, 2 * D])
        x = sb("read_x", [P, D])
        mT = sb("read_mT", [P, 2 * DB, P])
        x1, x2 = sb("read_x1", [P, D]), sb("read_x2", [P, D])
        hT = sb("read_hT", [P, DB, P])
        qT = sb("read_qT", [P, DB, P])
        p = sb("read_p", [P, MEM_HEADS, N_MEM])
        pT = sb("read_pT", [P, MEM_HEADS, 2, P])
        ms, rstd, scale = sb("read_ms", [P, 1]), sb("read_rstd", [P, 1]), sb("read_scale", [P, 1])
        ms2, rstd2 = sb("read_ms2", [P, 1]), sb("read_rstd2", [P, 1])
        half, part = sb("read_half", [P, 1]), sb("read_part", [P, 1])
        top, total = sb("read_top", [P, MEM_HEADS]), sb("read_total", [P, MEM_HEADS])
        xn, gain_ffn = sb("read_xn", [P, D]), sb("read_gain_ffn", [P, D])
        o = p[:].rearrange("p h m -> p (h m)")
        oT = qT

        front_fills = Fills(sem, "read_front", [("m0", 0), ("m1", 1), ("m2", 0), ("m3", 1), ("r0", 2), ("r1", 3)])
        back_fills = Fills(sem, "read_back", [
            ("h0", 4), ("h1", 5), ("q0", 6), ("q1", 7), ("s0", 4), ("s1", 5), ("t0", 6), ("t1", 7),
            ("o0", 4), ("o1", 5), ("u0", 6), ("u1", 7), ("y0", 4), ("y1", 5)])

        def fill(name):
            f = front_fills if name in front_fills.place else back_fills
            return f, f.bank(name), psum[f.bank(name)]

        w_mq_in, w_mo_in = sem("read_w_mq"), sem("read_w_mo")
        mixed_in, x_in = event("read_mixed_in", 1, 16), event("read_x_in", 1, 16)
        mixed_turned, x_added = event("read_mixed_turned"), event("read_x_added")
        mT_ready, mT_used = event("read_mT_ready"), event("read_mT_used")
        x1_ready = event("read_x1_ready")
        ms_ready, rstd_ready = event("read_ms_ready"), event("read_rstd_ready")
        hT_ready, qT_ready = event("read_hT_ready"), event("read_qT_ready")
        ntop_ready, p_ready, p_turned, pT_ready, o_ready, oT_ready = (
            event("read_" + n) for n in ("ntop_ready", "p_ready", "p_turned", "pT_ready", "o_ready", "oT_ready"))
        x2_ready, stored = event("read_x2_ready"), event("read_stored", 1, 16)
        ms2_ready, rstd2_ready = event("read_ms2_ready"), event("read_rstd2_ready")
        xn_ready, xn_stored = event("read_xn_ready"), event("read_xn_stored", 1, 16)
        gain_in = sem("read_gain_in")
        block = stage.block()

        @block.sync
        def _(sp):
            def rows(t):
                return bass.ds(t * P, P)

            def load_mixed(t):
                sp.wait_ge(mixed_turned.sem, mixed_turned.last(t))
                sp.dma_start(mixed[:], io["mixed"][rows(t), :]).then_inc(mixed_in.sem, 16)

            def load_x(t):
                sp.wait_ge(x_added.sem, x_added.last(t))
                sp.dma_start(x[:], io["x_prompt"][rows(t), :]).then_inc(x_in.sem, 16)

            def store_x2(t):
                sp.wait_ge(x2_ready.sem, x2_ready.this(t))
                sp.dma_start(io["x2"][rows(t), :], x2[:]).then_inc(stored.sem, 16)

            def store_xn(t):
                sp.wait_ge(xn_ready.sem, xn_ready.this(t))
                sp.dma_start(io["xn"][rows(t), :], xn[:]).then_inc(xn_stored.sem, 16)

            for e in (mixed_in, x_in, stored, xn_stored):
                sp.sem_inc(e.sem, 16)
            load_mixed(0)
            load_x(0)
            sp.dma_start(gain_ffn[:], io["norm_ffn_w"].broadcast_to([P, D])).then_inc(gain_in, 16)
            sp.dma_start(w_mq[:], io["w_mq"].rearrange("(b p) n -> p b n", p=P)).then_inc(w_mq_in, 16)
            load_mixed(1)
            sp.dma_start(w_mo[:], io["w_mo"].rearrange("(b p) n -> p b n", p=P)).then_inc(w_mo_in, 16)
            load_x(1)
            load_mixed(2)
            store_x2(0)
            with sp.Fori(1, TILES - 2) as t:
                load_x(t + 1)
                load_mixed(t + 2)
                store_xn(t - 1)
                store_x2(t)
            load_x(TILES - 1)
            for t in range(TILES - 2, TILES):
                store_xn(t - 1)
                store_x2(t)
            store_xn(TILES - 1)
            sp.wait_ge(stored.sem, stored.this(TILES - 1))
            sp.wait_ge(xn_stored.sem, xn_stored.this(TILES - 1))

        @block.tensor
        def _(pe):
            def begin(name, t):
                f, bank, out = fill(name)
                pe.wait_ge(f.free[bank], f.at(name, t))
                return out, f.full[bank]

            def turn_blocks(prefix, src, t, n=2):
                for h in range(n):
                    out, full = begin(f"{prefix}{h}", t)
                    for j in range(4):
                        ins = nc.tensor.transpose(out[:, j * P:(j + 1) * P], src[:, (4 * h + j) * P:(4 * h + j + 1) * P], ident[:])
                    ins.then_inc(full, 1)

            def turn_mixed(u):
                pe.wait_ge(mixed_in.sem, mixed_in.this(u))
                turn_blocks("m", mixed, u, 4)
                pe.drain()
                pe.sem_inc(mixed_turned.sem, 1)

            def residual(u, c, lo, hi):
                out = fill(f"r{c}")[2]
                if lo == 0:
                    begin(f"r{c}", u)
                    if c == 0:
                        pe.wait_ge(mT_ready.sem, mT_ready.this(u))
                for b in range(lo, hi):
                    ins = nc.tensor.matmul(out[:], mT[:, b, :], w_out[:, b, c * BANK:(c + 1) * BANK],
                                           start=(b == 0), stop=(b == 2 * DB - 1))
                if hi == 2 * DB:
                    f, bank, _ = fill(f"r{c}")
                    ins.then_inc(f.full[bank], 1)
                    if c == 1:
                        pe.drain()
                        pe.sem_inc(mT_used.sem, 1)

            def turn(t, u):
                front = u is not None
                if front:
                    turn_mixed(u)
                pe.wait_ge(x1_ready.sem, x1_ready.this(t))
                turn_blocks("h", x1, t)
                if front:
                    residual(u, 0, 0, 8)
                pe.wait_ge(hT_ready.sem, hT_ready.this(t))
                for h in range(2):
                    out, full = begin(f"q{h}", t)
                    for j in range(4):
                        d = 4 * h + j
                        for b in range(DB):
                            ins = nc.tensor.matmul(out[:, j * P:(j + 1) * P], w_mq[:, b, d * P:(d + 1) * P], hT[:, b, :],
                                                   start=(b == 0), stop=(b == DB - 1))
                    ins.then_inc(full, 1)
                if front:
                    residual(u, 0, 8, 12)
                pe.wait_ge(qT_ready.sem, qT_ready.this(t))
                for n in range(2):
                    out, full = begin(f"s{n}", t)
                    for r in range(2):
                        for k in range(2):
                            d = 2 * (2 * n + r) + k
                            ins = nc.tensor.matmul(out[:, r * N_MEM:(r + 1) * N_MEM], qT[:, d, :], mkT[:, d, :], start=(k == 0), stop=(k == 1))
                    ins.then_inc(full, 1)
                if front:
                    residual(u, 0, 12, 16)
                    residual(u, 1, 0, 4)
                pe.wait_ge(p_ready.sem, p_ready.this(t))
                turn_blocks("t", o, t)
                pe.drain()
                pe.sem_inc(p_turned.sem, 1)
                if front:
                    residual(u, 1, 4, 6)
                pe.wait_ge(pT_ready.sem, pT_ready.this(t))
                for n in range(2):
                    out, full = begin(f"o{n}", t)
                    for r in range(2):
                        h = 2 * n + r
                        for k in range(2):
                            ins = nc.tensor.matmul(out[:, r * MEM_HD:(r + 1) * MEM_HD], pT[:, h, k, :], mv[:, k, h * MEM_HD:(h + 1) * MEM_HD],
                                                   start=(k == 0), stop=(k == 1))
                    ins.then_inc(full, 1)
                if front:
                    residual(u, 1, 6, 12)
                pe.wait_ge(o_ready.sem, o_ready.this(t))
                turn_blocks("u", o, t)
                if front:
                    residual(u, 1, 12, 16)
                pe.wait_ge(oT_ready.sem, oT_ready.this(t))
                for c in range(2):
                    out, full = begin(f"y{c}", t)
                    for b in range(DB):
                        ins = nc.tensor.matmul(out[:], oT[:, b, :], w_mo[:, b, c * BANK:(c + 1) * BANK], start=(b == 0), stop=(b == DB - 1))
                    ins.then_inc(full, 1)

            front_fills.prime(pe)
            back_fills.prime(pe)
            for e in (mixed_turned, mT_used, p_turned):
                pe.sem_inc(e.sem, 1)
            turn_mixed(0)
            pe.wait_ge(w_out_in, 32)
            for c in range(2):
                residual(0, c, 0, 16)
            pe.wait_ge(w_mq_in, 16)
            pe.wait_ge(w_mo_in, 16)
            with pe.Fori(0, TILES - 1) as t:
                turn(t, t + 1)
            turn(TILES - 1, None)

        @block.scalar
        def _(act):
            def full(name, t):
                f, bank, src = fill(name)
                act.wait_ge(f.full[bank], f.at(name, t))
                return src, f.free[bank]

            def copy_blocks(prefix, dst, ready, t):
                for h in range(2):
                    src, free = full(f"{prefix}{h}", t)
                    nc.scalar.copy(dst[:, 4 * h:4 * h + 4, :], src[:].rearrange("p (b t) -> p b t", b=4)).then_inc(free, 1)
                act.drain()
                act.sem_inc(ready.sem, 1)

            def turn(t):
                act.wait_ge(x1_ready.sem, x1_ready.this(t))
                nc.scalar.activation(p[:].rearrange("p h m -> p (h m)"), x1[:], ACT.Square, accum_out=ms[:])
                act.drain()
                act.sem_inc(ms_ready.sem, 1)
                copy_blocks("q", qT, qT_ready, t)
                act.wait_ge(ntop_ready.sem, ntop_ready.this(t))
                for h in range(MEM_HEADS):
                    if h % 2 == 0:
                        src, _ = full(f"s{h // 2}", t)
                    nc.scalar.activation(p[:, h, :], src[:, (h % 2) * N_MEM:(h % 2 + 1) * N_MEM], ACT.Exp,
                                         bias=top[:, h:h + 1], scale=scale[:], accum_out=total[:, h:h + 1])
                act.drain()
                act.sem_inc(p_ready.sem, 1)
                for n in range(2):
                    act.sem_inc(fill(f"s{n}")[0].free[fill(f"s{n}")[1]], 1)
                copy_blocks("t", pT[:].rearrange("p h k t -> p (h k) t"), pT_ready, t)
                copy_blocks("u", oT, oT_ready, t)
                act.wait_ge(x2_ready.sem, x2_ready.this(t))
                nc.scalar.activation(p[:].rearrange("p h m -> p (h m)"), x2[:], ACT.Square, accum_out=ms2[:])
                act.drain()
                act.sem_inc(ms2_ready.sem, 1)

            for e in (ms2_ready, ms_ready, qT_ready, p_ready, pT_ready, oT_ready):
                act.sem_inc(e.sem, 1)
            with act.Fori(0, TILES) as t:
                turn(t)

        @block.gpsimd
        def _(pool):
            nc.gpsimd.memset(half[:], -0.5)
            nc.gpsimd.memset(part[:], 1.0 / D)
            pool.drain()
            pool.sem_inc(rstd_ready.sem, 1)
            pool.sem_inc(rstd2_ready.sem, 1)
            with pool.Fori(0, TILES) as t:
                for src, dst, ready, done in ((ms, rstd, ms_ready, rstd_ready), (ms2, rstd2, ms2_ready, rstd2_ready)):
                    pool.wait_ge(ready.sem, ready.this(t))
                    nc.gpsimd.tensor_tensor(src[:], src[:], part[:], ALU.mult)
                    pool.drain()
                    nc.gpsimd.tensor_scalar(src[:], src[:], EPS, None, ALU.add)
                    pool.drain()
                    nc.gpsimd.tensor_tensor(dst[:], src[:], half[:], ALU.pow)
                    pool.drain()
                    pool.sem_inc(done.sem, 1)

        @block.vector
        def _(dve):
            def full(name, t):
                f, bank, src = fill(name)
                dve.wait_ge(f.full[bank], f.at(name, t))
                return src, f.free[bank]

            def with_gain(dst, gain, prefix, first, t, n):
                for h in range(n):
                    src, free = full(f"{prefix}{first + h}", t)
                    nc.vector.tensor_tensor(dst[:, 4 * h:4 * h + 4, :], src[:].rearrange("p (b t) -> p b t", b=4),
                                            gain[:, 4 * h:4 * h + 4, None].broadcast_to([P, 4, P]), ALU.mult).then_inc(free, 1)

            def mixed_rows(u):
                dve.wait_ge(mT_used.sem, mT_used.last(u))
                with_gain(mT[:, 0:DB], shared["gain_att"], "m", 0, u, 2)
                with_gain(mT[:, DB:2 * DB], shared["gain_ssd"], "m", 2, u, 2)
                dve.drain()
                dve.sem_inc(mT_ready.sem, 1)

            def ffn_rows(t):
                dve.wait_ge(rstd2_ready.sem, rstd2_ready.this(t))
                dve.wait_ge(xn_stored.sem, xn_stored.last(t))
                nc.vector.scalar_tensor_tensor(xn[:], x2[:], rstd2[:], gain_ffn[:], ALU.mult, ALU.mult)
                dve.drain()
                dve.sem_inc(xn_ready.sem, 1)

            def turn(t, u, first=False):
                dve.wait_ge(x_in.sem, x_in.this(t))
                for c in range(2):
                    src, free = full(f"r{c}", t)
                    cols = slice(c * BANK, (c + 1) * BANK)
                    nc.vector.tensor_tensor(x1[:, cols], src[:], x[:, cols], ALU.add).then_inc(free, 1)
                dve.drain()
                dve.sem_inc(x1_ready.sem, 1)
                dve.sem_inc(x_added.sem, 1)
                if u is not None:
                    mixed_rows(u)
                with_gain(hT, shared["gain_read"], "h", 0, t, 2)
                dve.drain()
                dve.sem_inc(hT_ready.sem, 1)
                if not first:
                    ffn_rows(t - 1)
                dve.wait_ge(rstd_ready.sem, rstd_ready.this(t))
                nc.vector.tensor_scalar(scale[:], rstd[:], MEM_HD ** -0.5, None, ALU.mult)
                for n in range(2):
                    src, _ = full(f"s{n}", t)
                    nc.vector.tensor_reduce(top[:, 2 * n:2 * n + 2], src[:].rearrange("p (r m) -> p r m", r=2), AX.X, ALU.max)
                dve.drain()
                nc.vector.tensor_scalar(top[:], top[:], scale[:], -1.0, ALU.mult, ALU.mult)
                dve.drain()
                dve.sem_inc(ntop_ready.sem, 1)
                dve.wait_ge(p_ready.sem, p_ready.this(t))
                nc.vector.reciprocal(total[:], total[:])
                dve.drain()
                dve.wait_ge(p_turned.sem, p_turned.this(t))
                for n in range(2):
                    src, free = full(f"o{n}", t)
                    nc.vector.tensor_tensor(p[:, 2 * n:2 * n + 2, :], src[:].rearrange("p (r m) -> p r m", r=2),
                                            total[:, 2 * n:2 * n + 2, None].broadcast_to([P, 2, MEM_HD]), ALU.mult).then_inc(free, 1)
                dve.drain()
                dve.sem_inc(o_ready.sem, 1)
                dve.wait_ge(stored.sem, stored.last(t))
                for c in range(2):
                    src, free = full(f"y{c}", t)
                    cols = slice(c * BANK, (c + 1) * BANK)
                    nc.vector.tensor_tensor(x2[:, cols], src[:], x1[:, cols], ALU.add).then_inc(free, 1)
                dve.drain()
                dve.sem_inc(x2_ready.sem, 1)

            for e in (xn_ready, mT_ready, x1_ready, x_added, hT_ready, ntop_ready, o_ready, x2_ready):
                dve.sem_inc(e.sem, 1)
            dve.wait_ge(gain_in, 16)
            mixed_rows(0)
            turn(0, 1, first=True)
            with dve.Fori(1, TILES - 1) as t:
                turn(t, t + 1)
            turn(TILES - 1, None)
            ffn_rows(TILES - 1)


def memory_read_sample(nc, io, psum, shared, w_out, w_mq, w_mo, mkT, mv, x1):
    ident = shared["ident"]
    ROWS = DEC * MEM_HEADS
    with Stage(nc) as stage:
        sb, sem = stage.buffer, stage.semaphore

        mixed, x, junk, q = sb("rs_mixed", [DEC, 2 * D]), sb("rs_x", [DEC, D]), sb("rs_junk", [DEC, D]), sb("rs_q", [DEC, D])
        mT, hT = sb("rs_mT", [P, 2 * DB, DEC]), sb("rs_hT", [P, DB, DEC])
        ms, rstd, half = sb("rs_ms", [DEC, 1]), sb("rs_rstd", [DEC, 1]), sb("rs_half", [DEC, 1])
        ms2, rstd2 = sb("rs_ms2", [DEC, 1]), sb("rs_rstd2", [DEC, 1])
        q_wide = sb("rs_q_wide", [P, 2, D])
        sT = sb("rs_sT", [P, 2, DEC, MEM_HEADS])
        p = sb("rs_p", [ROWS, N_MEM])
        ntop, total = sb("rs_ntop", [ROWS, 1]), sb("rs_total", [ROWS, 1])
        own = sb("rs_own", [P, 2, ROWS, DEC])
        o, oT = sb("rs_o", [DEC, D]), sb("rs_oT", [P, DB, DEC])
        xn, gain_ffn = sb("rs_xn", [DEC, D]), sb("rs_gain_ffn", [DEC, D])
        blank = sb("rs_blank", [P - DEC, D])
        k = [w_out[:, 2 * b:2 * b + 2, :] for b in range(DEC)]
        places = [mkT[:].rearrange("p b n -> p (b n)").rearrange("p (m n) -> p m n", m=2), mv[:]]
        places += [w_mq[:, 2 * i:2 * i + 2, :] for i in range(4)]
        v = [places[b % 6] for b in range(DEC)]
        w_pq = w_out[:].rearrange("p (b k) n -> p b (k n)", k=2)

        loaded, turned, mT_ready, summed, x1_ready = (sem("rs_" + n) for n in ("loaded", "turned", "mT_ready", "summed", "x1_ready"))
        x1_turned, hT_ready, ms_ready, rstd_ready, projected, q_ready = (
            sem("rs_" + n) for n in ("x1_turned", "hT_ready", "ms_ready", "rstd_ready", "projected", "q_ready"))
        spread, q_wide_ready, reduced = sem("rs_spread"), sem("rs_q_wide_ready"), sem("rs_reduced")
        k_in = [sem(f"rs_k_in{b}") for b in range(DEC)]
        v_in = [sem(f"rs_v_in{i}") for i in range(6)]
        s_turned, ntop_ready, p_exp, p_ready, p_turned, own_ready = (
            sem("rs_" + n) for n in ("s_turned", "ntop_ready", "p_exp", "p_ready", "p_turned", "own_ready"))
        valued, o_ready, o_turned, oT_ready, read_projected, x2_ready = (
            sem("rs_" + n) for n in ("valued", "o_ready", "o_turned", "oT_ready", "read_projected", "x2_ready"))
        gain_in, blank_ready, ms2_ready, rstd2_ready, xn_ready, w_pq_in, stored = (
            sem("rs_" + n) for n in ("gain_in", "blank_ready", "ms2_ready", "rstd2_ready", "xn_ready", "w_pq_in", "stored"))
        block = stage.block()

        def bank_of_spread(b, c):
            return (2, 3, 6, 7)[2 * (b % 2) + c]

        def bank_of_head(h):
            return (2, 3, 6, 7)[h]

        @block.sync
        def _(sp):
            def load_v(b):
                sp.dma_start(v[b], io["cache_mem_v"][b].rearrange("(m p) n -> p m n", p=P)).then_inc(v_in[b % 6], 16)

            sp.dma_start(mixed[:], io["mixed"][SEQ:TOKENS, :]).then_inc(loaded, 16)
            sp.dma_start(x[:], io["x_sample"]).then_inc(loaded, 16)
            sp.dma_start(gain_ffn[:], io["norm_ffn_w"].broadcast_to([DEC, D])).then_inc(gain_in, 16)
            load_v(0)
            load_v(1)
            sp.wait_ge(blank_ready, 1)
            for name in ("x2", "xn"):
                sp.dma_start(io[name][TOKENS:SEQ + P, :], blank[:]).then_inc(stored, 16)
            sp.wait_ge(summed, 1)
            for b in range(DEC):
                sp.dma_start(k[b], io["cache_mem_k"][b].rearrange("(m p) n -> p m n", p=P)).then_inc(k_in[b], 16)
            sp.wait_ge(projected, 1)
            for b in range(2, 6):
                load_v(b)
            sp.wait_ge(reduced, DEC)
            sp.dma_start(w_pq, io["peer_wq"].rearrange("(b p) n -> p b n", p=P)).then_inc(w_pq_in, 16)
            for b in range(6, DEC):
                sp.wait_ge(valued, b - 5)
                load_v(b)
            sp.wait_ge(x2_ready, 1)
            sp.dma_start(io["x2"][SEQ:TOKENS, :], x1[:]).then_inc(stored, 16)
            sp.wait_ge(xn_ready, 1)
            sp.dma_start(io["xn"][SEQ:TOKENS, :], xn[:]).then_inc(stored, 16)
            sp.wait_ge(stored, 64)
            sp.wait_ge(w_pq_in, 16)

        @block.tensor
        def _(pe):
            def turn_rows(src, bank, n):
                for b in range(n):
                    ins = nc.tensor.transpose(psum[bank][:, b * DEC:(b + 1) * DEC], src[:, b * P:(b + 1) * P], ident[0:DEC, 0:DEC])
                return ins

            def project(lhsT, w, n, bank):
                for c in range(2):
                    for b in range(n):
                        ins = nc.tensor.matmul(psum[bank + c][0:DEC, :], lhsT[:, b, :], w[:, b, c * BANK:(c + 1) * BANK],
                                               start=(b == 0), stop=(b == n - 1))
                return ins

            pe.wait_ge(loaded, 32)
            turn_rows(mixed, 0, 2 * DB).then_inc(turned, 1)
            pe.wait_ge(mT_ready, 1)
            project(mT, w_out, 2 * DB, 1).then_inc(summed, 1)
            pe.wait_ge(x1_ready, 1)
            turn_rows(x1, 3, DB).then_inc(x1_turned, 1)
            pe.wait_ge(hT_ready, 1)
            project(hT, w_mq, DB, 4).then_inc(projected, 1)
            pe.wait_ge(q_ready, 1)
            for b in range(DEC):
                if b >= 2:
                    pe.wait_ge(q_wide_ready, b - 1)
                for c in range(2):
                    ins = nc.tensor.matmul(psum[bank_of_spread(b, c)][:], ident[0:DEC, b:b + 1].broadcast_to([DEC, P]),
                                           q[:, c * BANK:(c + 1) * BANK], start=True, stop=True)
                ins.then_inc(spread, 1)
            pe.wait_ge(reduced, DEC)
            for m in range(2):
                ins = nc.tensor.transpose(psum[0][0:ROWS, m * P:(m + 1) * P], sT[:, m].rearrange("p b h -> p (b h)"), ident[:])
            ins.then_inc(s_turned, 1)
            pe.wait_ge(p_ready, 1)
            for m in range(2):
                ins = nc.tensor.transpose(psum[1][:, m * ROWS:(m + 1) * ROWS], p[:, m * P:(m + 1) * P], ident[0:ROWS, 0:ROWS])
            ins.then_inc(p_turned, 1)
            pe.wait_ge(own_ready, 1)
            for b in range(DEC):
                pe.wait_ge(v_in[b % 6], 16 * (b // 6 + 1))
                for h in range(MEM_HEADS):
                    for m in range(2):
                        ins = nc.tensor.matmul(psum[bank_of_head(h)][0:DEC, 0:MEM_HD], own[:, m, b * MEM_HEADS + h, :],
                                               v[b][:, m, h * MEM_HD:(h + 1) * MEM_HD], start=(b == 0 and m == 0), stop=(b == DEC - 1 and m == 1))
                ins.then_inc(valued, 1)
            pe.wait_ge(o_ready, 1)
            turn_rows(o, 0, DB).then_inc(o_turned, 1)
            pe.wait_ge(oT_ready, 1)
            project(oT, w_mo, DB, 4).then_inc(read_projected, 1)

        @block.scalar
        def _(act):
            act.wait_ge(x1_ready, 1)
            nc.scalar.activation(junk[:], x1[:], ACT.Square, accum_out=ms[:]).then_inc(ms_ready, 1)
            for b in range(DEC):
                act.wait_ge(spread, b + 1)
                if b >= 2:
                    act.wait_ge(reduced, b - 1)
                for c in range(2):
                    ins = nc.scalar.copy(q_wide[:, b % 2, c * BANK:(c + 1) * BANK], psum[bank_of_spread(b, c)][:])
                act.drain()
                act.sem_inc(q_wide_ready, 1)
            act.wait_ge(ntop_ready, 1)
            nc.scalar.activation(p[:], psum[0][0:ROWS, 0:N_MEM], ACT.Exp, bias=ntop[:], accum_out=total[:])
            act.drain()
            act.sem_inc(p_exp, 1)
            act.wait_ge(x2_ready, 1)
            nc.scalar.activation(junk[:], x1[:], ACT.Square, accum_out=ms2[:]).then_inc(ms2_ready, 1)

        @block.gpsimd
        def _(pool):
            nc.gpsimd.memset(blank[:], 0.0).then_inc(blank_ready, 1)
            nc.gpsimd.memset(half[:], -0.5)
            for src, dst, ready, done in ((ms, rstd, ms_ready, rstd_ready), (ms2, rstd2, ms2_ready, rstd2_ready)):
                pool.wait_ge(ready, 1)
                nc.gpsimd.tensor_scalar(src[:], src[:], 1.0 / D, EPS, ALU.mult, ALU.add)
                pool.drain()
                nc.gpsimd.tensor_tensor(dst[:], src[:], half[:], ALU.pow).then_inc(done, 1)

        @block.vector
        def _(dve):
            nc.vector.memset(own[:], 0.0)
            dve.wait_ge(turned, 1)
            for i, gain in enumerate((shared["gain_att"], shared["gain_ssd"])):
                ins = nc.vector.tensor_tensor(mT[:, i * DB:(i + 1) * DB, :],
                                              psum[0][:, i * DB * DEC:(i + 1) * DB * DEC].rearrange("p (b t) -> p b t", b=DB),
                                              gain[:, :, None].broadcast_to([P, DB, DEC]), ALU.mult)
            ins.then_inc(mT_ready, 1)
            dve.wait_ge(loaded, 32)
            dve.wait_ge(summed, 1)
            for c in range(2):
                cols = slice(c * BANK, (c + 1) * BANK)
                ins = nc.vector.tensor_tensor(x1[:, cols], psum[1 + c][0:DEC, :], x[:, cols], ALU.add)
            ins.then_inc(x1_ready, 1)
            dve.wait_ge(x1_turned, 1)
            nc.vector.tensor_tensor(hT[:], psum[3][:, 0:DB * DEC].rearrange("p (b t) -> p b t", b=DB),
                                    shared["gain_read"][:, :, None].broadcast_to([P, DB, DEC]), ALU.mult).then_inc(hT_ready, 1)
            dve.wait_ge(rstd_ready, 1)
            dve.wait_ge(projected, 1)
            for c in range(2):
                ins = nc.vector.tensor_scalar(q[:, c * BANK:(c + 1) * BANK], psum[4 + c][0:DEC, :], rstd[:], MEM_HD ** -0.5, ALU.mult, ALU.mult)
            ins.then_inc(q_ready, 1)
            for b in range(DEC):
                dve.wait_ge(q_wide_ready, b + 1)
                dve.wait_ge(k_in[b], 16)
                for m in range(2):
                    for h in range(MEM_HEADS):
                        cols = slice(h * MEM_HD, (h + 1) * MEM_HD)
                        ins = nc.vector.tensor_tensor_reduce(k[b][:, m, cols], k[b][:, m, cols], q_wide[:, b % 2, cols], 1.0, 0.0,
                                                             ALU.mult, ALU.add, sT[:, m, b, h:h + 1])
                ins.then_inc(reduced, 1)
            dve.wait_ge(s_turned, 1)
            nc.vector.tensor_reduce(ntop[:], psum[0][0:ROWS, 0:N_MEM], AX.X, ALU.max)
            dve.drain()
            nc.vector.tensor_scalar(ntop[:], ntop[:], -1.0, None, ALU.mult).then_inc(ntop_ready, 1)
            dve.wait_ge(p_exp, 1)
            nc.vector.reciprocal(total[:], total[:])
            dve.drain()
            nc.vector.tensor_scalar(p[:], p[:], total[:], None, ALU.mult).then_inc(p_ready, 1)
            dve.wait_ge(p_turned, 1)
            for m in range(2):
                at = own[:, m]
                columns = bass.AP(at.tensor, at.offset, [list(at.ap[0]), [MEM_HEADS * DEC + 1, DEC], [DEC, MEM_HEADS]])
                ins = nc.vector.tensor_copy(columns, psum[1][:, m * ROWS:(m + 1) * ROWS].rearrange("p (b h) -> p b h", b=DEC))
            ins.then_inc(own_ready, 1)
            dve.wait_ge(valued, DEC)
            for h in range(MEM_HEADS):
                ins = nc.vector.tensor_copy(o[:, h * MEM_HD:(h + 1) * MEM_HD], psum[bank_of_head(h)][0:DEC, 0:MEM_HD])
            ins.then_inc(o_ready, 1)
            dve.wait_ge(o_turned, 1)
            nc.vector.tensor_copy(oT[:], psum[0][:, 0:DB * DEC].rearrange("p (b t) -> p b t", b=DB)).then_inc(oT_ready, 1)
            dve.wait_ge(read_projected, 1)
            for c in range(2):
                cols = slice(c * BANK, (c + 1) * BANK)
                ins = nc.vector.tensor_tensor(x1[:, cols], psum[4 + c][0:DEC, :], x1[:, cols], ALU.add)
            dve.drain()
            dve.sem_inc(x2_ready, 1)
            dve.wait_ge(gain_in, 16)
            dve.wait_ge(rstd2_ready, 1)
            nc.vector.scalar_tensor_tensor(xn[:], x1[:], rstd2[:], gain_ffn[:], ALU.mult, ALU.mult).then_inc(xn_ready, 1)


def expert_mix(nc, io, psum, shared, w_pq, idx, gate):
    ident = shared["ident"]
    PAIRS = PEER_HEADS // 2
    PER = 2 * TOPK
    RING = 8
    USES = PER // RING
    with Stage(nc) as stage:
        sb, sem, event = stage.buffer, stage.semaphore, stage.event
        keysT = sb("ex_keysT", [P, 2 * PEER_HEADS * N_KEYS])
        rows = sb("ex_rows", [P, D])
        x_next = sb("ex_x_next", [P, D])
        x_cur = sb("ex_x_cur", [P, D])
        xT, sample_xT = sb("ex_xT", [P, DB, P]), sb("ex_sample_xT", [P, DB, DEC])
        final_gain = sb("ex_final_gain", [P, D])
        total = sb("ex_total", [P, D])
        u_ring = sb("ex_u_ring", [P, RING, D])
        v_ring = sb("ex_v_ring", [P, RING, D])
        diag = sb("ex_diag", [P, 2, TOPK, P])
        u_idx, v_idx = sb("ex_u_idx", [P, 2, TOPK], U32), sb("ex_v_idx", [P, 2, TOPK], U32)
        dots, weight = sb("ex_dots", [P, 2, TOPK]), sb("ex_weight", [P, 2, TOPK])
        q, qT = sb("ex_q", [P, 2 * P]), sb("ex_qT", [P, 2, P])
        sub, sub_less = sb("ex_sub", [P, 2, N_KEYS]), sb("ex_sub_less", [P, 2, N_KEYS])
        top, top_at, top_atf = sb("ex_top", [P, 2, TOPK]), sb("ex_top_at", [P, 2, TOPK], U32), sb("ex_top_atf", [P, 2, TOPK])
        cand, cand_less = sb("ex_cand", [P, TOPK * TOPK]), sb("ex_cand_less", [P, TOPK * TOPK])
        best, best_at = sb("ex_best", [P, TOPK]), sb("ex_best_at", [P, TOPK], U32)
        halves, halvesf = sb("ex_halves", [P, 2, TOPK], U32), sb("ex_halvesf", [P, 2, TOPK])
        match = sb("ex_match", [P, 2 * TOPK, TOPK])
        picked, joined = sb("ex_picked", [P, 2, TOPK]), sb("ex_joined", [P, TOPK])
        count16 = sb("ex_count16", [P, TOPK])
        nbest, esum = sb("ex_nbest", [P, 1]), sb("ex_esum", [P, 1])
        ms, root, rstd, err = (sb("ex_" + n, [P, 1]) for n in ("ms", "root", "rstd", "err"))
        squares = sb("ex_squares", [P, D])
        raw_keys = u_ring[:, 0:2, :].rearrange("p a (b d) -> p (a b) d", d=P)

        route_fills = Fills(sem, "route", [("q0", 0), ("qT0", 1), ("sub0", 2), ("q1", 0), ("qT1", 1), ("sub1", 2)])
        prep_fills = Fills(sem, "prep", [("xT0", 3), ("xT1", 4)])
        loaded, keys_in, keys_turned, keys_ready = (sem("ex_" + n) for n in ("loaded", "keys_in", "keys_turned", "keys_ready"))
        x_in, x_turned, x_moved = event("ex_x_in", 1, 16), event("ex_x_turned"), event("ex_x_moved")
        rows_in, rows_used = event("ex_rows_in", 1, 16), event("ex_rows_used")
        xT_ready, sample_xT_ready = event("ex_xT_ready"), sem("ex_sample_xT_ready")
        mix_over, mix_read = event("ex_mix_over"), event("ex_mix_read")
        var_ready, root_ready, out_ready, stored = event("ex_var_ready"), event("ex_root_ready"), event("ex_out_ready"), event("ex_stored", 1, 16)
        ms_ready = event("ex_ms_ready")
        routed_pe = event("ex_routed_pe", 2)
        q_ready, qT_ready = event("ex_q_ready", 2), event("ex_qT_ready", 2)
        best_ready, exp_ready = event("ex_best_ready", 2), event("ex_exp_ready", 2)
        u_idx_ready = event("ex_u_idx_ready", 2)
        v_idx_ready = [event(f"ex_v_idx_ready{half}") for half in range(2)]
        dots_ready, gelu_ready, weight_ready, diag_ready = (
            event("ex_" + n, 2) for n in ("dots_ready", "gelu_ready", "weight_ready", "diag_ready"))
        mixed = [event(f"ex_mixed{half}") for half in range(2)]
        u_in = [sem(f"ex_u_in{r}") for r in range(RING)]
        v_in = [sem(f"ex_v_in{r}") for r in range(RING)]
        u_used, v_used = sem("ex_u_used"), sem("ex_v_used")
        gathers = sem("ex_gathers")
        last_routes = [[(0, "last", 1)], [(1, "last", 2), (2, "sample", 0)], [(3, "last", 3), (4, "sample", 1)],
                       [(5, "sample", 2), (6, "sample", 3)]]
        last_routes = [[(((TILES - 1) * PAIRS + 1) + m, which, i) for m, which, i in routes] for routes in last_routes]
        block = stage.block()

        @block.sync
        def _(sp):
            def load_x(tile):
                sp.wait_ge(x_turned.sem, x_turned.last(tile))
                sp.wait_ge(x_moved.sem, x_moved.last(tile))
                sp.dma_start(x_next[:], io["xn"][bass.ds(tile * P, P), :]).then_inc(x_in.sem, 16)

            def load_rows(tile):
                sp.wait_ge(rows_used.sem, rows_used.last(tile))
                sp.dma_start(rows[:], io["x2"][bass.ds(tile * P, P), :]).then_inc(rows_in.sem, 16)

            for e in (x_in, rows_in, stored):
                sp.sem_inc(e.sem, 16)
            sp.dma_start(raw_keys, io["peer_keys"].rearrange("h k d -> k h d")).then_inc(keys_in, 16)
            load_x(0)
            sp.dma_start(final_gain[:], io["final_norm_w"].broadcast_to([P, D])).then_inc(loaded, 16)
            load_rows(0)
            with sp.Fori(0, TILES) as t:
                load_x(t + 1)
                load_rows(t + 1)
                sp.wait_ge(out_ready.sem, out_ready.this(t))
                sp.dma_start(io["y_prompt"][bass.ds(t * P, P), :], total[:]).then_inc(stored.sem, 16)
            sp.wait_ge(stored.sem, stored.this(TILES - 1))
            sp.wait_ge(rows_in.sem, rows_in.this(TILES))

        @block.gpsimd
        def _(pool):
            def gather(table, ring, places, arrived, used, n, half, s):
                j = half * TOPK + s
                pool.wait_ge(used, n * PER + (j + 1))
                pool.sem_inc(gathers, 1)
                nc.gpsimd.indirect_dma_start(
                    out=ring[:, j % RING, :], out_offset=None, in_=io[table],
                    in_offset=bass.IndirectOffsetOnAxis(ap=places[:, half, s:s + 1], axis=0),
                ).then_inc(arrived[j % RING], 16)

            def rows_u(n, half, s):
                gather("peer_u", u_ring, u_idx, u_in, u_used, n, half, s)

            def rows_v(n, half, s):
                gather("peer_v", v_ring, v_idx, v_in, v_used, n, half, s)

            def pair(n, first=False):
                pool.wait_ge(u_idx_ready.sem, u_idx_ready.this(n, 1))
                pool.sem_inc(gathers, 1)
                if not first:
                    pool.wait_ge(v_idx_ready[1].sem, v_idx_ready[1].last(n))
                    pool.sem_inc(gathers, 1)
                for s in range(TOPK):
                    rows_u(n, 0, s)
                    if not first:
                        rows_v(n - 1, 1, s)
                pool.wait_ge(u_idx_ready.sem, u_idx_ready.this(n, 2))
                pool.sem_inc(gathers, 1)
                pool.wait_ge(v_idx_ready[0].sem, v_idx_ready[0].this(n))
                pool.sem_inc(gathers, 1)
                for s in range(TOPK):
                    rows_u(n, 1, s)
                    rows_v(n, 0, s)

            nc.gpsimd.iota(count16[:], [[1, TOPK]], base=0, channel_multiplier=0, allow_small_or_imprecise_dtypes=True)
            pool.drain()
            pool.sem_inc(loaded, 16)
            pool.wait_ge(keys_ready, 2)
            pair(0, first=True)
            with pool.Fori(1, TILES * PAIRS) as n:
                pair(n)
            pool.wait_ge(v_idx_ready[1].sem, v_idx_ready[1].last(TILES * PAIRS))
            for s in range(TOPK):
                rows_v(TILES * PAIRS - 1, 1, s)

        @block.tensor
        def _(pe):
            def prepare(tile):
                pe.wait_ge(x_in.sem, x_in.this(tile))
                for h in range(2):
                    f = f"xT{h}"
                    bank = prep_fills.bank(f)
                    pe.wait_ge(prep_fills.free[bank], prep_fills.at(f, tile))
                    for j in range(4):
                        ins = nc.tensor.transpose(psum[bank][:, j * P:(j + 1) * P], x_next[:, (4 * h + j) * P:(4 * h + j + 1) * P], ident[:])
                    ins.then_inc(prep_fills.full[bank], 1)
                pe.drain()
                pe.sem_inc(x_turned.sem, 1)

            def route(m, tile, head, half, sample=False):
                def begin(name):
                    pe.wait_ge(route_fills.free[route_fills.bank(name)], route_fills.at(name, m))
                    return psum[route_fills.bank(name)], route_fills.full[route_fills.bank(name)]

                out, full = begin(f"q{half}")
                if half == 0 and sample:
                    pe.wait_ge(sample_xT_ready, 1)
                elif half == 0:
                    pe.wait_ge(xT_ready.sem, xT_ready.this(tile))
                n, src = (DEC, sample_xT) if sample else (P, xT)
                for b in range(DB):
                    ins = nc.tensor.matmul(out[0:n, 0:2 * P], src[:, b, :], w_pq[:, b, bass.ds(head * 2 * P, 2 * P)], start=(b == 0), stop=(b == DB - 1))
                ins.then_inc(full, 1)
                pe.wait_ge(q_ready.sem, q_ready.this(m, half + 1))
                out, full = begin(f"qT{half}")
                for p in range(2):
                    ins = nc.tensor.transpose(out[:, p * P:(p + 1) * P], q[:, p * P:(p + 1) * P], ident[:])
                ins.then_inc(full, 1)
                pe.wait_ge(qT_ready.sem, qT_ready.this(m, half + 1))
                out, full = begin(f"sub{half}")
                for p in range(2):
                    ins = nc.tensor.matmul(out[:, p * P:(p + 1) * P], qT[:, p, :], keysT[:, bass.ds((head * 2 + p) * P, P)], start=True, stop=True)
                ins.then_inc(full, 1)
                pe.drain()
                pe.sem_inc(routed_pe.sem, 1)

            def mix(n, half):
                pe.wait_ge(diag_ready.sem, diag_ready.this(n, half + 1))
                for s in range(TOPK):
                    j = half * TOPK + s
                    pe.wait_ge(v_in[j % RING], 16 * (n * USES + (j // RING + 1)))
                    for c in range(2):
                        ins = nc.tensor.matmul(psum[6 + c][:], diag[:, half, s, :], v_ring[:, j % RING, c * BANK:(c + 1) * BANK],
                                               start=False, stop=False, skip_group_check=True)
                    ins.then_inc(v_used, 1)
                pe.drain()
                pe.sem_inc(mixed[half].sem, 1)

            def begin_sum(t):
                pe.wait_ge(rows_in.sem, rows_in.this(t))
                pe.wait_ge(mix_read.sem, mix_read.last(t))
                for c in range(2):
                    nc.tensor.matmul(psum[6 + c][:], ident[:], rows[:, c * BANK:(c + 1) * BANK], start=True, stop=False, skip_group_check=True)
                pe.drain()
                pe.sem_inc(rows_used.sem, 1)

            def pair(n, tile, i, boundary=False, first=False):
                route(n + 1, tile, i * 2, 0)
                if not first:
                    mix(n - 1, 1)
                if boundary:
                    pe.sem_inc(mix_over.sem, 1)
                if boundary or first:
                    begin_sum(tile)
                route(n + 1, tile, i * 2 + 1, 1)
                mix(n, 0)

            def turn(t, first=False):
                n = t * PAIRS
                pair(n, t, 1, boundary=not first, first=first)
                with pe.Fori(1, PAIRS - 1) as i:
                    pair(n + i, t, i + 1)
                prepare(t + 1)
                pair(n + PAIRS - 1, t + 1, 0)

            def last_turn():
                t, n = TILES - 1, (TILES - 1) * PAIRS
                for i, routes in enumerate(last_routes):
                    m, which, j = routes[0]
                    route(m, t, 2 * j, 0, which == "sample")
                    mix(n + i - 1, 1)
                    if i == 0:
                        pe.sem_inc(mix_over.sem, 1)
                        begin_sum(t)
                    route(m, t, 2 * j + 1, 1, which == "sample")
                    if i == 0:
                        prepare(TILES)
                    mix(n + i, 0)
                    for m, which, j in routes[1:]:
                        for half in range(2):
                            route(m, t, 2 * j + half, half, True)

            for f in (route_fills, prep_fills):
                f.prime(pe)
            for e in (x_turned, rows_used, routed_pe, mixed[0], mixed[1], mix_over):
                pe.sem_inc(e.sem, 1)
            pe.sem_inc(v_used, RING)
            pe.wait_ge(keys_in, 16)
            for n in range(4):
                for j in range(4):
                    ins = nc.tensor.transpose(psum[4 + n][:, j * P:(j + 1) * P], raw_keys[:, 4 * n + j, :], ident[:])
                ins.then_inc(keys_turned, 1)
            pe.wait_ge(keys_ready, 2)
            prepare(0)
            for half in range(2):
                route(0, 0, half, half)
            turn(0, first=True)
            with pe.Fori(1, TILES - 1) as t:
                turn(t)
            last_turn()
            mix(TILES * PAIRS - 1, 1)
            pe.sem_inc(mix_over.sem, 1)

        @block.scalar
        def _(act):
            def prepare(tile):
                act.wait_ge(routed_pe.sem, routed_pe.last(tile * PAIRS))
                for h in range(2):
                    bank = prep_fills.bank(f"xT{h}")
                    act.wait_ge(prep_fills.full[bank], prep_fills.at(f"xT{h}", tile))
                    nc.scalar.copy(xT[:, 4 * h:4 * h + 4, :], psum[bank][:].rearrange("p (b t) -> p b t", b=4)).then_inc(prep_fills.free[bank], 1)
                act.drain()
                act.sem_inc(xT_ready.sem, 1)

            def prepare_sample():
                for h in range(2):
                    bank = prep_fills.bank(f"xT{h}")
                    act.wait_ge(prep_fills.full[bank], prep_fills.at(f"xT{h}", TILES))
                    ins = nc.scalar.copy(sample_xT[:, 4 * h:4 * h + 4, :], psum[bank][:].rearrange("p (b t) -> p b t", b=4)[:, :, 0:DEC])
                ins.then_inc(sample_xT_ready, 1)

            def queries(m, half):
                for name, dst, ready in ((f"q{half}", q[:], q_ready), (f"qT{half}", qT[:].rearrange("p a t -> p (a t)"), qT_ready)):
                    bank = route_fills.bank(name)
                    act.wait_ge(route_fills.full[bank], route_fills.at(name, m))
                    nc.scalar.copy(dst, psum[bank][:, 0:2 * P]).then_inc(route_fills.free[bank], 1)
                    act.drain()
                    act.sem_inc(ready.sem, 1)

            def exponentials(m, half):
                act.wait_ge(best_ready.sem, best_ready.this(m, half + 1))
                nc.scalar.activation(best[:], best[:], ACT.Exp, bias=nbest[:], accum_out=esum[:])
                act.drain()
                act.sem_inc(exp_ready.sem, 1)

            def weights(n, half):
                act.wait_ge(dots_ready.sem, dots_ready.this(n, half + 1))
                nc.scalar.activation(dots[:, half, :], dots[:, half, :], ACT.Gelu)
                act.drain()
                act.sem_inc(gelu_ready.sem, 1)
                act.wait_ge(weight_ready.sem, weight_ready.this(n, half + 1))
                act.wait_ge(mixed[half].sem, mixed[half].last(n))
                for s in range(TOPK):
                    nc.scalar.activation(diag[:, half, s, :], ident[:], ACT.Copy, scale=weight[:, half, s:s + 1])
                act.drain()
                act.sem_inc(diag_ready.sem, 1)

            def finish(t):
                act.wait_ge(mix_over.sem, mix_over.this(t))
                act.wait_ge(stored.sem, stored.last(t))
                for c in range(2):
                    nc.scalar.copy(total[:, c * BANK:(c + 1) * BANK], psum[6 + c][:])
                act.drain()
                act.sem_inc(mix_read.sem, 1)
                nc.scalar.activation(squares[:], total[:], ACT.Square, accum_out=ms[:])
                act.drain()
                act.sem_inc(ms_ready.sem, 1)
                act.wait_ge(var_ready.sem, var_ready.this(t))
                nc.scalar.activation(root[:], ms[:], ACT.Sqrt)
                act.drain()
                act.sem_inc(root_ready.sem, 1)

            def pair(n, boundary=None):
                for half in range(2):
                    queries(n + 1, half)
                    weights(n, half)
                    exponentials(n + 1, half)
                    if boundary is not None and half == 0:
                        finish(boundary)

            def turn(t, first=False):
                n = t * PAIRS
                pair(n, boundary=None if first else t - 1)
                with act.Fori(1, PAIRS - 1) as i:
                    pair(n + i)
                prepare(t + 1)
                pair(n + PAIRS - 1)

            def last_turn():
                n = (TILES - 1) * PAIRS
                for i, routes in enumerate(last_routes):
                    m = routes[0][0]
                    queries(m, 0)
                    weights(n + i, 0)
                    exponentials(m, 0)
                    if i == 0:
                        finish(TILES - 2)
                    queries(m, 1)
                    if i == 0:
                        prepare_sample()
                    weights(n + i, 1)
                    if len(routes) == 2:
                        queries(routes[1][0], 0)
                    exponentials(m, 1)
                    if len(routes) == 2:
                        m = routes[1][0]
                        queries(m, 1)
                        exponentials(m, 0)
                        exponentials(m, 1)

            for e in (xT_ready, q_ready, qT_ready, exp_ready, gelu_ready, diag_ready, mix_read, ms_ready, root_ready):
                act.sem_inc(e.sem, 1)
            prepare(0)
            for half in range(2):
                queries(0, half)
                exponentials(0, half)
            turn(0, first=True)
            with act.Fori(1, TILES - 1) as t:
                turn(t)
            last_turn()
            finish(TILES - 1)

        @block.vector
        def _(dve):
            def link(ins):
                dve.drain()

            def top16(values, less, out, at):
                link(nc.vector.max(out[:, 0:8], values))
                nc.vector.max_index(at[:, 0:8], out[:, 0:8], values)
                link(nc.vector.match_replace(less, out[:, 0:8], values, FAR))
                link(nc.vector.max(out[:, 8:16], less))
                link(nc.vector.max_index(at[:, 8:16], out[:, 8:16], less))

            def route(m, half, at):
                name = f"sub{half}"
                bank = route_fills.bank(name)
                dve.wait_ge(route_fills.full[bank], route_fills.at(name, m))
                link(nc.vector.tensor_copy(sub[:], psum[bank][:, 0:2 * P].rearrange("p (a k) -> p a k", a=2)).then_inc(route_fills.free[bank], 1))
                for a in range(2):
                    top16(sub[:, a, :], sub_less[:, a, :], top[:, a, :], top_at[:, a, :])
                nc.vector.tensor_copy(top_atf[:], top_at[:])
                link(nc.vector.tensor_tensor(cand[:].rearrange("p (i j) -> p i j", i=TOPK), top[:, 0, :, None].broadcast_to([P, TOPK, TOPK]),
                                             top[:, 1, None, :].broadcast_to([P, TOPK, TOPK]), ALU.add))
                top16(cand[:], cand_less[:], best, best_at)
                link(nc.vector.tensor_scalar(nbest[:], best[:, 0:1], -1.0, None, ALU.mult))
                dve.sem_inc(best_ready.sem, 1)
                nc.vector.tensor_scalar(halves[:, 0, :], best_at[:], 4, None, ALU.logical_shift_right)
                link(nc.vector.tensor_scalar(halves[:, 1, :], best_at[:], 15, None, ALU.bitwise_and))
                link(nc.vector.tensor_copy(halvesf[:], halves[:]))
                link(nc.vector.tensor_tensor(match[:], halvesf[:].rearrange("p a k -> p (a k)")[:, :, None].broadcast_to([P, 2 * TOPK, TOPK]),
                                             count16[:, None, :].broadcast_to([P, 2 * TOPK, TOPK]), ALU.is_equal))
                for a in range(2):
                    rows_a = slice(a * TOPK, (a + 1) * TOPK)
                    ins = nc.vector.tensor_tensor(match[:, rows_a, :], match[:, rows_a, :], top_atf[:, a, None, :].broadcast_to([P, TOPK, TOPK]), ALU.mult)
                link(ins)
                link(nc.vector.tensor_reduce(picked[:].rearrange("p a k -> p (a k)"), match[:], AX.X, ALU.add))
                link(nc.vector.scalar_tensor_tensor(joined[:], picked[:, 0, :], float(N_KEYS), picked[:, 1, :], ALU.mult, ALU.add))
                nc.vector.tensor_copy(idx[:, bass.ds(at, TOPK)], joined[:])
                dve.wait_ge(exp_ready.sem, exp_ready.this(m, half + 1))
                link(nc.vector.reciprocal(esum[:], esum[:]))
                link(nc.vector.tensor_scalar(gate[:, bass.ds(at, TOPK)], best[:], esum[:], None, ALU.mult))

            def take_u(half, at):
                link(nc.vector.tensor_copy(u_idx[:, half, :], idx[:, bass.ds(at, TOPK)]))
                dve.sem_inc(u_idx_ready.sem, 1)

            def take_v(n, half, at):
                dve.wait_ge(mixed[half].sem, mixed[half].last(n))
                link(nc.vector.tensor_copy(v_idx[:, half, :], idx[:, bass.ds(at, TOPK)]))
                dve.sem_inc(v_idx_ready[half].sem, 1)

            def products(n, half, at):
                for s in range(TOPK):
                    j = half * TOPK + s
                    dve.wait_ge(u_in[j % RING], 16 * (n * USES + (j // RING + 1)))
                    nc.vector.tensor_tensor_reduce(u_ring[:, j % RING, :], u_ring[:, j % RING, :], x_cur[:], 1.0, 0.0, ALU.mult, ALU.add,
                                                   dots[:, half, s:s + 1]).then_inc(u_used, 1)
                dve.drain()
                dve.sem_inc(dots_ready.sem, 1)
                dve.wait_ge(gelu_ready.sem, gelu_ready.this(n, half + 1))
                nc.vector.tensor_tensor(weight[:, half, :], dots[:, half, :], gate[:, bass.ds(at, TOPK)], ALU.mult)
                dve.drain()
                dve.sem_inc(weight_ready.sem, 1)

            def finish(t):
                dve.wait_ge(ms_ready.sem, ms_ready.this(t))
                link(nc.vector.tensor_scalar(ms[:], ms[:], 1.0 / D, EPS, ALU.mult, ALU.add))
                dve.sem_inc(var_ready.sem, 1)
                dve.wait_ge(root_ready.sem, root_ready.this(t))
                link(nc.vector.reciprocal(rstd[:], root[:]))
                link(nc.vector.tensor_tensor(err[:], rstd[:], rstd[:], ALU.mult))
                link(nc.vector.tensor_tensor(err[:], err[:], ms[:], ALU.mult))
                link(nc.vector.tensor_scalar(err[:], err[:], -0.5, 1.5, ALU.mult, ALU.add))
                link(nc.vector.tensor_tensor(rstd[:], rstd[:], err[:], ALU.mult))
                nc.vector.scalar_tensor_tensor(total[:], total[:], rstd[:], final_gain[:], ALU.mult, ALU.mult)
                dve.drain()
                dve.sem_inc(out_ready.sem, 1)

            def pair(n, boundary=None):
                at = n * PER
                take_v(n, 0, at)
                for half in range(2):
                    products(n, half, at + half * TOPK)
                    if half == 1:
                        take_v(n, 1, at + TOPK)
                    route(n + 1, half, at + PER + half * TOPK)
                    take_u(half, at + PER + half * TOPK)
                    if boundary is not None and half == 0:
                        finish(boundary)

            def last_turn():
                n = (TILES - 1) * PAIRS
                begin(TILES - 1)
                for i, routes in enumerate(last_routes):
                    at = (n + i) * PER
                    take_v(n + i, 0, at)
                    for half in range(2):
                        products(n + i, half, at + half * TOPK)
                        if half == 1:
                            take_v(n + i, 1, at + TOPK)
                        m, which, j = routes[0]
                        place = ((n + j) if which == "last" else (n + PAIRS + j)) * PER + half * TOPK
                        route(m, half, place)
                        if which == "last":
                            take_u(half, place)
                        if i == 0 and half == 0:
                            finish(TILES - 2)
                    for m, which, j in routes[1:]:
                        for half in range(2):
                            route(m, half, (n + PAIRS + j) * PER + half * TOPK)

            def begin(t):
                dve.wait_ge(x_in.sem, x_in.this(t))
                nc.vector.tensor_copy(x_cur[:], x_next[:])
                dve.drain()
                dve.sem_inc(x_moved.sem, 1)

            def turn(t, first=False):
                n = t * PAIRS
                begin(t)
                pair(n, boundary=None if first else t - 1)
                with dve.Fori(1, PAIRS) as i:
                    pair(n + i)

            for e in (x_moved, best_ready, u_idx_ready, v_idx_ready[0], v_idx_ready[1], dots_ready, weight_ready, var_ready, out_ready):
                dve.sem_inc(e.sem, 1)
            dve.sem_inc(u_used, RING)
            for n in range(4):
                dve.wait_ge(keys_turned, n + 1)
                ins = nc.vector.tensor_copy(keysT[:, n * BANK:(n + 1) * BANK], psum[4 + n][:])
            dve.drain()
            dve.sem_inc(keys_ready, 2)
            dve.wait_ge(loaded, 32)
            for half in range(2):
                route(0, half, half * TOPK)
                take_u(half, half * TOPK)
            turn(0, first=True)
            with dve.Fori(1, TILES - 1) as t:
                turn(t)
            last_turn()
            finish(TILES - 1)


def expert_mix_sample(nc, io, psum, shared, idx, gate):
    ident = shared["ident"]
    at = TILES * SLOTS
    with Stage(nc) as stage:
        sb, sem = stage.buffer, stage.semaphore
        x = sb("es_x", [P, DEC, D])
        u, v = sb("es_u", [P, DEC, D]), sb("es_v", [P, DEC, D])
        rows, gain = sb("es_rows", [DEC, D]), sb("es_gain", [DEC, D])
        junk = sb("es_junk", [DEC, D])
        idxf, idxT, gateT = sb("es_idxf", [DEC, SLOTS]), sb("es_idxT", [P, DEC], U32), sb("es_gateT", [P, DEC])
        dots, weight = sb("es_dots", [P, DEC]), sb("es_weight", [P, DEC])
        own = sb("es_own", [P, DEC, DEC])
        ms, rstd, half = sb("es_ms", [DEC, 1]), sb("es_rstd", [DEC, 1]), sb("es_half", [DEC, 1])
        loaded, idxf_ready, turned, idxT_ready = (sem("es_" + n) for n in ("loaded", "idxf_ready", "turned", "idxT_ready"))
        u_in = [sem(f"es_u_in{b}") for b in range(DEC)]
        v_in = [sem(f"es_v_in{b}") for b in range(DEC)]
        dots_ready, gelu_ready, own_ready, mixed, sum_ready, ms_ready, rstd_ready, out_ready, stored = (
            sem("es_" + n) for n in ("dots_ready", "gelu_ready", "own_ready", "mixed", "sum_ready", "ms_ready", "rstd_ready", "out_ready", "stored"))
        block = stage.block()

        @block.sync
        def _(sp):
            for b in range(DEC):
                sp.dma_start(x[:, b, :], io["xn"][SEQ + b:SEQ + b + 1, :].broadcast_to([P, D])).then_inc(loaded, 16)
            sp.dma_start(rows[:], io["x2"][SEQ:TOKENS, :]).then_inc(loaded, 16)
            sp.dma_start(gain[:], io["final_norm_w"].broadcast_to([DEC, D])).then_inc(loaded, 16)
            sp.wait_ge(out_ready, 1)
            sp.dma_start(io["y_sample"], rows[:]).then_inc(stored, 16)
            sp.wait_ge(stored, 16)

        @block.gpsimd
        def _(pool):
            nc.gpsimd.memset(half[:], -0.5)
            pool.wait_ge(idxT_ready, 1)
            for b in range(DEC):
                for table, rows_in, arrived in (("peer_u", u, u_in), ("peer_v", v, v_in)):
                    nc.gpsimd.indirect_dma_start(out=rows_in[:, b, :], out_offset=None, in_=io[table],
                                                 in_offset=bass.IndirectOffsetOnAxis(ap=idxT[:, b:b + 1], axis=0)).then_inc(arrived[b], 16)
            pool.wait_ge(ms_ready, 1)
            nc.gpsimd.tensor_scalar(ms[:], ms[:], 1.0 / D, EPS, ALU.mult, ALU.add)
            pool.drain()
            nc.gpsimd.tensor_tensor(rstd[:], ms[:], half[:], ALU.pow).then_inc(rstd_ready, 1)

        @block.tensor
        def _(pe):
            pe.wait_ge(idxf_ready, 1)
            nc.tensor.transpose(psum[0][:, 0:DEC], idxf[:], ident[0:DEC, 0:DEC])
            nc.tensor.transpose(psum[0][:, 32:32 + DEC], gate[0:DEC, at:at + SLOTS], ident[0:DEC, 0:DEC]).then_inc(turned, 1)
            pe.wait_ge(own_ready, 1)
            for b in range(DEC):
                pe.wait_ge(v_in[b], 16)
                for c in range(2):
                    ins = nc.tensor.matmul(psum[1 + c][0:DEC, :], own[:, b, :], v[:, b, c * BANK:(c + 1) * BANK], start=(b == 0), stop=(b == DEC - 1))
            ins.then_inc(mixed, 1)

        @block.scalar
        def _(act):
            act.wait_ge(dots_ready, 1)
            nc.scalar.activation(dots[:], dots[:], ACT.Gelu).then_inc(gelu_ready, 1)
            act.wait_ge(sum_ready, 1)
            nc.scalar.activation(junk[:], rows[:], ACT.Square, accum_out=ms[:]).then_inc(ms_ready, 1)

        @block.vector
        def _(dve):
            nc.vector.memset(own[:], 0.0)
            nc.vector.tensor_copy(idxf[:], idx[0:DEC, at:at + SLOTS]).then_inc(idxf_ready, 1)
            dve.wait_ge(turned, 1)
            nc.vector.tensor_copy(gateT[:], psum[0][:, 32:32 + DEC])
            nc.vector.tensor_copy(idxT[:], psum[0][:, 0:DEC]).then_inc(idxT_ready, 1)
            dve.wait_ge(loaded, 16 * (DEC + 2))
            for b in range(DEC):
                dve.wait_ge(u_in[b], 16)
                nc.vector.tensor_tensor_reduce(u[:, b, :], u[:, b, :], x[:, b, :], 1.0, 0.0, ALU.mult, ALU.add, dots[:, b:b + 1])
            dve.drain()
            dve.sem_inc(dots_ready, 1)
            dve.wait_ge(gelu_ready, 1)
            nc.vector.tensor_tensor(weight[:], dots[:], gateT[:], ALU.mult)
            dve.drain()
            diagonal = bass.AP(own[:].tensor, own[:].offset, [list(own[:].ap[0]), [DEC + 1, DEC]])
            nc.vector.tensor_copy(diagonal, weight[:]).then_inc(own_ready, 1)
            dve.wait_ge(mixed, 1)
            for c in range(2):
                cols = slice(c * BANK, (c + 1) * BANK)
                ins = nc.vector.tensor_tensor(rows[:, cols], psum[1 + c][0:DEC, :], rows[:, cols], ALU.add)
            ins.then_inc(sum_ready, 1)
            dve.wait_ge(rstd_ready, 1)
            nc.vector.scalar_tensor_tensor(rows[:], rows[:], rstd[:], gain[:], ALU.mult, ALU.mult).then_inc(out_ready, 1)


def buckets(distance):
    n = np.arange(distance + 1)
    large = BUCKETS // 2 + (np.log(np.maximum(n, 1).astype(np.float32) / np.float32(BUCKETS // 2)) / np.log(128 / (BUCKETS // 2))
                            * (BUCKETS - BUCKETS // 2)).astype(np.int32)
    return np.where(n < BUCKETS // 2, n, np.minimum(large, BUCKETS - 1))


def constants():
    onehot = np.zeros((BUCKETS + 1, 384), np.float32)
    onehot[BUCKETS] = 1
    onehot[BUCKETS, 127:127 + WINDOW + 1] = 0
    onehot[buckets(WINDOW), 127 + np.arange(WINDOW + 1)] = 1
    s, l = np.arange(P)[:, None], np.arange(P)[None, :]
    tri = (s <= l).astype(np.float32)
    return {
        "ident": np.eye(P, dtype=np.float32),
        "tri": tri,
        "far": ((1 - tri) * np.float32(FAR)).astype(np.float32),
        "onehot": onehot,
        "head_mask": np.kron(np.eye(KV), np.ones((GROUP, 1))).astype(np.float32),
    }


def program(nc, io):
    with ExitStack() as scope:
        def sb(name, shape, dt=F32):
            return scope.enter_context(nc.sbuf_tensor(name, shape, dt))

        psum = [scope.enter_context(nc.psum_tensor(f"psum{b}", [P, BANK], F32)) for b in range(8)]
        shared = {
            "ident": sb("ident", [P, P]), "tri": sb("tri", [P, P]), "far": sb("far", [P, P]), "ones": sb("ones", [P, P]),
            "sinks": sb("sinks", [P, HEADS]), "sink_col": sb("sink_col", [HEADS, 1]),
            "head_mask": sb("head_mask", [HEADS, KV]), "bias_row": sb("bias_row", [HEADS, WINDOW + 1]),
            "gains": sb("gains", [P, 5, DB]), "conv": sb("conv", [P, CONV + 1, CB]),
        }
        for i, name in enumerate(("mix", "att", "ssd", "read", "mem")):
            shared["gain_" + name] = shared["gains"][:, i, :]
        with ExitStack() as ssd:
            w_zx = ssd.enter_context(nc.sbuf_tensor("w_zx", [P, DB, IN_COLS - 1536], F32))
            with ExitStack() as attention:
                w_qkv = attention.enter_context(nc.sbuf_tensor("w_qkv", [P, DB, 1536], F32))
                with ExitStack() as window:
                    shared["bias"] = window.enter_context(nc.sbuf_tensor("bias", [P, HEADS, 2 * P], F32))
                    setup(nc, io, psum, shared)
                    attention_prompt(nc, io, psum, shared, w_qkv, w_zx)
                attention_sample(nc, io, psum, shared, w_qkv)
            ssd_prompt(nc, io, psum, shared, w_zx)
            ssd_sample_inputs(nc, io, psum, shared, w_zx)
        w_out = sb("w_out", [P, 2 * DB, D])
        w_out_in = nc.alloc_semaphore("w_out_in")
        with ExitStack() as memory:
            x1 = memory.enter_context(nc.sbuf_tensor("sample_x1", [DEC, D], F32))
            mkT = memory.enter_context(nc.sbuf_tensor("mkT", [P, DB, N_MEM], F32))
            mv = memory.enter_context(nc.sbuf_tensor("mv", [P, N_MEM // P, D], F32))
            w_mo = memory.enter_context(nc.sbuf_tensor("w_mo", [P, DB, D], F32))
            memory_kv_and_sample_step(nc, io, psum, shared, mkT, mv, w_out, w_mo, w_out_in)
            w_mq = memory.enter_context(nc.sbuf_tensor("w_mq", [P, DB, D], F32))
            memory_read(nc, io, psum, shared, w_out, w_mq, w_mo, mkT, mv, w_out_in)
            memory_read_sample(nc, io, psum, shared, w_out, w_mq, w_mo, mkT, mv, x1)
        with ExitStack() as experts:
            n = (TILES + 1) * SLOTS
            w_pq = w_out[:].rearrange("p (b k) n -> p b (k n)", k=2)
            idx = experts.enter_context(nc.sbuf_tensor("expert_idx", [P, n + 2 * TOPK], U32))
            gate = experts.enter_context(nc.sbuf_tensor("expert_gate", [P, n + 2 * TOPK], F32))
            expert_mix(nc, io, psum, shared, w_pq, idx, gate)
            expert_mix_sample(nc, io, psum, shared, idx, gate)


_VIEWS = {
    "x_prompt": (SEQ, D), "x_sample": (DEC, D), "mem_prompt": (N_MEM, D),
    "cache_swa_k": (DEC, WINDOW, KV * HD), "cache_swa_v": (DEC, WINDOW, KV * HD),
    "state_ssm": (DEC * SSD_HEADS, HD, STATE), "state_conv": (DEC, CONV - 1, CONV_DIM),
    "cache_mem_k": (DEC, N_MEM, D), "cache_mem_v": (DEC, N_MEM, D),
    "norm_mix_w": (1, D), "w_in": (D, IN_COLS), "attn_sinks": (1, HEADS), "rel_bias": (BUCKETS, HEADS),
    "attn_norm_w": (1, D), "conv_w": (CONV, CONV_DIM), "conv_b": (1, CONV_DIM), "dt_bias": (1, SSD_HEADS),
    "a_log": (1, SSD_HEADS), "d_skip": (1, SSD_HEADS), "ssd_norm_w": (1, D), "w_out": (2 * D, D),
    "norm_mem_w": (1, D), "mem_norm_w": (1, D), "w_mq": (D, D), "w_mk": (D, D), "w_mv": (D, D), "w_mo": (D, D),
    "norm_ffn_w": (1, D), "peer_wq": (D, 2 * D), "peer_keys": (2 * PEER_HEADS, N_KEYS, P),
    "peer_u": (N_KEYS * N_KEYS, D), "peer_v": (N_KEYS * N_KEYS, D), "final_norm_w": (1, D),
}
_OUTS = {
    "y_prompt": ((SEQ, D), (1, SEQ, D)), "y_sample": ((DEC, D), (DEC, 1, D)),
    "p_swa_k": ((WINDOW, KV * HD), (1, 1, WINDOW, KV, HD)), "p_swa_v": ((WINDOW, KV * HD), (1, 1, WINDOW, KV, HD)),
    "p_ssm": ((SSD_HEADS * HD, STATE), (1, 1, SSD_HEADS, HD, STATE)), "p_conv": ((CONV - 1, CONV_DIM), (1, 1, CONV - 1, CONV_DIM)),
    "p_mem_k": ((N_MEM, D), (1, 1, N_MEM, MEM_HEADS, MEM_HD)), "p_mem_v": ((N_MEM, D), (1, 1, N_MEM, MEM_HEADS, MEM_HD)),
    "s_swa_k": ((DEC, WINDOW, KV * HD), (1, DEC, WINDOW, KV, HD)), "s_swa_v": ((DEC, WINDOW, KV * HD), (1, DEC, WINDOW, KV, HD)),
    "s_ssm": ((DEC * SSD_HEADS, HD, STATE), (1, DEC, SSD_HEADS, HD, STATE)),
    "s_conv": ((DEC, CONV - 1, CONV_DIM), (1, DEC, CONV - 1, CONV_DIM)),
}
_SCRATCH = {
    "mixed": (TOKENS, 2 * D), "bias_line": (HEADS, 384), "rows": (DEC, D), "rows2": (DEC, D), "rows3": (DEC, D), "gates": (DEC, D),
    "dts": (DEC, SSD_HEADS), "bcs": (DEC, 512), "x2": (SEQ + P, D), "xn": (SEQ + P, D),
}


def kernel(**inputs):
    import concourse.bacc as _bacc
    from concourse.bass_utils import run_bass_kernel_spmd as _run

    nc = _bacc.Bacc("TRN2", target_bir_lowering=False, num_devices=1)
    arrays, io = {}, {}
    laid = {name: np.ascontiguousarray(inputs[name]).reshape(shape) for name, shape in _VIEWS.items()}
    laid.update(constants())
    for name, a in laid.items():
        arrays[f"in_{name}"] = a
        io[name] = nc.dram_tensor(f"in_{name}", a.shape, mybir.dt.from_np(a.dtype), kind="ExternalInput").ap()
    for name, (shape, _) in _OUTS.items():
        io[name] = nc.dram_tensor(f"out_{name}", shape, F32, kind="ExternalOutput").ap()
    for name, shape in _SCRATCH.items():
        io[name] = nc.dram_tensor(f"scratch_{name}", shape, F32, kind="Internal").ap()
    program(nc, io)
    r = _run(nc, [arrays], core_ids=[0])
    return tuple(r.results[0][f"out_{name}"].reshape(shape) for name, (_, shape) in _OUTS.items())
```
